# Optimizing a Trainium2 kernel written in Bass

```python
import math
import jax, jax.numpy as jnp
from jax import lax
import numpy as np

D_MODEL = 1024
BATCH = 1
SEQ = 256
DEPTH = 2

GRID_W = 64
CTX_LEN = 256
EPS = 1e-6
ROPE_THETA = 10000.0
F32 = jnp.float32

A_HEADS = 4
A_QK_DIM = 64
A_V_DIM = 2 * A_QK_DIM
A_WIDTH = A_HEADS * A_V_DIM
A_PROJ = 2 * (A_HEADS * 2 * A_QK_DIM) + A_WIDTH
Q_BLOCK = 128

B_HEADS = 8
B_HEAD = 64
B_WIDTH = B_HEADS * B_HEAD
B_DECAY_LORA = 64
B_AAA_LORA = 64
B_GATE_LORA = 128
B_GN_EPS = 64e-5
B_PROJ = 3 * B_WIDTH + B_DECAY_LORA + B_AAA_LORA + B_GATE_LORA

C_HEADS = 8
C_HEAD = 64
C_WIDTH = C_HEADS * C_HEAD
C_GROUPS = 2
C_REP = C_HEADS // C_GROUPS
C_STATE = 128
C_CONV = 5
C_CHUNK = 128
C_CONV_DIM = C_WIDTH + 2 * C_GROUPS * C_STATE
C_PROJ = C_WIDTH + C_CONV_DIM + 2 * C_HEADS

D_HEADS = 4
D_KEY = 64
D_VAL = 128
D_WIDTH = D_HEADS * D_VAL
D_GATE_LORA = 16
D_GATE_TAU = 16.0
D_CHUNK = 64
D_PROJ = 2 * D_HEADS * D_KEY + 2 * D_WIDTH + D_GATE_LORA

MLP_HIDDEN = 4 * D_MODEL
EVEN_IN = A_PROJ + B_PROJ
ODD_IN = C_PROJ + D_PROJ
MIX_WIDTH = A_WIDTH + B_WIDTH


def rmsnorm(x, g, eps=EPS):
    xf = x.astype(F32)
    y = xf * lax.rsqrt(jnp.mean(xf * xf, axis=-1, keepdims=True) + eps)
    return (y * g.astype(F32)).astype(x.dtype)

def _split(t, sizes):
    idx = [int(s) for s in np.cumsum(sizes)[:-1]]
    return jnp.split(t, idx, axis=-1)

def _flip_seq(*ts):
    return tuple(jnp.flip(t, axis=1) for t in ts)

def axial_rope_tables(n, dim):
    rows = n // GRID_W
    t = jnp.arange(rows * GRID_W)
    row = (t // GRID_W).astype(F32)
    col = (t % GRID_W).astype(F32)
    nf = dim // 4
    inv = ROPE_THETA ** (-jnp.arange(nf, dtype=F32) / nf)
    ar = row[:, None] * inv[None, :]
    ac = col[:, None] * inv[None, :]
    return jnp.cos(ar), jnp.sin(ar), jnp.cos(ac), jnp.sin(ac)

def _rot_half(x, cos, sin):
    x1, x2 = jnp.split(x, 2, axis=-1)
    return jnp.concatenate([x1 * cos - x2 * sin, x2 * cos + x1 * sin], axis=-1)

def apply_axial_rope(x, tabs):
    cr, sr, cc, sc = tabs
    xr, xc = jnp.split(x.astype(F32), 2, axis=-1)
    return jnp.concatenate([_rot_half(xr, cr, sr), _rot_half(xc, cc, sc)], axis=-1)

def _diff_softmax_mix(q, k, v, lam):
    s = jnp.einsum('bhmqd,bhmkd->bhmqk', q.astype(F32), k.astype(F32)) * (A_QK_DIM ** -0.5)
    p = jax.nn.softmax(s, axis=-1)
    w = p[:, :, 0] - lam * p[:, :, 1]
    return jnp.einsum('bhqk,bhkd->bhqd', w, v.astype(F32))

def diff_attention(t_lat, t_ctx, lam_q1, lam_k1, lam_q2, lam_k2, subln, layer_idx, need_ctx):
    bsz, n = t_lat.shape[0], t_lat.shape[1]
    lam_init = 0.8 - 0.6 * math.exp(-0.3 * layer_idx)
    lam = (jnp.exp(jnp.sum(lam_q1.astype(F32) * lam_k1.astype(F32)))
           - jnp.exp(jnp.sum(lam_q2.astype(F32) * lam_k2.astype(F32))) + lam_init)

    def heads(t):
        m = t.shape[1]
        q, k, v = _split(t, [A_HEADS * 2 * A_QK_DIM, A_HEADS * 2 * A_QK_DIM, A_WIDTH])
        q = q.reshape(bsz, m, A_HEADS, 2, A_QK_DIM).transpose(0, 2, 3, 1, 4)
        k = k.reshape(bsz, m, A_HEADS, 2, A_QK_DIM).transpose(0, 2, 3, 1, 4)
        v = v.reshape(bsz, m, A_HEADS, A_V_DIM).transpose(0, 2, 1, 3)
        return q, k, v

    q_l, k_l, v_l = heads(t_lat)
    q_c, k_c, v_c = heads(t_ctx)
    tabs = axial_rope_tables(n, A_QK_DIM)
    q_l = apply_axial_rope(q_l, tabs)
    k_l = apply_axial_rope(k_l, tabs)
    k_all = jnp.concatenate([k_c.astype(F32), k_l], axis=3)
    v_all = jnp.concatenate([v_c, v_l], axis=2)
    nb = n // Q_BLOCK
    qb = jnp.moveaxis(q_l.reshape(bsz, A_HEADS, 2, nb, Q_BLOCK, A_QK_DIM), 3, 0)
    ob = lax.map(lambda qq: _diff_softmax_mix(qq, k_all, v_all, lam), qb)
    o_l = jnp.moveaxis(ob, 0, 2).reshape(bsz, A_HEADS, n, A_V_DIM)

    def post(o):
        o = rmsnorm(o, subln, eps=1e-5) * (1.0 - lam_init)
        return o.transpose(0, 2, 1, 3).reshape(bsz, o.shape[2], A_WIDTH)

    out_l = post(o_l)
    out_c = post(_diff_softmax_mix(q_c, k_c, v_c, lam)) if need_ctx else None
    return out_l, out_c

def _token_shift_mix(f, mu):
    prev = jnp.pad(f[:, :-1], ((0, 0), (1, 0), (0, 0)))
    nxt = jnp.pad(f[:, 1:], ((0, 0), (0, 1), (0, 0)))
    return f + (0.5 * (prev + nxt) - f) * mu

def _rwkv7_scan(S0, r, w, k, v, kk, a):
    def step(S, inp):
        r_t, w_t, k_t, v_t, kk_t, a_t = inp
        sa = jnp.einsum('bhvk,bhk->bhv', S, kk_t)
        S = (S * w_t[:, :, None, :] - sa[..., None] * (kk_t * a_t)[:, :, None, :]
             + v_t[..., None] * k_t[:, :, None, :])
        return S, jnp.einsum('bhvk,bhk->bhv', S, r_t)
    xs = tuple(jnp.swapaxes(t, 0, 1) for t in (r, w, k, v, kk, a))
    S, ys = lax.scan(step, S0, xs)
    return jnp.swapaxes(ys, 0, 1), S

def rwkv7_mix(t_lat, t_ctx, mu, w0_f, w2_f, w0_b, w2_b, a0, a2, g2, k_k, k_a, r_k, lnx_w, lnx_b, need_ctx):
    def prep(t):
        bsz, n = t.shape[0], t.shape[1]
        f = _token_shift_mix(t, mu).astype(F32)
        r, k, v, wd, ad, gd = _split(f, [B_WIDTH, B_WIDTH, B_WIDTH, B_DECAY_LORA, B_AAA_LORA, B_GATE_LORA])
        hd = lambda u: u.reshape(bsz, n, B_HEADS, B_HEAD)
        a = jax.nn.sigmoid(a0 + ad @ a2)
        tw = jnp.tanh(wd)
        def decay(w0, w2):
            wl = -jax.nn.softplus(-(w0 + tw @ w2)) - 0.5
            return hd(jnp.exp(-jnp.exp(wl)))
        kk = hd(k * k_k)
        kk = kk / jnp.maximum(jnp.sqrt(jnp.sum(kk * kk, axis=-1, keepdims=True)), 1e-12)
        k = k * (1.0 + (a - 1.0) * k_a)
        g = jax.nn.sigmoid(gd) @ g2
        return (hd(r), hd(k), hd(v), kk, hd(a), decay(w0_f, w2_f), decay(w0_b, w2_b), g)

    r_c, k_c, v_c, kk_c, a_c, wf_c, wb_c, g_c = prep(t_ctx)
    r_l, k_l, v_l, kk_l, a_l, wf_l, wb_l, g_l = prep(t_lat)
    S0 = jnp.zeros((t_lat.shape[0], B_HEADS, B_HEAD, B_HEAD), F32)
    yf_c, Sf_c = _rwkv7_scan(S0, r_c, wf_c, k_c, v_c, kk_c, a_c)
    yb_c, Sb_c = _rwkv7_scan(S0, *_flip_seq(r_c, wb_c, k_c, v_c, kk_c, a_c))
    yf_l, _ = _rwkv7_scan(Sf_c, r_l, wf_l, k_l, v_l, kk_l, a_l)
    yb_l, _ = _rwkv7_scan(Sb_c, *_flip_seq(r_l, wb_l, k_l, v_l, kk_l, a_l))

    def post(r, k, v, g, yf, yb):
        bsz, n = r.shape[0], r.shape[1]
        y = yf + jnp.flip(yb, axis=1)
        mean = jnp.mean(y, axis=-1, keepdims=True)
        var = jnp.mean(jnp.square(y - mean), axis=-1, keepdims=True)
        y = ((y - mean) * lax.rsqrt(var + B_GN_EPS)).reshape(bsz, n, B_WIDTH) * lnx_w + lnx_b
        bonus = jnp.sum(r * k * r_k.reshape(B_HEADS, B_HEAD), axis=-1, keepdims=True) * v
        return (y + bonus.reshape(bsz, n, B_WIDTH)) * g

    out_l = post(r_l, k_l, v_l, g_l, yf_l, yb_l)
    out_c = post(r_c, k_c, v_c, g_c, yf_c, yb_c) if need_ctx else None
    return out_l, out_c

def _dwconv_centred(t, w, b):
    y = lax.conv_general_dilated(t, w[:, None, :].astype(t.dtype), window_strides=(1,),
                                 padding=[(C_CONV // 2, C_CONV // 2)],
                                 dimension_numbers=('NWC', 'WIO', 'NWC'),
                                 feature_group_count=t.shape[-1])
    return y + b

def _ssd_chunk_scan(h0, x, dt, la, bm, cm):
    bsz, n = x.shape[0], x.shape[1]
    nc = n // C_CHUNK
    chunks = lambda t: jnp.swapaxes(t.reshape((bsz, nc, C_CHUNK) + t.shape[2:]), 0, 1)
    idx = jnp.arange(C_CHUNK)
    lower = (idx[:, None] >= idx[None, :])[None, :, :, None, None]

    def step(h, inp):
        xc, dtc, lac, bc, cc = inp
        cum = jnp.cumsum(lac, axis=1)
        lmat = jnp.exp(jnp.where(lower, cum[:, :, None] - cum[:, None, :], -jnp.inf))
        cb = jnp.einsum('bign,bjgn->bijg', cc, bc)
        xdt = xc * dtc[..., None]
        y = jnp.einsum('bijgr,bjgrp->bigrp', cb[..., None] * lmat, xdt)
        y = y + jnp.einsum('bign,bgrpn->bigrp', cc, h) * jnp.exp(cum)[..., None]
        w_end = jnp.exp(cum[:, -1:] - cum)
        h = h * jnp.exp(cum[:, -1])[..., None, None] + jnp.einsum('bjgn,bjgrp->bgrpn', bc, xdt * w_end[..., None])
        return h, y

    h, ys = lax.scan(step, h0, tuple(chunks(t) for t in (x, dt, la, bm, cm)))
    return jnp.swapaxes(ys, 0, 1).reshape(x.shape), h

def ssd_mix(t_lat, t_ctx, conv_w, conv_b, dt_bias_f, a_log_f, dt_bias_b, a_log_b, d_skip, norm_g, need_ctx):
    def prep(t):
        bsz, n = t.shape[0], t.shape[1]
        z, xbc, dt_f, dt_b = _split(t, [C_WIDTH, C_CONV_DIM, C_HEADS, C_HEADS])
        xbc = jax.nn.silu(_dwconv_centred(xbc, conv_w, conv_b).astype(F32))
        xs, bm, cm = _split(xbc, [C_WIDTH, C_GROUPS * C_STATE, C_GROUPS * C_STATE])
        xs = xs.reshape(bsz, n, C_GROUPS, C_REP, C_HEAD)
        bm = bm.reshape(bsz, n, C_GROUPS, C_STATE)
        cm = cm.reshape(bsz, n, C_GROUPS, C_STATE)
        def direction(dt_raw, dt_bias, a_log):
            dt = jax.nn.softplus(dt_raw.astype(F32) + dt_bias).reshape(bsz, n, C_GROUPS, C_REP)
            return dt, dt * (-jnp.exp(a_log.astype(F32))).reshape(C_GROUPS, C_REP)
        return z, xs, bm, cm, direction(dt_f, dt_bias_f, a_log_f), direction(dt_b, dt_bias_b, a_log_b)

    z_c, x_c, b_c, c_c, (dtf_c, laf_c), (dtb_c, lab_c) = prep(t_ctx)
    z_l, x_l, b_l, c_l, (dtf_l, laf_l), (dtb_l, lab_l) = prep(t_lat)
    h0 = jnp.zeros((t_lat.shape[0], C_GROUPS, C_REP, C_HEAD, C_STATE), F32)
    yf_c, hf_c = _ssd_chunk_scan(h0, x_c, dtf_c, laf_c, b_c, c_c)
    yb_c, hb_c = _ssd_chunk_scan(h0, *_flip_seq(x_c, dtb_c, lab_c, b_c, c_c))
    yf_l, _ = _ssd_chunk_scan(hf_c, x_l, dtf_l, laf_l, b_l, c_l)
    yb_l, _ = _ssd_chunk_scan(hb_c, *_flip_seq(x_l, dtb_l, lab_l, b_l, c_l))

    def post(z, xs, yf, yb):
        bsz, n = xs.shape[0], xs.shape[1]
        y = yf + jnp.flip(yb, axis=1) + xs * d_skip.astype(F32).reshape(C_GROUPS, C_REP, 1)
        y = y.reshape(bsz, n, C_WIDTH) * jax.nn.silu(z.astype(F32))
        y = rmsnorm(y.reshape(bsz, n, C_GROUPS, C_WIDTH // C_GROUPS), norm_g.reshape(C_GROUPS, C_WIDTH // C_GROUPS))
        return y.reshape(bsz, n, C_WIDTH)

    out_l = post(z_l, x_l, yf_l, yb_l)
    out_c = post(z_c, x_c, yf_c, yb_c) if need_ctx else None
    return out_l, out_c

def _gla_chunk_scan(S0, q, k, v, lg):
    bsz, n = q.shape[0], q.shape[1]
    nc = n // D_CHUNK
    chunks = lambda t: jnp.swapaxes(t.reshape((bsz, nc, D_CHUNK) + t.shape[2:]), 0, 1)
    idx = jnp.arange(D_CHUNK)
    lower = (idx[:, None] >= idx[None, :])[None, :, :, None, None]

    def step(S, inp):
        qc, kc, vc, gc = inp
        cum = jnp.cumsum(gc, axis=1)
        dec = jnp.exp(jnp.where(lower, cum[:, :, None] - cum[:, None, :], -jnp.inf))
        att = jnp.einsum('bihk,bjhk,bijhk->bhij', qc, kc, dec)
        y = jnp.einsum('bhij,bjhv->bihv', att, vc) + jnp.einsum('bihk,bhkv->bihv', qc * jnp.exp(cum), S)
        S = S * jnp.exp(cum[:, -1])[..., None] + jnp.einsum('bjhk,bjhv->bhkv', kc * jnp.exp(cum[:, -1:] - cum), vc)
        return S, y

    S, ys = lax.scan(step, S0, tuple(chunks(t) for t in (q, k, v, lg)))
    return jnp.swapaxes(ys, 0, 1).reshape(v.shape), S

def gla_mix(t_lat, t_ctx, gk_up_f, gk_b_f, gk_up_b, gk_b_b, norm_g, need_ctx):
    def prep(t):
        bsz, n = t.shape[0], t.shape[1]
        q, k, v, g, gd = _split(t.astype(F32), [D_HEADS * D_KEY, D_HEADS * D_KEY, D_WIDTH, D_WIDTH, D_GATE_LORA])
        hk = lambda u: u.reshape(bsz, n, D_HEADS, D_KEY)
        def log_gate(up, b):
            return hk(jax.nn.log_sigmoid(gd @ up + b) / D_GATE_TAU)
        return (hk(q) * (D_KEY ** -0.5), hk(k), v.reshape(bsz, n, D_HEADS, D_VAL), g,
                log_gate(gk_up_f, gk_b_f), log_gate(gk_up_b, gk_b_b))

    q_c, k_c, v_c, g_c, gf_c, gb_c = prep(t_ctx)
    q_l, k_l, v_l, g_l, gf_l, gb_l = prep(t_lat)
    S0 = jnp.zeros((t_lat.shape[0], D_HEADS, D_KEY, D_VAL), F32)
    yf_c, Sf_c = _gla_chunk_scan(S0, q_c, k_c, v_c, gf_c)
    yb_c, Sb_c = _gla_chunk_scan(S0, *_flip_seq(q_c, k_c, v_c, gb_c))
    yf_l, _ = _gla_chunk_scan(Sf_c, q_l, k_l, v_l, gf_l)
    yb_l, _ = _gla_chunk_scan(Sb_c, *_flip_seq(q_l, k_l, v_l, gb_l))

    def post(g, yf, yb):
        bsz, n = g.shape[0], g.shape[1]
        y = rmsnorm(yf + jnp.flip(yb, axis=1), norm_g)
        return y.reshape(bsz, n, D_WIDTH) * jax.nn.silu(g)

    out_l = post(g_l, yf_l, yb_l)
    out_c = post(g_c, yf_c, yb_c) if need_ctx else None
    return out_l, out_c

def even_mixer(p_lat, p_ctx, lam_q1, lam_k1, lam_q2, lam_k2, subln, mu, w0_f, w2_f, w0_b, w2_b,
               a0, a2, g2, k_k, k_a, r_k, lnx_w, lnx_b, layer_idx, need_ctx):
    oa_l, oa_c = diff_attention(p_lat[..., :A_PROJ], p_ctx[..., :A_PROJ],
                                lam_q1, lam_k1, lam_q2, lam_k2, subln, layer_idx, need_ctx)
    ob_l, ob_c = rwkv7_mix(p_lat[..., A_PROJ:], p_ctx[..., A_PROJ:], mu, w0_f, w2_f, w0_b, w2_b,
                           a0, a2, g2, k_k, k_a, r_k, lnx_w, lnx_b, need_ctx)
    o_l = jnp.concatenate([oa_l, ob_l], axis=-1)
    o_c = jnp.concatenate([oa_c, ob_c], axis=-1) if need_ctx else None
    return o_l, o_c

def odd_mixer(p_lat, p_ctx, conv_w, conv_b, dt_bias_f, a_log_f, dt_bias_b, a_log_b, d_skip, ssm_norm,
              gk_up_f, gk_b_f, gk_up_b, gk_b_b, gla_norm, need_ctx):
    oc_l, oc_c = ssd_mix(p_lat[..., :C_PROJ], p_ctx[..., :C_PROJ], conv_w, conv_b, dt_bias_f, a_log_f,
                         dt_bias_b, a_log_b, d_skip, ssm_norm, need_ctx)
    od_l, od_c = gla_mix(p_lat[..., C_PROJ:], p_ctx[..., C_PROJ:], gk_up_f, gk_b_f, gk_up_b, gk_b_b,
                         gla_norm, need_ctx)
    o_l = jnp.concatenate([oc_l, od_l], axis=-1)
    o_c = jnp.concatenate([oc_c, od_c], axis=-1) if need_ctx else None
    return o_l, o_c

def _ada(x, g, shift, scale):
    return rmsnorm(x, g) * (1.0 + scale) + shift

def _sq_relu_mlp(h, w1, w2):
    return jnp.square(jax.nn.relu(h @ w1)) @ w2

def first_inputs(seed: int = 0) -> dict:
    key = jax.random.key(seed)
    keys = iter(jax.random.split(key, 64))
    D = D_MODEL
    def nrm(shape, scale):
        return jax.random.normal(next(keys), shape, F32) * scale
    def gain(n):
        return 1.0 + 0.05 * jax.random.normal(next(keys), (n,), F32)
    def unif(shape, lo, hi):
        return jax.random.uniform(next(keys), shape, F32, lo, hi)
    def dt_bias(n):
        dt = jnp.exp(unif((n,), math.log(1e-3), math.log(1e-1)))
        return dt + jnp.log(-jnp.expm1(-dt))
    inp = {}
    inp['x'] = nrm((BATCH, SEQ, D), 1.0)
    inp['c'] = nrm((BATCH, D), 1.0)
    inp['ctx'] = nrm((BATCH, CTX_LEN, D), 1.0)
    inp['c_ctx'] = nrm((D,), 1.0)
    inp['l0_mod_w'] = nrm((D, 6 * D), 0.5 * D ** -0.5)
    inp['l0_mod_b'] = nrm((6 * D,), 0.02)
    inp['l0_norm1'] = gain(D)
    inp['l0_norm2'] = gain(D)
    inp['l0_w_in'] = nrm((D, EVEN_IN), D ** -0.5)
    inp['l0_w_out'] = nrm((MIX_WIDTH, D), MIX_WIDTH ** -0.5)
    inp['l0_mlp_w1'] = nrm((D, MLP_HIDDEN), D ** -0.5)
    inp['l0_mlp_w2'] = nrm((MLP_HIDDEN, D), MLP_HIDDEN ** -0.5)
    inp['l0_lam_q1'] = nrm((A_QK_DIM,), 0.1)
    inp['l0_lam_k1'] = nrm((A_QK_DIM,), 0.1)
    inp['l0_lam_q2'] = nrm((A_QK_DIM,), 0.1)
    inp['l0_lam_k2'] = nrm((A_QK_DIM,), 0.1)
    inp['l0_subln'] = gain(A_V_DIM)
    inp['l0_mu'] = unif((B_PROJ,), 0.0, 1.0)
    inp['l0_w0_f'] = unif((B_WIDTH,), -6.0, -1.0)
    inp['l0_w2_f'] = nrm((B_DECAY_LORA, B_WIDTH), 0.1 * B_DECAY_LORA ** -0.5)
    inp['l0_w0_b'] = unif((B_WIDTH,), -6.0, -1.0)
    inp['l0_w2_b'] = nrm((B_DECAY_LORA, B_WIDTH), 0.1 * B_DECAY_LORA ** -0.5)
    inp['l0_a0'] = nrm((B_WIDTH,), 0.1)
    inp['l0_a2'] = nrm((B_AAA_LORA, B_WIDTH), B_AAA_LORA ** -0.5)
    inp['l0_g2'] = nrm((B_GATE_LORA, B_WIDTH), B_GATE_LORA ** -0.5)
    inp['l0_k_k'] = 0.85 + nrm((B_WIDTH,), 0.05)
    inp['l0_k_a'] = gain(B_WIDTH)
    inp['l0_r_k'] = nrm((B_WIDTH,), 0.1)
    inp['l0_lnx_w'] = gain(B_WIDTH)
    inp['l0_lnx_b'] = nrm((B_WIDTH,), 0.02)
    inp['l1_mod_w'] = nrm((D, 6 * D), 0.5 * D ** -0.5)
    inp['l1_mod_b'] = nrm((6 * D,), 0.02)
    inp['l1_norm1'] = gain(D)
    inp['l1_norm2'] = gain(D)
    inp['l1_w_in'] = nrm((D, ODD_IN), D ** -0.5)
    inp['l1_w_out'] = nrm((MIX_WIDTH, D), MIX_WIDTH ** -0.5)
    inp['l1_mlp_w1'] = nrm((D, MLP_HIDDEN), D ** -0.5)
    inp['l1_mlp_w2'] = nrm((MLP_HIDDEN, D), MLP_HIDDEN ** -0.5)
    inp['l1_conv_w'] = nrm((C_CONV, C_CONV_DIM), C_CONV ** -0.5)
    inp['l1_conv_b'] = nrm((C_CONV_DIM,), 0.02)
    inp['l1_dt_bias_f'] = dt_bias(C_HEADS)
    inp['l1_a_log_f'] = jnp.log(unif((C_HEADS,), 1.0, 16.0))
    inp['l1_dt_bias_b'] = dt_bias(C_HEADS)
    inp['l1_a_log_b'] = jnp.log(unif((C_HEADS,), 1.0, 16.0))
    inp['l1_d_skip'] = gain(C_HEADS)
    inp['l1_ssm_norm'] = gain(C_WIDTH)
    inp['l1_gk_up_f'] = nrm((D_GATE_LORA, D_HEADS * D_KEY), D_GATE_LORA ** -0.5)
    inp['l1_gk_b_f'] = nrm((D_HEADS * D_KEY,), 0.1)
    inp['l1_gk_up_b'] = nrm((D_GATE_LORA, D_HEADS * D_KEY), D_GATE_LORA ** -0.5)
    inp['l1_gk_b_b'] = nrm((D_HEADS * D_KEY,), 0.1)
    inp['l1_gla_norm'] = gain(D_VAL)
    inp['final_norm'] = gain(D)
    return inp

def first_block(x, c, ctx, c_ctx,
              l0_mod_w, l0_mod_b, l0_norm1, l0_norm2, l0_w_in, l0_w_out, l0_mlp_w1, l0_mlp_w2,
              l0_lam_q1, l0_lam_k1, l0_lam_q2, l0_lam_k2, l0_subln,
              l0_mu, l0_w0_f, l0_w2_f, l0_w0_b, l0_w2_b, l0_a0, l0_a2, l0_g2, l0_k_k, l0_k_a, l0_r_k,
              l0_lnx_w, l0_lnx_b,
              l1_mod_w, l1_mod_b, l1_norm1, l1_norm2, l1_w_in, l1_w_out, l1_mlp_w1, l1_mlp_w2,
              l1_conv_w, l1_conv_b, l1_dt_bias_f, l1_a_log_f, l1_dt_bias_b, l1_a_log_b, l1_d_skip, l1_ssm_norm,
              l1_gk_up_f, l1_gk_b_f, l1_gk_up_b, l1_gk_b_b, l1_gla_norm,
              final_norm):
    shared = [
        (l0_mod_w, l0_mod_b, l0_norm1, l0_norm2, l0_w_in, l0_w_out, l0_mlp_w1, l0_mlp_w2),
        (l1_mod_w, l1_mod_b, l1_norm1, l1_norm2, l1_w_in, l1_w_out, l1_mlp_w1, l1_mlp_w2),
    ]
    for i in range(DEPTH):
        mod_w, mod_b, norm1, norm2, w_in, w_out, mlp_w1, mlp_w2 = shared[i]
        need_ctx = i < DEPTH - 1
        m_l = (jax.nn.silu(c) @ mod_w + mod_b)[:, None, :]
        m_c = jax.nn.silu(c_ctx) @ mod_w + mod_b
        sh1_l, sc1_l, g1_l, sh2_l, sc2_l, g2_l = jnp.split(m_l, 6, axis=-1)
        sh1_c, sc1_c, g1_c, sh2_c, sc2_c, g2_c = jnp.split(m_c, 6, axis=-1)
        p_lat = _ada(x, norm1, sh1_l, sc1_l) @ w_in
        p_ctx = _ada(ctx, norm1, sh1_c, sc1_c) @ w_in
        if i % 2 == 0:
            o_l, o_c = even_mixer(p_lat, p_ctx, l0_lam_q1, l0_lam_k1, l0_lam_q2, l0_lam_k2, l0_subln,
                                  l0_mu, l0_w0_f, l0_w2_f, l0_w0_b, l0_w2_b, l0_a0, l0_a2, l0_g2,
                                  l0_k_k, l0_k_a, l0_r_k, l0_lnx_w, l0_lnx_b, i, need_ctx)
        else:
            o_l, o_c = odd_mixer(p_lat, p_ctx, l1_conv_w, l1_conv_b, l1_dt_bias_f, l1_a_log_f,
                                 l1_dt_bias_b, l1_a_log_b, l1_d_skip, l1_ssm_norm,
                                 l1_gk_up_f, l1_gk_b_f, l1_gk_up_b, l1_gk_b_b, l1_gla_norm, need_ctx)
        x = x + g1_l * (o_l.astype(x.dtype) @ w_out)
        x = x + g2_l * _sq_relu_mlp(_ada(x, norm2, sh2_l, sc2_l), mlp_w1, mlp_w2)
        if need_ctx:
            ctx = ctx + g1_c * (o_c.astype(ctx.dtype) @ w_out)
            ctx = ctx + g2_c * _sq_relu_mlp(_ada(ctx, norm2, sh2_c, sc2_c), mlp_w1, mlp_w2)
    return rmsnorm(x, final_norm)


HEAD_DIM = 64
FOURIER_WIDTH = D_MODEL // 4
FOURIER_CH = HEAD_DIM
N_FOURIER_GROUPS = FOURIER_WIDTH // FOURIER_CH
ATTN_WIDTH = D_MODEL // 2
N_Q_HEADS = ATTN_WIDTH // HEAD_DIM
N_KV_HEADS = 2
KV_WIDTH = N_KV_HEADS * HEAD_DIM
MEM_WIDTH = D_MODEL // 4
N_MEM_HEADS = MEM_WIDTH // HEAD_DIM
N_MEM = 256
MIX_WIDTH_2 = FOURIER_WIDTH + ATTN_WIDTH + MEM_WIDTH
IN_WIDTH = FOURIER_WIDTH + ATTN_WIDTH + 2 * KV_WIDTH + MEM_WIDTH
WINDOW = 128
BLOCK = 128
D_FF = -(-8 * D_MODEL // (3 * 256)) * 256
NEG_INF = -1e30


def _rmsnorm(x, g):
    xf = x.astype(jnp.float32)
    y = xf * lax.rsqrt(jnp.mean(xf * xf, axis=-1, keepdims=True) + EPS)
    return (y * g.astype(jnp.float32)).astype(x.dtype)

def _rope(t, positions):
    half = HEAD_DIM // 2
    inv_freq = jnp.exp(-math.log(ROPE_THETA) * jnp.arange(half, dtype=jnp.float32) * (2.0 / HEAD_DIM))
    ang = positions.astype(jnp.float32)[:, :, None] * inv_freq
    cos = jnp.cos(ang)[:, :, None, :]
    sin = jnp.sin(ang)[:, :, None, :]
    tf = t.astype(jnp.float32)
    t1, t2 = tf[..., :half], tf[..., half:]
    return jnp.concatenate([t1 * cos - t2 * sin, t2 * cos + t1 * sin], axis=-1).astype(t.dtype)

def _fourier_mix(u, w_f):
    b, s, _ = u.shape
    ug = u.reshape(b, s, N_FOURIER_GROUPS, FOURIER_CH).astype(jnp.float32)
    spec = jnp.fft.fftn(ug, axes=(1, 3), norm='ortho').real
    y = jnp.einsum('bsgc,gce->bsge', spec.astype(u.dtype), w_f)
    return y.reshape(b, s, FOURIER_WIDTH)

def _window_attn(q, k, v, sink):
    b, s, _, _ = q.shape
    nb = s // BLOCK
    grp = N_Q_HEADS // N_KV_HEADS

    def bands(t):
        tp = jnp.pad(t, ((0, 0), (BLOCK, BLOCK), (0, 0), (0, 0)))
        tp = tp.reshape(b, nb + 2, BLOCK, N_KV_HEADS, HEAD_DIM)
        return jnp.concatenate([tp[:, :-2], tp[:, 1:-1], tp[:, 2:]], axis=2)

    kb, vb = bands(k), bands(v)
    qb = q.reshape(b, nb, BLOCK, N_KV_HEADS, grp, HEAD_DIM)
    scores = jnp.einsum('bnqhgd,bnjhd->bnhgqj', qb, kb).astype(jnp.float32) * (HEAD_DIM ** -0.5)
    blk = jnp.arange(nb)[:, None, None] * BLOCK
    qpos = blk + jnp.arange(BLOCK)[None, :, None]
    kpos = blk - BLOCK + jnp.arange(3 * BLOCK)[None, None, :]
    valid = (kpos >= 0) & (kpos < s) & (jnp.abs(qpos - kpos) <= WINDOW)
    scores = jnp.where(valid[None, :, None, None], scores, NEG_INF)
    sink_b = jnp.broadcast_to(sink.astype(jnp.float32).reshape(1, 1, N_KV_HEADS, grp, 1, 1),
                              scores.shape[:-1] + (1,))
    probs = jax.nn.softmax(jnp.concatenate([scores, sink_b], axis=-1), axis=-1)[..., :-1]
    out = jnp.einsum('bnhgqj,bnjhd->bnqhgd', probs.astype(v.dtype), vb)
    return out.reshape(b, s, N_Q_HEADS * HEAD_DIM)

def _memory_attn(q, km, vm):
    b, s, _, _ = q.shape
    scores = jnp.einsum('bshd,bmhd->bhsm', q, km).astype(jnp.float32) * (HEAD_DIM ** -0.5)
    probs = jax.nn.softmax(scores, axis=-1)
    out = jnp.einsum('bhsm,bmhd->bshd', probs.astype(vm.dtype), vm)
    return out.reshape(b, s, MEM_WIDTH)

def second_inputs(seed: int = 0) -> dict:
    key = jax.random.key(seed)
    ks = jax.random.split(key, 20)
    f32 = jnp.float32

    def nrm(k, shape, scale):
        return jax.random.normal(k, shape, f32) * scale

    def gain(k, shape):
        return 1.0 + 0.05 * jax.random.normal(k, shape, f32)

    x = jax.random.normal(ks[0], (BATCH, SEQ, D_MODEL), f32)
    mem = jax.random.normal(ks[1], (BATCH, N_MEM, D_MODEL), f32)
    positions = jnp.broadcast_to(jnp.arange(SEQ, dtype=jnp.int32)[None, :], (BATCH, SEQ))
    return {
        'x': x,
        'mem': mem,
        'positions': positions,
        'g_pre_mix': gain(ks[2], (DEPTH, D_MODEL)),
        'w_in': nrm(ks[3], (DEPTH, D_MODEL, IN_WIDTH), D_MODEL ** -0.5),
        'w_fourier': nrm(ks[4], (DEPTH, N_FOURIER_GROUPS, FOURIER_CH, FOURIER_CH), FOURIER_CH ** -0.5),
        'sink': nrm(ks[5], (DEPTH, N_Q_HEADS), 0.5),
        'g_mem': gain(ks[6], (DEPTH, D_MODEL)),
        'w_mem_kv': nrm(ks[7], (DEPTH, D_MODEL, 2 * MEM_WIDTH), D_MODEL ** -0.5),
        'g_grp': gain(ks[8], (DEPTH, MIX_WIDTH_2)),
        'w_out': nrm(ks[9], (DEPTH, MIX_WIDTH_2, D_MODEL), MIX_WIDTH_2 ** -0.5),
        'g_post_mix': gain(ks[10], (DEPTH, D_MODEL)),
        'g_pre_ffn': gain(ks[11], (DEPTH, D_MODEL)),
        'w_ffn_in': nrm(ks[12], (DEPTH, D_MODEL, 2 * D_FF), D_MODEL ** -0.5),
        'w_ffn_out': nrm(ks[13], (DEPTH, D_FF, D_MODEL), D_FF ** -0.5),
        'g_post_ffn': gain(ks[14], (DEPTH, D_MODEL)),
    }

def second_block(x, mem, positions, g_pre_mix, w_in, w_fourier, sink, g_mem, w_mem_kv, g_grp,
              w_out, g_post_mix, g_pre_ffn, w_ffn_in, w_ffn_out, g_post_ffn):
    b, s, _ = x.shape
    m = mem.shape[1]
    splits = [FOURIER_WIDTH,
              FOURIER_WIDTH + ATTN_WIDTH,
              FOURIER_WIDTH + ATTN_WIDTH + KV_WIDTH,
              FOURIER_WIDTH + ATTN_WIDTH + 2 * KV_WIDTH]
    for l in range(DEPTH):
        h = _rmsnorm(x, g_pre_mix[l])
        z = h @ w_in[l]
        zf, zq, zk, zv, zm = jnp.split(z, splits, axis=-1)

        y_f = _fourier_mix(zf, w_fourier[l])

        q = _rope(zq.reshape(b, s, N_Q_HEADS, HEAD_DIM), positions)
        k = _rope(zk.reshape(b, s, N_KV_HEADS, HEAD_DIM), positions)
        v = zv.reshape(b, s, N_KV_HEADS, HEAD_DIM)
        y_a = _window_attn(q, k, v, sink[l])

        mkv = _rmsnorm(mem, g_mem[l]) @ w_mem_kv[l]
        km, vm = jnp.split(mkv, 2, axis=-1)
        km = km.reshape(b, m, N_MEM_HEADS, HEAD_DIM)
        vm = vm.reshape(b, m, N_MEM_HEADS, HEAD_DIM)
        y_m = _memory_attn(zm.reshape(b, s, N_MEM_HEADS, HEAD_DIM), km, vm)

        gg = g_grp[l]
        y = jnp.concatenate([
            _rmsnorm(y_f, gg[:FOURIER_WIDTH]),
            _rmsnorm(y_a, gg[FOURIER_WIDTH:FOURIER_WIDTH + ATTN_WIDTH]),
            _rmsnorm(y_m, gg[FOURIER_WIDTH + ATTN_WIDTH:]),
        ], axis=-1) @ w_out[l]
        x = x + _rmsnorm(y, g_post_mix[l])

        h = _rmsnorm(x, g_pre_ffn[l])
        gate, up = jnp.split(h @ w_ffn_in[l], 2, axis=-1)
        f = (jax.nn.silu(gate) * up) @ w_ffn_out[l]
        x = x + _rmsnorm(f, g_post_ffn[l])
    return x


def setup_inputs(seed=0):
    out = dict(first_inputs(seed))
    for name, value in second_inputs(seed + 1).items():
        if name != "x":
            out[name + "_2"] = value
    return out


def reference(
    x, c, ctx, c_ctx, l0_mod_w, l0_mod_b, l0_norm1, l0_norm2, l0_w_in, l0_w_out, l0_mlp_w1,
    l0_mlp_w2, l0_lam_q1, l0_lam_k1, l0_lam_q2, l0_lam_k2, l0_subln, l0_mu, l0_w0_f, l0_w2_f,
    l0_w0_b, l0_w2_b, l0_a0, l0_a2, l0_g2, l0_k_k, l0_k_a, l0_r_k, l0_lnx_w, l0_lnx_b, l1_mod_w,
    l1_mod_b, l1_norm1, l1_norm2, l1_w_in, l1_w_out, l1_mlp_w1, l1_mlp_w2, l1_conv_w, l1_conv_b,
    l1_dt_bias_f, l1_a_log_f, l1_dt_bias_b, l1_a_log_b, l1_d_skip, l1_ssm_norm, l1_gk_up_f,
    l1_gk_b_f, l1_gk_up_b, l1_gk_b_b, l1_gla_norm, final_norm, mem_2, positions_2, g_pre_mix_2,
    w_in_2, w_fourier_2, sink_2, g_mem_2, w_mem_kv_2, g_grp_2, w_out_2, g_post_mix_2,
    g_pre_ffn_2, w_ffn_in_2, w_ffn_out_2, g_post_ffn_2,
):
    x = first_block(
        x, c, ctx, c_ctx, l0_mod_w, l0_mod_b, l0_norm1, l0_norm2, l0_w_in, l0_w_out, l0_mlp_w1,
        l0_mlp_w2, l0_lam_q1, l0_lam_k1, l0_lam_q2, l0_lam_k2, l0_subln, l0_mu, l0_w0_f,
        l0_w2_f, l0_w0_b, l0_w2_b, l0_a0, l0_a2, l0_g2, l0_k_k, l0_k_a, l0_r_k, l0_lnx_w,
        l0_lnx_b, l1_mod_w, l1_mod_b, l1_norm1, l1_norm2, l1_w_in, l1_w_out, l1_mlp_w1,
        l1_mlp_w2, l1_conv_w, l1_conv_b, l1_dt_bias_f, l1_a_log_f, l1_dt_bias_b, l1_a_log_b,
        l1_d_skip, l1_ssm_norm, l1_gk_up_f, l1_gk_b_f, l1_gk_up_b, l1_gk_b_b, l1_gla_norm,
        final_norm,
    )
    return second_block(
        x, mem_2, positions_2, g_pre_mix_2, w_in_2, w_fourier_2, sink_2, g_mem_2, w_mem_kv_2,
        g_grp_2, w_out_2, g_post_mix_2, g_pre_ffn_2, w_ffn_in_2, w_ffn_out_2, g_post_ffn_2,
    )


_drawn_inputs = setup_inputs


def setup_inputs(seed=0):
    import zlib

    import numpy as np

    out = dict(_drawn_inputs(seed))
    spreads = {}
    factors = {'l0_norm1': 3.296,
     'l0_lam_q1': 4.634,
     'l0_lam_q2': 64.0,
     'l0_lam_k2': 4.171,
     'l0_subln': 10.654,
     'l0_w2_f': 8.0,
     'l0_w2_b': 8.0,
     'l0_a0': 8.0,
     'l0_k_k': 10.434,
     'l0_k_a': 3.922,
     'l0_lnx_w': 7.284,
     'l0_lnx_b': 43.844,
     'l1_conv_b': 6.772,
     'l1_d_skip': 200.0,
     'l1_ssm_norm': 28.752,
     'l1_gk_b_f': 8.0,
     'l1_gk_b_b': 8.0,
     'l1_gla_norm': 43.996,
     'sink_2': 8.0,
     'l0_norm2': 3.631,
     'l1_norm2': 5.185,
     'l1_dt_bias_f': 26.616,
     'l1_dt_bias_b': 29.624,
     'l1_a_log_b': 26.816,
     'l1_a_log_f': 8.0}
    for name, (base, spread) in spreads.items():
        noise = np.random.default_rng([zlib.crc32(name.encode()), seed]).standard_normal(out[name].shape)
        drawn = base * np.exp(spread * noise) if base else spread * noise
        out[name] = __import__('jax').numpy.asarray(drawn.astype(out[name].dtype))
    for name, factor in factors.items():
        out[name] = (out[name] * factor).astype(out[name].dtype)
    return out
```

```python
from contextlib import ExitStack

import numpy as np

import concourse.bass as bass
from concourse import mybir

F32 = mybir.dt.float32
I32 = mybir.dt.int32
ALU = mybir.AluOpType
ACT = mybir.ActivationFunctionType
AX_X = mybir.AxisListType.X

P = 128
D = 1024
KT = D // P
LAT = 256
TOK = 512
CH = 128
NCH = TOK // CH
HID = 4096
FF = 2816
SLOTS = 4
SW = 256
EPS = 1e-6
LAM_INIT = 0.2
DECAY = float(np.exp(-0.5))
GLA_CLAMP = 43.0


C_IDENT, C_ONES, C_BLK, C_LE, C_GE = (P * n for n in range(5))
C_OVER = 5 * P
C_MASK4 = C_OVER
C_LEVEL = C_MASK4 + 1024
C_ROTA = C_LEVEL + 2 * 7 * P
C_COSA = C_ROTA + P
C_SINA = C_COSA + LAT
N_CONST = C_SINA + LAT
C_DFTC = C_OVER
C_DFTS = C_DFTC + 2 * P
C_WIN = C_DFTS + 4 * LAT
C_ROTB = C_WIN + 2 * LAT
C_INVF = C_ROTB + P
N_CONST2 = C_INVF + 1 - C_OVER


def first_constants():
    j, i = np.arange(P)[:, None], np.arange(P)[None, :]
    out = np.zeros((P, N_CONST), np.float32)
    out[:, C_IDENT:C_IDENT + P] = j == i
    out[:, C_ONES:C_ONES + P] = 1.0
    out[:, C_BLK:C_BLK + P] = j // 64 == i // 64
    out[:, C_LE:C_LE + P] = j <= i
    out[:, C_GE:C_GE + P] = j >= i
    for n, (strict, incl) in enumerate(((j < i, j <= i), (j > i, j >= i))):
        out[:, C_MASK4 + 512 * n:C_MASK4 + 512 * (n + 1)] = np.concatenate([strict, incl, strict, incl], 1)
    for lv in range(7):
        b = 1 << lv
        low = (j // (2 * b) == i // (2 * b)) & ((j // b) % 2 == 1) & ((i // b) % 2 == 0)
        out[:, C_LEVEL + P * lv:C_LEVEL + P * (lv + 1)] = low.T
        out[:, C_LEVEL + P * (7 + lv):C_LEVEL + P * (8 + lv)] = low
    rot = np.zeros((P, P), np.float32)
    for r in range(P):
        if r % 32 < 16:
            rot[r, r + 16] = -1.0
        else:
            rot[r, r - 16] = 1.0
    out[:, C_ROTA:C_ROTA + P] = rot.T
    t = np.arange(LAT)
    inv = (np.float32(10000.0) ** (-np.arange(16, dtype=np.float32) / np.float32(16))).astype(np.float32)
    for r in range(P):
        pos = (t // 64 if r % 64 < 32 else t % 64).astype(np.float32)
        ang = pos * inv[r % 16]
        out[r, C_COSA:C_COSA + LAT] = np.cos(ang)
        out[r, C_SINA:C_SINA + LAT] = np.sin(ang)
    return out


def second_constants():
    out = np.zeros((P, N_CONST2), np.float32)
    o = -C_OVER
    c = np.arange(64)
    ang = 2 * np.pi * ((c[:, None] * c[None, :]) % 64) / 64
    for n, m in enumerate((np.cos(ang), np.sin(ang))):
        for g in range(2):
            out[64 * g:64 * g + 64, o + C_DFTC + P * n + 64 * g:o + C_DFTC + P * n + 64 * g + 64] = m / 128.0
    s = np.arange(LAT)
    ang = 2 * np.pi * ((s[:, None] * s[None, :]) % LAT) / LAT
    for n, m in enumerate((np.cos(ang), -np.sin(ang))):
        for h in range(2):
            at = o + C_DFTS + (2 * n + h) * LAT
            out[:, at:at + LAT] = m[P * h:P * h + P]
    q, k = np.arange(P)[:, None], np.arange(LAT)[None, :]
    for h in range(2):
        at = o + C_WIN + h * LAT
        out[:, at:at + LAT] = np.where(np.abs(q + P * h - k) <= 128, 0.0, -1e30)
    for r in range(P):
        if r % 64 < 32:
            out[r + 32, o + C_ROTB + r] = -1.0
        else:
            out[r - 32, o + C_ROTB + r] = 1.0
    inv = np.exp(-np.float32(np.log(10000.0)) * np.arange(32, dtype=np.float32) * np.float32(2.0 / 64))
    out[:, o + C_INVF] = inv.astype(np.float32)[np.arange(P) % 32]
    return out


ROWS = [
    [("c", 8), ("c_ctx", 8), ("l0_mod_b", 48), ("l0_norm1", 8), ("l0_norm2", 8), ("l0_mu", 14), ("l0_w0_f", 4),
     ("l0_w0_b", 4), ("l0_a0", 4), ("l0_k_k", 4), ("l0_k_a", 4), ("l0_r_k", 4), ("l0_lnx_w", 4), ("l0_lnx_b", 4),
     ("l0_subln", 1)],
    [("l1_mod_b", 48), ("l1_norm1", 8), ("l1_norm2", 8), ("l1_conv_w", 40), ("l1_conv_b", 8), ("l1_ssm_norm", 4),
     ("l1_gk_b_f", 2), ("l1_gk_b_b", 2), ("l1_gla_norm", 1)],
    [("final_norm", 8), ("g_pre_mix_2", 16), ("g_mem_2", 16), ("g_grp_2", 16), ("g_post_mix_2", 16),
     ("g_pre_ffn_2", 16), ("g_post_ffn_2", 16)],
]
COL = {}
for _n, _tile in enumerate(ROWS):
    _r = 0
    for _name, _count in _tile:
        COL[_name] = P * _n + _r
        _r += _count
    assert _r <= P


class Stage:

    def __init__(self, net, name):
        self.net, self.nc, self.name, self.sems = net, net.nc, name, []

    def sem(self, what):
        s = self.nc.alloc_semaphore(f"{self.name}_{what}")
        self.sems.append(s)
        return s

    def __enter__(self):
        self.block = self.nc.Block(name=self.name, no_gpsimd_drain=True)
        self.block.__enter__()
        self.scalar, self.vector, self.tensor = self.block.scalar, self.block.vector, self.block.tensor
        self.gpsimd, self.sync = self.block.gpsimd, self.block.sync
        return self

    def __exit__(self, *failed):
        self.block.__exit__(*failed)
        if failed[0]:
            return
        for s in self.sems:
            self.nc.gpsimd.sem_clear(s)
        for s in self.net.cleared:
            self.nc.release_semaphore(s)
        self.net.cleared = self.sems


class Chain:

    def __init__(self, engine, sem):
        self.engine, self.sem, self.n = engine, sem, 0

    def __call__(self, step):
        self.n += 1
        step.then_inc(self.sem, 1)
        self.engine.wait_ge(self.sem, self.n)


class Weights:

    def __init__(self, loops, tail, slot, kts=(KT,) * SLOTS):
        self.loops, self.tail, self.slot, self.kts = loops, tail, slot, kts

    def first(self):
        return SLOTS if self.loops else min(self.tail, SLOTS)


def columns(w, first, count):
    view = w[:, first:first + count].rearrange("(t k) (n m) -> n k t m", k=P, m=SW)
    return Weights(count // SW // SLOTS, count // SW % SLOTS, lambda i, s: view[SLOTS * i + s])


def deep(w, parts):
    view = w.rearrange("(t k) (n m) -> n k t m", k=P, m=SW)
    ends = np.cumsum((0,) + parts)
    return Weights(D // SW, 0, lambda i, s: view[i, :, int(ends[s]):int(ends[s + 1]), :], parts)


class Net:

    def __init__(self, nc, ctx, ins, out):
        self.nc, self.ins, self.out, self.cleared = nc, ins, out, []

        def sb(name, shape):
            return ctx.enter_context(nc.sbuf_tensor(name, shape, F32))

        self.XT = sb("XT", [P, KT, TOK])
        self.HT = sb("HT", [P, KT, TOK])
        self.PT = sb("PT", [P, 32, TOK])
        self.OT = sb("OT", [P, KT, TOK])
        self.RING = sb("RING", [P, SLOTS, KT * SW])
        self.CONST = sb("CONST", [P, N_CONST])
        self.PAR = sb("PAR", [P, 3 * P])
        self.MOD = sb("MOD", [P, 48, 2])
        self.AFF = sb("AFF", [P, 2, KT, 2])
        self.CACT = sb("CACT", [P, KT, 2])
        self.DER = sb("DER", [P, 40])
        self.LORA = sb("LORA", [P, 2, 512])
        self.G2 = sb("G2", [P, 512])
        self.WDG = sb("WDG", [P, KT, 32])
        self.GUP = sb("GUP", [16, 2, 256])
        self.WF = sb("WF", [P, 2, 2, P])
        self.HEADROW = sb("HEADROW", [P, 40])
        self.DSKIP = sb("DSKIP", [P, 4])
        self.SINKROW = sb("SINKROW", [P, 16])
        self.LAMROW = sb("LAMROW", [P, 4, 64])
        self.LAM = sb("LAM", [P, 4])
        self.SC = sb("SC", [P, 7900])
        self.ps = [ctx.enter_context(nc.psum_tensor(f"bank{b}", [P, 512], F32)) for b in range(8)]
        self.ring_loaded = [ctx.enter_context(nc.semaphore(f"ring{s}_loaded")) for s in range(SLOTS)]
        self.ring_base = [0] * SLOTS
        self.smalls_in = ctx.enter_context(nc.semaphore("smalls_in"))

    def const(self, at, width=P):
        return self.CONST[:, at:at + width]

    def par(self, name, n=0):
        return self.PAR[:, COL[name] + n:COL[name] + n + 1]

    def ring(self, s, kt, m):
        return self.RING[:, s, kt * SW + m * P:kt * SW + m * P + P]

    def fetch(self, sync, w, i, s):
        view = self.RING[:, s, 0:w.kts[s] * SW].rearrange("p (t m) -> p t m", m=SW)
        sync.dma_start(view, w.slot(i, s)).then_inc(self.ring_loaded[s], 16)

    def spent(self, w):
        for s in range(SLOTS):
            self.ring_base[s] += 16 * (w.loops + (s < w.tail))


def load_stage(net, first_weights):
    nc, ins = net.nc, net.ins
    rows = net.SC[:, 0:3 * P].rearrange("p (g m) -> p g m", m=P)
    tokens = net.PT[:, 0:2 * NCH, :].rearrange("p t m -> p (t m)").rearrange("p (t d) -> p t d", d=D)
    with Stage(net, "load") as st:
        const_in, rows_in, x_in = st.sem("const_in"), st.sem("rows_in"), st.sem("x_in")
        small_in, zeroed = st.sem("small_in"), st.sem("wf_zeroed")
        turned, copied, cols_ready = st.sem("turned"), st.sem("copied"), st.sem("cols_ready")
        own = st.sem("dve_own")
        lam_exp, lam_sums, act_own = st.sem("lam_exp"), st.sem("lam_sums"), st.sem("act_own")
        smalls_in = net.smalls_in
        n_rows = sum(len(t) for t in ROWS)

        @st.sync
        def _(sp):
            sp.dma_start(net.CONST[:, :], ins["const_1"]).then_inc(const_in, 16)
            for t in range(2):
                sp.dma_start(tokens[:, t, :], ins["x"][0, P * t:P * t + P, :]).then_inc(x_in, 16)
            for t in range(2):
                sp.dma_start(tokens[:, 2 + t, :], ins["ctx"][0, P * t:P * t + P, :]).then_inc(x_in, 16)
            for s in range(first_weights.first()):
                net.fetch(sp, first_weights, 0, s)
            w1 = ins["l1_w_in"]
            for at, col in ((0, 1536), (16, 3088)):
                sp.dma_start(net.WDG[:, :, at:at + 16],
                             w1[:, col:col + 16].rearrange("(t k) m -> k t m", k=P)).then_inc(small_in, 16)
            sp.wait_ge(small_in, 32)

        @st.scalar
        def _(act):
            n = 0
            for g, tile in enumerate(ROWS):
                r = 0
                for name, count in tile:
                    a = ins[name]
                    if len(a.shape) == 2:
                        a = a.rearrange("a b -> (a b)")
                    flat = a.rearrange("(t p) -> t p", p=P)
                    act.dma_start(rows[r:r + count, g, :], flat).then_inc(rows_in, 16)
                    r += count
            link = Chain(act, act_own)
            act.wait_ge(cols_ready, 3)
            for n, name in enumerate(("c", "c_ctx")):
                act.activation(net.CACT[:, :, n], net.PAR[:, COL[name]:COL[name] + 8], ACT.Silu)
            act.wait_ge(lam_sums, 1)
            act.activation(net.LAM[:, 2:4], net.LAM[:, 0:2], ACT.Exp).then_inc(lam_exp, 1)

        @st.gpsimd
        def _(pool):
            pool.memset(net.WF[:, :, :, :], 0.0).then_inc(zeroed, 1)
            small = [(net.LORA[0:64, 0, :], ins["l0_w2_f"]), (net.LORA[0:64, 1, :], ins["l0_w2_b"]),
                     (net.LORA[64:128, 0, :], ins["l0_a2"]), (net.G2[:, :], ins["l0_g2"]),
                     (net.GUP[:, 0, :], ins["l1_gk_up_f"]), (net.GUP[:, 1, :], ins["l1_gk_up_b"])]
            for n, name in enumerate(("l1_dt_bias_f", "l1_dt_bias_b", "l1_a_log_f", "l1_a_log_b",
                                      "l1_d_skip")):
                small.append((net.HEADROW[:, 8 * n:8 * n + 8], ins[name].partition_broadcast(P)))
            small.append((net.SINKROW[:, :], ins["sink_2"].rearrange("a b -> (a b)").partition_broadcast(P)))
            for n, name in enumerate(("l0_lam_q1", "l0_lam_k1", "l0_lam_q2", "l0_lam_k2")):
                small.append((net.LAMROW[:, n, :], ins[name].partition_broadcast(P)))
            for into, of in small:
                pool.dma_start(into, of).then_inc(smalls_in, 16)
            pool.wait_ge(zeroed, 1)
            for layer in range(2):
                for g in range(4):
                    o = 64 * (g % 2)
                    pool.dma_start(net.WF[o:o + 64, layer, g // 2, o:o + 64],
                                   ins["w_fourier_2"][layer, g]).then_inc(smalls_in, 16)
            pool.wait_ge(smalls_in, 16 * (len(small) + 8))

        @st.tensor
        def _(pe):
            ident = net.const(C_IDENT)
            pe.wait_ge(const_in, 16)
            pe.wait_ge(rows_in, 16 * n_rows)
            for g, tile in enumerate(ROWS):
                r = sum(count for _, count in tile)
                nc.tensor.transpose(net.ps[g][:, 0:r], rows[0:r, g, :], ident[0:r, 0:r]).then_inc(turned, 1)
            pe.wait_ge(x_in, 64)
            for f in range(KT):
                bank = (f + 3) % 8
                if f >= 5:
                    pe.wait_ge(cols_ready, f - 4)
                for t in range(4):
                    last = nc.tensor.transpose(net.ps[bank][:, P * t:P * t + P],
                                               tokens[:, t, P * f:P * f + P], ident)
                last.then_inc(turned, 1)

        @st.vector
        def _(dve):
            link = Chain(dve, own)
            for g, tile in enumerate(ROWS):
                r = sum(count for _, count in tile)
                dve.wait_ge(turned, g + 1)
                nc.vector.tensor_copy(net.PAR[:, P * g:P * g + r], net.ps[g][:, 0:r]).then_inc(cols_ready, 1)
            for f in range(KT):
                dve.wait_ge(turned, f + 4)
                nc.vector.tensor_copy(net.XT[:, f, :], net.ps[(f + 3) % 8][:, :])
            dve.wait_ge(cols_ready, 3)
            mu = net.PAR[:, COL["l0_mu"]:COL["l0_mu"] + 14]
            nc.vector.tensor_scalar(net.DER[:, 0:14], mu, 0.5, None, ALU.mult)
            nc.vector.tensor_scalar(net.DER[:, 14:28], mu, -1.0, 1.0, ALU.mult, ALU.add)
            k_a = net.PAR[:, COL["l0_k_a"]:COL["l0_k_a"] + 4]
            nc.vector.tensor_scalar(net.DER[:, 28:32], k_a, -1.0, 1.0, ALU.mult, ALU.add)
            nc.vector.tensor_scalar(net.DER[:, 32:33], net.par("l0_subln"), 1.0 - LAM_INIT, None, ALU.mult)
            dve.wait_ge(smalls_in, 16 * (6 + 5 + 1 + 4 + 8))
            skip = net.HEADROW[:, 32:40].rearrange("p (t h) -> p t h", h=2)
            for h in range(2):
                nc.vector.tensor_copy(net.DSKIP[64 * h:64 * h + 64, :], skip[64 * h:64 * h + 64, :, h])
            lam = net.LAMROW[:, :, :].rearrange("p (a b) d -> p a b d", b=2)
            link(nc.vector.tensor_tensor(lam[:, :, 0, :], lam[:, :, 0, :], lam[:, :, 1, :], ALU.mult))
            nc.vector.tensor_reduce(net.LAM[:, 0:2], lam[:, :, 0, :], AX_X, ALU.add).then_inc(lam_sums, 1)
            dve.wait_ge(lam_exp, 1)
            link(nc.vector.tensor_tensor(net.LAM[:, 0:1], net.LAM[:, 3:4], net.LAM[:, 2:3], ALU.subtract))
            link(nc.vector.tensor_scalar(net.LAM[:, 0:1], net.LAM[:, 0:1], LAM_INIT, None, ALU.subtract))


def feed(net, sp, w, used, following, straight=False):
    if w.loops > 1 and straight:
        for i in range(w.loops - 1):
            for s in range(SLOTS):
                sp.wait_ge(*used(i, s))
                net.fetch(sp, w, i + 1, s)
    elif w.loops > 1:
        with sp.Fori(0, w.loops - 1) as i:
            for s in range(SLOTS):
                sp.wait_ge(*used(i, s))
                net.fetch(sp, w, i + 1, s)
    if w.loops:
        for s in range(w.tail):
            sp.wait_ge(*used(w.loops - 1, s))
            net.fetch(sp, w, w.loops, s)
    if following:
        for s in range(following.first()):
            if w.loops or s < w.tail:
                sp.wait_ge(*used(w.loops - (s >= w.tail), s))
            net.fetch(sp, following, 0, s)


def turns(engine, w, turn, straight=False):
    if straight:
        for i in range(w.loops):
            turn(i, range(SLOTS))
    elif w.loops == 1:
        turn(0, range(SLOTS))
    elif w.loops:
        with engine.Fori(0, w.loops) as i:
            turn(i, range(SLOTS))
    if w.tail:
        turn(w.loops, range(w.tail))


def product_on_pe(net, pe, w, src, widths, tile_ready, tile_free, straight=False):
    base = list(net.ring_base)

    def turn(i, slots):
        for s in slots:
            n = widths(i, s)
            pe.wait_ge(net.ring_loaded[s], 16 * (i + 1) + base[s])
            for m in range(2):
                pe.wait_ge(tile_free[m], SLOTS * i + s + 1)
                for kt in range(KT):
                    last = net.nc.tensor.matmul(net.ps[2 * s + m][:, 0:n], net.ring(s, kt, m), src[:, kt, 0:n],
                                                start=(kt == 0), stop=(kt == KT - 1))
                last.then_inc(tile_ready[m], 1)

    turns(pe, w, turn, straight)


def deep_on_pe(net, pe, w, src, n, tile_ready, tile_free, slot_read):
    base = list(net.ring_base)

    def turn(i, slots):
        k0 = 0
        for s in slots:
            pe.wait_ge(net.ring_loaded[s], 16 * (i + 1) + base[s])
            for m in range(2):
                if s == 0:
                    pe.wait_ge(tile_free[m], i + 1)
                for kt in range(w.kts[s]):
                    last = net.nc.tensor.matmul(net.ps[m][:, 0:n], net.ring(s, kt, m), src[:, k0 + kt, 0:n],
                                                start=(s == 0 and kt == 0),
                                                stop=(s == SLOTS - 1 and kt == w.kts[s] - 1))
                if s == SLOTS - 1:
                    last.then_inc(tile_ready[m], 1)
            if s < SLOTS - 1:
                last.then_inc(slot_read, 1)
            k0 += w.kts[s]

    turns(pe, w, turn)


def modulation_stage(net, layer, w, following):
    nc = net.nc
    with Stage(net, f"mod{layer}") as st:
        tile_ready = [st.sem(f"tile_ready{m}") for m in range(2)]
        own = st.sem("dve_own")
        base = list(net.ring_base)
        sums = net.ps[0][:, 0:96].rearrange("p (t n) -> p t n", n=2)

        @st.sync
        def _(sp):
            feed(net, sp, w, lambda i, s: (tile_ready[1], SLOTS * i + s + 1), following)

        @st.tensor
        def _(pe):
            def turn(i, slots):
                for s in slots:
                    pe.wait_ge(net.ring_loaded[s], 16 * (i + 1) + base[s])
                    for m in range(2):
                        for kt in range(KT):
                            last = nc.tensor.matmul(sums[:, 2 * (SLOTS * i + s) + m, :], net.ring(s, kt, m),
                                                    net.CACT[:, kt, :], start=(kt == 0), stop=(kt == KT - 1))
                        last.then_inc(tile_ready[m], 1)

            turns(pe, w, turn)

        @st.vector
        def _(dve):
            link = Chain(dve, own)
            dve.wait_ge(tile_ready[1], SLOTS * w.loops)
            bias = COL[f"l{layer}_mod_b"]
            link(nc.vector.tensor_tensor(net.MOD[:, :, :], sums,
                                         net.PAR[:, bias:bias + 48].unsqueeze(2).to_broadcast([P, 48, 2]), ALU.add))
            for h in range(2):
                gain = COL[f"l{layer}_norm{h + 1}"]
                link(nc.vector.scalar_tensor_tensor(net.AFF[:, h], net.MOD[:, 24 * h + 8:24 * h + 16, :], 1.0,
                                                    net.PAR[:, gain:gain + 8].unsqueeze(2).to_broadcast([P, KT, 2]),
                                                    ALU.add, ALU.mult))
        net.spent(w)


def ada_stage(net, layer, half, n):
    nc, square = net.nc, net.PT
    with Stage(net, f"ada{layer}{half}") as st:
        squared, summed, scaled = st.sem("squared"), st.sem("summed"), st.sem("scaled")
        mean_ready, root_ready, own = st.sem("mean_ready"), st.sem("root_ready"), st.sem("dve_own")
        total, rstd = net.ps[0][:, 0:n], net.SC[:, 0:n]
        parts = [(0, 0)] + ([(1, LAT)] if n > LAT else [])

        @st.scalar
        def _(act):
            for t in range(KT):
                act.activation(square[:, t, 0:n], net.XT[:, t, 0:n], ACT.Square).then_inc(squared, 1)
            act.wait_ge(mean_ready, 1)
            act.activation(rstd, rstd, ACT.Sqrt).then_inc(root_ready, 1)
            for t in range(KT):
                act.wait_ge(scaled, t + 1)
                for j, at in parts:
                    act.activation(net.HT[:, t, at:at + LAT], net.HT[:, t, at:at + LAT], ACT.Identity,
                                   bias=net.MOD[:, 24 * half + t, j:j + 1])

        @st.tensor
        def _(pe):
            for t in range(KT):
                pe.wait_ge(squared, t + 1)
                last = nc.tensor.matmul(total, net.const(C_ONES), square[:, t, 0:n], start=(t == 0), stop=(t == KT - 1))
            last.then_inc(summed, 1)

        @st.vector
        def _(dve):
            link = Chain(dve, own)
            dve.wait_ge(summed, 1)
            nc.vector.tensor_scalar(rstd, total, 1.0 / D, EPS, ALU.mult, ALU.add).then_inc(mean_ready, 1)
            dve.wait_ge(root_ready, 1)
            link(nc.vector.reciprocal(rstd, rstd))
            for t in range(KT):
                for j, at in parts:
                    last = nc.vector.scalar_tensor_tensor(net.HT[:, t, at:at + LAT], net.XT[:, t, at:at + LAT],
                                                          net.AFF[:, half, t, j:j + 1], rstd[:, at:at + LAT],
                                                          ALU.mult, ALU.mult)
                last.then_inc(scaled, 1)


def project_stage(net, name, w, src, widths, dst, following, straight=False, dst_tile=lambda n: n):
    nc = net.nc
    with Stage(net, name) as st:
        tile_ready = [st.sem(f"tile_ready{m}") for m in range(2)]
        tile_free = [st.sem(f"tile_free{m}") for m in range(2)]

        @st.sync
        def _(sp):
            feed(net, sp, w, lambda i, s: (tile_ready[1], SLOTS * i + s + 1), following, straight)

        @st.tensor
        def _(pe):
            product_on_pe(net, pe, w, src, widths, tile_ready, tile_free, straight)

        @st.scalar
        def _(act):
            act.sem_inc(tile_free[0], SLOTS)

            def turn(i, slots):
                for s in slots:
                    n = widths(i, s)
                    act.wait_ge(tile_ready[0], SLOTS * i + s + 1)
                    act.activation(dst[:, dst_tile(2 * (SLOTS * i + s)), 0:n], net.ps[2 * s][:, 0:n],
                                   ACT.Copy).then_inc(tile_free[0], 1)

            turns(act, w, turn, straight)

        @st.vector
        def _(dve):
            dve.sem_inc(tile_free[1], SLOTS)

            def turn(i, slots):
                for s in slots:
                    n = widths(i, s)
                    dve.wait_ge(tile_ready[1], SLOTS * i + s + 1)
                    nc.vector.tensor_copy(dst[:, dst_tile(2 * (SLOTS * i + s) + 1), 0:n],
                                          net.ps[2 * s + 1][:, 0:n]).then_inc(tile_free[1], 1)

            turns(dve, w, turn, straight)
        net.spent(w)


def relu_squared_stage(net, name, w, n, following):
    nc = net.nc
    raised = net.SC[:, 0:8 * TOK].rearrange("p (b m) -> p b m", m=TOK)
    with Stage(net, name) as st:
        tile_ready = [st.sem(f"tile_ready{m}") for m in range(2)]
        tile_free = [st.sem(f"tile_free{m}") for m in range(2)]
        raised_ready = [st.sem(f"raised_ready{m}") for m in range(2)]

        @st.sync
        def _(sp):
            feed(net, sp, w, lambda i, s: (tile_ready[1], SLOTS * i + s + 1), following)

        @st.tensor
        def _(pe):
            product_on_pe(net, pe, w, net.HT, lambda i, s: n, tile_ready, tile_free)

        @st.scalar
        def _(act):
            def turn(i, slots):
                for s in slots:
                    for m in range(2):
                        act.wait_ge(tile_ready[m], SLOTS * i + s + 1)
                        act.activation(raised[:, 2 * s + m, 0:n], net.ps[2 * s + m][:, 0:n],
                                       ACT.Relu).then_inc(raised_ready[m], 1)

            turns(act, w, turn)

        @st.vector
        def _(dve):
            for m in range(2):
                dve.sem_inc(tile_free[m], SLOTS)

            def turn(i, slots):
                for s in slots:
                    for m in range(2):
                        dve.wait_ge(raised_ready[m], SLOTS * i + s + 1)
                        nc.vector.tensor_tensor(net.PT[:, 2 * (SLOTS * i + s) + m, 0:n], raised[:, 2 * s + m, 0:n],
                                                raised[:, 2 * s + m, 0:n], ALU.mult).then_inc(tile_free[m], 1)

            turns(dve, w, turn)
        net.spent(w)


def add_gated(net, dve, tile, bank, gate, n):
    for j, at in ((0, 0), (1, LAT))[:n // LAT]:
        step = net.nc.vector.scalar_tensor_tensor(net.XT[:, tile, at:at + LAT], bank[:, at:at + LAT],
                                                  net.MOD[:, gate + tile, j:j + 1], net.XT[:, tile, at:at + LAT],
                                                  ALU.mult, ALU.add)
    return step


def mixed_out_stage(net, name, w, n, following):
    with Stage(net, name) as st:
        tile_ready = [st.sem(f"tile_ready{m}") for m in range(2)]
        tile_free = [st.sem(f"tile_free{m}") for m in range(2)]

        @st.sync
        def _(sp):
            feed(net, sp, w, lambda i, s: (tile_ready[1], SLOTS * i + s + 1), following)

        @st.tensor
        def _(pe):
            product_on_pe(net, pe, w, net.OT, lambda i, s: n, tile_ready, tile_free)

        @st.vector
        def _(dve):
            for m in range(2):
                dve.sem_inc(tile_free[m], SLOTS)
            for s in range(SLOTS):
                for m in range(2):
                    dve.wait_ge(tile_ready[m], s + 1)
                    add_gated(net, dve, 2 * s + m, net.ps[2 * s + m], 16, n)
        net.spent(w)


def mlp_out_stage(net, name, w, n, following):
    with Stage(net, name) as st:
        tile_ready = [st.sem(f"tile_ready{m}") for m in range(2)]
        tile_free = [st.sem(f"tile_free{m}") for m in range(2)]
        slot_read = st.sem("slot_read")

        @st.sync
        def _(sp):
            feed(net, sp, w, lambda i, s: (slot_read, (SLOTS - 1) * i + s + 1) if s < SLOTS - 1 else (tile_ready[1], i + 1),
                 following)

        @st.tensor
        def _(pe):
            deep_on_pe(net, pe, w, net.PT, n, tile_ready, tile_free, slot_read)

        @st.vector
        def _(dve):
            for m in range(2):
                dve.sem_inc(tile_free[m], 1)

            def turn(i, slots):
                for m in range(2):
                    dve.wait_ge(tile_ready[m], i + 1)
                    for j, at in ((0, 0), (1, LAT))[:n // LAT]:
                        into = net.XT[:, 2 * i + m, at:at + LAT]
                        step = net.nc.vector.scalar_tensor_tensor(into, net.ps[m][:, at:at + LAT],
                                                                  net.MOD[:, 40 + 2 * i + m, j:j + 1], into,
                                                                  ALU.mult, ALU.add)
                    step.then_inc(tile_free[m], 1)

            turns(dve, w, turn)
        net.spent(w)


def first_fetch_stage(net, w):
    with Stage(net, "fetch") as st:
        @st.sync
        def _(sp):
            for s in range(w.first()):
                net.fetch(sp, w, 0, s)


def diff_prepare_stage(net):
    nc = net.nc
    values = net.SC[:, 0:2048].rearrange("p (t m) -> p t m", m=512)
    part = net.SC[:, 2048:2048 + 2 * LAT].rearrange("p (b m) -> p b m", m=LAT)
    with Stage(net, "diff_prepare") as st:
        rotated, added, turned, own = st.sem("rotated"), st.sem("added"), st.sem("turned"), st.sem("dve_own")

        @st.tensor
        def _(pe):
            for t in range(8):
                if t >= 4:
                    pe.wait_ge(added, t - 3)
                nc.tensor.matmul(net.ps[t % 4][:, 0:LAT], net.const(C_ROTA), net.PT[:, t, 0:LAT],
                                 start=True, stop=True).then_inc(rotated, 1)
            for t in range(NCH):
                for h in range(4):
                    last = nc.tensor.transpose(net.ps[4 + t][:, P * h:P * h + P],
                                               net.PT[:, 8 + h, CH * t:CH * t + CH], net.const(C_IDENT))
                last.then_inc(turned, 1)

        @st.scalar
        def _(act):
            for t in range(NCH):
                act.wait_ge(turned, t + 1)
                act.activation(values[:, t, :], net.ps[4 + t][:, :], ACT.Copy)

        @st.vector
        def _(dve):
            link = Chain(dve, own)
            for t in range(8):
                dve.wait_ge(rotated, t + 1)
                x = net.PT[:, t, 0:LAT]
                nc.vector.tensor_tensor(part[:, t % 2], net.ps[t % 4][:, 0:LAT], net.const(C_SINA, LAT),
                                        ALU.mult).then_inc(added, 1)
                link(nc.vector.tensor_tensor(x, x, net.const(C_COSA, LAT), ALU.mult))
                dve.wait_ge(added, t + 1)
                link(nc.vector.tensor_tensor(x, x, part[:, t % 2], ALU.add))


def diff_attention_stage(net):
    nc = net.nc
    values = net.SC[:, 0:2048].rearrange("p (t m) -> p t m", m=512)
    prob = net.SC[:, 2048:4096].rearrange("p (b m k) -> p b m k", b=2, m=2)
    mixed = net.SC[:, 4096:5120].rearrange("p (b k) -> p b k", b=2)
    mixed_t = net.SC[:, 5120:6144].rearrange("p (b k) -> p b k", b=2)
    stat = net.SC[:, 6144:6144 + 8 * 16].rearrange("p (u n) -> p u n", n=8)
    units = [(h, q) for h in range(4) for q in range(NCH)]
    first_key = lambda q: 0 if q < 2 else 2
    scale = 64 ** -0.5
    with Stage(net, "diff_attention") as st:
        scored, max_ready, exp_ready = st.sem("scored"), st.sem("max_ready"), st.sem("exp_ready")
        mixed_ready, turned, turned_copied = st.sem("mixed_ready"), st.sem("turned"), st.sem("turned_copied")
        out_ready, out_taken, own = st.sem("out_ready"), st.sem("out_taken"), st.sem("dve_own")

        @st.tensor
        def _(pe):
            def score(u):
                h, q = units[u]
                if u >= 2:
                    pe.wait_ge(exp_ready, 2 * (u - 1))
                k0 = first_key(q) * P
                for m in range(2):
                    rows = slice(64 * m, 64 * m + 64)
                    last = nc.tensor.matmul(net.ps[2 * (u % 2) + m][:, k0:TOK], net.PT[rows, h, P * q:P * q + P],
                                            net.PT[rows, 4 + h, k0:TOK], start=True, stop=True)
                last.then_inc(scored, 1)

            score(0)
            score(1)
            for u, (h, q) in enumerate(units):
                pe.wait_ge(mixed_ready, u + 1)
                if u >= 2:
                    pe.wait_ge(turned_copied, u - 1)
                for t in range(first_key(q), NCH):
                    last = nc.tensor.transpose(net.ps[4 + u % 2][:, P * t:P * t + P],
                                               mixed[:, u % 2, P * t:P * t + P], net.const(C_IDENT))
                last.then_inc(turned, 1)
                if u + 2 < len(units):
                    score(u + 2)
                pe.wait_ge(turned_copied, u + 1)
                if q == 0 and h >= 2:
                    pe.wait_ge(out_taken, h - 1)
                for t in range(first_key(q), NCH):
                    last = nc.tensor.matmul(net.ps[6 + h % 2][:, P * q:P * q + P], values[:, t, P * h:P * h + P],
                                            mixed_t[:, u % 2, P * t:P * t + P],
                                            start=(t == first_key(q)), stop=(t == NCH - 1))
                last.then_inc(out_ready, 1)

        @st.scalar
        def _(act):
            def exps(u):
                k0 = first_key(units[u][1]) * P
                act.wait_ge(max_ready, u + 1)
                if u >= 2:
                    act.wait_ge(mixed_ready, u - 1)
                for m in range(2):
                    act.activation(prob[:, u % 2, m, k0:TOK], net.ps[2 * (u % 2) + m][:, k0:TOK], ACT.Exp,
                                   bias=stat[:, u, m:m + 1], scale=scale,
                                   accum_out=stat[:, u, 2 + m:3 + m]).then_inc(exp_ready, 1)

            exps(0)
            exps(1)
            for u, (h, q) in enumerate(units):
                k0 = first_key(q) * P
                act.wait_ge(turned, u + 1)
                if u >= 2:
                    act.wait_ge(out_ready, u - 1)
                act.activation(mixed_t[:, u % 2, k0:TOK], net.ps[4 + u % 2][:, k0:TOK],
                               ACT.Copy).then_inc(turned_copied, 1)
                if u + 2 < len(units):
                    exps(u + 2)

        @st.vector
        def _(dve):
            link = Chain(dve, own)

            def maxima(u):
                k0 = first_key(units[u][1]) * P
                dve.wait_ge(scored, u + 1)
                for m in range(2):
                    link(nc.vector.reduce_max(stat[:, u, m:m + 1], net.ps[2 * (u % 2) + m][:, k0:TOK], AX_X))
                nc.vector.tensor_scalar(stat[:, u, 0:2], stat[:, u, 0:2], -scale, None,
                                        ALU.mult).then_inc(max_ready, 1)

            maxima(0)
            maxima(1)
            for u, (h, q) in enumerate(units):
                k0 = first_key(q) * P
                dve.wait_ge(exp_ready, 2 * (u + 1))
                link(nc.vector.reciprocal(stat[:, u, 4:6], stat[:, u, 2:4]))
                link(nc.vector.tensor_tensor(stat[:, u, 5:6], stat[:, u, 5:6], net.LAM[:, 0:1], ALU.mult))
                link(nc.vector.tensor_scalar(prob[:, u % 2, 1, k0:TOK], prob[:, u % 2, 1, k0:TOK],
                                             stat[:, u, 5:6], None, ALU.mult))
                if u >= 2:
                    dve.wait_ge(turned, u - 1)
                nc.vector.scalar_tensor_tensor(mixed[:, u % 2, k0:TOK], prob[:, u % 2, 0, k0:TOK], stat[:, u, 4:5],
                                               prob[:, u % 2, 1, k0:TOK], ALU.mult, ALU.add).then_inc(mixed_ready, 1)
                if u + 2 < len(units):
                    maxima(u + 2)
                if q == 1 and h >= 1:
                    dve.wait_ge(out_ready, 4 * h)
                    nc.vector.tensor_copy(net.OT[:, h - 1, :], net.ps[6 + (h - 1) % 2][:, :]).then_inc(out_taken, 1)
            dve.wait_ge(out_ready, len(units))
            nc.vector.tensor_copy(net.OT[:, 3, :], net.ps[7][:, :])


def group_norm_stage(net, name, groups, n, eps, adds=()):
    nc = net.nc
    rstd = net.SC[:, 7900 - 512 * 1:7900]
    with Stage(net, name) as st:
        squared, summed, mean_ready = st.sem("squared"), st.sem("summed"), st.sem("mean_ready")
        root_ready, own = st.sem("root_ready"), st.sem("dve_own")
        steps = [t for g in groups for t in zip(g[0], g[3])]

        @st.scalar
        def _(act):
            for src, square in steps:
                act.activation(square, src, ACT.Square).then_inc(squared, 1)
            for g in range(len(groups)):
                act.wait_ge(mean_ready, g + 1)
                act.activation(rstd[:, 0:n], rstd[:, 0:n], ACT.Sqrt).then_inc(root_ready, 1)

        @st.tensor
        def _(pe):
            at = 0
            for g, (srcs, _, _, squares) in enumerate(groups):
                for k, square in enumerate(squares):
                    at += 1
                    pe.wait_ge(squared, at)
                    last = nc.tensor.matmul(net.ps[g % 8][:, 0:n], net.const(C_ONES), square,
                                            start=(k == 0), stop=(k == len(squares) - 1))
                last.then_inc(summed, 1)

        @st.vector
        def _(dve):
            link = Chain(dve, own)
            for g, (srcs, dsts, gains, _) in enumerate(groups):
                dve.wait_ge(summed, g + 1)
                nc.vector.tensor_scalar(rstd[:, 0:n], net.ps[g % 8][:, 0:n], 1.0 / (P * len(srcs)), eps,
                                        ALU.mult, ALU.add).then_inc(mean_ready, 1)
                dve.wait_ge(root_ready, g + 1)
                link(nc.vector.reciprocal(rstd[:, 0:n], rstd[:, 0:n]))
                for src, dst, gain in zip(srcs, dsts, gains):
                    link(nc.vector.scalar_tensor_tensor(dst, src, gain, rstd[:, 0:n], ALU.mult, ALU.mult))
                for dst, x in zip(dsts, adds):
                    nc.vector.tensor_tensor(x, x, dst, ALU.add)


def rwkv_prepare_stage(net):
    nc = net.nc
    r0, k0, lora, gate = 12, 16, 24, 25
    kk = net.HT[:, 4:8, :]
    b = net.PT[:, 26:30, :]
    near = net.SC[:, 0:7 * TOK].rearrange("p (t m) -> p t m", m=TOK)
    square = net.SC[:, 3584:3584 + 2048].rearrange("p (t m) -> p t m", m=TOK)
    norm = net.SC[:, 5632:5632 + 2048].rearrange("p (t m) -> p t m", m=TOK)
    with Stage(net, "rwkv_prepare") as st:
        near_ready, shifted, own = st.sem("near_ready"), st.sem("shifted"), st.sem("dve_own")
        tanh_ready, a_summed, a_ready = st.sem("tanh_ready"), st.sem("a_summed"), st.sem("a_ready")
        squared, normed, floor_ready, root_ready = (st.sem("squared"), st.sem("normed"), st.sem("floor_ready"),
                                                    st.sem("root_ready"))

        @st.gpsimd
        def _(pool):
            for lot in range(2):
                if lot:
                    pool.wait_ge(shifted, 7)
                f = net.PT[:, r0 + 7 * lot:r0 + 7 * lot + 7, :].rearrange("p t (s m) -> p (t s) m", m=LAT)
                s = near[:, :, :].rearrange("p t (s m) -> p (t s) m", m=LAT)
                pool.tensor_tensor(s[:, :, 1:LAT - 1], f[:, :, 0:LAT - 2], f[:, :, 2:LAT], ALU.add).then_inc(near_ready, 1)
                pool.tensor_copy(s[:, :, 0:1], f[:, :, 1:2]).then_inc(near_ready, 1)
                pool.tensor_copy(s[:, :, LAT - 1:LAT], f[:, :, LAT - 2:LAT - 1]).then_inc(near_ready, 1)

        @st.vector
        def _(dve):
            link = Chain(dve, own)
            for lot in range(2):
                dve.wait_ge(near_ready, 3 * (lot + 1))
                for t in range(7 * lot, 7 * lot + 7):
                    f = net.PT[:, r0 + t, :]
                    link(nc.vector.tensor_scalar(f, f, net.DER[:, 14 + t:15 + t], None, ALU.mult))
                    nc.vector.scalar_tensor_tensor(f, near[:, t - 7 * lot, :], net.DER[:, t:t + 1], f,
                                                   ALU.mult, ALU.add).then_inc(shifted, 1)
            dve.wait_ge(shifted, 14)
            for t in range(4):
                dve.wait_ge(normed, t + 1)
                nc.vector.tensor_scalar(norm[:, t], net.ps[4 + t][:, :], 1e-24, None, ALU.max).then_inc(floor_ready, 1)
            for t in range(4):
                k = net.PT[:, k0 + t, :]
                dve.wait_ge(root_ready, t + 1)
                link(nc.vector.reciprocal(norm[:, t], norm[:, t]))
                link(nc.vector.scalar_tensor_tensor(kk[:, t, :], k, net.par("l0_k_k", t), norm[:, t], ALU.mult, ALU.mult))
                dve.wait_ge(a_ready, t + 1)
                link(nc.vector.tensor_scalar(norm[:, t], b[:, t, :], net.par("l0_k_a", t), net.DER[:, 28 + t:29 + t],
                                             ALU.mult, ALU.add))
                link(nc.vector.tensor_tensor(k, k, norm[:, t], ALU.mult))
                link(nc.vector.tensor_tensor(b[:, t, :], b[:, t, :], kk[:, t, :], ALU.mult))

        @st.scalar
        def _(act):
            act.wait_ge(shifted, 14)
            for t in range(4):
                act.activation(square[:, t], net.PT[:, k0 + t, :], ACT.Square,
                               scale=net.par("l0_k_k", t)).then_inc(squared, 1)
            act.activation(net.PT[0:64, lora, :], net.PT[0:64, lora, :], ACT.Tanh).then_inc(tanh_ready, 1)
            act.activation(net.PT[:, gate, :], net.PT[:, gate, :], ACT.Sigmoid)
            for t in range(4):
                act.wait_ge(a_summed, t + 1)
                act.activation(b[:, t, :], net.ps[t][:, :], ACT.Sigmoid, bias=net.par("l0_a0", t)).then_inc(a_ready, 1)
            for t in range(4):
                act.wait_ge(floor_ready, t + 1)
                act.activation(norm[:, t], norm[:, t], ACT.Sqrt).then_inc(root_ready, 1)

        @st.tensor
        def _(pe):
            pe.wait_ge(shifted, 14)
            for t in range(4):
                nc.tensor.matmul(net.ps[t][:, :], net.LORA[64:128, 0, P * t:P * t + P], net.PT[64:128, lora, :],
                                 start=True, stop=True).then_inc(a_summed, 1)
            for t in range(4):
                pe.wait_ge(squared, t + 1)
                nc.tensor.matmul(net.ps[4 + t][:, :], net.const(C_BLK), square[:, t], start=True,
                                 stop=True).then_inc(normed, 1)


class RwkvMemory:

    def __init__(self, net):
        chunks = lambda v: v.rearrange("p t (c m) -> p t c m", m=CH)
        flat = lambda v, n: v.rearrange("p t m -> p (t m)")[:, 0:n]
        self.r, self.k, self.v = (chunks(net.PT[:, n:n + 4, :]) for n in (12, 16, 20))
        self.kk, self.b = chunks(net.HT[:, 4:8, :]), chunks(net.PT[:, 26:30, :])
        self.kr = flat(net.PT[:, 0:8, :], 4096).rearrange("p (t c n m) -> p t c n m", t=4, c=NCH, n=2)
        self.bd, self.kd = chunks(net.PT[:, 8:12, :]), chunks(net.HT[:, 0:4, :])
        self.sig, self.cum = (net.SC[:, n:n + 2048].rearrange("p (t c m) -> p t c m", t=4, c=NCH) for n in (0, 2048))
        self.vtok = net.SC[:, 4096:6144].rearrange("p (c m) -> p c m", m=512)
        self.state = net.SC[:, 6144:6656].rearrange("p (t m) -> p t m", m=P)
        self.rhs, self.minus_u = net.SC[:, 6656:7168], net.SC[:, 7168:7680]
        small = net.SC[:, 7680:7680 + 64].rearrange("p (n t c) -> p n t c", n=4, t=4)
        self.mid, self.end, self.carry = small[:, 0], small[:, 1], small[:, 2]
        self.btok, self.ktok = net.PT[:, 30, :], net.PT[:, 31, :]
        ring = net.RING[:, :, :].rearrange("p s m -> p (s m)")
        self.gram = ring[:, 0:4096].rearrange("p (h m) -> p h m", m=512)
        four = ring[:, 4096:8192].rearrange("p (q n h m) -> p q n h m", q=2, n=4, h=4)
        self.level, self.inv, self.inv_t, self.y = (four[:, :, n] for n in range(4))
        self.out = chunks(net.OT[:, 4:8, :])


def rwkv_decay_stage(net, d):
    nc, mem = net.nc, RwkvMemory(net)
    order = [2, 3, 0, 1] if d == 0 else [3, 2, 1, 0]
    mid, end = (63, CH - 1) if d == 0 else (64, 0)
    flat = lambda v: v.rearrange("p t c m -> p (t c) m")
    with Stage(net, f"rwkv_decay{d}") as st:
        summed, gated, cum_ready, exped, own = (st.sem("summed"), st.sem("gated"), st.sem("cum_ready"),
                                                st.sem("exped"), st.sem("dve_own"))
        turned, carry_ready = st.sem("turned"), st.sem("carry_ready")

        @st.tensor
        def _(pe):
            for t in range(4):
                nc.tensor.matmul(net.ps[t][:, :], net.LORA[0:64, d, P * t:P * t + P], net.PT[0:64, 24, :],
                                 start=True, stop=True).then_inc(summed, 1)
            if d == 0:
                for c in range(NCH):
                    for t in range(4):
                        last = nc.tensor.transpose(net.ps[4 + c][:, P * t:P * t + P], mem.v[:, t, c, :],
                                                   net.const(C_IDENT))
                    last.then_inc(turned, 1)

        @st.scalar
        def _(act):
            bias = "l0_w0_f" if d == 0 else "l0_w0_b"
            for t in range(4):
                act.wait_ge(summed, t + 1)
                act.activation(mem.sig[:, t].rearrange("p c m -> p (c m)"), net.ps[t][:, :], ACT.Sigmoid,
                               bias=net.par(bias, t)).then_inc(gated, 1)
            if d == 0:
                for c in range(NCH):
                    act.wait_ge(turned, c + 1)
                    act.activation(mem.vtok[:, c, :], net.ps[4 + c][:, :], ACT.Copy)
            kr = mem.kr.rearrange("p t c n m -> p (t c) n m")
            act.wait_ge(cum_ready, 1)
            act.activation(kr[:, :, 1, :], flat(mem.cum), ACT.Exp, scale=-DECAY).then_inc(exped, 1)
            act.activation(flat(mem.bd), flat(mem.cum), ACT.Exp, scale=DECAY).then_inc(exped, 1)
            act.wait_ge(cum_ready, 2)
            act.activation(kr[:, :, 0, :], flat(mem.sig), ACT.Exp, scale=-DECAY).then_inc(exped, 1)
            act.wait_ge(carry_ready, 1)
            act.activation(mem.carry[:, :, 0:3], mem.carry[:, :, 0:3], ACT.Exp, scale=-DECAY)

        @st.vector
        def _(dve):
            link = Chain(dve, own)
            ones = net.const(C_ONES)
            for t in range(4):
                dve.wait_ge(gated, t + 1)
                for c in range(NCH):
                    into, of = mem.cum[:, t, c, :], mem.sig[:, t, c, :]
                    if d:
                        into, of = into[:, ::-1], of[:, ::-1]
                    last = nc.vector.tensor_tensor_scan(into, ones, of, 0.0, ALU.mult, ALU.add)
            link(last)
            link(nc.vector.tensor_copy(mem.mid, mem.cum[:, :, :, mid]))
            link(nc.vector.tensor_copy(mem.end, mem.cum[:, :, :, end]))
            nc.vector.tensor_tensor(flat(mem.cum), flat(mem.cum),
                                    mem.mid.rearrange("p t c -> p (t c)").unsqueeze(2).to_broadcast([P, 16, CH]),
                                    ALU.subtract).then_inc(cum_ready, 1)
            dve.wait_ge(cum_ready, 1)
            nc.vector.tensor_tensor(flat(mem.sig), flat(mem.cum), flat(mem.sig), ALU.subtract).then_inc(cum_ready, 1)
            for j in range(3):
                c, after = order[j], order[j + 1]
                link(nc.vector.tensor_tensor(mem.carry[:, :, j], mem.end[:, :, c], mem.mid[:, :, c], ALU.subtract))
                step = nc.vector.tensor_tensor(mem.carry[:, :, j], mem.carry[:, :, j], mem.mid[:, :, after], ALU.add)
                step.then_inc(carry_ready, 1) if j == 2 else link(step)
            kr = mem.kr.rearrange("p t c n m -> p (t c) n m")
            dve.wait_ge(exped, 2)
            nc.vector.tensor_tensor(kr[:, :, 1, :], kr[:, :, 1, :], flat(mem.r), ALU.mult)
            link(nc.vector.tensor_tensor(flat(mem.kd), flat(mem.bd), flat(mem.k), ALU.mult))
            nc.vector.tensor_tensor(flat(mem.bd), flat(mem.bd), flat(mem.b), ALU.mult)
            dve.wait_ge(exped, 3)
            nc.vector.tensor_tensor(kr[:, :, 0, :], kr[:, :, 0, :], flat(mem.kk), ALU.mult)


def rwkv_chunks_stage(net, d):
    nc, mem = net.nc, RwkvMemory(net)
    order = [2, 3, 0, 1] if d == 0 else [3, 2, 1, 0]
    mask4 = net.const(C_MASK4 + 512 * d, 512)
    level_mask = lambda lv: net.const(C_LEVEL + P * (7 * d + lv)).unsqueeze(1).to_broadcast([P, 4, P])
    ident = net.const(C_IDENT)
    four = lambda bank: bank[:, :].rearrange("p (h m) -> p h m", m=P)
    head = lambda h: (h // 2, slice(64 * (h % 2), 64 * (h % 2) + 64))
    LV = range(1, 7)
    with Stage(net, f"rwkv_chunks{d}") as st:
        gram_ready, gram_masked = st.sem("gram_ready"), st.sem("gram_masked")
        start_ready, start_turned, start_copied = st.sem("start_ready"), st.sem("start_turned"), st.sem("start_copied")
        level_ready, y_ready, y_copied = st.sem("level_ready"), st.sem("y_ready"), st.sem("y_copied")
        dd_ready, doubled = st.sem("dd_ready"), st.sem("doubled")
        rhs_ready, rhs_copied, u_ready, u_copied = st.sem("rhs_ready"), st.sem("rhs_copied"), st.sem("u_ready"), st.sem("u_copied")
        tok_turned, tok_copied = st.sem("tok_turned"), st.sem("tok_copied")
        out_ready, out_taken, state_summed, state_ready = (st.sem("out_ready"), st.sem("out_taken"),
                                                           st.sem("state_summed"), st.sem("state_ready"))
        own, act_own = st.sem("dve_own"), st.sem("act_own")

        @st.tensor
        def _(pe):
            for j, c in enumerate(order):
                for h in range(8):
                    t, rows = head(h)
                    bank = net.ps[h % 2]
                    if 8 * j + h >= 2:
                        pe.wait_ge(gram_masked, 8 * j + h - 1)
                    if h < 2 and j:
                        pe.wait_ge(tok_copied, 2 * j)
                    nc.tensor.matmul(bank[:, 0:256], mem.bd[rows, t, c, :],
                                     mem.kr[rows, t, c].rearrange("p n m -> p (n m)"), start=True, stop=True)
                    nc.tensor.matmul(bank[:, 256:512], mem.kd[rows, t, c, :],
                                     mem.kr[rows, t, c].rearrange("p n m -> p (n m)"),
                                     start=True, stop=True).then_inc(gram_ready, 1)
                for q in range(2):
                    pe.wait_ge(start_ready, 2 * j + q + 1)
                    if j:
                        pe.wait_ge(out_taken, j)
                        pe.wait_ge(state_ready, j)
                    for h in range(4):
                        last = nc.tensor.transpose(net.ps[4 + q][:, P * h:P * h + P], mem.inv_t[:, q, h, :], ident)
                    last.then_inc(start_turned, 1)
                for lv in LV:
                    n = 12 * j + 2 * (lv - 1)
                    for q in range(2):
                        if lv == 1:
                            pe.wait_ge(start_copied, 2 * j + q + 1)
                        else:
                            pe.wait_ge(doubled, n - 2 + q + 1)
                        pe.wait_ge(level_ready, n + q + 1)
                        for h in range(4):
                            last = nc.tensor.matmul(four(net.ps[2 + q])[:, h, :], mem.level[:, q, h, :],
                                                    mem.inv[:, q, h, :], start=True, stop=True)
                        last.then_inc(y_ready, 1)
                    for q in range(2):
                        pe.wait_ge(y_copied, n + q + 1)
                        for h in range(4):
                            if lv < 6:
                                nc.tensor.matmul(four(net.ps[4 + q])[:, h, :], mem.inv_t[:, q, h, :],
                                                 mem.y[:, q, h, :], start=True, stop=True)
                            last = nc.tensor.matmul(four(net.ps[6 + q])[:, h, :], mem.y[:, q, h, :],
                                                    mem.inv_t[:, q, h, :], start=True, stop=True)
                        last.then_inc(dd_ready, 1)
                if j < 3:
                    pe.wait_ge(gram_masked, 8 * (j + 1))
                    for bank, part in ((net.ps[0], mem.bd), (net.ps[1], mem.kd)):
                        for t in range(4):
                            last = nc.tensor.transpose(bank[:, P * t:P * t + P], part[:, t, c, :], ident)
                        last.then_inc(tok_turned, 1)
                pe.wait_ge(y_copied, 12 * (j + 1))
                if j:
                    pe.wait_ge(state_ready, j)
                for h in range(8):
                    t, v = h // 2, slice(64 * h, 64 * h + 64)
                    if j and h % 2 == 0:
                        nc.tensor.matmul(net.ps[2][:, P * t:P * t + P], mem.kr[:, t, c, 0, :], mem.state[:, t, :],
                                         start=True, stop=False)
                    last = nc.tensor.matmul(net.ps[2][:, v], mem.gram[:, h, 256:384], mem.vtok[:, c, v],
                                            start=(j == 0), stop=(j == 0 or h % 2 == 1))
                last.then_inc(rhs_ready, 1)
                pe.wait_ge(rhs_copied, j + 1)
                pe.wait_ge(doubled, 12 * (j + 1))
                for h in range(8):
                    last = nc.tensor.matmul(net.ps[3][:, 64 * h:64 * h + 64], mem.inv_t[:, h // 4, h % 4, :],
                                            mem.rhs[:, 64 * h:64 * h + 64], start=True, stop=True)
                last.then_inc(u_ready, 1)
                pe.wait_ge(u_copied, j + 1)
                if j < 3:
                    pe.wait_ge(tok_copied, 2 * (j + 1))
                    for h in range(8):
                        t, rows = head(h)
                        into, v = net.ps[5][rows, 64 * t:64 * t + 64], slice(64 * h, 64 * h + 64)
                        nc.tensor.matmul(into, mem.ktok[:, v], mem.vtok[:, c, v], start=True, stop=False)
                        last = nc.tensor.matmul(into, mem.btok[:, v], mem.minus_u[:, v], start=False, stop=True)
                    last.then_inc(state_summed, 1)
                for h in range(8):
                    t, rows = head(h)
                    into, v = net.ps[4][rows, P * t:P * t + P], slice(64 * h, 64 * h + 64)
                    if j and h % 2 == 0:
                        nc.tensor.matmul(net.ps[4][:, P * t:P * t + P], mem.state[:, t, :], mem.kr[:, t, c, 1, :],
                                         start=True, stop=False)
                    nc.tensor.matmul(into, mem.vtok[:, c, v], mem.gram[:, h, 384:512], start=(j == 0), stop=False)
                    last = nc.tensor.matmul(into, mem.minus_u[:, v], mem.gram[:, h, 128:256], start=False, stop=True)
                last.then_inc(out_ready, 1)

        @st.gpsimd
        def _(pool):
            for j in range(NCH):
                for lv in LV:
                    n = 12 * j + 2 * (lv - 1)
                    for q in range(2):
                        if lv == 1:
                            pool.wait_ge(gram_masked, 8 * j + 4 * (q + 1))
                            if j:
                                pool.wait_ge(y_ready, 12 * j)
                        else:
                            pool.wait_ge(y_ready, n - 2 + q + 1)
                        pool.tensor_tensor(mem.level[:, q], mem.gram[:, 4 * q:4 * q + 4, 0:P], level_mask(lv),
                                           ALU.mult).then_inc(level_ready, 1)

        @st.scalar
        def _(act):
            for j in range(NCH):
                for q in range(2):
                    act.wait_ge(start_turned, 2 * j + q + 1)
                    act.activation(mem.inv[:, q], four(net.ps[4 + q]), ACT.Copy).then_inc(start_copied, 1)
                for lv in LV:
                    n = 12 * j + 2 * (lv - 1)
                    for q in range(2):
                        act.wait_ge(y_ready, n + q + 1)
                        if n + q >= 2:
                            act.wait_ge(dd_ready, n + q - 1)
                        act.activation(mem.y[:, q], four(net.ps[2 + q]), ACT.Copy).then_inc(y_copied, 1)
                if j < 3:
                    for n, (bank, part) in enumerate(((net.ps[0], mem.btok), (net.ps[1], mem.ktok))):
                        act.wait_ge(tok_turned, 2 * j + n + 1)
                        if j:
                            act.wait_ge(state_summed, j)
                        act.activation(part, bank[:, :], ACT.Copy).then_inc(tok_copied, 1)
                act.wait_ge(rhs_ready, j + 1)
                act.activation(mem.rhs, net.ps[2][:, :], ACT.Copy).then_inc(rhs_copied, 1)

        @st.vector
        def _(dve):
            link = Chain(dve, own)
            for j, c in enumerate(order):
                for h in range(8):
                    dve.wait_ge(gram_ready, 8 * j + h + 1)
                    if j and h == 0:
                        dve.wait_ge(out_ready, j)
                        dve.wait_ge(level_ready, 12 * j)
                    nc.vector.tensor_tensor(mem.gram[:, h, :], net.ps[h % 2][:, :], mask4, ALU.mult).then_inc(gram_masked, 1)
                    if h % 4 == 3:
                        q = h // 4
                        dve.wait_ge(gram_masked, 8 * j + h + 1)
                        link(nc.vector.tensor_tensor(mem.inv_t[:, q], mem.gram[:, 4 * q:4 * q + 4, 0:P], level_mask(0),
                                                     ALU.mult))
                        nc.vector.tensor_tensor(mem.inv_t[:, q], ident.unsqueeze(1).to_broadcast([P, 4, P]),
                                                mem.inv_t[:, q], ALU.subtract).then_inc(start_ready, 1)
                for lv in LV:
                    n = 12 * j + 2 * (lv - 1)
                    for q in range(2):
                        dve.wait_ge(dd_ready, n + q + 1)
                        if lv < 6:
                            link(nc.vector.tensor_tensor(mem.inv[:, q], mem.inv[:, q], four(net.ps[4 + q]), ALU.subtract))
                        nc.vector.tensor_tensor(mem.inv_t[:, q], mem.inv_t[:, q], four(net.ps[6 + q]),
                                                ALU.subtract).then_inc(doubled, 1)
                dve.wait_ge(u_ready, j + 1)
                nc.vector.tensor_scalar(mem.minus_u, net.ps[3][:, :], -1.0, None, ALU.mult).then_inc(u_copied, 1)
                if j < 3:
                    sums = net.ps[5][:, 0:256].rearrange("p (t m) -> p t m", m=64)
                    carry = mem.carry[:, :, j].unsqueeze(2).to_broadcast([P, 4, P])
                    dve.wait_ge(state_summed, j + 1)
                    dve.wait_ge(out_ready, j + 1)
                    if j == 0:
                        link(nc.vector.memset(mem.state, 0.0))
                    for o in (0, 64):
                        block = mem.state[o:o + 64, :, o:o + 64]
                        link(nc.vector.tensor_tensor(block, block, sums[o:o + 64], ALU.add))
                    nc.vector.tensor_tensor(mem.state, mem.state, carry, ALU.mult).then_inc(state_ready, 1)
                dve.wait_ge(out_ready, j + 1)
                if d == 0:
                    nc.vector.tensor_copy(mem.out[:, :, c, :], four(net.ps[4])).then_inc(out_taken, 1)
                else:
                    nc.vector.tensor_tensor(mem.out[:, :, c, :], mem.out[:, :, c, :], four(net.ps[4]),
                                            ALU.add).then_inc(out_taken, 1)


def rwkv_finish_stage(net):
    nc, eps = net.nc, 64e-5
    y = net.OT[:, 4:8, :]
    r, k, v = net.PT[:, 12:16, :], net.PT[:, 16:20, :], net.PT[:, 20:24, :]
    rk = net.PT[:, 0:4, :]
    square = net.PT[:, 4:8, :]
    rstd = net.PT[:, 8:12, :]
    with Stage(net, "rwkv_finish") as st:
        rk_ready, bonus_ready, gate_ready = st.sem("rk_ready"), st.sem("bonus_ready"), st.sem("gate_ready")
        mean_ready, centred, squared, var_ready = (st.sem("mean_ready"), st.sem("centred"), st.sem("squared"),
                                                   st.sem("var_ready"))
        var_copied, root_ready, own = st.sem("var_copied"), st.sem("root_ready"), st.sem("dve_own")
        bonus_used = st.sem("bonus_used")

        @st.gpsimd
        def _(pool):
            pool.tensor_tensor(rk[:, :, :], r, k, ALU.mult).then_inc(rk_ready, 1)

        @st.tensor
        def _(pe):
            for t in range(4):
                nc.tensor.matmul(net.ps[t][:, :], net.const(C_BLK), y[:, t, :], start=True, stop=True).then_inc(mean_ready, 1)
            for t in range(4):
                pe.wait_ge(squared, t + 1)
                nc.tensor.matmul(net.ps[4 + t][:, :], net.const(C_BLK), square[:, t, :], start=True,
                                 stop=True).then_inc(var_ready, 1)
            pe.wait_ge(centred, 4)
            pe.wait_ge(rk_ready, 5)
            for t in range(4):
                nc.tensor.matmul(net.ps[t][:, :], net.const(C_BLK), rk[:, t, :], start=True, stop=True).then_inc(bonus_ready, 1)
            for t in range(4):
                pe.wait_ge(var_copied, t + 1)
                nc.tensor.matmul(net.ps[4 + t][:, :], net.G2[:, P * t:P * t + P], net.PT[:, 25, :], start=True,
                                 stop=True).then_inc(gate_ready, 1)

        @st.scalar
        def _(act):
            act.wait_ge(rk_ready, 1)
            for t in range(4):
                act.activation(rk[:, t, :], rk[:, t, :], ACT.Copy, scale=net.par("l0_r_k", t)).then_inc(rk_ready, 1)
            for t in range(4):
                act.wait_ge(centred, t + 1)
                act.activation(square[:, t, :], y[:, t, :], ACT.Square).then_inc(squared, 1)
            for t in range(4):
                act.wait_ge(var_copied, t + 1)
                act.activation(rstd[:, t, :], rstd[:, t, :], ACT.Sqrt).then_inc(root_ready, 1)

        @st.vector
        def _(dve):
            link = Chain(dve, own)
            for t in range(4):
                dve.wait_ge(mean_ready, t + 1)
                nc.vector.scalar_tensor_tensor(y[:, t, :], net.ps[t][:, :], -1.0 / 64, y[:, t, :], ALU.mult,
                                               ALU.add).then_inc(centred, 1)
            for t in range(4):
                dve.wait_ge(var_ready, t + 1)
                nc.vector.tensor_scalar(rstd[:, t, :], net.ps[4 + t][:, :], 1.0 / 64, eps, ALU.mult,
                                        ALU.add).then_inc(var_copied, 1)
            dve.wait_ge(squared, 4)
            for t in range(4):
                dve.wait_ge(root_ready, t + 1)
                link(nc.vector.reciprocal(rstd[:, t, :], rstd[:, t, :]))
                link(nc.vector.tensor_tensor(y[:, t, :], y[:, t, :], rstd[:, t, :], ALU.mult))
                link(nc.vector.tensor_scalar(y[:, t, :], y[:, t, :], net.par("l0_lnx_w", t), net.par("l0_lnx_b", t),
                                             ALU.mult, ALU.add))
                dve.wait_ge(bonus_ready, t + 1)
                link(nc.vector.tensor_tensor(rstd[:, t, :], net.ps[t][:, :], v[:, t, :], ALU.mult))
                link(nc.vector.tensor_tensor(y[:, t, :], y[:, t, :], rstd[:, t, :], ALU.add))
                dve.wait_ge(gate_ready, t + 1)
                link(nc.vector.tensor_tensor(y[:, t, :], y[:, t, :], net.ps[4 + t][:, :], ALU.mult))


def odd_projection(w):
    starts = [0, 256, 512, 768, 1024, 1280, 1552, 1808, 2064, 2320, 2576, 2832]
    views = [w[:, c:c + SW].rearrange("(t k) m -> k t m", k=P) for c in starts]
    latents_only = {0, 1, 5, 6, 10, 11}
    return (Weights(3, 0, lambda i, s: views[SLOTS * i + s]),
            lambda i, s: LAT if SLOTS * i + s in latents_only else TOK)


class SsdMemory:

    def __init__(self, net):
        sc = net.SC
        self.gate_down = sc[0:16, 0:512]
        (self.dt, self.la, self.cum, self.tot, self.to_end, self.e_cum, self.e_tot, self.x, self.e, self.s, self.s2,
         self.poly) = (sc[:, 512 + 64 * n:576 + 64 * n].rearrange("p (c h) -> p c h", h=16) for n in range(12))
        self.e_a = sc[:, 1280:1296]
        self.acc = sc[:, 1600:2624].rearrange("p (b m) -> p b m", m=TOK)
        self.xdt = sc[:, 1600:3648].rearrange("p (c d m) -> p c d m", c=2, d=2)
        self.state = sc[:, 3648:4672].rearrange("p (d m) -> p d m", d=2)
        self.cb = sc[:, 4672:5184].rearrange("p (d g m) -> p d g m", d=2, g=2)
        self.y = sc[:, 5184:6208].rearrange("p (c m) -> p c m", c=2)
        self.part = sc[:, 6208:6720]
        ht = net.HT[:, :, :].rearrange("p t m -> p (t m)")
        self.xtok = ht[:, 0:2048].rearrange("p (c m) -> p c m", c=NCH)
        self.btok = ht[:, 2048:3072].rearrange("p (c m) -> p c m", c=NCH)
        self.xw = ht[:, 3072:4096].rearrange("p (d m) -> p d m", d=2)
        self.att = net.PT[:, 24:32, :].rearrange("p (c t) (h m) -> p c (t h) m", c=2, m=P)


def ssd_steps_stage(net):
    nc, mem = net.nc, SsdMemory(net)
    with Stage(net, "ssd_steps") as st:
        dt_raw, down_ready, own, act_own = st.sem("dt_raw"), st.sem("down_ready"), st.sem("dve_own"), st.sem("act_own")
        abs_ready, e_ready, la_ready, cum_summed = (st.sem("abs_ready"), st.sem("e_ready"), st.sem("la_ready"),
                                                    st.sem("cum_summed"))
        cum_ready, e_a_ready = st.sem("cum_ready"), st.sem("e_a_ready")
        all_of = lambda v: v.rearrange("p c h -> p (c h)")
        per_head = lambda v: v.unsqueeze(1).to_broadcast([P, NCH, 16])

        @st.tensor
        def _(pe):
            for c in range(NCH):
                for kt in range(KT):
                    last = nc.tensor.matmul(net.ps[0][:, 16 * c:16 * c + 16], net.HT[:, kt, CH * c:CH * c + CH],
                                            net.WDG[:, kt, 0:16], start=(kt == 0), stop=(kt == KT - 1))
            last.then_inc(dt_raw, 1)
            for kt in range(KT):
                last = nc.tensor.matmul(net.ps[1][0:16, :], net.WDG[:, kt, 16:32], net.HT[:, kt, :],
                                        start=(kt == 0), stop=(kt == KT - 1))
            last.then_inc(down_ready, 1)
            pe.wait_ge(la_ready, 1)
            for c in range(NCH):
                for d, tri in enumerate((C_LE, C_GE)):
                    nc.tensor.matmul(net.ps[2][:, 16 * c + 8 * d:16 * c + 8 * d + 8], net.const(tri),
                                     mem.la[:, c, 8 * d:8 * d + 8], start=True, stop=True)
            nc.tensor.matmul(net.ps[3][:, 0:64], net.const(C_ONES), all_of(mem.la), start=True,
                             stop=True).then_inc(cum_summed, 1)

        @st.scalar
        def _(act):
            act.activation(mem.e_a, net.HEADROW[:, 16:32], ACT.Exp).then_inc(e_a_ready, 1)
            act.wait_ge(abs_ready, 1)
            act.activation(mem.e, mem.e, ACT.Exp, scale=-1.0).then_inc(e_ready, 1)
            act.wait_ge(down_ready, 1)
            act.activation(mem.gate_down, net.ps[1][0:16, :], ACT.Copy)
            act.wait_ge(cum_ready, 1)
            for into, of in ((mem.e_cum, mem.cum), (mem.e_tot, mem.tot), (mem.to_end, mem.to_end)):
                act.activation(into, of, ACT.Exp)

        @st.vector
        def _(dve):
            link = Chain(dve, own)
            raw = net.ps[0][:, 0:64].rearrange("p (c h) -> p c h", h=16)
            dve.wait_ge(dt_raw, 1)
            link(nc.vector.tensor_tensor(mem.x, raw, per_head(net.HEADROW[:, 0:16]), ALU.add))
            link(nc.vector.tensor_scalar(mem.s, mem.x, -1.0, None, ALU.mult))
            nc.vector.tensor_tensor(mem.e, mem.x, mem.s, ALU.max).then_inc(abs_ready, 1)
            dve.wait_ge(e_ready, 1)
            link(nc.vector.tensor_scalar(mem.s, mem.e, 2.0, None, ALU.add))
            link(nc.vector.reciprocal(mem.s, mem.s))
            link(nc.vector.tensor_tensor(mem.s, mem.s, mem.e, ALU.mult))
            link(nc.vector.tensor_tensor(mem.s2, mem.s, mem.s, ALU.mult))
            link(nc.vector.tensor_scalar(mem.poly, mem.s2, 1.0 / 15, None, ALU.mult))
            for odd in (13, 11, 9, 7, 5, 3):
                link(nc.vector.scalar_tensor_tensor(mem.poly, mem.poly, 1.0 / odd, mem.s2, ALU.add, ALU.mult))
            link(nc.vector.scalar_tensor_tensor(mem.poly, mem.poly, 1.0, mem.s, ALU.add, ALU.mult))
            link(nc.vector.tensor_scalar(mem.x, mem.x, 0.0, None, ALU.max))
            link(nc.vector.scalar_tensor_tensor(mem.dt, mem.poly, 2.0, mem.x, ALU.mult, ALU.add))
            dve.wait_ge(e_a_ready, 1)
            nc.vector.scalar_tensor_tensor(mem.la, mem.dt, -1.0, per_head(mem.e_a), ALU.mult, ALU.mult).then_inc(la_ready, 1)
            dve.wait_ge(cum_summed, 1)
            link(nc.vector.tensor_copy(all_of(mem.cum), net.ps[2][:, 0:64]))
            link(nc.vector.tensor_copy(all_of(mem.tot), net.ps[3][:, 0:64]))
            nc.vector.tensor_tensor(mem.to_end, mem.tot, mem.cum, ALU.subtract).then_inc(cum_ready, 1)


def ssd_conv_stage(net):
    nc, mem = net.nc, SsdMemory(net)
    with Stage(net, "ssd_conv") as st:
        summed, silu_ready, turned, own = st.sem("summed"), st.sem("silu_ready"), st.sem("turned"), st.sem("dve_own")

        @st.vector
        def _(dve):
            link = Chain(dve, own)
            for t in range(8):
                n = TOK if t < 6 else LAT
                x = net.PT[:, 4 + t, 0:n].rearrange("p (s m) -> p s m", m=LAT)
                acc = mem.acc[:, t % 2, 0:n].rearrange("p (s m) -> p s m", m=LAT)
                if t >= 2:
                    dve.wait_ge(silu_ready, t - 1)
                tap = lambda k: net.par("l1_conv_w", 8 * k + t)
                link(nc.vector.tensor_scalar(acc, x, tap(2), None, ALU.mult))
                for k in (0, 1, 3, 4):
                    o = k - 2
                    to, of = slice(max(0, -o), LAT - max(0, o)), slice(max(0, o), LAT - max(0, -o))
                    step = nc.vector.scalar_tensor_tensor(acc[:, :, to], x[:, :, of], tap(k), acc[:, :, to],
                                                          ALU.mult, ALU.add)
                    step.then_inc(summed, 1) if k == 4 else link(step)

        @st.scalar
        def _(act):
            for t in range(8):
                n = TOK if t < 6 else LAT
                act.wait_ge(summed, t + 1)
                act.activation(net.PT[:, 4 + t, 0:n], mem.acc[:, t % 2, 0:n], ACT.Silu,
                               bias=net.par("l1_conv_b", t)).then_inc(silu_ready, 1)
            for c in range(NCH):
                act.wait_ge(turned, 2 * c + 1)
                act.activation(mem.xtok[:, c, :], net.ps[2 * c][:, :], ACT.Copy)
                act.wait_ge(turned, 2 * c + 2)
                act.activation(mem.btok[:, c, :], net.ps[2 * c + 1][:, 0:256], ACT.Copy)

        @st.tensor
        def _(pe):
            pe.wait_ge(silu_ready, 6)
            for c in range(NCH):
                for n, (first, count) in enumerate(((4, 4), (8, 2))):
                    for t in range(count):
                        last = nc.tensor.transpose(net.ps[2 * c + n][:, P * t:P * t + P],
                                                   net.PT[:, first + t, CH * c:CH * c + CH], net.const(C_IDENT))
                    last.then_inc(turned, 1)


def ssd_scan_stage(net):
    nc, mem = net.nc, SsdMemory(net)
    heads = lambda v: v.rearrange("p (h m) -> p h m", m=64)
    wide = lambda v: v.unsqueeze(2).to_broadcast([P, 8, 64])
    updates = [(0, 2), (1, 3), (0, 3), (1, 2), (0, 0), (1, 1)]
    serves = {2: (0, 0), 3: (1, 1), 4: (0, 1), 5: (1, 0)}
    with Stage(net, "ssd_scan") as st:
        row_ready, row_used, exp_ready, att_ready = (st.sem("row_ready"), st.sem("row_used"), st.sem("exp_ready"),
                                                     st.sem("att_ready"))
        cb_ready, cb_masked, xdt_ready = st.sem("cb_ready"), st.sem("cb_masked"), st.sem("xdt_ready")
        y_ready, xw_ready, state_summed, state_ready = (st.sem("y_ready"), st.sem("xw_ready"), st.sem("state_summed"),
                                                        st.sem("state_ready"))
        served, served_used, own = st.sem("served"), st.sem("served_used"), st.sem("dve_own")

        @st.tensor
        def _(pe):
            for c in range(2):
                for n in range(4):
                    at = 4 * c + n
                    if at >= 2:
                        pe.wait_ge(row_used, at - 1)
                    for h in range(4 * n, 4 * n + 4):
                        last = nc.tensor.matmul(net.ps[at % 2][:, P * (h % 4):P * (h % 4) + P],
                                                mem.la[:, c, h:h + 1].to_broadcast([P, P]),
                                                net.const(C_LE if h < 8 else C_GE), start=True, stop=True)
                    last.then_inc(row_ready, 1)
                for g in range(2):
                    last = nc.tensor.matmul(net.ps[2 + c][:, P * g:P * g + P], net.PT[:, 8 + g, CH * c:CH * c + CH],
                                            net.PT[:, 10 + g, CH * c:CH * c + CH], start=True, stop=True)
                last.then_inc(cb_ready, 1)
            for n, (d, c) in enumerate(updates):
                pe.wait_ge(xw_ready, n + 1)
                if n >= 2:
                    pe.wait_ge(state_ready, n - 1)
                for g in range(2):
                    last = nc.tensor.matmul(net.ps[6 + d][:, 256 * g:256 * g + 256], mem.btok[:, c, P * g:P * g + P],
                                            mem.xw[:, d, 256 * g:256 * g + 256], start=True, stop=True)
                last.then_inc(state_summed, 1)
                if n < 2:
                    continue
                if n >= 4:
                    pe.wait_ge(served_used, n - 3)
                pe.wait_ge(state_ready, n + 1 if n < 4 else n + 1)
                to = serves[n][1]
                for g in range(2):
                    last = nc.tensor.matmul(net.ps[n % 2][:, 256 * g:256 * g + 256],
                                            net.PT[:, 10 + g, CH * to:CH * to + CH],
                                            mem.state[:, d, 256 * g:256 * g + 256], start=True, stop=True)
                last.then_inc(served, 1)
            pe.wait_ge(xdt_ready, 4)
            for c in range(2):
                pe.wait_ge(att_ready, 4 * (c + 1))
                for h in range(8):
                    v = slice(64 * h, 64 * h + 64)
                    for d in range(2):
                        last = nc.tensor.matmul(net.ps[4 + c][:, v], mem.att[:, c, 8 * d + h, :], mem.xdt[:, c, d, v],
                                                start=(d == 0), stop=(d == 1))
                last.then_inc(y_ready, 1)

        @st.gpsimd
        def _(pool):
            for c in range(2):
                for d in range(2):
                    pool.tensor_tensor(heads(mem.xdt[:, c, d, :]), heads(mem.xtok[:, c, :]),
                                       wide(mem.dt[:, c, 8 * d:8 * d + 8]), ALU.mult).then_inc(xdt_ready, 1)

        @st.scalar
        def _(act):
            for c in range(2):
                act.wait_ge(row_used, 4 * (c + 1))
                act.activation(mem.att[:, c], mem.att[:, c], ACT.Exp).then_inc(exp_ready, 1)

        @st.vector
        def _(dve):
            link = Chain(dve, own)
            link(nc.vector.tensor_tensor(mem.to_end, mem.to_end, mem.dt, ALU.mult))
            for c in range(2):
                for n in range(4):
                    dve.wait_ge(row_ready, 4 * c + n + 1)
                    for h in range(4 * n, 4 * n + 4):
                        last = nc.vector.tensor_scalar(mem.att[:, c, h, :],
                                                       net.ps[(4 * c + n) % 2][:, P * (h % 4):P * (h % 4) + P],
                                                       mem.cum[:, c, h:h + 1], 0.0, ALU.subtract, ALU.min)
                    last.then_inc(row_used, 1)
            for n, (d, c) in enumerate(updates):
                if n >= 2:
                    dve.wait_ge(state_summed, n - 1)
                nc.vector.tensor_tensor(heads(mem.xw[:, d, :]), heads(mem.xtok[:, c, :]),
                                        wide(mem.to_end[:, c, 8 * d:8 * d + 8]), ALU.mult).then_inc(xw_ready, 1)
                dve.wait_ge(state_summed, n + 1)
                if n < 2:
                    nc.vector.tensor_copy(mem.state[:, d, :], net.ps[6 + d][:, :]).then_inc(state_ready, 1)
                else:
                    if n >= 4:
                        dve.wait_ge(served, n - 3)
                    dve.wait_ge(state_ready, n)
                    link(nc.vector.tensor_tensor(heads(mem.state[:, d, :]), heads(mem.state[:, d, :]),
                                                 wide(mem.e_tot[:, c, 8 * d:8 * d + 8]), ALU.mult))
                    nc.vector.tensor_tensor(mem.state[:, d, :], mem.state[:, d, :], net.ps[6 + d][:, :],
                                            ALU.add).then_inc(state_ready, 1)
                    to = serves[n][1]
                    dve.wait_ge(served, n - 1)
                    into = mem.y[:, to, :] if n < 4 else mem.part
                    step = nc.vector.tensor_tensor(heads(into), heads(net.ps[n % 2][:, :]),
                                                   wide(mem.e_cum[:, to, 8 * d:8 * d + 8]), ALU.mult)
                    step.then_inc(served_used, 1)
                    dve.wait_ge(served_used, n - 1)
                    if n >= 4:
                        link(nc.vector.tensor_tensor(mem.y[:, to, :], mem.y[:, to, :], mem.part, ALU.add))
            for c in range(2):
                dve.wait_ge(cb_ready, c + 1)
                for d, tri in enumerate((C_LE, C_GE)):
                    if c:
                        dve.wait_ge(att_ready, 4)
                    for g in range(2):
                        link(nc.vector.tensor_tensor(mem.cb[:, d, g, :], net.ps[2 + c][:, P * g:P * g + P],
                                                     net.const(tri), ALU.mult))
                dve.wait_ge(exp_ready, c + 1)
                for d in range(2):
                    for g in range(2):
                        four = mem.att[:, c, 8 * d + 4 * g:8 * d + 4 * g + 4, :]
                        nc.vector.tensor_tensor(four, four, mem.cb[:, d, g, :].unsqueeze(1).to_broadcast([P, 4, P]),
                                                ALU.mult).then_inc(att_ready, 1)
            for c in range(2):
                dve.wait_ge(y_ready, c + 1)
                link(nc.vector.tensor_tensor(mem.y[:, c, :], mem.y[:, c, :], net.ps[4 + c][:, :], ALU.add))


def ssd_gate_stage(net):
    nc, mem = net.nc, SsdMemory(net)
    with Stage(net, "ssd_gate") as st:
        turned, z_ready, own = st.sem("turned"), st.sem("z_ready"), st.sem("dve_own")

        @st.tensor
        def _(pe):
            for t in range(4):
                for c in range(2):
                    last = nc.tensor.transpose(net.ps[t][:, P * c:P * c + P], mem.y[:, c, P * t:P * t + P],
                                               net.const(C_IDENT))
                last.then_inc(turned, 1)

        @st.scalar
        def _(act):
            act.activation(net.PT[:, 0:4, 0:LAT], net.PT[:, 0:4, 0:LAT], ACT.Silu).then_inc(z_ready, 1)

        @st.vector
        def _(dve):
            link = Chain(dve, own)
            dve.wait_ge(z_ready, 1)
            for t in range(4):
                dve.wait_ge(turned, t + 1)
                link(nc.vector.scalar_tensor_tensor(net.OT[:, t, 0:LAT], net.PT[:, 4 + t, 0:LAT], net.DSKIP[:, t:t + 1],
                                                    net.ps[t][:, 0:LAT], ALU.mult, ALU.add))
                link(nc.vector.tensor_tensor(net.OT[:, t, 0:LAT], net.OT[:, t, 0:LAT], net.PT[:, t, 0:LAT], ALU.mult))


class GlaMemory:

    def __init__(self, net):
        sc = net.SC
        self.gate_down = sc[0:16, 0:512]
        self.cum = sc[:, 512:2560].rearrange("p (d t c m) -> p d t c m", d=2, t=2, c=NCH)
        lat = lambda at: sc[:, at:at + 1024].rearrange("p (d t c m) -> p d t c m", d=2, t=2, c=2)
        self.q_in, self.k_in, self.q_state = lat(2560), lat(3584), lat(4608)
        half = lambda at: sc[:, at:at + 512].rearrange("p (d t c m) -> p d t c m", d=2, t=2, c=2)
        self.q_cross, self.k_cross = half(5632), half(6144)
        self.e_end = sc[:, 6656:6672].rearrange("p (d t c) -> p d t c", d=2, t=2)
        ht = net.HT[:, :, :].rearrange("p t m -> p (t m)")
        self.k_end = ht[:, 0:2048].rearrange("p (d t c m) -> p d t c m", d=2, t=2, c=NCH)
        self.vtok = ht[:, 2048:4096].rearrange("p (c m) -> p c m", c=NCH)
        pt = net.PT[:, 0:12, :].rearrange("p t m -> p (t m)")
        self.gate = pt[:, 0:2048].rearrange("p (d t m) -> p d t m", d=2, t=2)
        self.low = pt[:, 2048:4096].rearrange("p (d t m) -> p d t m", d=2, t=2)
        self.shift = pt[:, 4096:6144].rearrange("p (d t c m) -> p d t c m", d=2, t=2, c=NCH)
        pt = net.PT[:, 24:32, :].rearrange("p t m -> p (t m)")
        self.att = pt[:, 0:2048].rearrange("p (d c h m) -> p d c h m", d=2, c=2, h=4)
        self.state = pt[:, 2048:3072].rearrange("p (d c t m) -> p d c t m", d=2, c=2, t=2)
        self.ktok = pt[:, 3072:4096].rearrange("p (b m) -> p b m", b=4)


def gla_gates_stage(net):
    nc, mem = net.nc, GlaMemory(net)
    q, k = (net.PT[:, n:n + 2, :].rearrange("p t (c m) -> p t c m", m=CH) for n in (12, 14))
    tau = 1.0 / 16.0
    with Stage(net, "gla_gates") as st:
        gate_raw, low_ready, log_ready, turned = (st.sem("gate_raw"), st.sem("low_ready"), st.sem("log_ready"),
                                                  st.sem("turned"))
        own, act_own, shifted, exped = st.sem("dve_own"), st.sem("act_own"), st.sem("shifted"), st.sem("exped")

        @st.tensor
        def _(pe):
            for d in range(2):
                for t in range(2):
                    nc.tensor.matmul(net.ps[2 * d + t][:, :], net.GUP[:, d, P * t:P * t + P], mem.gate_down,
                                     start=True, stop=True).then_inc(gate_raw, 1)
            for c in range(NCH):
                for t in range(4):
                    last = nc.tensor.transpose(net.ps[4 + c][:, P * t:P * t + P], net.PT[:, 16 + t, CH * c:CH * c + CH],
                                               net.const(C_IDENT))
                last.then_inc(turned, 1)

        @st.scalar
        def _(act):
            link = Chain(act, act_own)
            bias = lambda d, t: net.par("l1_gk_b_f" if d == 0 else "l1_gk_b_b", t)
            every = mem.gate.rearrange("p d t m -> p (d t m)")
            for d in range(2):
                for t in range(2):
                    act.wait_ge(gate_raw, 2 * d + t + 1)
                    link(act.activation(mem.gate[:, d, t, :], net.ps[2 * d + t][:, :], ACT.Abs, bias=bias(d, t)))
            link(act.activation(every, every, ACT.Exp, scale=-1.0))
            act.activation(every, every, ACT.Ln, bias=1.0).then_inc(log_ready, 1)
            act.activation(net.PT[:, 20:24, 0:LAT], net.PT[:, 20:24, 0:LAT], ACT.Silu)
            for c in range(NCH):
                act.wait_ge(turned, c + 1)
                act.activation(mem.vtok[:, c, :], net.ps[4 + c][:, :], ACT.Copy)
            for d in range(2):
                qh, kh = ((64, 0), (0, 64))[d]
                lat = mem.shift[:, d, :, 0:2, :]
                act.wait_ge(shifted, 4 * d + 1)
                for t in range(2):
                    act.activation(mem.q_in[:, d, t], lat[:, t], ACT.Exp, scale=tau)
                    act.activation(mem.k_in[:, d, t], lat[:, t], ACT.Exp, scale=-tau).then_inc(exped, 1)
                act.wait_ge(shifted, 4 * d + 2)
                for t in range(2):
                    act.activation(mem.q_cross[:, d, t], lat[:, t, :, qh:qh + 64], ACT.Exp, scale=tau)
                    act.activation(mem.k_cross[:, d, t], lat[:, t, :, kh:kh + 64], ACT.Exp, scale=-tau).then_inc(exped, 1)
                act.wait_ge(shifted, 4 * d + 3)
                for t in range(2):
                    act.activation(mem.k_end[:, d, t], mem.shift[:, d, t], ACT.Exp, scale=-tau)
                    act.activation(mem.q_state[:, d, t], mem.cum[:, d, t, 0:2], ACT.Exp, scale=tau).then_inc(exped, 1)
                act.wait_ge(shifted, 4 * d + 4)
                act.activation(mem.e_end[:, d], mem.e_end[:, d], ACT.Exp, scale=tau)

        @st.vector
        def _(dve):
            link = Chain(dve, own)
            ones = net.const(C_ONES)
            for d in range(2):
                for t in range(2):
                    dve.wait_ge(gate_raw, 2 * d + t + 1)
                    dve.wait_ge(act_own, 2 * d + t + 1)
                    nc.vector.tensor_scalar(mem.low[:, d, t, :], net.ps[2 * d + t][:, :],
                                            net.par("l1_gk_b_f" if d == 0 else "l1_gk_b_b", t), 0.0, ALU.add,
                                            ALU.min).then_inc(low_ready, 1)
            dve.wait_ge(low_ready, 4)
            dve.wait_ge(log_ready, 1)
            link(nc.vector.tensor_tensor(mem.low, mem.low, mem.gate, ALU.subtract))
            for d in range(2):
                for t in range(2):
                    for c in range(NCH):
                        into, of = mem.cum[:, d, t, c, :], mem.low[:, d, t, CH * c:CH * c + CH]
                        if d:
                            into, of = into[:, ::-1], of[:, ::-1]
                        last = nc.vector.tensor_tensor_scan(into, ones, of, 0.0, ALU.mult, ALU.add)
            link(last)
            clamp = GLA_CLAMP / tau
            for d in range(2):
                qh, kh = ((64, 0), (0, 64))[d]
                cum, shift = mem.cum[:, d], mem.shift[:, d]
                mids, edge, end = (((31, 95), 63, CH - 1), ((32, 96), 64, 0))[d]
                for t in range(2):
                    for h in range(2):
                        part = slice(64 * h, 64 * h + 64)
                        link(nc.vector.tensor_tensor(shift[:, t, 0:2, part], cum[:, t, 0:2, part],
                                                     cum[:, t, 0:2, mids[h]:mids[h] + 1].to_broadcast([P, 2, 64]),
                                                     ALU.subtract))
                step = nc.vector.tensor_scalar(shift[:, :, 0:2, :], shift[:, :, 0:2, :], clamp, -clamp, ALU.min, ALU.max)
                step.then_inc(shifted, 1)
                dve.wait_ge(exped, 6 * d + 2)
                for t in range(2):
                    link(nc.vector.scalar_tensor_tensor(mem.q_in[:, d, t], mem.q_in[:, d, t], 0.125, q[:, t, 0:2],
                                                        ALU.mult, ALU.mult))
                    link(nc.vector.tensor_tensor(mem.k_in[:, d, t], mem.k_in[:, d, t], k[:, t, 0:2], ALU.mult))
                    step = nc.vector.tensor_tensor(shift[:, t, 0:2, :], cum[:, t, 0:2, :],
                                                   cum[:, t, 0:2, edge:edge + 1].to_broadcast([P, 2, CH]), ALU.subtract)
                    link(step) if t == 0 else step.then_inc(shifted, 1)
                dve.wait_ge(exped, 6 * d + 4)
                for t in range(2):
                    link(nc.vector.scalar_tensor_tensor(mem.q_cross[:, d, t], mem.q_cross[:, d, t], 0.125,
                                                        q[:, t, 0:2, qh:qh + 64], ALU.mult, ALU.mult))
                    link(nc.vector.tensor_tensor(mem.k_cross[:, d, t], mem.k_cross[:, d, t], k[:, t, 0:2, kh:kh + 64],
                                                 ALU.mult))
                    step = nc.vector.tensor_tensor(shift[:, t], cum[:, t],
                                                   cum[:, t, :, end:end + 1].to_broadcast([P, NCH, CH]), ALU.subtract)
                    link(step) if t == 0 else step.then_inc(shifted, 1)
                nc.vector.tensor_copy(mem.e_end[:, d], cum[:, :, :, end]).then_inc(shifted, 1)
                dve.wait_ge(exped, 6 * d + 6)
                for t in range(2):
                    link(nc.vector.tensor_tensor(mem.k_end[:, d, t], mem.k_end[:, d, t], k[:, t], ALU.mult))
                    link(nc.vector.scalar_tensor_tensor(mem.q_state[:, d, t], mem.q_state[:, d, t], 0.125, q[:, t, 0:2],
                                                        ALU.mult, ALU.mult))


def gla_scan_stage(net):
    nc, mem = net.nc, GlaMemory(net)
    head = lambda h: (h // 2, slice(64 * (h % 2), 64 * (h % 2) + 64))
    ident = net.const(C_IDENT)
    updates = [(0, 2, None), (1, 3, None), (0, 3, 0), (1, 2, 1), (0, 0, 1), (1, 1, 0)]
    units = [(d, c) for d in range(2) for c in range(2)]
    with Stage(net, "gla_scan") as st:
        zeroed, att_raw, att_ready = st.sem("zeroed"), st.sem("att_raw"), st.sem("att_ready")
        turned, ktok_ready, state_summed, state_ready = (st.sem("turned"), st.sem("ktok_ready"), st.sem("state_summed"),
                                                         st.sem("state_ready"))
        y_ready, own = st.sem("y_ready"), st.sem("dve_own")

        @st.tensor
        def _(pe):
            for n, (d, c) in enumerate(units):
                if n:
                    pe.wait_ge(att_ready, 4 * n)
                for h in range(4):
                    t, rows = head(h)
                    bank, at = net.ps[h % 2], P * (h // 2)
                    for half in range(2):
                        part = slice(64 * half, 64 * half + 64)
                        nc.tensor.matmul(bank[part, at + 64 * half:at + 64 * half + 64], mem.k_in[rows, d, t, c, part],
                                         mem.q_in[rows, d, t, c, part], start=True, stop=True)
                    jh, ih = ((0, 1), (1, 0))[d]
                    last = nc.tensor.matmul(bank[64 * jh:64 * jh + 64, at + 64 * ih:at + 64 * ih + 64],
                                            mem.k_cross[rows, d, t, c], mem.q_cross[rows, d, t, c], start=True, stop=True)
                    if h >= 2:
                        last.then_inc(att_raw, 1)
            for n, (d, c, _) in enumerate(updates):
                if n >= 2:
                    pe.wait_ge(state_ready, n - 1)
                for t in range(2):
                    last = nc.tensor.transpose(net.ps[2 + n % 2][:, P * t:P * t + P], mem.k_end[:, d, t, c, :], ident)
                last.then_inc(turned, 1)
                pe.wait_ge(ktok_ready, n + 1)
                for h in range(4):
                    t, rows = head(h)
                    last = nc.tensor.matmul(net.ps[2 + n % 2][rows, 256 + P * t:384 + P * t],
                                            mem.ktok[:, n % 2, 64 * h:64 * h + 64], mem.vtok[:, c, P * h:P * h + P],
                                            start=True, stop=True)
                last.then_inc(state_summed, 1)
            pe.wait_ge(state_ready, len(updates))
            pe.wait_ge(att_ready, 16)
            for h in range(4):
                t, rows = head(h)
                for c in range(2):
                    into = net.ps[4 + h][:, P * c:P * c + P]
                    for d in range(2):
                        nc.tensor.matmul(into, mem.vtok[:, c, P * h:P * h + P], mem.att[:, d, c, h, :],
                                         start=(d == 0), stop=False)
                    for d in range(2):
                        last = nc.tensor.matmul(into, mem.state[rows, d, c, t, :], mem.q_state[rows, d, t, c, :],
                                                start=False, stop=(d == 1))
                last.then_inc(y_ready, 1)

        @st.gpsimd
        def _(pool):
            pool.memset(mem.att, 0.0).then_inc(zeroed, 1)

        @st.scalar
        def _(act):
            for n in range(len(updates)):
                act.wait_ge(turned, n + 1)
                if n >= 2:
                    act.wait_ge(state_summed, n - 1)
                act.activation(mem.ktok[:, n % 2, :], net.ps[2 + n % 2][:, 0:256], ACT.Copy).then_inc(ktok_ready, 1)

        @st.vector
        def _(dve):
            link = Chain(dve, own)
            dve.wait_ge(zeroed, 1)
            for n, (d, c) in enumerate(units):
                tri = net.const((C_LE, C_GE)[d]).unsqueeze(1).to_broadcast([P, 2, P])
                whole, rest = ((slice(0, 64), slice(64, 128)), (slice(64, 128), slice(0, 64)))[d]
                for odd in range(2):
                    dve.wait_ge(att_raw, 2 * n + 2)
                    raw = net.ps[odd][:, 0:256].rearrange("p (h m) -> p h m", m=P)
                    into = mem.att[:, d, c, odd::2, :]
                    nc.vector.tensor_tensor(into[whole], raw[whole], tri[whole], ALU.mult).then_inc(att_ready, 1)
                    nc.vector.tensor_tensor(into[rest, :, rest], raw[rest, :, rest], tri[rest, :, rest],
                                            ALU.mult).then_inc(att_ready, 1)
            held = {}
            for n, (d, c, to) in enumerate(updates):
                sums = net.ps[2 + n % 2][:, 256:512].rearrange("p (t m) -> p t m", m=P)
                dve.wait_ge(state_summed, n + 1)
                if n < 2:
                    into = mem.state[:, d, 1 - d]
                    last = nc.vector.tensor_copy(into, sums)
                else:
                    into = mem.state[:, d, to]
                    dve.wait_ge(state_ready, n)
                    decay = mem.e_end[:, d, :, c:c + 1].to_broadcast([P, 2, P])
                    link(nc.vector.tensor_tensor(into, held[d], decay, ALU.mult))
                    last = nc.vector.tensor_tensor(into, into, sums, ALU.add)
                last.then_inc(state_ready, 1)
                held[d] = into
            for h in range(4):
                dve.wait_ge(y_ready, h + 1)
                nc.vector.tensor_copy(net.OT[:, 4 + h, 0:LAT], net.ps[4 + h][:, 0:LAT])


def times_stage(net, name, pairs):
    with Stage(net, name) as st:
        @st.vector
        def _(dve):
            for a, b in pairs:
                net.nc.vector.tensor_tensor(a, a, b, ALU.mult)


class SecondMemory:

    def __init__(self, net):
        sc = net.SC
        self.spectrum_in = sc[:, 0:1024].rearrange("p (a t n m) -> p a t n m", a=2, t=2, n=2)
        self.spectrum = sc[:, 1024:1536].rearrange("p (t m) -> p t m", m=LAT)
        self.vtok = sc[:, 1536:1792].rearrange("p (a m) -> p a m", a=2)
        self.mem_vtok = sc[:, 1792:2304].rearrange("p (a m) -> p a m", a=2)
        self.prob = sc[:, 2304:3328].rearrange("p (b q k) -> p b q k", b=2, q=2)
        self.prob_t = sc[:, 3328:4352].rearrange("p (b m) -> p b m", b=2)
        self.stat = sc[:, 4352:4352 + 12 * 8].rearrange("p (h n) -> p h n", n=8)
        self.part = sc[:, 4500:5012].rearrange("p (b m) -> p b m", m=LAT)
        self.angle, self.turn = sc[:, 5100:5356], sc[:, 5356:5612]
        self.sin, self.cos = sc[:, 6300:6556], sc[:, 6556:6812]
        self.memory, self.memory_normed = net.HT[:, :, LAT:TOK], net.OT[:, :, LAT:TOK]
        self.k_swapped = net.PT[:, 14, 0:LAT]


def second_load_stage(net):
    nc, mem = net.nc, SecondMemory(net)
    rows = net.PT[:, 24:28, :].rearrange("p t m -> p (t m)").rearrange("p (a d) -> p a d", a=2)
    where = mem.turn.bitcast(I32)
    with Stage(net, "second_load") as st:
        const_in, memory_in, where_in, turned = (st.sem("const_in"), st.sem("memory_in"), st.sem("where_in"),
                                                 st.sem("turned"))
        own, reduced, sin_ready = st.sem("dve_own"), st.sem("reduced"), st.sem("sin_ready")

        @st.sync
        def _(sp):
            sp.dma_start(where, net.ins["positions_2"][0].partition_broadcast(P)).then_inc(where_in, 16)
            sp.dma_start(net.CONST[:, C_OVER:C_OVER + N_CONST2], net.ins["const_2"]).then_inc(const_in, 16)
            sp.dma_start(rows, net.ins["mem_2"][0].rearrange("(a p) d -> p a d", p=P)).then_inc(memory_in, 16)

        @st.tensor
        def _(pe):
            pe.wait_ge(memory_in, 16)
            for f in range(KT):
                for a in range(2):
                    last = nc.tensor.transpose(net.ps[f][:, P * a:P * a + P], rows[:, a, P * f:P * f + P],
                                               net.const(C_IDENT))
                last.then_inc(turned, 1)

        @st.scalar
        def _(act):
            for f in range(KT):
                act.wait_ge(turned, f + 1)
                act.activation(mem.memory[:, f, :], net.ps[f][:, 0:LAT], ACT.Copy)
            act.wait_ge(reduced, 2)
            act.activation(mem.sin, mem.angle, ACT.Sin)
            act.activation(mem.cos, mem.angle, ACT.Sin, scale=0.5).then_inc(sin_ready, 1)

        @st.vector
        def _(dve):
            link = Chain(dve, own)
            two_pi = 2.0 * np.pi
            high = float(np.float32(6.28125))
            middle = float(np.float32(np.float64(two_pi - high)))
            low = float(np.float32(two_pi - high - middle))
            rounder = 1.5 * 2.0 ** 23
            dve.wait_ge(where_in, 16)
            dve.wait_ge(const_in, 16)
            link(nc.vector.tensor_copy(mem.angle, where))
            link(nc.vector.tensor_scalar(mem.angle, mem.angle, net.CONST[:, C_INVF:C_INVF + 1], None, ALU.mult))
            link(nc.vector.tensor_scalar(mem.turn, mem.angle, 1.0 / two_pi, rounder, ALU.mult, ALU.add))
            link(nc.vector.tensor_scalar(mem.turn, mem.turn, -rounder, None, ALU.add))
            for part in (high, middle, low):
                link(nc.vector.scalar_tensor_tensor(mem.angle, mem.turn, -part, mem.angle, ALU.mult, ALU.add))
            nc.vector.tensor_scalar(mem.angle, mem.angle, 3.1415925, -3.1415925, ALU.min, ALU.max).then_inc(reduced, 2)
            dve.wait_ge(sin_ready, 1)
            link(nc.vector.tensor_tensor(mem.cos, mem.cos, mem.cos, ALU.mult))
            nc.vector.tensor_scalar(mem.cos, mem.cos, -2.0, 1.0, ALU.mult, ALU.add)


def second_prepare_stage(net, layer):
    nc, mem = net.nc, SecondMemory(net)
    with Stage(net, f"second_prepare{layer}") as st:
        rotated, added, turned, own = st.sem("rotated"), st.sem("added"), st.sem("turned"), st.sem("dve_own")

        @st.tensor
        def _(pe):
            for n in range(5):
                if n == 4:
                    pe.wait_ge(added, 1)
                nc.tensor.matmul(net.ps[n % 4][:, 0:LAT], net.const(C_ROTB), net.PT[:, 2 + n, 0:LAT],
                                 start=True, stop=True).then_inc(rotated, 1)
            for a in range(2):
                for n, t in enumerate((7, 12, 13)):
                    last = nc.tensor.transpose(net.ps[4 + a][:, P * n:P * n + P], net.PT[:, t, P * a:P * a + P],
                                               net.const(C_IDENT))
                last.then_inc(turned, 1)

        @st.scalar
        def _(act):
            for a in range(2):
                act.wait_ge(turned, a + 1)
                act.activation(mem.vtok[:, a, :], net.ps[4 + a][:, 0:P], ACT.Copy)
                act.activation(mem.mem_vtok[:, a, :], net.ps[4 + a][:, P:3 * P], ACT.Copy)

        @st.vector
        def _(dve):
            link = Chain(dve, own)
            for n in range(5):
                x = net.PT[:, 2 + n, 0:LAT]
                dve.wait_ge(rotated, n + 1)
                nc.vector.tensor_tensor(mem.part[:, n % 2], net.ps[n % 4][:, 0:LAT], mem.sin, ALU.mult).then_inc(added, 1)
                link(nc.vector.tensor_tensor(x, x, mem.cos, ALU.mult))
                dve.wait_ge(added, n + 1)
                link(nc.vector.tensor_tensor(x, x, mem.part[:, n % 2], ALU.add))
            keys = net.PT[:, 6, 0:LAT]
            nc.vector.tensor_copy(mem.k_swapped[64:128], keys[0:64])
            nc.vector.tensor_copy(mem.k_swapped[0:64], keys[64:128])


def fourier_stage(net, layer):
    nc, mem = net.nc, SecondMemory(net)
    with Stage(net, f"fourier{layer}") as st:
        by_channel, by_channel_copied, by_token, by_token_copied, mixed = (
            st.sem("by_channel"), st.sem("by_channel_copied"), st.sem("by_token"), st.sem("by_token_copied"), st.sem("mixed"))

        @st.tensor
        def _(pe):
            for a in range(2):
                for t in range(2):
                    last = nc.tensor.matmul(net.ps[a][:, 256 * t:256 * t + 256], net.PT[:, t, P * a:P * a + P],
                                            net.const(C_DFTC, 256), start=True, stop=True)
                last.then_inc(by_channel, 1)
            pe.wait_ge(by_channel_copied, 2)
            for t in range(2):
                for n in range(2):
                    for a in range(2):
                        last = nc.tensor.matmul(net.ps[2 + t][:, 0:LAT], mem.spectrum_in[:, a, t, n, :],
                                                net.const(C_DFTS + (2 * n + a) * LAT, LAT),
                                                start=(n == 0 and a == 0), stop=(n == 1 and a == 1))
                last.then_inc(by_token, 1)
            for t in range(2):
                pe.wait_ge(by_token_copied, t + 1)
                nc.tensor.matmul(net.ps[4 + t][:, 0:LAT], net.WF[:, layer, t, :], mem.spectrum[:, t, :], start=True,
                                 stop=True).then_inc(mixed, 1)

        @st.scalar
        def _(act):
            for a in range(2):
                act.wait_ge(by_channel, a + 1)
                act.activation(mem.spectrum_in[:, a].rearrange("p t n m -> p (t n m)"), net.ps[a][:, :],
                               ACT.Copy).then_inc(by_channel_copied, 1)
            for t in range(2):
                act.wait_ge(by_token, t + 1)
                act.activation(mem.spectrum[:, t, :], net.ps[2 + t][:, 0:LAT], ACT.Copy).then_inc(by_token_copied, 1)
            for t in range(2):
                act.wait_ge(mixed, t + 1)
                act.activation(net.OT[:, t, 0:LAT], net.ps[4 + t][:, 0:LAT], ACT.Copy)


def second_attention_stage(net, layer):
    nc, mem = net.nc, SecondMemory(net)
    scale = 64 ** -0.5
    window = net.const(C_WIN, 2 * LAT)
    heads = []
    for h in range(8):
        rows, kv = slice(64 * (h % 2), 64 * (h % 2) + 64), h // 4
        keys = net.PT[rows, 6, 0:LAT] if kv == h % 2 else mem.k_swapped[rows]
        heads.append((net.PT[rows, 2 + h // 2, 0:LAT], keys, mem.vtok[:, :, 64 * kv:64 * kv + 64],
                      net.SINKROW[:, 8 * layer + h:8 * layer + h + 1]))
    for h in range(4):
        rows = slice(64 * (h % 2), 64 * (h % 2) + 64)
        heads.append((net.PT[rows, 8 + h // 2, 0:LAT], net.PT[rows, 10 + h // 2, 0:LAT],
                      mem.mem_vtok[:, :, 64 * h:64 * h + 64], None))
    N = len(heads)
    with Stage(net, f"attention{layer}") as st:
        scored, score_used, max_ready, exp_ready = (st.sem("scored"), st.sem("score_used"), st.sem("max_ready"),
                                                    st.sem("exp_ready"))
        prob_ready, turned, turned_copied, out_ready = (st.sem("prob_ready"), st.sem("turned"), st.sem("turned_copied"),
                                                        st.sem("out_ready"))
        out_taken, own = st.sem("out_taken"), st.sem("dve_own")

        @st.tensor
        def _(pe):
            def score(u):
                q, k, _, _ = heads[u]
                if u >= 2:
                    pe.wait_ge(score_used, u - 1)
                for t in range(2):
                    last = nc.tensor.matmul(net.ps[u % 2][:, LAT * t:LAT * t + LAT], q[:, P * t:P * t + P], k,
                                            start=True, stop=True)
                last.then_inc(scored, 1)

            score(0)
            score(1)
            for u, (_, _, v, _) in enumerate(heads):
                pe.wait_ge(prob_ready, u + 1)
                if u >= 2:
                    pe.wait_ge(turned_copied, u - 1)
                for kt in range(2):
                    for t in range(2):
                        last = nc.tensor.transpose(net.ps[2 + u % 2][:, LAT * kt + P * t:LAT * kt + P * t + P],
                                                   mem.prob[:, u % 2, t, P * kt:P * kt + P], net.const(C_IDENT))
                last.then_inc(turned, 1)
                if u + 2 < N:
                    score(u + 2)
                pe.wait_ge(turned_copied, u + 1)
                if u % 2 == 0 and u >= 4:
                    pe.wait_ge(out_taken, u // 2 - 1)
                rows = slice(64 * (u % 2), 64 * (u % 2) + 64)
                for kt in range(2):
                    last = nc.tensor.matmul(net.ps[4 + (u // 2) % 2][rows, 0:LAT], v[:, kt, :],
                                            mem.prob_t[:, u % 2, LAT * kt:LAT * kt + LAT], start=(kt == 0), stop=(kt == 1))
                last.then_inc(out_ready, 1)

        @st.scalar
        def _(act):
            def exps(u):
                act.wait_ge(max_ready, u + 1)
                for t in range(2):
                    act.activation(mem.prob[:, u % 2, t, :], mem.prob[:, u % 2, t, :], ACT.Exp,
                                   bias=mem.stat[:, u, t:t + 1], accum_out=mem.stat[:, u, 2 + t:3 + t]).then_inc(exp_ready, 1)
                sink = heads[u][3]
                if sink is not None:
                    act.activation(mem.stat[:, u, 4:6], mem.stat[:, u, 0:2], ACT.Exp, bias=sink).then_inc(exp_ready, 1)

            exps(0)
            for u in range(N):
                if u + 1 < N:
                    exps(u + 1)
                act.wait_ge(turned, u + 1)
                if u >= 2:
                    act.wait_ge(out_ready, u - 1)
                act.activation(mem.prob_t[:, u % 2, :], net.ps[2 + u % 2][:, :], ACT.Copy).then_inc(turned_copied, 1)

        @st.vector
        def _(dve):
            link = Chain(dve, own)
            exps_before = [sum(3 if x[3] is not None else 2 for x in heads[:u]) for u in range(N + 1)]

            def maxima(u):
                sink, most = heads[u][3], mem.stat[:, u, 0:2]
                dve.wait_ge(scored, u + 1)
                if u >= 2:
                    dve.wait_ge(turned, u - 1)
                both = mem.prob[:, u % 2].rearrange("p q k -> p (q k)")
                if sink is not None:
                    step = nc.vector.scalar_tensor_tensor(both, net.ps[u % 2][:, :], scale, window, ALU.mult, ALU.add)
                else:
                    step = nc.vector.tensor_scalar(both, net.ps[u % 2][:, :], scale, None, ALU.mult)
                step.then_inc(score_used, 1)
                dve.wait_ge(score_used, u + 1)
                link(nc.vector.reduce_max(most, mem.prob[:, u % 2], AX_X))
                if sink is not None:
                    nc.vector.tensor_scalar(most, most, sink, -1.0, ALU.max, ALU.mult).then_inc(max_ready, 1)
                else:
                    nc.vector.tensor_scalar(most, most, -1.0, None, ALU.mult).then_inc(max_ready, 1)

            maxima(0)
            for u in range(N):
                if u + 1 < N:
                    maxima(u + 1)
                dve.wait_ge(exp_ready, exps_before[u + 1])
                total = mem.stat[:, u, 2:4]
                if heads[u][3] is not None:
                    link(nc.vector.tensor_tensor(total, total, mem.stat[:, u, 4:6], ALU.add))
                link(nc.vector.reciprocal(total, total))
                for t in range(2):
                    last = nc.vector.tensor_scalar(mem.prob[:, u % 2, t, :], mem.prob[:, u % 2, t, :],
                                                   mem.stat[:, u, 2 + t:3 + t], None, ALU.mult)
                last.then_inc(prob_ready, 1)
                if u % 2 == 0 and u >= 2:
                    dve.wait_ge(out_ready, u)
                    pair = u // 2 - 1
                    nc.vector.tensor_copy(net.OT[:, 2 + pair, 0:LAT], net.ps[4 + pair % 2][:, 0:LAT]).then_inc(out_taken, 1)
            dve.wait_ge(out_ready, N)
            nc.vector.tensor_copy(net.OT[:, 7, 0:LAT], net.ps[5][:, 0:LAT])


def swiglu_weights(w):
    gate, up = (w[:, o:o + FF].rearrange("(t k) (n m) -> n k t m", k=P, m=SW) for o in (0, FF))
    pairs = FF // SW
    return Weights(pairs // 2, 2 * (pairs % 2), lambda i, s: (up if s % 2 else gate)[2 * i + s // 2])


def swiglu_stage(net, name, w, following):
    nc = net.nc
    with Stage(net, name) as st:
        tile_ready = [st.sem(f"tile_ready{m}") for m in range(2)]
        gate_free = [st.sem(f"gate_free{m}") for m in range(2)]
        up_free = [st.sem(f"up_free{m}") for m in range(2)]
        base = list(net.ring_base)

        @st.sync
        def _(sp):
            feed(net, sp, w, lambda i, s: (tile_ready[1], SLOTS * i + s + 1), following)

        @st.tensor
        def _(pe):
            def turn(i, slots):
                for s in slots:
                    pe.wait_ge(net.ring_loaded[s], 16 * (i + 1) + base[s])
                    for m in range(2):
                        pe.wait_ge((up_free if s % 2 else gate_free)[m], 2 * i + s // 2 + 1)
                        for kt in range(KT):
                            last = nc.tensor.matmul(net.ps[2 * s + m][:, 0:LAT], net.ring(s, kt, m),
                                                    net.HT[:, kt, 0:LAT], start=(kt == 0), stop=(kt == KT - 1))
                        last.then_inc(tile_ready[m], 1)

            turns(pe, w, turn)

        @st.scalar
        def _(act):
            for m in range(2):
                act.sem_inc(gate_free[m], 2)

            def turn(i, slots):
                for s in slots[::2]:
                    for m in range(2):
                        act.wait_ge(tile_ready[m], SLOTS * i + s + 1)
                        act.activation(net.PT[:, 4 * i + s + m, 0:LAT], net.ps[2 * s + m][:, 0:LAT],
                                       ACT.Silu).then_inc(gate_free[m], 1)

            turns(act, w, turn)

        @st.vector
        def _(dve):
            for m in range(2):
                dve.sem_inc(up_free[m], 2)

            def turn(i, slots):
                for s in slots[1::2]:
                    for m in range(2):
                        into = net.PT[:, 4 * i + s - 1 + m, 0:LAT]
                        dve.wait_ge(gate_free[m], 2 + 2 * i + s // 2 + 1)
                        dve.wait_ge(tile_ready[m], SLOTS * i + s + 1)
                        nc.vector.tensor_tensor(into, into, net.ps[2 * s + m][:, 0:LAT], ALU.mult).then_inc(up_free[m], 1)

            turns(dve, w, turn)
        net.spent(w)


def deep_project_stage(net, name, w, src, dst, following):
    with Stage(net, name) as st:
        tile_ready = [st.sem(f"tile_ready{m}") for m in range(2)]
        tile_free = [st.sem(f"tile_free{m}") for m in range(2)]
        slot_read = st.sem("slot_read")

        @st.sync
        def _(sp):
            feed(net, sp, w, lambda i, s: (slot_read, (SLOTS - 1) * i + s + 1) if s < SLOTS - 1 else (tile_ready[1], i + 1),
                 following)

        @st.tensor
        def _(pe):
            deep_on_pe(net, pe, w, src, LAT, tile_ready, tile_free, slot_read)

        @st.vector
        def _(dve):
            for m in range(2):
                dve.sem_inc(tile_free[m], 1)

            def turn(i, slots):
                for m in range(2):
                    dve.wait_ge(tile_ready[m], i + 1)
                    net.nc.vector.tensor_copy(dst[:, 2 * i + m, 0:LAT], net.ps[m][:, 0:LAT]).then_inc(tile_free[m], 1)

            turns(dve, w, turn)
        net.spent(w)


def store_stage(net):
    nc = net.nc
    rows = net.PT[:, 0:4, :].rearrange("p t m -> p (t m)").rearrange("p (a d) -> p a d", a=2)
    with Stage(net, "store") as st:
        turned, copied, stored = st.sem("turned"), st.sem("copied"), st.sem("stored")

        @st.tensor
        def _(pe):
            for a in range(2):
                for f in range(KT):
                    last = nc.tensor.transpose(net.ps[2 * a + f // 4][:, P * (f % 4):P * (f % 4) + P],
                                               net.XT[:, f, P * a:P * a + P], net.const(C_IDENT))
                    if f % 4 == 3:
                        last.then_inc(turned, 1)

        @st.vector
        def _(dve):
            for n in range(4):
                dve.wait_ge(turned, n + 1)
                nc.vector.tensor_copy(rows[:, n // 2, 512 * (n % 2):512 * (n % 2) + 512], net.ps[n][:, :]).then_inc(copied, 1)

        @st.sync
        def _(sp):
            for a in range(2):
                sp.wait_ge(copied, 2 * (a + 1))
                sp.dma_start(net.out[0, P * a:P * a + P, :], rows[:, a, :]).then_inc(stored, 16)
            sp.wait_ge(stored, 32)


def program(nc, ins, out):
    with ExitStack() as ctx:
        net = Net(nc, ctx, ins, out)
        both, lat = (lambda i, s: TOK), (lambda i, s: LAT)
        mod = [columns(ins[f"l{n}_mod_w"], 0, 6 * D) for n in range(2)]
        w_in0 = columns(ins["l0_w_in"], 0, 3328)
        w_in1, in1_widths = odd_projection(ins["l1_w_in"])
        w_out = [columns(ins[f"l{n}_w_out"], 0, D) for n in range(2)]
        w_up = [columns(ins[f"l{n}_mlp_w1"], 0, HID) for n in range(2)]
        w_down = [deep(ins[f"l{n}_mlp_w2"], (8, 8, 8, 8)) for n in range(2)]

        w_in2 = [columns(ins["w_in_2"][n], 0, 1280) for n in range(2)]
        w_kv = [columns(ins["w_mem_kv_2"][n], 0, 512) for n in range(2)]
        w_out2 = [columns(ins["w_out_2"][n], 0, D) for n in range(2)]
        w_ffn_in = [swiglu_weights(ins["w_ffn_in_2"][n]) for n in range(2)]
        w_ffn_out = [deep(ins["w_ffn_out_2"][n], (6, 6, 5, 5)) for n in range(2)]

        load_stage(net, mod[0])
        modulation_stage(net, 0, mod[0], w_in0)
        ada_stage(net, 0, 0, TOK)
        project_stage(net, "in0", w_in0, net.HT, both, net.PT, None)
        diff_prepare_stage(net)
        diff_attention_stage(net)
        heads = [net.OT[:, h, :] for h in range(4)]
        group_norm_stage(net, "diff_norm", [([o], [o], [net.DER[:, 32:33]], [net.PT[:, h, :]])
                                            for h, o in enumerate(heads)], TOK, 1e-5)
        rwkv_prepare_stage(net)
        for d in range(2):
            rwkv_decay_stage(net, d)
            rwkv_chunks_stage(net, d)
        rwkv_finish_stage(net)
        first_fetch_stage(net, w_out[0])
        mixed_out_stage(net, "out0", w_out[0], TOK, w_up[0])
        ada_stage(net, 0, 1, TOK)
        relu_squared_stage(net, "up0", w_up[0], TOK, w_down[0])
        mlp_out_stage(net, "down0", w_down[0], TOK, mod[1])

        modulation_stage(net, 1, mod[1], w_in1)
        ada_stage(net, 1, 0, TOK)
        project_stage(net, "in1", w_in1, net.HT, in1_widths, net.PT, w_out[1], straight=True)
        ssd_steps_stage(net)
        ssd_conv_stage(net)
        ssd_scan_stage(net)
        ssd_gate_stage(net)
        group_norm_stage(net, "ssd_norm", [([net.OT[:, 2 * g + t, 0:LAT] for t in range(2)],) * 2 +
                                           ([net.par("l1_ssm_norm", 2 * g + t) for t in range(2)],
                                            [net.PT[:, 2 * g + t, 0:LAT] for t in range(2)]) for g in range(2)], LAT, EPS)
        gla_gates_stage(net)
        gla_scan_stage(net)
        group_norm_stage(net, "gla_norm", [([net.OT[:, 4 + h, 0:LAT]],) * 2 + ([net.par("l1_gla_norm")],
                                            [net.PT[:, h, 0:LAT]]) for h in range(4)], LAT, EPS)
        times_stage(net, "gla_gate", [(net.OT[:, 4 + h, 0:LAT], net.PT[:, 20 + h, 0:LAT]) for h in range(4)])
        mixed_out_stage(net, "out1", w_out[1], LAT, w_up[1])
        ada_stage(net, 1, 1, LAT)
        relu_squared_stage(net, "up1", w_up[1], LAT, w_down[1])
        mlp_out_stage(net, "down1", w_down[1], LAT, w_in2[0])
        x = [net.XT[:, t, 0:LAT] for t in range(KT)]
        h = [net.HT[:, t, 0:LAT] for t in range(KT)]
        scratch = [net.PT[:, t, 0:LAT] for t in range(24, 32)]
        gains = lambda name, layer: [net.par(name, KT * layer + t) for t in range(KT)]
        group_norm_stage(net, "final_norm", [(x, x, gains("final_norm", 0), scratch)], LAT, EPS)

        second_load_stage(net)
        mem = SecondMemory(net)
        mem_scratch = [net.PT[:, t, LAT:TOK] for t in range(24, 32)]
        for n in range(2):
            raw, normed = ([v[:, t, :] for t in range(KT)] for v in (mem.memory, mem.memory_normed))
            group_norm_stage(net, f"pre_mix{n}", [(x, h, gains("g_pre_mix_2", n), scratch),
                                                  (raw, normed, gains("g_mem_2", n), mem_scratch)], LAT, EPS)
            project_stage(net, f"second_in{n}", w_in2[n], net.HT, lat, net.PT, w_kv[n])
            project_stage(net, f"memory_in{n}", w_kv[n], mem.memory_normed, lat, net.PT, w_out2[n],
                          dst_tile=lambda t: 10 + t)
            second_prepare_stage(net, n)
            fourier_stage(net, n)
            second_attention_stage(net, n)
            o = [net.OT[:, t, 0:LAT] for t in range(KT)]
            gain = gains("g_grp_2", n)
            group_norm_stage(net, f"mix_norm{n}", [(o[a:b], o[a:b], gain[a:b], scratch[a:b])
                                                   for a, b in ((0, 2), (2, 6), (6, 8))], LAT, EPS)
            project_stage(net, f"second_out{n}", w_out2[n], net.OT, lat, net.PT, w_ffn_in[n])
            y = [net.PT[:, t, 0:LAT] for t in range(KT)]
            group_norm_stage(net, f"post_mix{n}", [(y, y, gains("g_post_mix_2", n), scratch)], LAT, EPS, adds=x)
            group_norm_stage(net, f"pre_ffn{n}", [(x, h, gains("g_pre_ffn_2", n), scratch)], LAT, EPS)
            swiglu_stage(net, f"ffn_in{n}", w_ffn_in[n], w_ffn_out[n])
            deep_project_stage(net, f"ffn_out{n}", w_ffn_out[n], net.PT, net.OT, w_in2[1] if n == 0 else None)
            group_norm_stage(net, f"post_ffn{n}", [(o, o, gains("g_post_ffn_2", n), scratch)], LAT, EPS, adds=x)
        store_stage(net)




def kernel(**inputs):
    import concourse.bacc as bacc
    from concourse.bass_utils import run_bass_kernel_spmd

    nc = bacc.Bacc("TRN2", target_bir_lowering=False, num_devices=1)
    arrays = {name: np.ascontiguousarray(a) for name, a in inputs.items()}
    arrays |= {"const_1": first_constants(), "const_2": second_constants()}
    ins = {name: nc.dram_tensor(f"in_{name}", a.shape, mybir.dt.from_np(a.dtype), kind="ExternalInput").ap()
           for name, a in arrays.items()}
    out = nc.dram_tensor("out", (1, LAT, D), F32, kind="ExternalOutput").ap()
    program(nc, ins, out)
    result = run_bass_kernel_spmd(nc, [{f"in_{name}": a for name, a in arrays.items()}], core_ids=[0])
    return result.results[0]["out"]
```

```python
from contextlib import ExitStack

import numpy as np

import concourse.bass as bass
from concourse import mybir

F32 = mybir.dt.float32
F32R = mybir.dt.float32r
I32 = mybir.dt.int32
ALU = mybir.AluOpType
ACT = mybir.ActivationFunctionType
AX_X = mybir.AxisListType.X

P = 128
D = 1024
KT = D // P
LAT = 256
TOK = 512
CH = 128
NCH = TOK // CH
HID = 4096
FF = 2816
SLOTS = 4
SW = 256
EPS = 1e-6
LAM_INIT = 0.2
DECAY = float(np.exp(-0.5))
GLA_CLAMP = 43.0


C_IDENT, C_ONES, C_BLK, C_LE, C_GE = (P * n for n in range(5))
C_EPS = 5 * P
EPSILONS = (EPS, 1e-5, 64e-5)
C_OVER = C_EPS + 4
C_MASK4 = C_OVER
C_LEVEL = C_MASK4 + 1024
C_ROTA = C_LEVEL + 2 * 7 * P
C_COSA = C_ROTA + P
C_SINA = C_COSA + LAT
C_FOLD = C_SINA + LAT
N_CONST = C_FOLD + 2
C_DFTC = C_OVER
C_DFTS = C_DFTC + 2 * P
C_WIN = C_DFTS + 4 * LAT
C_ROTB = C_WIN + 2 * LAT
C_INVF = C_ROTB + P
N_CONST2 = C_INVF + 1 - C_OVER


def first_constants():
    j, i = np.arange(P)[:, None], np.arange(P)[None, :]
    out = np.zeros((P, N_CONST), np.float32)
    out[:, C_IDENT:C_IDENT + P] = j == i
    out[:, C_ONES:C_ONES + P] = 1.0
    out[:, C_BLK:C_BLK + P] = j // 64 == i // 64
    out[:, C_LE:C_LE + P] = j <= i
    out[:, C_GE:C_GE + P] = j >= i
    out[:, C_EPS:C_EPS + len(EPSILONS)] = EPSILONS
    for n, (strict, incl) in enumerate(((j < i, j <= i), (j > i, j >= i))):
        out[:, C_MASK4 + 512 * n:C_MASK4 + 512 * (n + 1)] = np.concatenate([strict, incl, strict, incl], 1)
    for lv in range(7):
        b = 1 << lv
        low = (j // (2 * b) == i // (2 * b)) & ((j // b) % 2 == 1) & ((i // b) % 2 == 0)
        out[:, C_LEVEL + P * lv:C_LEVEL + P * (lv + 1)] = low.T
        out[:, C_LEVEL + P * (7 + lv):C_LEVEL + P * (8 + lv)] = low
    rot = np.zeros((P, P), np.float32)
    for r in range(P):
        if r % 32 < 16:
            rot[r, r + 16] = -1.0
        else:
            rot[r, r - 16] = 1.0
    out[:, C_ROTA:C_ROTA + P] = rot.T
    t = np.arange(LAT)
    inv = (np.float32(10000.0) ** (-np.arange(16, dtype=np.float32) / np.float32(16))).astype(np.float32)
    for r in range(P):
        pos = (t // 64 if r % 64 < 32 else t % 64).astype(np.float32)
        ang = pos * inv[r % 16]
        out[r, C_COSA:C_COSA + LAT] = np.cos(ang)
        out[r, C_SINA:C_SINA + LAT] = np.sin(ang)
    for r in range(4):
        out[r, C_FOLD + r % 2] = 1.0
    return out


def second_constants():
    out = np.zeros((P, N_CONST2), np.float32)
    o = -C_OVER
    c = np.arange(64)
    ang = 2 * np.pi * ((c[:, None] * c[None, :]) % 64) / 64
    for n, m in enumerate((np.cos(ang), np.sin(ang))):
        for g in range(2):
            out[64 * g:64 * g + 64, o + C_DFTC + P * n + 64 * g:o + C_DFTC + P * n + 64 * g + 64] = m / 128.0
    s = np.arange(LAT)
    ang = 2 * np.pi * ((s[:, None] * s[None, :]) % LAT) / LAT
    for n, m in enumerate((np.cos(ang), -np.sin(ang))):
        for h in range(2):
            at = o + C_DFTS + (2 * n + h) * LAT
            out[:, at:at + LAT] = m[P * h:P * h + P]
    q, k = np.arange(P)[:, None], np.arange(LAT)[None, :]
    for h in range(2):
        at = o + C_WIN + h * LAT
        out[:, at:at + LAT] = np.where(np.abs(q + P * h - k) <= 128, 0.0, -1e30)
    for r in range(P):
        if r % 64 < 32:
            out[r + 32, o + C_ROTB + r] = -1.0
        else:
            out[r - 32, o + C_ROTB + r] = 1.0
    inv = np.exp(-np.float32(np.log(10000.0)) * np.arange(32, dtype=np.float32) * np.float32(2.0 / 64))
    out[:, o + C_INVF] = inv.astype(np.float32)[np.arange(P) % 32]
    return out


ROWS = [
    [("c", 8), ("c_ctx", 8), ("l0_mod_b", 48), ("l0_norm1", 8), ("l0_norm2", 8), ("l0_mu", 14), ("l0_w0_f", 4),
     ("l0_w0_b", 4), ("l0_a0", 4), ("l0_k_k", 4), ("l0_k_a", 4), ("l0_r_k", 4), ("l0_lnx_w", 4), ("l0_lnx_b", 4),
     ("l0_subln", 1)],
    [("l1_mod_b", 48), ("l1_norm1", 8), ("l1_norm2", 8), ("l1_conv_w", 40), ("l1_conv_b", 8), ("l1_ssm_norm", 4),
     ("l1_gk_b_f", 2), ("l1_gk_b_b", 2), ("l1_gla_norm", 1)],
    [("final_norm", 8), ("g_pre_mix_2", 16), ("g_mem_2", 16), ("g_grp_2", 16), ("g_post_mix_2", 16),
     ("g_pre_ffn_2", 16), ("g_post_ffn_2", 16)],
]
COL = {}
for _n, _tile in enumerate(ROWS):
    _r = 0
    for _name, _count in _tile:
        COL[_name] = P * _n + _r
        _r += _count
    assert _r <= P


class Stage:

    def __init__(self, net, name):
        self.net, self.nc, self.name, self.sems = net, net.nc, name, []

    def sem(self, what):
        s = self.nc.alloc_semaphore(f"{self.name}_{what}")
        self.sems.append(s)
        return s

    def __enter__(self):
        self.block = self.nc.Block(name=self.name, no_gpsimd_drain=True)
        self.block.__enter__()
        self.scalar, self.vector, self.tensor = self.block.scalar, self.block.vector, self.block.tensor
        self.gpsimd, self.sync = self.block.gpsimd, self.block.sync
        return self

    def __exit__(self, *failed):
        self.block.__exit__(*failed)
        if failed[0]:
            return
        for s in self.sems:
            self.nc.gpsimd.sem_clear(s)
        for s in self.net.cleared:
            self.nc.release_semaphore(s)
        self.net.cleared = self.sems


class Chain:

    def __init__(self, engine, sem):
        self.engine, self.sem, self.n = engine, sem, 0

    def __call__(self, step):
        self.n += 1
        step.then_inc(self.sem, 1)
        self.engine.wait_ge(self.sem, self.n)


class Weights:

    def __init__(self, loops, tail, slot, kts=(KT,) * SLOTS, depth=1):
        self.loops, self.tail, self.slot, self.kts, self.depth = loops, tail, slot, kts, depth

    def first(self):
        return SLOTS if self.loops else min(self.tail, SLOTS)

    def last(self):
        return (self.loops, self.tail - 1) if self.tail else (self.loops - 1, SLOTS - 1)


def columns(w, first, count):
    view = w[:, first:first + count].rearrange("(t k) (n m) -> n k t m", k=P, m=SW)
    return Weights(count // SW // SLOTS, count // SW % SLOTS, lambda i, s: view[SLOTS * i + s])


def deep(w, parts):
    view = w.rearrange("(t k) (n m) -> n k t m", k=P, m=SW)
    depth = len(parts)
    ends = [0, *(int(n) for n in np.cumsum(parts))]
    across = SLOTS // depth
    return Weights(D // SW // across, 0,
                   lambda i, s: view[across * i + s // depth, :, ends[s % depth]:ends[s % depth + 1], :],
                   tuple(parts) * across, depth)


class Net:

    def __init__(self, nc, ctx, ins, out):
        self.nc, self.ins, self.out, self.cleared = nc, ins, out, []

        self.places, self.at = {}, -(-nc.sbuf_base // 32) * 32

        def sb(name, shape):
            self.places[name] = self.at
            tensor = nc.alloc_sbuf_tensor_at(name, shape, F32, offset=self.at)
            self.at += -(-4 * int(np.prod(shape[1:])) // 32) * 32
            return tensor

        self.XT = sb("XT", [P, KT, TOK])
        self.HT = sb("HT", [P, KT, TOK])
        self.PT = sb("PT", [P, 32, TOK])
        self.OT = sb("OT", [P, KT, TOK])
        self.RING = sb("RING", [P, SLOTS, KT * SW])
        self.CONST = sb("CONST", [P, N_CONST])
        self.PAR = sb("PAR", [P, 3 * P])
        self.MOD = sb("MOD", [P, 48, 2])
        self.AFF = sb("AFF", [P, 2, KT, 2])
        self.CACT = sb("CACT", [P, KT, 2])
        self.CSPLIT = nc.alloc_sbuf_tensor_at("CSPLIT", [P, KT, 4], F32R, offset=self.at)
        self.at += 4 * KT * 4
        self.DER = sb("DER", [P, 40])
        self.LORA = sb("LORA", [P, 2, 512])
        self.G2 = sb("G2", [P, 512])
        self.WDG = sb("WDG", [P, KT, 32])
        self.GUP = sb("GUP", [16, 2, 256])
        self.WF = sb("WF", [P, 2, 2, P])
        self.HEADROW = sb("HEADROW", [P, 40])
        self.DSKIP = sb("DSKIP", [P, 4])
        self.SINKROW = sb("SINKROW", [P, 16])
        self.LAMROW = sb("LAMROW", [P, 4, 64])
        self.LAM = sb("LAM", [P, 4])
        self.SC = sb("SC", [P, 7900])
        self.HR, self.OR = (self.rounded(name, [P, KT, TOK]) for name in ("HT", "OT"))
        self.PR = self.rounded("PT", [P, 32, TOK])
        self.RINGR = self.rounded("RING", [P, SLOTS, KT * SW])
        self.SCR = self.rounded("SC", [P, 2 * KT * SW])
        self.ps = [ctx.enter_context(nc.psum_tensor(f"bank{b}", [P, 512], F32)) for b in range(8)]
        self.ring_loaded = [ctx.enter_context(nc.semaphore(f"ring{s}_loaded")) for s in range(SLOTS)]
        self.ring_base = [0] * SLOTS
        self.smalls_in = ctx.enter_context(nc.semaphore("smalls_in"))

    def rounded(self, name, shape):
        return self.nc.alloc_sbuf_tensor_at(name + "_rounded", shape, F32R, offset=self.places[name])

    def const(self, at, width=P):
        return self.CONST[:, at:at + width]

    def eps(self, value):
        at = C_EPS + EPSILONS.index(value)
        return self.CONST[:, at:at + 1]

    def par(self, name, n=0):
        return self.PAR[:, COL[name] + n:COL[name] + n + 1]

    def low(self, s, kt, m):
        return self.RINGR[:, s, kt * SW + m * P:kt * SW + m * P + P]

    def ring_half(self, ring, s, m, kts):
        return ring[:, s, 0:kts * SW].rearrange("p (t m) -> p t m", m=SW)[:, :, m * P:m * P + P]

    def high(self, s, m):
        at = (2 * (s % 2) + m) * KT * P
        return self.SCR[:, at:at + KT * P].rearrange("p (t m) -> p t m", m=P)

    def fetch(self, sync, w, i, s):
        view = self.RING[:, s, 0:w.kts[s] * SW].rearrange("p (t m) -> p t m", m=SW)
        sync.dma_start(view, w.slot(i, s)).then_inc(self.ring_loaded[s], 16)

    def spent(self, w):
        for s in range(SLOTS):
            self.ring_base[s] += 16 * (w.loops + (s < w.tail))


def load_stage(net, first_weights):
    nc, ins = net.nc, net.ins
    rows = net.SC[:, 0:3 * P].rearrange("p (g m) -> p g m", m=P)
    tokens = net.PT[:, 0:2 * NCH, :].rearrange("p t m -> p (t m)").rearrange("p (t d) -> p t d", d=D)
    with Stage(net, "load") as st:
        const_in, rows_in, x_in = st.sem("const_in"), st.sem("rows_in"), st.sem("x_in")
        small_in, zeroed = st.sem("small_in"), st.sem("wf_zeroed")
        turned, copied, cols_ready = st.sem("turned"), st.sem("copied"), st.sem("cols_ready")
        own = st.sem("dve_own")
        lam_exp, lam_sums, act_own = st.sem("lam_exp"), st.sem("lam_sums"), st.sem("act_own")
        smalls_in = net.smalls_in
        n_rows = sum(len(t) for t in ROWS)

        @st.sync
        def _(sp):
            sp.dma_start(net.CONST[:, :], ins["const_1"]).then_inc(const_in, 16)
            for t in range(2):
                sp.dma_start(tokens[:, t, :], ins["x"][0, P * t:P * t + P, :]).then_inc(x_in, 16)
            for t in range(2):
                sp.dma_start(tokens[:, 2 + t, :], ins["ctx"][0, P * t:P * t + P, :]).then_inc(x_in, 16)
            for s in range(first_weights.first()):
                net.fetch(sp, first_weights, 0, s)
            w1 = ins["l1_w_in"]
            for at, col in ((0, 1536), (16, 3088)):
                sp.dma_start(net.WDG[:, :, at:at + 16],
                             w1[:, col:col + 16].rearrange("(t k) m -> k t m", k=P)).then_inc(small_in, 16)
            sp.wait_ge(small_in, 32)

        @st.scalar
        def _(act):
            n = 0
            for g, tile in enumerate(ROWS):
                r = 0
                for name, count in tile:
                    a = ins[name]
                    if len(a.shape) == 2:
                        a = a.rearrange("a b -> (a b)")
                    flat = a.rearrange("(t p) -> t p", p=P)
                    act.dma_start(rows[r:r + count, g, :], flat).then_inc(rows_in, 16)
                    r += count
            link = Chain(act, act_own)
            act.wait_ge(cols_ready, 3)
            for n, name in enumerate(("c", "c_ctx")):
                act.activation(net.CACT[:, :, n], net.PAR[:, COL[name]:COL[name] + 8], ACT.Silu)
            act.wait_ge(lam_sums, 1)
            act.activation(net.LAM[:, 2:4], net.LAM[:, 0:2], ACT.Exp).then_inc(lam_exp, 1)

        @st.gpsimd
        def _(pool):
            pool.memset(net.WF[:, :, :, :], 0.0).then_inc(zeroed, 1)
            small = [(net.LORA[0:64, 0, :], ins["l0_w2_f"]), (net.LORA[0:64, 1, :], ins["l0_w2_b"]),
                     (net.LORA[64:128, 0, :], ins["l0_a2"]), (net.G2[:, :], ins["l0_g2"]),
                     (net.GUP[:, 0, :], ins["l1_gk_up_f"]), (net.GUP[:, 1, :], ins["l1_gk_up_b"])]
            for n, name in enumerate(("l1_dt_bias_f", "l1_dt_bias_b", "l1_a_log_f", "l1_a_log_b",
                                      "l1_d_skip")):
                small.append((net.HEADROW[:, 8 * n:8 * n + 8], ins[name].partition_broadcast(P)))
            small.append((net.SINKROW[:, :], ins["sink_2"].rearrange("a b -> (a b)").partition_broadcast(P)))
            for n, name in enumerate(("l0_lam_q1", "l0_lam_k1", "l0_lam_q2", "l0_lam_k2")):
                small.append((net.LAMROW[:, n, :], ins[name].partition_broadcast(P)))
            for into, of in small:
                pool.dma_start(into, of).then_inc(smalls_in, 16)
            pool.wait_ge(zeroed, 1)
            for layer in range(2):
                for g in range(4):
                    o = 64 * (g % 2)
                    pool.dma_start(net.WF[o:o + 64, layer, g // 2, o:o + 64],
                                   ins["w_fourier_2"][layer, g]).then_inc(smalls_in, 16)
            pool.wait_ge(smalls_in, 16 * (len(small) + 8))

        @st.tensor
        def _(pe):
            ident = net.const(C_IDENT)
            pe.wait_ge(const_in, 16)
            pe.wait_ge(rows_in, 16 * n_rows)
            for g, tile in enumerate(ROWS):
                r = sum(count for _, count in tile)
                nc.tensor.transpose(net.ps[g][:, 0:r], rows[0:r, g, :], ident[0:r, 0:r]).then_inc(turned, 1)
            pe.wait_ge(x_in, 64)
            for f in range(KT):
                bank = (f + 3) % 8
                if f >= 5:
                    pe.wait_ge(cols_ready, f - 4)
                for t in range(4):
                    last = nc.tensor.transpose(net.ps[bank][:, P * t:P * t + P],
                                               tokens[:, t, P * f:P * f + P], ident)
                last.then_inc(turned, 1)

        @st.vector
        def _(dve):
            link = Chain(dve, own)
            for g, tile in enumerate(ROWS):
                r = sum(count for _, count in tile)
                dve.wait_ge(turned, g + 1)
                nc.vector.tensor_copy(net.PAR[:, P * g:P * g + r], net.ps[g][:, 0:r]).then_inc(cols_ready, 1)
            for f in range(KT):
                dve.wait_ge(turned, f + 4)
                nc.vector.tensor_copy(net.XT[:, f, :], net.ps[(f + 3) % 8][:, :])
            dve.wait_ge(cols_ready, 3)
            mu = net.PAR[:, COL["l0_mu"]:COL["l0_mu"] + 14]
            nc.vector.tensor_scalar(net.DER[:, 0:14], mu, 0.5, None, ALU.mult)
            nc.vector.tensor_scalar(net.DER[:, 14:28], mu, -1.0, 1.0, ALU.mult, ALU.add)
            k_a = net.PAR[:, COL["l0_k_a"]:COL["l0_k_a"] + 4]
            nc.vector.tensor_scalar(net.DER[:, 28:32], k_a, -1.0, 1.0, ALU.mult, ALU.add)
            nc.vector.tensor_scalar(net.DER[:, 32:33], net.par("l0_subln"), 1.0 - LAM_INIT, None, ALU.mult)
            dve.wait_ge(smalls_in, 16 * (6 + 5 + 1 + 4 + 8))
            skip = net.HEADROW[:, 32:40].rearrange("p (t h) -> p t h", h=2)
            for h in range(2):
                nc.vector.tensor_copy(net.DSKIP[64 * h:64 * h + 64, :], skip[64 * h:64 * h + 64, :, h])
            lam = net.LAMROW[:, :, :].rearrange("p (a b) d -> p a b d", b=2)
            link(nc.vector.tensor_tensor(lam[:, :, 0, :], lam[:, :, 0, :], lam[:, :, 1, :], ALU.mult))
            nc.vector.tensor_reduce(net.LAM[:, 0:2], lam[:, :, 0, :], AX_X, ALU.add).then_inc(lam_sums, 1)
            dve.wait_ge(lam_exp, 1)
            link(nc.vector.tensor_tensor(net.LAM[:, 0:1], net.LAM[:, 3:4], net.LAM[:, 2:3], ALU.subtract))
            link(nc.vector.tensor_scalar(net.LAM[:, 0:1], net.LAM[:, 0:1], LAM_INIT, None, ALU.subtract))


def feed(net, sp, w, used, following, straight=False):
    if w.loops > 1 and straight:
        for i in range(w.loops - 1):
            for s in range(SLOTS):
                sp.wait_ge(*used(i, s))
                net.fetch(sp, w, i + 1, s)
    elif w.loops > 1:
        with sp.Fori(0, w.loops - 1) as i:
            for s in range(SLOTS):
                sp.wait_ge(*used(i, s))
                net.fetch(sp, w, i + 1, s)
    if w.loops:
        for s in range(w.tail):
            sp.wait_ge(*used(w.loops - 1, s))
            net.fetch(sp, w, w.loops, s)
    if following:
        for s in range(following.first()):
            if w.loops or s < w.tail:
                sp.wait_ge(*used(w.loops - (s >= w.tail), s))
            net.fetch(sp, following, 0, s)


def turns(engine, w, turn, straight=False, peel=False):
    first = w.loops if straight else min(w.loops, 1) if peel else 0
    for i in range(first):
        turn(i, range(SLOTS))
    if w.loops - first == 1:
        turn(first, range(SLOTS))
    elif w.loops > first:
        with engine.Fori(first, w.loops) as i:
            turn(i, range(SLOTS))
    if w.tail:
        turn(w.loops, range(w.tail))


class Operand:

    def __init__(self, high, low, whole=None):
        self.high, self.low, self.whole = high, low, whole

    def tiles(self):
        return self.whole.shape[1]


class Split:

    def __init__(self, st):
        self.high_ready = [st.sem(f"high_ready{m}") for m in range(2)]
        self.split_ready = [st.sem(f"split_ready{m}") for m in range(2)]
        self.used = [st.sem(f"used{m}") for m in range(2)]
        self.operand_high = st.sem("operand_high")
        self.operand_split = st.sem("operand_split")


def is_first(i, s):
    return isinstance(i, int) and i == 0 and s == 0


def high_on_act(net, act, w, sems, x=None, take=None, straight=False):
    base = list(net.ring_base)

    def turn(i, slots):
        for s in slots:
            for m in range(2):
                if m == 0:
                    act.wait_ge(net.ring_loaded[s], 16 * (i + 1) + base[s])
                if not (isinstance(i, int) and i == 0 and s < 2):
                    act.wait_ge(sems.used[m], SLOTS * i + s - 1)
                act.activation(net.high(s, m)[:, 0:w.kts[s], :], net.ring_half(net.RING, s, m, w.kts[s]),
                               ACT.Copy).then_inc(sems.high_ready[m], 1)
                if is_first(i, s) and m == 0 and x is not None and x.whole is not None:
                    for t in range(x.tiles()):
                        act.activation(x.high[:, t], x.whole[:, t], ACT.Copy).then_inc(sems.operand_high, 1)
                if take and not is_first(i, s):
                    take(*((i, s - 1) if s else (i - 1, SLOTS - 1)), m)

    turns(act, w, turn, straight, peel=True)
    if take:
        for m in range(2):
            take(*w.last(), m)


def low_on_dve(net, dve, w, sems, x=None, take=None, straight=False):
    def turn(i, slots):
        for s in slots:
            for m in range(2):
                whole, low = (net.ring_half(ring, s, m, w.kts[s]) for ring in (net.RING, net.RINGR))
                dve.wait_ge(sems.high_ready[m], SLOTS * i + s + 1)
                net.nc.vector.tensor_tensor(low, whole, net.high(s, m)[:, 0:w.kts[s], :].bitcast(F32),
                                            ALU.subtract).then_inc(sems.split_ready[m], 1)
                if is_first(i, s) and m == 0 and x is not None and x.whole is not None:
                    for t in range(x.tiles()):
                        dve.wait_ge(sems.operand_high, t + 1)
                        net.nc.vector.tensor_tensor(x.low[:, t], x.whole[:, t], x.high[:, t].bitcast(F32),
                                                    ALU.subtract).then_inc(sems.operand_split, 1)
                if take and not is_first(i, s):
                    take(*((i, s - 1) if s else (i - 1, SLOTS - 1)), m)

    turns(dve, w, turn, straight, peel=True)
    if take:
        for m in range(2):
            take(*w.last(), m)


def product_on_pe(net, pe, w, sems, x, widths, tile_free, straight=False):
    def turn(i, slots):
        for s in slots:
            first = is_first(i, s)
            for m in range(2):
                pe.wait_ge(tile_free[m], SLOTS * i + s + 1)
                pe.wait_ge(sems.split_ready[m], SLOTS * i + s + 1)
                for kt in range(KT):
                    if first and m == 0 and x.whole is not None:
                        pe.wait_ge(sems.operand_split, kt + 1)
                    last = three_passes(net, net.ps[2 * s + m], s, m, kt, x, kt, widths(i, s), kt == 0, kt == KT - 1)
                last.then_inc(sems.used[m], 1)

    turns(pe, w, turn, straight, peel=True)


def three_passes(net, bank, s, m, kt, x, at, n, start, stop):
    high, low = net.high(s, m)[:, kt, :], net.low(s, kt, m)
    x_high, x_low = x.high[:, at, 0:n], x.low[:, at, 0:n]
    net.nc.tensor.matmul(bank[:, 0:n], high, x_high, start=start, stop=False)
    net.nc.tensor.matmul(bank[:, 0:n], high, x_low, start=False, stop=False)
    return net.nc.tensor.matmul(bank[:, 0:n], low, x_high, start=False, stop=stop)


def deep_on_pe(net, pe, w, sems, x, n, tile_free):
    def turn(i, slots):
        for s in slots:
            part, group, at = s % w.depth, s // w.depth, sum(w.kts[s - s % w.depth:s])
            for m in range(2):
                if part == 0:
                    pe.wait_ge(tile_free[m], SLOTS // w.depth * i + group + 1)
                pe.wait_ge(sems.split_ready[m], SLOTS * i + s + 1)
                for kt in range(w.kts[s]):
                    last = three_passes(net, net.ps[2 * group + m], s, m, kt, x, at + kt, n, part == 0 and kt == 0,
                                        part == w.depth - 1 and kt == w.kts[s] - 1)
                last.then_inc(sems.used[m], 1)

    turns(pe, w, turn)


def modulation_stage(net, layer, w, following):
    nc = net.nc
    high, low = (net.PR[:, t:t + 16, :].rearrange("p t m -> p (t m)").rearrange("p (b m) -> p b m", b=SLOTS)
                 for t in (0, 16))
    rows = net.SC[0:4, 0:SLOTS * SW].rearrange("p (s m) -> p s m", m=SW)
    with Stage(net, f"mod{layer}") as st:
        own, c_split, high_ready, split_ready = (st.sem("dve_own"), st.sem("c_split"), st.sem("high_ready"),
                                                 st.sem("split_ready"))
        used, copied, turned = st.sem("used"), st.sem("copied"), st.sem("turned")
        base = list(net.ring_base)
        columns_at = net.ps[0][:, 0:96].rearrange("p (t n) -> p t n", n=2)

        @st.sync
        def _(sp):
            feed(net, sp, w, lambda i, s: (split_ready, SLOTS * i + s + 1), following)

        @st.scalar
        def _(act):
            def copy_rows(i, s):
                act.wait_ge(used, SLOTS * i + s + 1)
                if not (isinstance(i, int) and i == 0):
                    act.wait_ge(turned, SLOTS * (i - 1) + s + 1)
                act.activation(rows[:, s, :], net.ps[1 + s][0:4, 0:SW], ACT.Copy).then_inc(copied, 1)

            def turn(i, slots):
                for s in slots:
                    first = isinstance(i, int) and i == 0
                    act.wait_ge(net.ring_loaded[s], 16 * (i + 1) + base[s])
                    if not first:
                        act.wait_ge(used, SLOTS * (i - 1) + s + 1)
                    act.activation(high[:, s], net.RING[:, s, :], ACT.Copy).then_inc(high_ready, 1)
                    if s >= 2 or not first:
                        copy_rows(*((i, s - 2) if s >= 2 else (i - 1, s + 2)))

            turn(0, range(SLOTS))
            turn(1, range(SLOTS))
            with act.Fori(2, w.loops) as i:
                turn(i, range(SLOTS))
            for s in (SLOTS - 2, SLOTS - 1):
                copy_rows(w.loops - 1, s)

        @st.tensor
        def _(pe):
            pe.wait_ge(c_split, 1)

            def to_columns(i, s):
                pe.wait_ge(copied, SLOTS * i + s + 1)
                for m in range(2):
                    last = nc.tensor.matmul(columns_at[:, 2 * (SLOTS * i + s) + m, :], rows[:, s, P * m:P * m + P],
                                            net.CONST[0:4, C_FOLD:C_FOLD + 2], start=True, stop=True)
                last.then_inc(turned, 1)

            def turn(i, slots):
                for s in slots:
                    first = isinstance(i, int) and i == 0
                    if not first:
                        pe.wait_ge(copied, SLOTS * (i - 1) + s + 1)
                    pe.wait_ge(split_ready, SLOTS * i + s + 1)
                    for kt in range(KT):
                        c = net.CSPLIT[:, kt, :]
                        at = slice(SW * kt, SW * kt + SW)
                        nc.tensor.matmul(net.ps[1 + s][0:4, 0:SW], c, high[:, s, at], start=(kt == 0), stop=False)
                        last = nc.tensor.matmul(net.ps[1 + s][0:4, 0:SW], c, low[:, s, at], start=False,
                                                stop=(kt == KT - 1))
                    last.then_inc(used, 1)
                    if s >= 2 or not first:
                        to_columns(*((i, s - 2) if s >= 2 else (i - 1, s + 2)))

            turns(pe, w, turn, peel=True)
            for s in (SLOTS - 2, SLOTS - 1):
                to_columns(w.loops - 1, s)

        @st.vector
        def _(dve):
            link = Chain(dve, own)
            c_high, c_low = net.CSPLIT[:, :, 0:2], net.CSPLIT[:, :, 2:4]
            link(nc.vector.tensor_copy(c_high, net.CACT[:, :, :]))
            nc.vector.tensor_tensor(c_low, net.CACT[:, :, :], c_high.bitcast(F32), ALU.subtract).then_inc(c_split, 1)

            def turn(i, slots):
                for s in slots:
                    dve.wait_ge(high_ready, SLOTS * i + s + 1)
                    if not (isinstance(i, int) and i == 0):
                        dve.wait_ge(used, SLOTS * (i - 1) + s + 1)
                    nc.vector.tensor_tensor(low[:, s], net.RING[:, s, :], high[:, s].bitcast(F32),
                                            ALU.subtract).then_inc(split_ready, 1)

            turns(dve, w, turn, peel=True)
            dve.wait_ge(turned, SLOTS * w.loops)
            bias = COL[f"l{layer}_mod_b"]
            link(nc.vector.tensor_tensor(net.MOD[:, :, :], columns_at,
                                         net.PAR[:, bias:bias + 48].unsqueeze(2).to_broadcast([P, 48, 2]), ALU.add))
            for h in range(2):
                gain = COL[f"l{layer}_norm{h + 1}"]
                link(nc.vector.scalar_tensor_tensor(net.AFF[:, h], net.MOD[:, 24 * h + 8:24 * h + 16, :], 1.0,
                                                    net.PAR[:, gain:gain + 8].unsqueeze(2).to_broadcast([P, KT, 2]),
                                                    ALU.add, ALU.mult))
        net.spent(w)


def ada_stage(net, layer, half, n):
    nc, square = net.nc, net.PT
    with Stage(net, f"ada{layer}{half}") as st:
        squared, summed, scaled = st.sem("squared"), st.sem("summed"), st.sem("scaled")
        rstd_ready, act_own = st.sem("rstd_ready"), st.sem("act_own")
        total, rstd = net.ps[0][:, 0:n], net.SC[:, 0:n]
        parts = [(0, 0)] + ([(1, LAT)] if n > LAT else [])

        @st.scalar
        def _(act):
            for t in range(KT):
                act.activation(square[:, t, 0:n], net.XT[:, t, 0:n], ACT.Square).then_inc(squared, 1)
            inverse_roots(act, Chain(act, act_own), rstd_ready, [(summed, 1, rstd, total, 1.0 / D, net.eps(EPS))])
            for t in range(KT):
                act.wait_ge(scaled, t + 1)
                for j, at in parts:
                    act.activation(net.HT[:, t, at:at + LAT], net.HT[:, t, at:at + LAT], ACT.Identity,
                                   bias=net.MOD[:, 24 * half + t, j:j + 1])

        @st.tensor
        def _(pe):
            for t in range(KT):
                pe.wait_ge(squared, t + 1)
                last = nc.tensor.matmul(total, net.const(C_ONES), square[:, t, 0:n], start=(t == 0), stop=(t == KT - 1))
            last.then_inc(summed, 1)

        @st.vector
        def _(dve):
            dve.wait_ge(rstd_ready, 1)
            for t in range(KT):
                for j, at in parts:
                    last = nc.vector.scalar_tensor_tensor(net.HT[:, t, at:at + LAT], net.XT[:, t, at:at + LAT],
                                                          net.AFF[:, half, t, j:j + 1], rstd[:, at:at + LAT],
                                                          ALU.mult, ALU.mult)
                last.then_inc(scaled, 1)


def project_stage(net, name, w, x, widths, dst, following, straight=False, dst_tile=lambda n: n):
    with Stage(net, name) as st:
        sems = Split(st)
        tile_free = [st.sem(f"tile_free{m}") for m in range(2)]

        @st.sync
        def _(sp):
            feed(net, sp, w, lambda i, s: (sems.used[1], SLOTS * i + s + 1), following, straight)

        @st.tensor
        def _(pe):
            product_on_pe(net, pe, w, sems, x, widths, tile_free, straight)

        @st.scalar
        def _(act):
            for m in range(2):
                act.sem_inc(tile_free[m], SLOTS)

            def take(i, s, m):
                n = widths(i, s)
                act.wait_ge(sems.used[m], SLOTS * i + s + 1)
                act.activation(dst[:, dst_tile(2 * (SLOTS * i + s) + m), 0:n], net.ps[2 * s + m][:, 0:n],
                               ACT.Copy).then_inc(tile_free[m], 1)

            high_on_act(net, act, w, sems, x, take, straight)

        @st.vector
        def _(dve):
            low_on_dve(net, dve, w, sems, x, straight=straight)
        net.spent(w)


def relu_squared_stage(net, name, w, x, n, hidden, following):
    nc = net.nc
    with Stage(net, name) as st:
        sems = Split(st)
        raised, squared, high = ([st.sem(f"{what}{m}") for m in range(2)] for what in ("raised", "squared", "hidden_high"))

        @st.sync
        def _(sp):
            feed(net, sp, w, lambda i, s: (sems.used[1], SLOTS * i + s + 1), following)

        @st.tensor
        def _(pe):
            product_on_pe(net, pe, w, sems, x, lambda i, s: n, raised)

        @st.scalar
        def _(act):
            for m in range(2):
                act.sem_inc(raised[m], SLOTS)

            def take(i, s, m):
                act.wait_ge(sems.used[m], SLOTS * i + s + 1)
                act.activation(hidden.whole[:, 2 * (SLOTS * i + s) + m, :], net.ps[2 * s + m][:, 0:n],
                               ACT.Relu).then_inc(raised[m], 1)

            high_on_act(net, act, w, sems, x, take)

        @st.vector
        def _(dve):
            def take(i, s, m):
                low, top, whole = (v[:, 2 * (SLOTS * i + s) + m, :] for v in (hidden.low, hidden.high, hidden.whole))
                done = SLOTS * i + s + 1
                dve.wait_ge(raised[m], SLOTS + done)
                nc.vector.tensor_tensor(whole, whole, whole, ALU.mult).then_inc(squared[m], 1)
                dve.wait_ge(squared[m], done)
                nc.vector.tensor_scalar(top, whole, 1.0, None, ALU.mult).then_inc(high[m], 1)
                dve.wait_ge(high[m], done)
                nc.vector.tensor_tensor(low, whole, top.bitcast(F32), ALU.subtract)

            low_on_dve(net, dve, w, sems, x, take)
        net.spent(w)


def mixed_out_stage(net, name, w, x, n, following):
    with Stage(net, name) as st:
        sems = Split(st)
        tile_free = [st.sem(f"tile_free{m}") for m in range(2)]

        @st.sync
        def _(sp):
            feed(net, sp, w, lambda i, s: (sems.used[1], SLOTS * i + s + 1), following)

        @st.tensor
        def _(pe):
            product_on_pe(net, pe, w, sems, x, lambda i, s: n, tile_free)

        @st.scalar
        def _(act):
            high_on_act(net, act, w, sems, x)

        @st.vector
        def _(dve):
            for m in range(2):
                dve.sem_inc(tile_free[m], SLOTS)

            def take(i, s, m):
                dve.wait_ge(sems.used[m], SLOTS * i + s + 1)
                add_gated(net, 2 * (SLOTS * i + s) + m, net.ps[2 * s + m], 16, n)

            low_on_dve(net, dve, w, sems, x, take)
        net.spent(w)


def add_gated(net, tile, bank, gate, n):
    for j, at in ((0, 0), (1, LAT))[:n // LAT]:
        into = net.XT[:, tile, at:at + LAT]
        step = net.nc.vector.scalar_tensor_tensor(into, bank[:, at:at + LAT], net.MOD[:, gate + tile, j:j + 1], into,
                                                  ALU.mult, ALU.add)
    return step


def deep_stage(net, name, w, x, n, take, following):
    with Stage(net, name) as st:
        sems = Split(st)
        tile_free = [st.sem(f"tile_free{m}") for m in range(2)]
        across = SLOTS // w.depth

        @st.sync
        def _(sp):
            feed(net, sp, w, lambda i, s: (sems.used[1], SLOTS * i + s + 1), following)

        @st.tensor
        def _(pe):
            deep_on_pe(net, pe, w, sems, x, n, tile_free)

        @st.scalar
        def _(act):
            high_on_act(net, act, w, sems)

        @st.vector
        def _(dve):
            for m in range(2):
                dve.sem_inc(tile_free[m], across)

            def take_last(i, s, m):
                if s % w.depth == w.depth - 1:
                    dve.wait_ge(sems.used[m], SLOTS * i + s + 1)
                    group = s // w.depth
                    take(2 * (across * i + group) + m, net.ps[2 * group + m]).then_inc(tile_free[m], 1)

            low_on_dve(net, dve, w, sems, take=take_last)
        net.spent(w)


def first_fetch_stage(net, w):
    with Stage(net, "fetch") as st:
        @st.sync
        def _(sp):
            for s in range(w.first()):
                net.fetch(sp, w, 0, s)


def diff_prepare_stage(net):
    nc = net.nc
    values = net.SC[:, 0:2048].rearrange("p (t m) -> p t m", m=512)
    part = net.SC[:, 2048:2048 + 2 * LAT].rearrange("p (b m) -> p b m", m=LAT)
    with Stage(net, "diff_prepare") as st:
        rotated, added, turned, own = st.sem("rotated"), st.sem("added"), st.sem("turned"), st.sem("dve_own")

        @st.tensor
        def _(pe):
            for t in range(8):
                if t >= 4:
                    pe.wait_ge(added, t - 3)
                nc.tensor.matmul(net.ps[t % 4][:, 0:LAT], net.const(C_ROTA), net.PT[:, t, 0:LAT],
                                 start=True, stop=True).then_inc(rotated, 1)
            for t in range(NCH):
                for h in range(4):
                    last = nc.tensor.transpose(net.ps[4 + t][:, P * h:P * h + P],
                                               net.PT[:, 8 + h, CH * t:CH * t + CH], net.const(C_IDENT))
                last.then_inc(turned, 1)

        @st.scalar
        def _(act):
            for t in range(NCH):
                act.wait_ge(turned, t + 1)
                act.activation(values[:, t, :], net.ps[4 + t][:, :], ACT.Copy)

        @st.vector
        def _(dve):
            link = Chain(dve, own)
            for t in range(8):
                dve.wait_ge(rotated, t + 1)
                x = net.PT[:, t, 0:LAT]
                nc.vector.tensor_tensor(part[:, t % 2], net.ps[t % 4][:, 0:LAT], net.const(C_SINA, LAT),
                                        ALU.mult).then_inc(added, 1)
                link(nc.vector.tensor_tensor(x, x, net.const(C_COSA, LAT), ALU.mult))
                dve.wait_ge(added, t + 1)
                link(nc.vector.tensor_tensor(x, x, part[:, t % 2], ALU.add))


def diff_attention_stage(net):
    nc = net.nc
    near = [net.HT[:, t, :] for t in range(KT)] + [net.PT[:, t, :] for t in range(26, 32)]
    values = net.SC[:, 0:2048].rearrange("p (t m) -> p t m", m=512)
    prob = net.SC[:, 2048:4096].rearrange("p (b m k) -> p b m k", b=2, m=2)
    mixed = net.SC[:, 4096:5120].rearrange("p (b k) -> p b k", b=2)
    mixed_t = net.SC[:, 5120:6144].rearrange("p (b k) -> p b k", b=2)
    stat = net.SC[:, 6144:6144 + 8 * 16].rearrange("p (u n) -> p u n", n=8)
    units = [(h, q) for h in range(4) for q in range(NCH)]
    first_key = lambda q: 0 if q < 2 else 2
    scale = 64 ** -0.5
    with Stage(net, "diff_attention") as st:
        scored, max_ready, exp_ready = st.sem("scored"), st.sem("max_ready"), st.sem("exp_ready")
        mixed_ready, turned, turned_copied = st.sem("mixed_ready"), st.sem("turned"), st.sem("turned_copied")
        out_ready, out_taken, own = st.sem("out_ready"), st.sem("out_taken"), st.sem("dve_own")
        near_ready, damped = st.sem("near_ready"), st.sem("damped")

        @st.gpsimd
        def _(pool):
            by_part = lambda v: v.rearrange("p (s m) -> p s m", m=LAT)
            for t, sums in enumerate(near):
                of, into = by_part(net.PT[:, 12 + t, :]), by_part(sums)
                pool.tensor_tensor(into[:, :, 1:LAT - 1], of[:, :, 0:LAT - 2], of[:, :, 2:LAT],
                                   ALU.add).then_inc(near_ready, 1)
                pool.tensor_copy(into[:, :, 0:1], of[:, :, 1:2]).then_inc(near_ready, 1)
                pool.tensor_copy(into[:, :, LAT - 1:LAT], of[:, :, LAT - 2:LAT - 1]).then_inc(near_ready, 1)

        @st.tensor
        def _(pe):
            def score(u):
                h, q = units[u]
                if u >= 2:
                    pe.wait_ge(exp_ready, 2 * (u - 1))
                k0 = first_key(q) * P
                for m in range(2):
                    rows = slice(64 * m, 64 * m + 64)
                    last = nc.tensor.matmul(net.ps[2 * (u % 2) + m][:, k0:TOK], net.PT[rows, h, P * q:P * q + P],
                                            net.PT[rows, 4 + h, k0:TOK], start=True, stop=True)
                last.then_inc(scored, 1)

            def weigh(u):
                h, q = units[u]
                pe.wait_ge(turned_copied, u + 1)
                if q == 0 and h >= 2:
                    pe.wait_ge(out_taken, h - 1)
                for t in range(first_key(q), NCH):
                    last = nc.tensor.matmul(net.ps[6 + h % 2][:, P * q:P * q + P], values[:, t, P * h:P * h + P],
                                            mixed_t[:, u % 2, P * t:P * t + P],
                                            start=(t == first_key(q)), stop=(t == NCH - 1))
                last.then_inc(out_ready, 1)

            score(0)
            score(1)
            for u, (h, q) in enumerate(units):
                if u + 2 < len(units):
                    score(u + 2)
                pe.wait_ge(mixed_ready, u + 1)
                if u >= 2:
                    pe.wait_ge(turned_copied, u - 1)
                for t in range(first_key(q), NCH):
                    last = nc.tensor.transpose(net.ps[4 + u % 2][:, P * t:P * t + P],
                                               mixed[:, u % 2, P * t:P * t + P], net.const(C_IDENT))
                last.then_inc(turned, 1)
                if u:
                    weigh(u - 1)
            weigh(len(units) - 1)

        @st.scalar
        def _(act):
            def exps(u):
                k0 = first_key(units[u][1]) * P
                act.wait_ge(max_ready, u + 1)
                if u >= 2:
                    act.wait_ge(mixed_ready, u - 1)
                for m in range(2):
                    act.activation(prob[:, u % 2, m, k0:TOK], net.ps[2 * (u % 2) + m][:, k0:TOK], ACT.Exp,
                                   bias=stat[:, u, m:m + 1], scale=scale,
                                   accum_out=stat[:, u, 2 + m:3 + m]).then_inc(exp_ready, 1)

            exps(0)
            exps(1)
            for u, (h, q) in enumerate(units):
                k0 = first_key(q) * P
                act.wait_ge(turned, u + 1)
                if u >= 2:
                    act.wait_ge(out_ready, u - 1)
                act.activation(mixed_t[:, u % 2, k0:TOK], net.ps[4 + u % 2][:, k0:TOK],
                               ACT.Copy).then_inc(turned_copied, 1)
                if u + 2 < len(units):
                    exps(u + 2)
                t = u - 2
                if t >= 0:
                    f = net.PT[:, 12 + t, :]
                    act.wait_ge(near_ready, 3 * (t + 1))
                    act.activation(f, f, ACT.Copy, scale=net.DER[:, 14 + t:15 + t]).then_inc(damped, 1)

        @st.vector
        def _(dve):
            link = Chain(dve, own)

            def maxima(u):
                k0 = first_key(units[u][1]) * P
                dve.wait_ge(scored, u + 1)
                for m in range(2):
                    link(nc.vector.reduce_max(stat[:, u, m:m + 1], net.ps[2 * (u % 2) + m][:, k0:TOK], AX_X))
                nc.vector.tensor_scalar(stat[:, u, 0:2], stat[:, u, 0:2], -scale, None,
                                        ALU.mult).then_inc(max_ready, 1)

            def shift(t):
                f = net.PT[:, 12 + t, :]
                dve.wait_ge(damped, t + 1)
                nc.vector.scalar_tensor_tensor(f, near[t], net.DER[:, t:t + 1], f, ALU.mult, ALU.add)

            maxima(0)
            maxima(1)
            for u, (h, q) in enumerate(units):
                k0 = first_key(q) * P
                dve.wait_ge(exp_ready, 2 * (u + 1))
                link(nc.vector.reciprocal(stat[:, u, 4:6], stat[:, u, 2:4]))
                link(nc.vector.tensor_tensor(stat[:, u, 5:6], stat[:, u, 5:6], net.LAM[:, 0:1], ALU.mult))
                link(nc.vector.tensor_scalar(prob[:, u % 2, 1, k0:TOK], prob[:, u % 2, 1, k0:TOK],
                                             stat[:, u, 5:6], None, ALU.mult))
                if u >= 2:
                    dve.wait_ge(turned, u - 1)
                nc.vector.scalar_tensor_tensor(mixed[:, u % 2, k0:TOK], prob[:, u % 2, 0, k0:TOK], stat[:, u, 4:5],
                                               prob[:, u % 2, 1, k0:TOK], ALU.mult, ALU.add).then_inc(mixed_ready, 1)
                if u + 2 < len(units):
                    maxima(u + 2)
                t = u - 3
                if t >= 0:
                    shift(t)
                if q == 1 and h >= 1:
                    dve.wait_ge(out_ready, 4 * h)
                    nc.vector.tensor_copy(net.OT[:, h - 1, :], net.ps[6 + (h - 1) % 2][:, :]).then_inc(out_taken, 1)
            shift(len(near) - 1)
            dve.wait_ge(out_ready, len(units))
            nc.vector.tensor_copy(net.OT[:, 3, :], net.ps[7][:, :])


def inverse_roots(act, own, ready, steps):
    for n, (sem, value, into, of, scale, eps) in enumerate(steps):
        act.wait_ge(sem, value)
        step = act.activation(into, of, ACT.Ln, scale=scale, bias=eps)
        if n + 1 < len(steps):
            step.then_inc(own.sem, 1)
            own.n += 1
    own(step)
    for _, _, into, _, _, _ in steps:
        act.activation(into, into, ACT.Exp, scale=-0.5).then_inc(ready, 1)


def group_norm_stage(net, name, groups, n, eps, adds=()):
    nc = net.nc
    with Stage(net, name) as st:
        squared, summed, rstd_ready = st.sem("squared"), st.sem("summed"), st.sem("rstd_ready")
        own, act_own = st.sem("dve_own"), st.sem("act_own")
        steps = [t for g in groups for t in zip(g[0], g[3])]

        @st.scalar
        def _(act):
            link = Chain(act, act_own)
            for src, square in steps:
                act.activation(square, src, ACT.Square).then_inc(squared, 1)
            inverse_roots(act, link, rstd_ready, [(summed, g + 1, squares[0], net.ps[g % 8][:, 0:n],
                                                   1.0 / (P * len(srcs)), net.eps(eps))
                                                  for g, (srcs, _, _, squares) in enumerate(groups)])

        @st.tensor
        def _(pe):
            at = 0
            for g, (srcs, _, _, squares) in enumerate(groups):
                for k, square in enumerate(squares):
                    at += 1
                    pe.wait_ge(squared, at)
                    last = nc.tensor.matmul(net.ps[g % 8][:, 0:n], net.const(C_ONES), square,
                                            start=(k == 0), stop=(k == len(squares) - 1))
                last.then_inc(summed, 1)

        @st.vector
        def _(dve):
            link = Chain(dve, own)
            for g, (srcs, dsts, gains, squares) in enumerate(groups):
                dve.wait_ge(rstd_ready, g + 1)
                for src, dst, gain in zip(srcs, dsts, gains):
                    last = nc.vector.scalar_tensor_tensor(dst, src, gain, squares[0], ALU.mult, ALU.mult)
                if adds:
                    link(last)
                for dst, x in zip(dsts, adds):
                    nc.vector.tensor_tensor(x, x, dst, ALU.add)


def rwkv_prepare_stage(net):
    nc = net.nc
    r0, k0, lora, gate = 12, 16, 24, 25
    kk = net.HT[:, 4:8, :]
    b = net.PT[:, 26:30, :]
    square = net.SC[:, 3584:3584 + 2048].rearrange("p (t m) -> p t m", m=TOK)
    norm = net.SC[:, 5632:5632 + 2048].rearrange("p (t m) -> p t m", m=TOK)
    with Stage(net, "rwkv_prepare") as st:
        own, act_own = st.sem("dve_own"), st.sem("act_own")
        tanh_ready, a_summed, a_ready = st.sem("tanh_ready"), st.sem("a_summed"), st.sem("a_ready")
        squared, normed, floor_ready, root_ready = (st.sem("squared"), st.sem("normed"), st.sem("floor_ready"),
                                                    st.sem("root_ready"))

        @st.vector
        def _(dve):
            link = Chain(dve, own)
            for t in range(4):
                dve.wait_ge(normed, t + 1)
                nc.vector.tensor_scalar(norm[:, t], net.ps[4 + t][:, :], 1e-24, None, ALU.max).then_inc(floor_ready, 1)
            for t in range(4):
                k = net.PT[:, k0 + t, :]
                dve.wait_ge(root_ready, t + 1)
                link(nc.vector.scalar_tensor_tensor(kk[:, t, :], k, net.par("l0_k_k", t), norm[:, t], ALU.mult, ALU.mult))
                dve.wait_ge(a_ready, t + 1)
                link(nc.vector.tensor_scalar(norm[:, t], b[:, t, :], net.par("l0_k_a", t), net.DER[:, 28 + t:29 + t],
                                             ALU.mult, ALU.add))
                link(nc.vector.tensor_tensor(k, k, norm[:, t], ALU.mult))
                link(nc.vector.tensor_tensor(b[:, t, :], b[:, t, :], kk[:, t, :], ALU.mult))

        @st.scalar
        def _(act):
            link = Chain(act, act_own)
            for t in range(4):
                act.activation(square[:, t], net.PT[:, k0 + t, :], ACT.Square,
                               scale=net.par("l0_k_k", t)).then_inc(squared, 1)
            act.activation(net.PT[0:64, lora, :], net.PT[0:64, lora, :], ACT.Tanh).then_inc(tanh_ready, 1)
            act.activation(net.PT[:, gate, :], net.PT[:, gate, :], ACT.Sigmoid)
            for t in range(4):
                act.wait_ge(a_summed, t + 1)
                act.activation(b[:, t, :], net.ps[t][:, :], ACT.Sigmoid, bias=net.par("l0_a0", t)).then_inc(a_ready, 1)
            inverse_roots(act, link, root_ready, [(floor_ready, t + 1, norm[:, t], norm[:, t], 1.0, 0.0)
                                                  for t in range(4)])

        @st.tensor
        def _(pe):
            for t in range(4):
                nc.tensor.matmul(net.ps[t][:, :], net.LORA[64:128, 0, P * t:P * t + P], net.PT[64:128, lora, :],
                                 start=True, stop=True).then_inc(a_summed, 1)
            for t in range(4):
                pe.wait_ge(squared, t + 1)
                nc.tensor.matmul(net.ps[4 + t][:, :], net.const(C_BLK), square[:, t], start=True,
                                 stop=True).then_inc(normed, 1)


class RwkvMemory:

    def __init__(self, net):
        chunks = lambda v: v.rearrange("p t (c m) -> p t c m", m=CH)
        flat = lambda v, n: v.rearrange("p t m -> p (t m)")[:, 0:n]
        self.r, self.k, self.v = (chunks(net.PT[:, n:n + 4, :]) for n in (12, 16, 20))
        self.kk, self.b = chunks(net.HT[:, 4:8, :]), chunks(net.PT[:, 26:30, :])
        self.kr = flat(net.PT[:, 0:8, :], 4096).rearrange("p (t c n m) -> p t c n m", t=4, c=NCH, n=2)
        self.bd, self.kd = chunks(net.PT[:, 8:12, :]), chunks(net.HT[:, 0:4, :])
        self.sig, self.cum = (net.SC[:, n:n + 2048].rearrange("p (t c m) -> p t c m", t=4, c=NCH) for n in (0, 2048))
        self.vtok = net.SC[:, 4096:6144].rearrange("p (c m) -> p c m", m=512)
        self.state = net.SC[:, 6144:6656].rearrange("p (t m) -> p t m", m=P)
        self.rhs, self.minus_u = net.SC[:, 6656:7168], net.SC[:, 7168:7680]
        small = net.SC[:, 7680:7680 + 64].rearrange("p (n t c) -> p n t c", n=4, t=4)
        self.mid, self.end, self.carry = small[:, 0], small[:, 1], small[:, 2]
        self.btok, self.ktok = net.PT[:, 30, :], net.PT[:, 31, :]
        ring = net.RING[:, :, :].rearrange("p s m -> p (s m)")
        self.grams = [place.rearrange("p (h m) -> p h m", m=512) for place in (ring[:, 0:4096], net.SC[:, 0:4096])]
        four = ring[:, 4096:8192].rearrange("p (q n h m) -> p q n h m", q=2, n=4, h=4)
        self.level, self.inv, self.first_inv_t, self.y = (four[:, :, n] for n in range(4))
        self.out = chunks(net.OT[:, 4:8, :])

    def inv_t(self, order, j, q):
        return (self.bd, self.kd)[q][:, :, order[j - 1], :] if j else self.first_inv_t[:, q]


def rwkv_decay_stage(net, d):
    nc, mem = net.nc, RwkvMemory(net)
    order = [2, 3, 0, 1] if d == 0 else [3, 2, 1, 0]
    mid, end = (63, CH - 1) if d == 0 else (64, 0)
    flat = lambda v: v.rearrange("p t c m -> p (t c) m")
    with Stage(net, f"rwkv_decay{d}") as st:
        summed, gated, cum_ready, exped, own = (st.sem("summed"), st.sem("gated"), st.sem("cum_ready"),
                                                st.sem("exped"), st.sem("dve_own"))
        turned, carry_ready = st.sem("turned"), st.sem("carry_ready")

        @st.tensor
        def _(pe):
            for t in range(4):
                nc.tensor.matmul(net.ps[t][:, :], net.LORA[0:64, d, P * t:P * t + P], net.PT[0:64, 24, :],
                                 start=True, stop=True).then_inc(summed, 1)
            if d == 0:
                for c in range(NCH):
                    for t in range(4):
                        last = nc.tensor.transpose(net.ps[4 + c][:, P * t:P * t + P], mem.v[:, t, c, :],
                                                   net.const(C_IDENT))
                    last.then_inc(turned, 1)

        @st.scalar
        def _(act):
            bias = "l0_w0_f" if d == 0 else "l0_w0_b"
            for t in range(4):
                act.wait_ge(summed, t + 1)
                act.activation(mem.sig[:, t].rearrange("p c m -> p (c m)"), net.ps[t][:, :], ACT.Sigmoid,
                               bias=net.par(bias, t)).then_inc(gated, 1)
            if d == 0:
                for c in range(NCH):
                    act.wait_ge(turned, c + 1)
                    act.activation(mem.vtok[:, c, :], net.ps[4 + c][:, :], ACT.Copy)
            kr = mem.kr.rearrange("p t c n m -> p (t c) n m")
            act.wait_ge(cum_ready, 1)
            act.activation(kr[:, :, 1, :], flat(mem.cum), ACT.Exp, scale=-DECAY).then_inc(exped, 1)
            act.activation(flat(mem.bd), flat(mem.cum), ACT.Exp, scale=DECAY).then_inc(exped, 1)
            act.wait_ge(cum_ready, 2)
            act.activation(kr[:, :, 0, :], flat(mem.sig), ACT.Exp, scale=-DECAY).then_inc(exped, 1)
            act.wait_ge(carry_ready, 1)
            act.activation(mem.carry[:, :, 0:3], mem.carry[:, :, 0:3], ACT.Exp, scale=-DECAY)

        @st.vector
        def _(dve):
            link = Chain(dve, own)
            ones = net.const(C_ONES)
            for t in range(4):
                dve.wait_ge(gated, t + 1)
                for c in range(NCH):
                    into, of = mem.cum[:, t, c, :], mem.sig[:, t, c, :]
                    if d:
                        into, of = into[:, ::-1], of[:, ::-1]
                    last = nc.vector.tensor_tensor_scan(into, ones, of, 0.0, ALU.mult, ALU.add)
            link(last)
            link(nc.vector.tensor_copy(mem.mid, mem.cum[:, :, :, mid]))
            link(nc.vector.tensor_copy(mem.end, mem.cum[:, :, :, end]))
            nc.vector.tensor_tensor(flat(mem.cum), flat(mem.cum),
                                    mem.mid.rearrange("p t c -> p (t c)").unsqueeze(2).to_broadcast([P, 16, CH]),
                                    ALU.subtract).then_inc(cum_ready, 1)
            dve.wait_ge(cum_ready, 1)
            nc.vector.tensor_tensor(flat(mem.sig), flat(mem.cum), flat(mem.sig), ALU.subtract).then_inc(cum_ready, 1)
            for j in range(3):
                c, after = order[j], order[j + 1]
                link(nc.vector.tensor_tensor(mem.carry[:, :, j], mem.end[:, :, c], mem.mid[:, :, c], ALU.subtract))
                step = nc.vector.tensor_tensor(mem.carry[:, :, j], mem.carry[:, :, j], mem.mid[:, :, after], ALU.add)
                step.then_inc(carry_ready, 1) if j == 2 else link(step)
            kr = mem.kr.rearrange("p t c n m -> p (t c) n m")
            dve.wait_ge(exped, 2)
            nc.vector.tensor_tensor(kr[:, :, 1, :], kr[:, :, 1, :], flat(mem.r), ALU.mult)
            link(nc.vector.tensor_tensor(flat(mem.kd), flat(mem.bd), flat(mem.k), ALU.mult))
            nc.vector.tensor_tensor(flat(mem.bd), flat(mem.bd), flat(mem.b), ALU.mult)
            dve.wait_ge(exped, 3)
            nc.vector.tensor_tensor(kr[:, :, 0, :], kr[:, :, 0, :], flat(mem.kk), ALU.mult)


def rwkv_chunks_stage(net, d):
    nc, mem = net.nc, RwkvMemory(net)
    order = [2, 3, 0, 1] if d == 0 else [3, 2, 1, 0]
    mask4 = net.const(C_MASK4 + 512 * d, 512)
    level_mask = lambda lv: net.const(C_LEVEL + P * (7 * d + lv)).unsqueeze(1).to_broadcast([P, 4, P])
    ident = net.const(C_IDENT)
    four = lambda bank: bank[:, :].rearrange("p (h m) -> p h m", m=P)
    head = lambda h: (h // 2, slice(64 * (h % 2), 64 * (h % 2) + 64))
    inv_t = lambda j, q: mem.inv_t(order, j, q)
    LV = range(1, 7)
    EVEN_ODD = (0, 2, 4, 6, 1, 3, 5, 7)
    with Stage(net, f"rwkv_chunks{d}") as st:
        gram_ready, gram_masked = st.sem("gram_ready"), st.sem("gram_masked")
        start_ready, start_turned, start_copied = st.sem("start_ready"), st.sem("start_turned"), st.sem("start_copied")
        level_ready, y_ready, y_copied = st.sem("level_ready"), st.sem("y_ready"), st.sem("y_copied")
        dd_ready, inv_doubled, doubled = st.sem("dd_ready"), st.sem("inv_doubled"), st.sem("doubled")
        rhs_ready, rhs_copied, u_ready, u_copied = st.sem("rhs_ready"), st.sem("rhs_copied"), st.sem("u_ready"), st.sem("u_copied")
        tok_turned, tok_copied = st.sem("tok_turned"), st.sem("tok_copied")
        out_ready, out_taken, state_summed, state_ready = (st.sem("out_ready"), st.sem("out_taken"),
                                                           st.sem("state_summed"), st.sem("state_ready"))
        own = st.sem("dve_own")

        @st.tensor
        def _(pe):
            def token_products(j, heads):
                c = order[j]
                for h in heads:
                    t, rows = head(h)
                    bank = net.ps[h % 2]
                    if 8 * j + h >= 2:
                        pe.wait_ge(gram_masked, 8 * j + h - 1)
                    both = mem.kr[rows, t, c].rearrange("p n m -> p (n m)")
                    nc.tensor.matmul(bank[:, 0:256], mem.bd[rows, t, c, :], both, start=True, stop=True)
                    nc.tensor.matmul(bank[:, 256:512], mem.kd[rows, t, c, :], both,
                                     start=True, stop=True).then_inc(gram_ready, 1)

            token_products(0, range(8))
            for j, c in enumerate(order):
                gram = mem.grams[j % 2]
                for q in range(2):
                    pe.wait_ge(start_ready, 2 * j + q + 1)
                    if j:
                        pe.wait_ge(tok_copied, 2 * j)
                    for h in range(4):
                        last = nc.tensor.transpose(net.ps[4 + q][:, P * h:P * h + P], inv_t(j, q)[:, h, :], ident)
                    last.then_inc(start_turned, 1)
                for lv in LV:
                    n = 12 * j + 2 * (lv - 1)
                    for q in range(2):
                        if lv == 1:
                            pe.wait_ge(start_copied, 2 * j + q + 1)
                        else:
                            pe.wait_ge(inv_doubled, 10 * j + 2 * (lv - 2) + q + 1)
                        pe.wait_ge(level_ready, n + q + 1)
                        for h in range(4):
                            last = nc.tensor.matmul(four(net.ps[2 + q])[:, h, :], mem.level[:, q, h, :],
                                                    mem.inv[:, q, h, :], start=True, stop=True)
                        last.then_inc(y_ready, 1)
                    for q in range(2):
                        pe.wait_ge(y_copied, n + q + 1)
                        if lv > 1:
                            pe.wait_ge(doubled, n - 2 + q + 1)
                        if j and lv == 1:
                            pe.wait_ge(out_taken if q else state_ready, j)
                        for h in range(4):
                            if lv < 6:
                                nc.tensor.matmul(four(net.ps[4 + q])[:, h, :], inv_t(j, q)[:, h, :],
                                                 mem.y[:, q, h, :], start=True, stop=True)
                            last = nc.tensor.matmul(four(net.ps[6 + q])[:, h, :], mem.y[:, q, h, :],
                                                    inv_t(j, q)[:, h, :], start=True, stop=True)
                        last.then_inc(dd_ready, 1)
                if j < 3:
                    for bank, part in ((net.ps[4], mem.bd), (net.ps[5], mem.kd)):
                        for t in range(4):
                            last = nc.tensor.transpose(bank[:, P * t:P * t + P], part[:, t, c, :], ident)
                        last.then_inc(tok_turned, 1)
                pe.wait_ge(y_copied, 12 * (j + 1))
                if j:
                    pe.wait_ge(state_ready, j)
                for h in range(8):
                    t, v = h // 2, slice(64 * h, 64 * h + 64)
                    if j and h % 2 == 0:
                        nc.tensor.matmul(net.ps[2][:, P * t:P * t + P], mem.kr[:, t, c, 0, :], mem.state[:, t, :],
                                         start=True, stop=False)
                    last = nc.tensor.matmul(net.ps[2][:, v], gram[:, h, 256:384], mem.vtok[:, c, v],
                                            start=(j == 0), stop=(j == 0 or h % 2 == 1))
                last.then_inc(rhs_ready, 1)
                if j < 3:
                    token_products(j + 1, range(0, 4))
                pe.wait_ge(rhs_copied, j + 1)
                pe.wait_ge(doubled, 12 * (j + 1))
                for h in range(8):
                    last = nc.tensor.matmul(net.ps[3][:, 64 * h:64 * h + 64], inv_t(j, h // 4)[:, h % 4, :],
                                            mem.rhs[:, 64 * h:64 * h + 64], start=True, stop=True)
                last.then_inc(u_ready, 1)
                if j < 3:
                    token_products(j + 1, range(4, 8))
                pe.wait_ge(u_copied, j + 1)
                if j < 3:
                    pe.wait_ge(tok_copied, 2 * (j + 1))
                    for h in EVEN_ODD:
                        t, rows = head(h)
                        into, v = net.ps[6][rows, 64 * t:64 * t + 64], slice(64 * h, 64 * h + 64)
                        nc.tensor.matmul(into, mem.ktok[:, v], mem.vtok[:, c, v], start=True, stop=False)
                        last = nc.tensor.matmul(into, mem.btok[:, v], mem.minus_u[:, v], start=False, stop=True)
                    last.then_inc(state_summed, 1)
                for h in range(8):
                    t, rows = head(h)
                    into, v = net.ps[7][rows, P * t:P * t + P], slice(64 * h, 64 * h + 64)
                    if j and h % 2 == 0:
                        nc.tensor.matmul(net.ps[7][:, P * t:P * t + P], mem.state[:, t, :], mem.kr[:, t, c, 1, :],
                                         start=True, stop=False)
                    nc.tensor.matmul(into, mem.vtok[:, c, v], gram[:, h, 384:512], start=(j == 0), stop=False)
                    last = nc.tensor.matmul(into, mem.minus_u[:, v], gram[:, h, 128:256], start=False, stop=True)
                last.then_inc(out_ready, 1)

        @st.gpsimd
        def _(pool):
            for j in range(NCH):
                for lv in LV:
                    n = 12 * j + 2 * (lv - 1)
                    for q in range(2):
                        if lv == 1:
                            pool.wait_ge(gram_masked, 8 * j + 4 * (q + 1))
                            if j:
                                pool.wait_ge(y_ready, 12 * j)
                        else:
                            pool.wait_ge(y_ready, n - 2 + q + 1)
                        pool.tensor_tensor(mem.level[:, q], mem.grams[j % 2][:, 4 * q:4 * q + 4, 0:P], level_mask(lv),
                                           ALU.mult).then_inc(level_ready, 1)

        @st.scalar
        def _(act):
            for j in range(NCH):
                for q in range(2):
                    act.wait_ge(start_turned, 2 * j + q + 1)
                    act.activation(mem.inv[:, q], four(net.ps[4 + q]), ACT.Copy).then_inc(start_copied, 1)
                for lv in LV:
                    n = 12 * j + 2 * (lv - 1)
                    for q in range(2):
                        act.wait_ge(y_ready, n + q + 1)
                        if n + q >= 2:
                            act.wait_ge(dd_ready, n + q - 1)
                        act.activation(mem.y[:, q], four(net.ps[2 + q]), ACT.Copy).then_inc(y_copied, 1)
                act.wait_ge(rhs_ready, j + 1)
                act.activation(mem.rhs, net.ps[2][:, :], ACT.Copy).then_inc(rhs_copied, 1)
                if j < 3:
                    for n, (bank, part) in enumerate(((net.ps[4], mem.btok), (net.ps[5], mem.ktok))):
                        act.wait_ge(tok_turned, 2 * j + n + 1)
                        if j:
                            act.wait_ge(state_summed, j)
                        act.activation(part, bank[:, :], ACT.Copy).then_inc(tok_copied, 1)

        @st.vector
        def _(dve):
            link = Chain(dve, own)

            def mask_products(j, q):
                gram = mem.grams[j % 2]
                if j >= 2 and q == 0:
                    dve.wait_ge(out_ready, j - 1)
                    dve.wait_ge(level_ready, 12 * (j - 1))
                for h in range(4 * q, 4 * q + 4):
                    dve.wait_ge(gram_ready, 8 * j + h + 1)
                    nc.vector.tensor_tensor(gram[:, h, :], net.ps[h % 2][:, :], mask4, ALU.mult).then_inc(gram_masked, 1)

            def start(j, q):
                dve.wait_ge(gram_masked, 8 * j + 4 * q + 4)
                link(nc.vector.tensor_tensor(inv_t(j, q), mem.grams[j % 2][:, 4 * q:4 * q + 4, 0:P], level_mask(0),
                                             ALU.mult))
                nc.vector.tensor_tensor(inv_t(j, q), ident.unsqueeze(1).to_broadcast([P, 4, P]), inv_t(j, q),
                                        ALU.subtract).then_inc(start_ready, 1)

            for q in range(2):
                mask_products(0, q)
                start(0, q)
            for j, c in enumerate(order):
                for lv in LV:
                    n = 12 * j + 2 * (lv - 1)
                    for q in range(2):
                        dve.wait_ge(dd_ready, n + q + 1)
                        if lv < 6:
                            nc.vector.tensor_tensor(mem.inv[:, q], mem.inv[:, q], four(net.ps[4 + q]),
                                                    ALU.subtract).then_inc(inv_doubled, 1)
                        nc.vector.tensor_tensor(inv_t(j, q), inv_t(j, q), four(net.ps[6 + q]),
                                                ALU.subtract).then_inc(doubled, 1)
                if j < 3:
                    mask_products(j + 1, 0)
                dve.wait_ge(u_ready, j + 1)
                nc.vector.tensor_scalar(mem.minus_u, net.ps[3][:, :], -1.0, None, ALU.mult).then_inc(u_copied, 1)
                if j < 3:
                    start(j + 1, 0)
                    mask_products(j + 1, 1)
                    start(j + 1, 1)
                    sums = net.ps[6][:, 0:256].rearrange("p (t m) -> p t m", m=64)
                    carry = mem.carry[:, :, j].unsqueeze(2).to_broadcast([P, 4, P])
                    dve.wait_ge(state_summed, j + 1)
                    dve.wait_ge(out_ready, j + 1)
                    if j == 0:
                        link(nc.vector.memset(mem.state, 0.0))
                    for o in (0, 64):
                        block = mem.state[o:o + 64, :, o:o + 64]
                        link(nc.vector.tensor_tensor(block, block, sums[o:o + 64], ALU.add))
                    nc.vector.tensor_tensor(mem.state, mem.state, carry, ALU.mult).then_inc(state_ready, 1)
                dve.wait_ge(out_ready, j + 1)
                if d == 0:
                    nc.vector.tensor_copy(mem.out[:, :, c, :], four(net.ps[7])).then_inc(out_taken, 1)
                else:
                    nc.vector.tensor_tensor(mem.out[:, :, c, :], mem.out[:, :, c, :], four(net.ps[7]),
                                            ALU.add).then_inc(out_taken, 1)


def rwkv_finish_stage(net):
    nc, eps = net.nc, 64e-5
    y = net.OT[:, 4:8, :]
    r, k, v = net.PT[:, 12:16, :], net.PT[:, 16:20, :], net.PT[:, 20:24, :]
    rk = net.PT[:, 0:4, :]
    square = net.PT[:, 4:8, :]
    rstd = net.PT[:, 8:12, :]
    with Stage(net, "rwkv_finish") as st:
        rk_ready, bonus_ready, gate_ready = st.sem("rk_ready"), st.sem("bonus_ready"), st.sem("gate_ready")
        mean_ready, centred, squared, var_ready = (st.sem("mean_ready"), st.sem("centred"), st.sem("squared"),
                                                   st.sem("var_ready"))
        root_ready, own, act_own = st.sem("root_ready"), st.sem("dve_own"), st.sem("act_own")
        bonus_used = st.sem("bonus_used")

        @st.gpsimd
        def _(pool):
            pool.tensor_tensor(rk[:, :, :], r, k, ALU.mult).then_inc(rk_ready, 1)

        @st.tensor
        def _(pe):
            for t in range(4):
                nc.tensor.matmul(net.ps[t][:, :], net.const(C_BLK), y[:, t, :], start=True, stop=True).then_inc(mean_ready, 1)
            for t in range(4):
                pe.wait_ge(squared, t + 1)
                nc.tensor.matmul(net.ps[4 + t][:, :], net.const(C_BLK), square[:, t, :], start=True,
                                 stop=True).then_inc(var_ready, 1)
            pe.wait_ge(centred, 4)
            pe.wait_ge(rk_ready, 5)
            for t in range(4):
                nc.tensor.matmul(net.ps[t][:, :], net.const(C_BLK), rk[:, t, :], start=True, stop=True).then_inc(bonus_ready, 1)
            for t in range(4):
                pe.wait_ge(root_ready, t + 1)
                nc.tensor.matmul(net.ps[4 + t][:, :], net.G2[:, P * t:P * t + P], net.PT[:, 25, :], start=True,
                                 stop=True).then_inc(gate_ready, 1)

        @st.scalar
        def _(act):
            link = Chain(act, act_own)
            act.wait_ge(rk_ready, 1)
            for t in range(4):
                act.activation(rk[:, t, :], rk[:, t, :], ACT.Copy, scale=net.par("l0_r_k", t)).then_inc(rk_ready, 1)
            for t in range(4):
                act.wait_ge(centred, t + 1)
                act.activation(square[:, t, :], y[:, t, :], ACT.Square).then_inc(squared, 1)
            inverse_roots(act, link, root_ready, [(var_ready, t + 1, rstd[:, t, :], net.ps[4 + t][:, :], 1.0 / 64,
                                                   net.eps(eps)) for t in range(4)])

        @st.vector
        def _(dve):
            link = Chain(dve, own)
            for t in range(4):
                dve.wait_ge(mean_ready, t + 1)
                nc.vector.scalar_tensor_tensor(y[:, t, :], net.ps[t][:, :], -1.0 / 64, y[:, t, :], ALU.mult,
                                               ALU.add).then_inc(centred, 1)
            dve.wait_ge(squared, 4)
            for t in range(4):
                dve.wait_ge(root_ready, t + 1)
                link(nc.vector.tensor_tensor(y[:, t, :], y[:, t, :], rstd[:, t, :], ALU.mult))
                link(nc.vector.tensor_scalar(y[:, t, :], y[:, t, :], net.par("l0_lnx_w", t), net.par("l0_lnx_b", t),
                                             ALU.mult, ALU.add))
                dve.wait_ge(bonus_ready, t + 1)
                link(nc.vector.tensor_tensor(rstd[:, t, :], net.ps[t][:, :], v[:, t, :], ALU.mult))
                link(nc.vector.tensor_tensor(y[:, t, :], y[:, t, :], rstd[:, t, :], ALU.add))
                dve.wait_ge(gate_ready, t + 1)
                link(nc.vector.tensor_tensor(y[:, t, :], y[:, t, :], net.ps[4 + t][:, :], ALU.mult))


def odd_projection(w):
    starts = [0, 256, 512, 768, 1024, 1280, 1552, 1808, 2064, 2320, 2576, 2832]
    views = [w[:, c:c + SW].rearrange("(t k) m -> k t m", k=P) for c in starts]
    latents_only = {0, 1, 5, 6, 10, 11}
    return (Weights(3, 0, lambda i, s: views[SLOTS * i + s]),
            lambda i, s: LAT if SLOTS * i + s in latents_only else TOK)


class SsdMemory:

    def __init__(self, net):
        sc = net.SC
        self.gate_down = sc[0:16, 0:512]
        (self.dt, self.la, self.cum, self.tot, self.to_end, self.e_cum, self.e_tot, self.x, self.e, self.s, self.s2,
         self.poly) = (sc[:, 512 + 64 * n:576 + 64 * n].rearrange("p (c h) -> p c h", h=16) for n in range(12))
        self.e_a = sc[:, 1280:1296]
        self.acc = sc[:, 1600:2624].rearrange("p (b m) -> p b m", m=TOK)
        self.xdt = sc[:, 1600:3648].rearrange("p (c d m) -> p c d m", c=2, d=2)
        self.state = sc[:, 3648:4672].rearrange("p (d m) -> p d m", d=2)
        self.cb = sc[:, 4672:5184].rearrange("p (d g m) -> p d g m", d=2, g=2)
        self.y = sc[:, 5184:6208].rearrange("p (c m) -> p c m", c=2)
        self.part = sc[:, 6208:6720]
        ht = net.HT[:, :, :].rearrange("p t m -> p (t m)")
        self.xtok = ht[:, 0:2048].rearrange("p (c m) -> p c m", c=NCH)
        self.btok = ht[:, 2048:3072].rearrange("p (c m) -> p c m", c=NCH)
        self.xw = ht[:, 3072:4096].rearrange("p (d m) -> p d m", d=2)
        self.att = net.PT[:, 24:32, :].rearrange("p (c t) (h m) -> p c (t h) m", c=2, m=P)


def ssd_steps_stage(net):
    nc, mem = net.nc, SsdMemory(net)
    with Stage(net, "ssd_steps") as st:
        dt_raw, down_ready, own, act_own = st.sem("dt_raw"), st.sem("down_ready"), st.sem("dve_own"), st.sem("act_own")
        abs_ready, e_ready, la_ready, cum_summed = (st.sem("abs_ready"), st.sem("e_ready"), st.sem("la_ready"),
                                                    st.sem("cum_summed"))
        cum_ready, e_a_ready = st.sem("cum_ready"), st.sem("e_a_ready")
        all_of = lambda v: v.rearrange("p c h -> p (c h)")
        per_head = lambda v: v.unsqueeze(1).to_broadcast([P, NCH, 16])

        @st.tensor
        def _(pe):
            for c in range(NCH):
                for kt in range(KT):
                    last = nc.tensor.matmul(net.ps[0][:, 16 * c:16 * c + 16], net.HT[:, kt, CH * c:CH * c + CH],
                                            net.WDG[:, kt, 0:16], start=(kt == 0), stop=(kt == KT - 1))
            last.then_inc(dt_raw, 1)
            for kt in range(KT):
                last = nc.tensor.matmul(net.ps[1][0:16, :], net.WDG[:, kt, 16:32], net.HT[:, kt, :],
                                        start=(kt == 0), stop=(kt == KT - 1))
            last.then_inc(down_ready, 1)
            pe.wait_ge(la_ready, 1)
            for c in range(NCH):
                for d, tri in enumerate((C_LE, C_GE)):
                    nc.tensor.matmul(net.ps[2][:, 16 * c + 8 * d:16 * c + 8 * d + 8], net.const(tri),
                                     mem.la[:, c, 8 * d:8 * d + 8], start=True, stop=True)
            nc.tensor.matmul(net.ps[3][:, 0:64], net.const(C_ONES), all_of(mem.la), start=True,
                             stop=True).then_inc(cum_summed, 1)

        @st.scalar
        def _(act):
            act.activation(mem.e_a, net.HEADROW[:, 16:32], ACT.Exp).then_inc(e_a_ready, 1)
            act.wait_ge(abs_ready, 1)
            act.activation(mem.e, mem.e, ACT.Exp, scale=-1.0).then_inc(e_ready, 1)
            act.wait_ge(down_ready, 1)
            act.activation(mem.gate_down, net.ps[1][0:16, :], ACT.Copy)
            act.wait_ge(cum_ready, 1)
            for into, of in ((mem.e_cum, mem.cum), (mem.e_tot, mem.tot), (mem.to_end, mem.to_end)):
                act.activation(into, of, ACT.Exp)

        @st.vector
        def _(dve):
            link = Chain(dve, own)
            raw = net.ps[0][:, 0:64].rearrange("p (c h) -> p c h", h=16)
            dve.wait_ge(dt_raw, 1)
            link(nc.vector.tensor_tensor(mem.x, raw, per_head(net.HEADROW[:, 0:16]), ALU.add))
            link(nc.vector.tensor_scalar(mem.s, mem.x, -1.0, None, ALU.mult))
            nc.vector.tensor_tensor(mem.e, mem.x, mem.s, ALU.max).then_inc(abs_ready, 1)
            dve.wait_ge(e_ready, 1)
            link(nc.vector.tensor_scalar(mem.s, mem.e, 2.0, None, ALU.add))
            link(nc.vector.reciprocal(mem.s, mem.s))
            link(nc.vector.tensor_tensor(mem.s, mem.s, mem.e, ALU.mult))
            link(nc.vector.tensor_tensor(mem.s2, mem.s, mem.s, ALU.mult))
            link(nc.vector.tensor_scalar(mem.poly, mem.s2, 1.0 / 15, None, ALU.mult))
            for odd in (13, 11, 9, 7, 5, 3):
                link(nc.vector.scalar_tensor_tensor(mem.poly, mem.poly, 1.0 / odd, mem.s2, ALU.add, ALU.mult))
            link(nc.vector.scalar_tensor_tensor(mem.poly, mem.poly, 1.0, mem.s, ALU.add, ALU.mult))
            link(nc.vector.tensor_scalar(mem.x, mem.x, 0.0, None, ALU.max))
            link(nc.vector.scalar_tensor_tensor(mem.dt, mem.poly, 2.0, mem.x, ALU.mult, ALU.add))
            dve.wait_ge(e_a_ready, 1)
            nc.vector.scalar_tensor_tensor(mem.la, mem.dt, -1.0, per_head(mem.e_a), ALU.mult, ALU.mult).then_inc(la_ready, 1)
            dve.wait_ge(cum_summed, 1)
            link(nc.vector.tensor_copy(all_of(mem.cum), net.ps[2][:, 0:64]))
            link(nc.vector.tensor_copy(all_of(mem.tot), net.ps[3][:, 0:64]))
            nc.vector.tensor_tensor(mem.to_end, mem.tot, mem.cum, ALU.subtract).then_inc(cum_ready, 1)


def ssd_conv_stage(net):
    nc, mem = net.nc, SsdMemory(net)
    with Stage(net, "ssd_conv") as st:
        summed, silu_ready, turned, own = st.sem("summed"), st.sem("silu_ready"), st.sem("turned"), st.sem("dve_own")

        @st.vector
        def _(dve):
            link = Chain(dve, own)
            for t in range(8):
                n = TOK if t < 6 else LAT
                x = net.PT[:, 4 + t, 0:n].rearrange("p (s m) -> p s m", m=LAT)
                acc = mem.acc[:, t % 2, 0:n].rearrange("p (s m) -> p s m", m=LAT)
                if t >= 2:
                    dve.wait_ge(silu_ready, t - 1)
                tap = lambda k: net.par("l1_conv_w", 8 * k + t)
                link(nc.vector.tensor_scalar(acc, x, tap(2), None, ALU.mult))
                for k in (0, 1, 3, 4):
                    o = k - 2
                    to, of = slice(max(0, -o), LAT - max(0, o)), slice(max(0, o), LAT - max(0, -o))
                    step = nc.vector.scalar_tensor_tensor(acc[:, :, to], x[:, :, of], tap(k), acc[:, :, to],
                                                          ALU.mult, ALU.add)
                    step.then_inc(summed, 1) if k == 4 else link(step)

        @st.scalar
        def _(act):
            for t in range(8):
                n = TOK if t < 6 else LAT
                act.wait_ge(summed, t + 1)
                act.activation(net.PT[:, 4 + t, 0:n], mem.acc[:, t % 2, 0:n], ACT.Silu,
                               bias=net.par("l1_conv_b", t)).then_inc(silu_ready, 1)
            for c in range(NCH):
                act.wait_ge(turned, 2 * c + 1)
                act.activation(mem.xtok[:, c, :], net.ps[2 * c][:, :], ACT.Copy)
                act.wait_ge(turned, 2 * c + 2)
                act.activation(mem.btok[:, c, :], net.ps[2 * c + 1][:, 0:256], ACT.Copy)

        @st.tensor
        def _(pe):
            pe.wait_ge(silu_ready, 6)
            for c in range(NCH):
                for n, (first, count) in enumerate(((4, 4), (8, 2))):
                    for t in range(count):
                        last = nc.tensor.transpose(net.ps[2 * c + n][:, P * t:P * t + P],
                                                   net.PT[:, first + t, CH * c:CH * c + CH], net.const(C_IDENT))
                    last.then_inc(turned, 1)


def ssd_scan_stage(net):
    nc, mem = net.nc, SsdMemory(net)
    heads = lambda v: v.rearrange("p (h m) -> p h m", m=64)
    wide = lambda v: v.unsqueeze(2).to_broadcast([P, 8, 64])
    updates = [(0, 2), (1, 3), (0, 3), (1, 2), (0, 0), (1, 1)]
    serves = {2: (0, 0), 3: (1, 1), 4: (0, 1), 5: (1, 0)}
    with Stage(net, "ssd_scan") as st:
        row_ready, row_used, exp_ready, att_ready = (st.sem("row_ready"), st.sem("row_used"), st.sem("exp_ready"),
                                                     st.sem("att_ready"))
        cb_ready, cb_masked, xdt_ready = st.sem("cb_ready"), st.sem("cb_masked"), st.sem("xdt_ready")
        y_ready, xw_ready, state_summed, state_ready = (st.sem("y_ready"), st.sem("xw_ready"), st.sem("state_summed"),
                                                        st.sem("state_ready"))
        served, served_used, own = st.sem("served"), st.sem("served_used"), st.sem("dve_own")

        @st.tensor
        def _(pe):
            for c in range(2):
                for n in range(4):
                    at = 4 * c + n
                    if at >= 2:
                        pe.wait_ge(row_used, at - 1)
                    for h in range(4 * n, 4 * n + 4):
                        last = nc.tensor.matmul(net.ps[at % 2][:, P * (h % 4):P * (h % 4) + P],
                                                mem.la[:, c, h:h + 1].to_broadcast([P, P]),
                                                net.const(C_LE if h < 8 else C_GE), start=True, stop=True)
                    last.then_inc(row_ready, 1)
                for g in range(2):
                    last = nc.tensor.matmul(net.ps[2 + c][:, P * g:P * g + P], net.PT[:, 8 + g, CH * c:CH * c + CH],
                                            net.PT[:, 10 + g, CH * c:CH * c + CH], start=True, stop=True)
                last.then_inc(cb_ready, 1)
            for n, (d, c) in enumerate(updates):
                pe.wait_ge(xw_ready, n + 1)
                if n >= 2:
                    pe.wait_ge(state_ready, n - 1)
                for g in range(2):
                    last = nc.tensor.matmul(net.ps[6 + d][:, 256 * g:256 * g + 256], mem.btok[:, c, P * g:P * g + P],
                                            mem.xw[:, d, 256 * g:256 * g + 256], start=True, stop=True)
                last.then_inc(state_summed, 1)
                if n < 2:
                    continue
                if n >= 4:
                    pe.wait_ge(served_used, n - 3)
                pe.wait_ge(state_ready, n + 1 if n < 4 else n + 1)
                to = serves[n][1]
                for g in range(2):
                    last = nc.tensor.matmul(net.ps[n % 2][:, 256 * g:256 * g + 256],
                                            net.PT[:, 10 + g, CH * to:CH * to + CH],
                                            mem.state[:, d, 256 * g:256 * g + 256], start=True, stop=True)
                last.then_inc(served, 1)
            pe.wait_ge(xdt_ready, 4)
            for c in range(2):
                pe.wait_ge(att_ready, 4 * (c + 1))
                for h in range(8):
                    v = slice(64 * h, 64 * h + 64)
                    for d in range(2):
                        last = nc.tensor.matmul(net.ps[4 + c][:, v], mem.att[:, c, 8 * d + h, :], mem.xdt[:, c, d, v],
                                                start=(d == 0), stop=(d == 1))
                last.then_inc(y_ready, 1)

        @st.gpsimd
        def _(pool):
            for c in range(2):
                for d in range(2):
                    pool.tensor_tensor(heads(mem.xdt[:, c, d, :]), heads(mem.xtok[:, c, :]),
                                       wide(mem.dt[:, c, 8 * d:8 * d + 8]), ALU.mult).then_inc(xdt_ready, 1)

        @st.scalar
        def _(act):
            for c in range(2):
                act.wait_ge(row_used, 4 * (c + 1))
                act.activation(mem.att[:, c], mem.att[:, c], ACT.Exp).then_inc(exp_ready, 1)

        @st.vector
        def _(dve):
            link = Chain(dve, own)
            link(nc.vector.tensor_tensor(mem.to_end, mem.to_end, mem.dt, ALU.mult))
            for c in range(2):
                for n in range(4):
                    dve.wait_ge(row_ready, 4 * c + n + 1)
                    for h in range(4 * n, 4 * n + 4):
                        last = nc.vector.tensor_scalar(mem.att[:, c, h, :],
                                                       net.ps[(4 * c + n) % 2][:, P * (h % 4):P * (h % 4) + P],
                                                       mem.cum[:, c, h:h + 1], 0.0, ALU.subtract, ALU.min)
                    last.then_inc(row_used, 1)
            for n, (d, c) in enumerate(updates):
                if n >= 2:
                    dve.wait_ge(state_summed, n - 1)
                nc.vector.tensor_tensor(heads(mem.xw[:, d, :]), heads(mem.xtok[:, c, :]),
                                        wide(mem.to_end[:, c, 8 * d:8 * d + 8]), ALU.mult).then_inc(xw_ready, 1)
                dve.wait_ge(state_summed, n + 1)
                if n < 2:
                    nc.vector.tensor_copy(mem.state[:, d, :], net.ps[6 + d][:, :]).then_inc(state_ready, 1)
                else:
                    if n >= 4:
                        dve.wait_ge(served, n - 3)
                    dve.wait_ge(state_ready, n)
                    link(nc.vector.tensor_tensor(heads(mem.state[:, d, :]), heads(mem.state[:, d, :]),
                                                 wide(mem.e_tot[:, c, 8 * d:8 * d + 8]), ALU.mult))
                    nc.vector.tensor_tensor(mem.state[:, d, :], mem.state[:, d, :], net.ps[6 + d][:, :],
                                            ALU.add).then_inc(state_ready, 1)
                    to = serves[n][1]
                    dve.wait_ge(served, n - 1)
                    into = mem.y[:, to, :] if n < 4 else mem.part
                    step = nc.vector.tensor_tensor(heads(into), heads(net.ps[n % 2][:, :]),
                                                   wide(mem.e_cum[:, to, 8 * d:8 * d + 8]), ALU.mult)
                    step.then_inc(served_used, 1)
                    dve.wait_ge(served_used, n - 1)
                    if n >= 4:
                        link(nc.vector.tensor_tensor(mem.y[:, to, :], mem.y[:, to, :], mem.part, ALU.add))
            for c in range(2):
                dve.wait_ge(cb_ready, c + 1)
                for d, tri in enumerate((C_LE, C_GE)):
                    if c:
                        dve.wait_ge(att_ready, 4)
                    for g in range(2):
                        link(nc.vector.tensor_tensor(mem.cb[:, d, g, :], net.ps[2 + c][:, P * g:P * g + P],
                                                     net.const(tri), ALU.mult))
                dve.wait_ge(exp_ready, c + 1)
                for d in range(2):
                    for g in range(2):
                        four = mem.att[:, c, 8 * d + 4 * g:8 * d + 4 * g + 4, :]
                        nc.vector.tensor_tensor(four, four, mem.cb[:, d, g, :].unsqueeze(1).to_broadcast([P, 4, P]),
                                                ALU.mult).then_inc(att_ready, 1)
            for c in range(2):
                dve.wait_ge(y_ready, c + 1)
                link(nc.vector.tensor_tensor(mem.y[:, c, :], mem.y[:, c, :], net.ps[4 + c][:, :], ALU.add))


def ssd_gate_stage(net):
    nc, mem = net.nc, SsdMemory(net)
    with Stage(net, "ssd_gate") as st:
        turned, z_ready, own = st.sem("turned"), st.sem("z_ready"), st.sem("dve_own")

        @st.tensor
        def _(pe):
            for t in range(4):
                for c in range(2):
                    last = nc.tensor.transpose(net.ps[t][:, P * c:P * c + P], mem.y[:, c, P * t:P * t + P],
                                               net.const(C_IDENT))
                last.then_inc(turned, 1)

        @st.scalar
        def _(act):
            act.activation(net.PT[:, 0:4, 0:LAT], net.PT[:, 0:4, 0:LAT], ACT.Silu).then_inc(z_ready, 1)

        @st.vector
        def _(dve):
            link = Chain(dve, own)
            dve.wait_ge(z_ready, 1)
            for t in range(4):
                dve.wait_ge(turned, t + 1)
                link(nc.vector.scalar_tensor_tensor(net.OT[:, t, 0:LAT], net.PT[:, 4 + t, 0:LAT], net.DSKIP[:, t:t + 1],
                                                    net.ps[t][:, 0:LAT], ALU.mult, ALU.add))
                link(nc.vector.tensor_tensor(net.OT[:, t, 0:LAT], net.OT[:, t, 0:LAT], net.PT[:, t, 0:LAT], ALU.mult))


class GlaMemory:

    def __init__(self, net):
        sc = net.SC
        self.gate_down = sc[0:16, 0:512]
        self.cum = sc[:, 512:2560].rearrange("p (d t c m) -> p d t c m", d=2, t=2, c=NCH)
        lat = lambda at: sc[:, at:at + 1024].rearrange("p (d t c m) -> p d t c m", d=2, t=2, c=2)
        self.q_in, self.k_in, self.q_state = lat(2560), lat(3584), lat(4608)
        half = lambda at: sc[:, at:at + 512].rearrange("p (d t c m) -> p d t c m", d=2, t=2, c=2)
        self.q_cross, self.k_cross = half(5632), half(6144)
        self.e_end = sc[:, 6656:6672].rearrange("p (d t c) -> p d t c", d=2, t=2)
        ht = net.HT[:, :, :].rearrange("p t m -> p (t m)")
        self.k_end = ht[:, 0:2048].rearrange("p (d t c m) -> p d t c m", d=2, t=2, c=NCH)
        self.vtok = ht[:, 2048:4096].rearrange("p (c m) -> p c m", c=NCH)
        pt = net.PT[:, 0:12, :].rearrange("p t m -> p (t m)")
        self.gate = pt[:, 0:2048].rearrange("p (d t m) -> p d t m", d=2, t=2)
        self.low = pt[:, 2048:4096].rearrange("p (d t m) -> p d t m", d=2, t=2)
        self.shift = pt[:, 4096:6144].rearrange("p (d t c m) -> p d t c m", d=2, t=2, c=NCH)
        pt = net.PT[:, 24:32, :].rearrange("p t m -> p (t m)")
        self.att = pt[:, 0:2048].rearrange("p (d c h m) -> p d c h m", d=2, c=2, h=4)
        self.state = pt[:, 2048:3072].rearrange("p (d c t m) -> p d c t m", d=2, c=2, t=2)
        self.ktok = pt[:, 3072:4096].rearrange("p (b m) -> p b m", b=4)


def gla_gates_stage(net):
    nc, mem = net.nc, GlaMemory(net)
    q, k = (net.PT[:, n:n + 2, :].rearrange("p t (c m) -> p t c m", m=CH) for n in (12, 14))
    tau = 1.0 / 16.0
    with Stage(net, "gla_gates") as st:
        gate_raw, low_ready, log_ready, turned = (st.sem("gate_raw"), st.sem("low_ready"), st.sem("log_ready"),
                                                  st.sem("turned"))
        own, act_own, shifted, exped = st.sem("dve_own"), st.sem("act_own"), st.sem("shifted"), st.sem("exped")

        @st.tensor
        def _(pe):
            for d in range(2):
                for t in range(2):
                    nc.tensor.matmul(net.ps[2 * d + t][:, :], net.GUP[:, d, P * t:P * t + P], mem.gate_down,
                                     start=True, stop=True).then_inc(gate_raw, 1)
            for c in range(NCH):
                for t in range(4):
                    last = nc.tensor.transpose(net.ps[4 + c][:, P * t:P * t + P], net.PT[:, 16 + t, CH * c:CH * c + CH],
                                               net.const(C_IDENT))
                last.then_inc(turned, 1)

        @st.scalar
        def _(act):
            link = Chain(act, act_own)
            bias = lambda d, t: net.par("l1_gk_b_f" if d == 0 else "l1_gk_b_b", t)
            every = mem.gate.rearrange("p d t m -> p (d t m)")
            for d in range(2):
                for t in range(2):
                    act.wait_ge(gate_raw, 2 * d + t + 1)
                    link(act.activation(mem.gate[:, d, t, :], net.ps[2 * d + t][:, :], ACT.Abs, bias=bias(d, t)))
            link(act.activation(every, every, ACT.Exp, scale=-1.0))
            act.activation(every, every, ACT.Ln, bias=1.0).then_inc(log_ready, 1)
            act.activation(net.PT[:, 20:24, 0:LAT], net.PT[:, 20:24, 0:LAT], ACT.Silu)
            for c in range(NCH):
                act.wait_ge(turned, c + 1)
                act.activation(mem.vtok[:, c, :], net.ps[4 + c][:, :], ACT.Copy)
            for d in range(2):
                qh, kh = ((64, 0), (0, 64))[d]
                lat = mem.shift[:, d, :, 0:2, :]
                act.wait_ge(shifted, 4 * d + 1)
                for t in range(2):
                    act.activation(mem.q_in[:, d, t], lat[:, t], ACT.Exp, scale=tau)
                    act.activation(mem.k_in[:, d, t], lat[:, t], ACT.Exp, scale=-tau).then_inc(exped, 1)
                act.wait_ge(shifted, 4 * d + 2)
                for t in range(2):
                    act.activation(mem.q_cross[:, d, t], lat[:, t, :, qh:qh + 64], ACT.Exp, scale=tau)
                    act.activation(mem.k_cross[:, d, t], lat[:, t, :, kh:kh + 64], ACT.Exp, scale=-tau).then_inc(exped, 1)
                act.wait_ge(shifted, 4 * d + 3)
                for t in range(2):
                    act.activation(mem.k_end[:, d, t], mem.shift[:, d, t], ACT.Exp, scale=-tau)
                    act.activation(mem.q_state[:, d, t], mem.cum[:, d, t, 0:2], ACT.Exp, scale=tau).then_inc(exped, 1)
                act.wait_ge(shifted, 4 * d + 4)
                act.activation(mem.e_end[:, d], mem.e_end[:, d], ACT.Exp, scale=tau)

        @st.vector
        def _(dve):
            link = Chain(dve, own)
            ones = net.const(C_ONES)
            for d in range(2):
                for t in range(2):
                    dve.wait_ge(gate_raw, 2 * d + t + 1)
                    dve.wait_ge(act_own, 2 * d + t + 1)
                    nc.vector.tensor_scalar(mem.low[:, d, t, :], net.ps[2 * d + t][:, :],
                                            net.par("l1_gk_b_f" if d == 0 else "l1_gk_b_b", t), 0.0, ALU.add,
                                            ALU.min).then_inc(low_ready, 1)
            dve.wait_ge(low_ready, 4)
            dve.wait_ge(log_ready, 1)
            link(nc.vector.tensor_tensor(mem.low, mem.low, mem.gate, ALU.subtract))
            for d in range(2):
                for t in range(2):
                    for c in range(NCH):
                        into, of = mem.cum[:, d, t, c, :], mem.low[:, d, t, CH * c:CH * c + CH]
                        if d:
                            into, of = into[:, ::-1], of[:, ::-1]
                        last = nc.vector.tensor_tensor_scan(into, ones, of, 0.0, ALU.mult, ALU.add)
            link(last)
            clamp = GLA_CLAMP / tau
            for d in range(2):
                qh, kh = ((64, 0), (0, 64))[d]
                cum, shift = mem.cum[:, d], mem.shift[:, d]
                mids, edge, end = (((31, 95), 63, CH - 1), ((32, 96), 64, 0))[d]
                for t in range(2):
                    for h in range(2):
                        part = slice(64 * h, 64 * h + 64)
                        link(nc.vector.tensor_tensor(shift[:, t, 0:2, part], cum[:, t, 0:2, part],
                                                     cum[:, t, 0:2, mids[h]:mids[h] + 1].to_broadcast([P, 2, 64]),
                                                     ALU.subtract))
                step = nc.vector.tensor_scalar(shift[:, :, 0:2, :], shift[:, :, 0:2, :], clamp, -clamp, ALU.min, ALU.max)
                step.then_inc(shifted, 1)
                dve.wait_ge(exped, 6 * d + 2)
                for t in range(2):
                    link(nc.vector.scalar_tensor_tensor(mem.q_in[:, d, t], mem.q_in[:, d, t], 0.125, q[:, t, 0:2],
                                                        ALU.mult, ALU.mult))
                    link(nc.vector.tensor_tensor(mem.k_in[:, d, t], mem.k_in[:, d, t], k[:, t, 0:2], ALU.mult))
                    step = nc.vector.tensor_tensor(shift[:, t, 0:2, :], cum[:, t, 0:2, :],
                                                   cum[:, t, 0:2, edge:edge + 1].to_broadcast([P, 2, CH]), ALU.subtract)
                    link(step) if t == 0 else step.then_inc(shifted, 1)
                dve.wait_ge(exped, 6 * d + 4)
                for t in range(2):
                    link(nc.vector.scalar_tensor_tensor(mem.q_cross[:, d, t], mem.q_cross[:, d, t], 0.125,
                                                        q[:, t, 0:2, qh:qh + 64], ALU.mult, ALU.mult))
                    link(nc.vector.tensor_tensor(mem.k_cross[:, d, t], mem.k_cross[:, d, t], k[:, t, 0:2, kh:kh + 64],
                                                 ALU.mult))
                    step = nc.vector.tensor_tensor(shift[:, t], cum[:, t],
                                                   cum[:, t, :, end:end + 1].to_broadcast([P, NCH, CH]), ALU.subtract)
                    link(step) if t == 0 else step.then_inc(shifted, 1)
                nc.vector.tensor_copy(mem.e_end[:, d], cum[:, :, :, end]).then_inc(shifted, 1)
                dve.wait_ge(exped, 6 * d + 6)
                for t in range(2):
                    link(nc.vector.tensor_tensor(mem.k_end[:, d, t], mem.k_end[:, d, t], k[:, t], ALU.mult))
                    link(nc.vector.scalar_tensor_tensor(mem.q_state[:, d, t], mem.q_state[:, d, t], 0.125, q[:, t, 0:2],
                                                        ALU.mult, ALU.mult))


def gla_scan_stage(net):
    nc, mem = net.nc, GlaMemory(net)
    head = lambda h: (h // 2, slice(64 * (h % 2), 64 * (h % 2) + 64))
    ident = net.const(C_IDENT)
    updates = [(0, 2, None), (1, 3, None), (0, 3, 0), (1, 2, 1), (0, 0, 1), (1, 1, 0)]
    units = [(d, c) for d in range(2) for c in range(2)]
    with Stage(net, "gla_scan") as st:
        zeroed, att_raw, att_ready = st.sem("zeroed"), st.sem("att_raw"), st.sem("att_ready")
        turned, ktok_ready, state_summed, state_ready = (st.sem("turned"), st.sem("ktok_ready"), st.sem("state_summed"),
                                                         st.sem("state_ready"))
        y_ready, own = st.sem("y_ready"), st.sem("dve_own")

        @st.tensor
        def _(pe):
            for n, (d, c) in enumerate(units):
                if n:
                    pe.wait_ge(att_ready, 4 * n)
                for h in range(4):
                    t, rows = head(h)
                    bank, at = net.ps[h % 2], P * (h // 2)
                    for half in range(2):
                        part = slice(64 * half, 64 * half + 64)
                        nc.tensor.matmul(bank[part, at + 64 * half:at + 64 * half + 64], mem.k_in[rows, d, t, c, part],
                                         mem.q_in[rows, d, t, c, part], start=True, stop=True)
                    jh, ih = ((0, 1), (1, 0))[d]
                    last = nc.tensor.matmul(bank[64 * jh:64 * jh + 64, at + 64 * ih:at + 64 * ih + 64],
                                            mem.k_cross[rows, d, t, c], mem.q_cross[rows, d, t, c], start=True, stop=True)
                    if h >= 2:
                        last.then_inc(att_raw, 1)
            for n, (d, c, _) in enumerate(updates):
                if n >= 2:
                    pe.wait_ge(state_ready, n - 1)
                for t in range(2):
                    last = nc.tensor.transpose(net.ps[2 + n % 2][:, P * t:P * t + P], mem.k_end[:, d, t, c, :], ident)
                last.then_inc(turned, 1)
                pe.wait_ge(ktok_ready, n + 1)
                for h in range(4):
                    t, rows = head(h)
                    last = nc.tensor.matmul(net.ps[2 + n % 2][rows, 256 + P * t:384 + P * t],
                                            mem.ktok[:, n % 2, 64 * h:64 * h + 64], mem.vtok[:, c, P * h:P * h + P],
                                            start=True, stop=True)
                last.then_inc(state_summed, 1)
            pe.wait_ge(state_ready, len(updates))
            pe.wait_ge(att_ready, 16)
            for h in range(4):
                t, rows = head(h)
                for c in range(2):
                    into = net.ps[4 + h][:, P * c:P * c + P]
                    for d in range(2):
                        nc.tensor.matmul(into, mem.vtok[:, c, P * h:P * h + P], mem.att[:, d, c, h, :],
                                         start=(d == 0), stop=False)
                    for d in range(2):
                        last = nc.tensor.matmul(into, mem.state[rows, d, c, t, :], mem.q_state[rows, d, t, c, :],
                                                start=False, stop=(d == 1))
                last.then_inc(y_ready, 1)

        @st.gpsimd
        def _(pool):
            pool.memset(mem.att, 0.0).then_inc(zeroed, 1)

        @st.scalar
        def _(act):
            for n in range(len(updates)):
                act.wait_ge(turned, n + 1)
                if n >= 2:
                    act.wait_ge(state_summed, n - 1)
                act.activation(mem.ktok[:, n % 2, :], net.ps[2 + n % 2][:, 0:256], ACT.Copy).then_inc(ktok_ready, 1)

        @st.vector
        def _(dve):
            link = Chain(dve, own)
            dve.wait_ge(zeroed, 1)
            for n, (d, c) in enumerate(units):
                tri = net.const((C_LE, C_GE)[d]).unsqueeze(1).to_broadcast([P, 2, P])
                whole, rest = ((slice(0, 64), slice(64, 128)), (slice(64, 128), slice(0, 64)))[d]
                for odd in range(2):
                    dve.wait_ge(att_raw, 2 * n + 2)
                    raw = net.ps[odd][:, 0:256].rearrange("p (h m) -> p h m", m=P)
                    into = mem.att[:, d, c, odd::2, :]
                    nc.vector.tensor_tensor(into[whole], raw[whole], tri[whole], ALU.mult).then_inc(att_ready, 1)
                    nc.vector.tensor_tensor(into[rest, :, rest], raw[rest, :, rest], tri[rest, :, rest],
                                            ALU.mult).then_inc(att_ready, 1)
            held = {}
            for n, (d, c, to) in enumerate(updates):
                sums = net.ps[2 + n % 2][:, 256:512].rearrange("p (t m) -> p t m", m=P)
                dve.wait_ge(state_summed, n + 1)
                if n < 2:
                    into = mem.state[:, d, 1 - d]
                    last = nc.vector.tensor_copy(into, sums)
                else:
                    into = mem.state[:, d, to]
                    dve.wait_ge(state_ready, n)
                    decay = mem.e_end[:, d, :, c:c + 1].to_broadcast([P, 2, P])
                    link(nc.vector.tensor_tensor(into, held[d], decay, ALU.mult))
                    last = nc.vector.tensor_tensor(into, into, sums, ALU.add)
                last.then_inc(state_ready, 1)
                held[d] = into
            for h in range(4):
                dve.wait_ge(y_ready, h + 1)
                nc.vector.tensor_copy(net.OT[:, 4 + h, 0:LAT], net.ps[4 + h][:, 0:LAT])


def times_stage(net, name, pairs):
    with Stage(net, name) as st:
        @st.vector
        def _(dve):
            for a, b in pairs:
                net.nc.vector.tensor_tensor(a, a, b, ALU.mult)


class SecondMemory:

    def __init__(self, net):
        sc = net.SC
        self.spectrum_in = sc[:, 0:1024].rearrange("p (a t n m) -> p a t n m", a=2, t=2, n=2)
        self.spectrum = sc[:, 1024:1536].rearrange("p (t m) -> p t m", m=LAT)
        self.vtok = sc[:, 1536:1792].rearrange("p (a m) -> p a m", a=2)
        self.mem_vtok = sc[:, 1792:2304].rearrange("p (a m) -> p a m", a=2)
        self.prob = sc[:, 2304:3328].rearrange("p (b q k) -> p b q k", b=2, q=2)
        self.prob_t = sc[:, 3328:4352].rearrange("p (b m) -> p b m", b=2)
        self.stat = sc[:, 4352:4352 + 12 * 8].rearrange("p (h n) -> p h n", n=8)
        self.part = sc[:, 4500:5012].rearrange("p (b m) -> p b m", m=LAT)
        self.angle, self.turn = sc[:, 5100:5356], sc[:, 5356:5612]
        self.sin, self.cos = sc[:, 6300:6556], sc[:, 6556:6812]
        self.memory, self.memory_normed = net.HT[:, :, LAT:TOK], net.OT[:, :, LAT:TOK]
        self.k_swapped = net.PT[:, 14, 0:LAT]


def second_load_stage(net):
    nc, mem = net.nc, SecondMemory(net)
    rows = net.PT[:, 24:28, :].rearrange("p t m -> p (t m)").rearrange("p (a d) -> p a d", a=2)
    where = mem.turn.bitcast(I32)
    with Stage(net, "second_load") as st:
        const_in, memory_in, where_in, turned = (st.sem("const_in"), st.sem("memory_in"), st.sem("where_in"),
                                                 st.sem("turned"))
        own, reduced, sin_ready = st.sem("dve_own"), st.sem("reduced"), st.sem("sin_ready")

        @st.sync
        def _(sp):
            sp.dma_start(where, net.ins["positions_2"][0].partition_broadcast(P)).then_inc(where_in, 16)
            sp.dma_start(net.CONST[:, C_OVER:C_OVER + N_CONST2], net.ins["const_2"]).then_inc(const_in, 16)
            sp.dma_start(rows, net.ins["mem_2"][0].rearrange("(a p) d -> p a d", p=P)).then_inc(memory_in, 16)

        @st.tensor
        def _(pe):
            pe.wait_ge(memory_in, 16)
            for f in range(KT):
                for a in range(2):
                    last = nc.tensor.transpose(net.ps[f][:, P * a:P * a + P], rows[:, a, P * f:P * f + P],
                                               net.const(C_IDENT))
                last.then_inc(turned, 1)

        @st.scalar
        def _(act):
            for f in range(KT):
                act.wait_ge(turned, f + 1)
                act.activation(mem.memory[:, f, :], net.ps[f][:, 0:LAT], ACT.Copy)
            act.wait_ge(reduced, 2)
            act.activation(mem.sin, mem.angle, ACT.Sin)
            act.activation(mem.cos, mem.angle, ACT.Sin, scale=0.5).then_inc(sin_ready, 1)

        @st.vector
        def _(dve):
            link = Chain(dve, own)
            two_pi = 2.0 * np.pi
            high = float(np.float32(6.28125))
            middle = float(np.float32(np.float64(two_pi - high)))
            low = float(np.float32(two_pi - high - middle))
            rounder = 1.5 * 2.0 ** 23
            dve.wait_ge(where_in, 16)
            dve.wait_ge(const_in, 16)
            link(nc.vector.tensor_copy(mem.angle, where))
            link(nc.vector.tensor_scalar(mem.angle, mem.angle, net.CONST[:, C_INVF:C_INVF + 1], None, ALU.mult))
            link(nc.vector.tensor_scalar(mem.turn, mem.angle, 1.0 / two_pi, rounder, ALU.mult, ALU.add))
            link(nc.vector.tensor_scalar(mem.turn, mem.turn, -rounder, None, ALU.add))
            for part in (high, middle, low):
                link(nc.vector.scalar_tensor_tensor(mem.angle, mem.turn, -part, mem.angle, ALU.mult, ALU.add))
            nc.vector.tensor_scalar(mem.angle, mem.angle, 3.1415925, -3.1415925, ALU.min, ALU.max).then_inc(reduced, 2)
            dve.wait_ge(sin_ready, 1)
            link(nc.vector.tensor_tensor(mem.cos, mem.cos, mem.cos, ALU.mult))
            nc.vector.tensor_scalar(mem.cos, mem.cos, -2.0, 1.0, ALU.mult, ALU.add)


def second_prepare_stage(net, layer):
    nc, mem = net.nc, SecondMemory(net)
    with Stage(net, f"second_prepare{layer}") as st:
        rotated, added, turned, own = st.sem("rotated"), st.sem("added"), st.sem("turned"), st.sem("dve_own")

        @st.tensor
        def _(pe):
            for n in range(5):
                if n == 4:
                    pe.wait_ge(added, 1)
                nc.tensor.matmul(net.ps[n % 4][:, 0:LAT], net.const(C_ROTB), net.PT[:, 2 + n, 0:LAT],
                                 start=True, stop=True).then_inc(rotated, 1)
            for a in range(2):
                for n, t in enumerate((7, 12, 13)):
                    last = nc.tensor.transpose(net.ps[4 + a][:, P * n:P * n + P], net.PT[:, t, P * a:P * a + P],
                                               net.const(C_IDENT))
                last.then_inc(turned, 1)

        @st.scalar
        def _(act):
            for a in range(2):
                act.wait_ge(turned, a + 1)
                act.activation(mem.vtok[:, a, :], net.ps[4 + a][:, 0:P], ACT.Copy)
                act.activation(mem.mem_vtok[:, a, :], net.ps[4 + a][:, P:3 * P], ACT.Copy)

        @st.vector
        def _(dve):
            link = Chain(dve, own)
            for n in range(5):
                x = net.PT[:, 2 + n, 0:LAT]
                dve.wait_ge(rotated, n + 1)
                nc.vector.tensor_tensor(mem.part[:, n % 2], net.ps[n % 4][:, 0:LAT], mem.sin, ALU.mult).then_inc(added, 1)
                link(nc.vector.tensor_tensor(x, x, mem.cos, ALU.mult))
                dve.wait_ge(added, n + 1)
                link(nc.vector.tensor_tensor(x, x, mem.part[:, n % 2], ALU.add))
            keys = net.PT[:, 6, 0:LAT]
            nc.vector.tensor_copy(mem.k_swapped[64:128], keys[0:64])
            nc.vector.tensor_copy(mem.k_swapped[0:64], keys[64:128])


def fourier_stage(net, layer):
    nc, mem = net.nc, SecondMemory(net)
    with Stage(net, f"fourier{layer}") as st:
        by_channel, by_channel_copied, by_token, by_token_copied, mixed = (
            st.sem("by_channel"), st.sem("by_channel_copied"), st.sem("by_token"), st.sem("by_token_copied"), st.sem("mixed"))

        @st.tensor
        def _(pe):
            for a in range(2):
                for t in range(2):
                    last = nc.tensor.matmul(net.ps[a][:, 256 * t:256 * t + 256], net.PT[:, t, P * a:P * a + P],
                                            net.const(C_DFTC, 256), start=True, stop=True)
                last.then_inc(by_channel, 1)
            pe.wait_ge(by_channel_copied, 2)
            for t in range(2):
                for n in range(2):
                    for a in range(2):
                        last = nc.tensor.matmul(net.ps[2 + t][:, 0:LAT], mem.spectrum_in[:, a, t, n, :],
                                                net.const(C_DFTS + (2 * n + a) * LAT, LAT),
                                                start=(n == 0 and a == 0), stop=(n == 1 and a == 1))
                last.then_inc(by_token, 1)
            for t in range(2):
                pe.wait_ge(by_token_copied, t + 1)
                nc.tensor.matmul(net.ps[4 + t][:, 0:LAT], net.WF[:, layer, t, :], mem.spectrum[:, t, :], start=True,
                                 stop=True).then_inc(mixed, 1)

        @st.scalar
        def _(act):
            for a in range(2):
                act.wait_ge(by_channel, a + 1)
                act.activation(mem.spectrum_in[:, a].rearrange("p t n m -> p (t n m)"), net.ps[a][:, :],
                               ACT.Copy).then_inc(by_channel_copied, 1)
            for t in range(2):
                act.wait_ge(by_token, t + 1)
                act.activation(mem.spectrum[:, t, :], net.ps[2 + t][:, 0:LAT], ACT.Copy).then_inc(by_token_copied, 1)
            for t in range(2):
                act.wait_ge(mixed, t + 1)
                act.activation(net.OT[:, t, 0:LAT], net.ps[4 + t][:, 0:LAT], ACT.Copy)


def second_attention_stage(net, layer):
    nc, mem = net.nc, SecondMemory(net)
    scale = 64 ** -0.5
    window = net.const(C_WIN, 2 * LAT)
    heads = []
    for h in range(8):
        rows, kv = slice(64 * (h % 2), 64 * (h % 2) + 64), h // 4
        keys = net.PT[rows, 6, 0:LAT] if kv == h % 2 else mem.k_swapped[rows]
        heads.append((net.PT[rows, 2 + h // 2, 0:LAT], keys, mem.vtok[:, :, 64 * kv:64 * kv + 64],
                      net.SINKROW[:, 8 * layer + h:8 * layer + h + 1]))
    for h in range(4):
        rows = slice(64 * (h % 2), 64 * (h % 2) + 64)
        heads.append((net.PT[rows, 8 + h // 2, 0:LAT], net.PT[rows, 10 + h // 2, 0:LAT],
                      mem.mem_vtok[:, :, 64 * h:64 * h + 64], None))
    N = len(heads)
    with Stage(net, f"attention{layer}") as st:
        scored, score_used, max_ready, exp_ready = (st.sem("scored"), st.sem("score_used"), st.sem("max_ready"),
                                                    st.sem("exp_ready"))
        prob_ready, turned, turned_copied, out_ready = (st.sem("prob_ready"), st.sem("turned"), st.sem("turned_copied"),
                                                        st.sem("out_ready"))
        out_taken, own = st.sem("out_taken"), st.sem("dve_own")

        @st.tensor
        def _(pe):
            def score(u):
                q, k, _, _ = heads[u]
                if u >= 2:
                    pe.wait_ge(score_used, u - 1)
                for t in range(2):
                    last = nc.tensor.matmul(net.ps[u % 2][:, LAT * t:LAT * t + LAT], q[:, P * t:P * t + P], k,
                                            start=True, stop=True)
                last.then_inc(scored, 1)

            def weigh(u):
                v = heads[u][2]
                pe.wait_ge(turned_copied, u + 1)
                if u % 2 == 0 and u >= 4:
                    pe.wait_ge(out_taken, u // 2 - 1)
                rows = slice(64 * (u % 2), 64 * (u % 2) + 64)
                for kt in range(2):
                    last = nc.tensor.matmul(net.ps[4 + (u // 2) % 2][rows, 0:LAT], v[:, kt, :],
                                            mem.prob_t[:, u % 2, LAT * kt:LAT * kt + LAT], start=(kt == 0), stop=(kt == 1))
                last.then_inc(out_ready, 1)

            score(0)
            score(1)
            for u in range(N):
                if u + 2 < N:
                    score(u + 2)
                pe.wait_ge(prob_ready, u + 1)
                if u >= 2:
                    pe.wait_ge(turned_copied, u - 1)
                for kt in range(2):
                    for t in range(2):
                        last = nc.tensor.transpose(net.ps[2 + u % 2][:, LAT * kt + P * t:LAT * kt + P * t + P],
                                                   mem.prob[:, u % 2, t, P * kt:P * kt + P], net.const(C_IDENT))
                last.then_inc(turned, 1)
                if u:
                    weigh(u - 1)
            weigh(N - 1)

        @st.scalar
        def _(act):
            def exps(u):
                act.wait_ge(max_ready, u + 1)
                for t in range(2):
                    act.activation(mem.prob[:, u % 2, t, :], mem.prob[:, u % 2, t, :], ACT.Exp,
                                   bias=mem.stat[:, u, t:t + 1], accum_out=mem.stat[:, u, 2 + t:3 + t]).then_inc(exp_ready, 1)
                sink = heads[u][3]
                if sink is not None:
                    act.activation(mem.stat[:, u, 4:6], mem.stat[:, u, 0:2], ACT.Exp, bias=sink).then_inc(exp_ready, 1)

            exps(0)
            for u in range(N):
                if u + 1 < N:
                    exps(u + 1)
                act.wait_ge(turned, u + 1)
                if u >= 2:
                    act.wait_ge(out_ready, u - 1)
                act.activation(mem.prob_t[:, u % 2, :], net.ps[2 + u % 2][:, :], ACT.Copy).then_inc(turned_copied, 1)

        @st.vector
        def _(dve):
            link = Chain(dve, own)
            exps_before = [sum(3 if x[3] is not None else 2 for x in heads[:u]) for u in range(N + 1)]

            def maxima(u):
                sink, most = heads[u][3], mem.stat[:, u, 0:2]
                dve.wait_ge(scored, u + 1)
                if u >= 2:
                    dve.wait_ge(turned, u - 1)
                both = mem.prob[:, u % 2].rearrange("p q k -> p (q k)")
                if sink is not None:
                    step = nc.vector.scalar_tensor_tensor(both, net.ps[u % 2][:, :], scale, window, ALU.mult, ALU.add)
                else:
                    step = nc.vector.tensor_scalar(both, net.ps[u % 2][:, :], scale, None, ALU.mult)
                step.then_inc(score_used, 1)
                dve.wait_ge(score_used, u + 1)
                link(nc.vector.reduce_max(most, mem.prob[:, u % 2], AX_X))
                if sink is not None:
                    nc.vector.tensor_scalar(most, most, sink, -1.0, ALU.max, ALU.mult).then_inc(max_ready, 1)
                else:
                    nc.vector.tensor_scalar(most, most, -1.0, None, ALU.mult).then_inc(max_ready, 1)

            maxima(0)
            for u in range(N):
                if u + 1 < N:
                    maxima(u + 1)
                dve.wait_ge(exp_ready, exps_before[u + 1])
                total = mem.stat[:, u, 2:4]
                if heads[u][3] is not None:
                    link(nc.vector.tensor_tensor(total, total, mem.stat[:, u, 4:6], ALU.add))
                link(nc.vector.reciprocal(total, total))
                for t in range(2):
                    last = nc.vector.tensor_scalar(mem.prob[:, u % 2, t, :], mem.prob[:, u % 2, t, :],
                                                   mem.stat[:, u, 2 + t:3 + t], None, ALU.mult)
                last.then_inc(prob_ready, 1)
                if u % 2 == 0 and u >= 2:
                    dve.wait_ge(out_ready, u)
                    pair = u // 2 - 1
                    nc.vector.tensor_copy(net.OT[:, 2 + pair, 0:LAT], net.ps[4 + pair % 2][:, 0:LAT]).then_inc(out_taken, 1)
            dve.wait_ge(out_ready, N)
            nc.vector.tensor_copy(net.OT[:, 7, 0:LAT], net.ps[5][:, 0:LAT])


def swiglu_weights(w):
    gate, up = (w[:, o:o + FF].rearrange("(t k) (n m) -> n k t m", k=P, m=SW) for o in (0, FF))
    pairs = FF // SW
    return Weights(pairs // 2, 2 * (pairs % 2), lambda i, s: (up if s % 2 else gate)[2 * i + s // 2])


def swiglu_stage(net, name, w, x, hidden, following):
    nc = net.nc
    with Stage(net, name) as st:
        sems = Split(st)
        gate_free, up_free, high = ([st.sem(f"{what}{m}") for m in range(2)]
                                           for what in ("gate_free", "up_free", "hidden_high"))

        @st.sync
        def _(sp):
            feed(net, sp, w, lambda i, s: (sems.used[1], SLOTS * i + s + 1), following)

        @st.tensor
        def _(pe):
            def turn(i, slots):
                for s in slots:
                    first = is_first(i, s)
                    for m in range(2):
                        pe.wait_ge((up_free if s % 2 else gate_free)[m], 2 * i + s // 2 + 1)
                        pe.wait_ge(sems.split_ready[m], SLOTS * i + s + 1)
                        for kt in range(KT):
                            if first and m == 0:
                                pe.wait_ge(sems.operand_split, kt + 1)
                            last = three_passes(net, net.ps[2 * s + m], s, m, kt, x, kt, LAT, kt == 0, kt == KT - 1)
                        last.then_inc(sems.used[m], 1)

            turns(pe, w, turn, peel=True)

        @st.scalar
        def _(act):
            for m in range(2):
                act.sem_inc(gate_free[m], 2)

            def take(i, s, m):
                if s % 2 == 0:
                    act.wait_ge(sems.used[m], SLOTS * i + s + 1)
                    act.activation(hidden.whole[:, 4 * i + s + m, :], net.ps[2 * s + m][:, 0:LAT],
                                   ACT.Silu).then_inc(gate_free[m], 1)

            high_on_act(net, act, w, sems, x, take)

        @st.vector
        def _(dve):
            for m in range(2):
                dve.sem_inc(up_free[m], 2)

            def take(i, s, m):
                if s % 2 == 0:
                    return
                low, top, whole = (v[:, 4 * i + s - 1 + m, :] for v in (hidden.low, hidden.high, hidden.whole))
                done = 2 * i + s // 2 + 1
                dve.wait_ge(gate_free[m], 2 + done)
                dve.wait_ge(sems.used[m], SLOTS * i + s + 1)
                nc.vector.tensor_tensor(whole, whole, net.ps[2 * s + m][:, 0:LAT], ALU.mult).then_inc(up_free[m], 1)
                dve.wait_ge(up_free[m], 2 + done)
                nc.vector.tensor_scalar(top, whole, 1.0, None, ALU.mult).then_inc(high[m], 1)
                dve.wait_ge(high[m], done)
                nc.vector.tensor_tensor(low, whole, top.bitcast(F32), ALU.subtract)

            low_on_dve(net, dve, w, sems, x, take)
        net.spent(w)


def store_stage(net):
    nc = net.nc
    rows = net.PT[:, 0:4, :].rearrange("p t m -> p (t m)").rearrange("p (a d) -> p a d", a=2)
    with Stage(net, "store") as st:
        turned, copied, stored = st.sem("turned"), st.sem("copied"), st.sem("stored")

        @st.tensor
        def _(pe):
            for a in range(2):
                for f in range(KT):
                    last = nc.tensor.transpose(net.ps[2 * a + f // 4][:, P * (f % 4):P * (f % 4) + P],
                                               net.XT[:, f, P * a:P * a + P], net.const(C_IDENT))
                    if f % 4 == 3:
                        last.then_inc(turned, 1)

        @st.vector
        def _(dve):
            for n in range(4):
                dve.wait_ge(turned, n + 1)
                nc.vector.tensor_copy(rows[:, n // 2, 512 * (n % 2):512 * (n % 2) + 512], net.ps[n][:, :]).then_inc(copied, 1)

        @st.sync
        def _(sp):
            for a in range(2):
                sp.wait_ge(copied, 2 * (a + 1))
                sp.dma_start(net.out[0, P * a:P * a + P, :], rows[:, a, :]).then_inc(stored, 16)
            sp.wait_ge(stored, 32)


def program(nc, ins, out):
    with ExitStack() as ctx:
        net = Net(nc, ctx, ins, out)
        both, lat = (lambda i, s: TOK), (lambda i, s: LAT)
        mod = [columns(ins[f"l{n}_mod_w"], 0, 6 * D) for n in range(2)]
        w_in0 = columns(ins["l0_w_in"], 0, 3328)
        w_in1, in1_widths = odd_projection(ins["l1_w_in"])
        w_out = [columns(ins[f"l{n}_w_out"], 0, D) for n in range(2)]
        half = HID // 2
        w_up0 = [columns(ins["l0_mlp_w1"], half * n, half) for n in range(2)]
        w_down0 = [deep(ins["l0_mlp_w2"][half * n:half * n + half, :], (8, 8)) for n in range(2)]
        w_up1, w_down1 = columns(ins["l1_mlp_w1"], 0, HID), deep(ins["l1_mlp_w2"], (8, 8, 8, 8))

        w_in2 = [columns(ins["w_in_2"][n], 0, 1280) for n in range(2)]
        w_kv = [columns(ins["w_mem_kv_2"][n], 0, 512) for n in range(2)]
        w_out2 = [columns(ins["w_out_2"][n], 0, D) for n in range(2)]
        w_ffn_in = [swiglu_weights(ins["w_ffn_in_2"][n]) for n in range(2)]
        w_ffn_out = [deep(ins["w_ffn_out_2"][n], (6, 6, 5, 5)) for n in range(2)]

        HT, PT, OT = net.HT[:, :, :], net.PT[:, :, :], net.OT[:, :, :]
        lats = slice(0, LAT)
        HR, PR, OR = net.HR[:, :, :], net.PR[:, :, :], net.OR[:, :, :]
        halves = Operand(PR[:, 0:16, :], PR[:, 16:32, :], PT[:, 16:32, :])
        hidden = Operand(PR[:, :, lats], PR[:, :, LAT:TOK], PT[:, :, LAT:TOK])
        h_lat = Operand(OR[:, :, lats], HR[:, :, lats], HT[:, :, lats])
        o_lat = Operand(HR[:, :, lats], OR[:, :, lats], OT[:, :, lats])
        mlp_gated = lambda n: lambda tile, bank: add_gated(net, tile, bank, 40, n)

        load_stage(net, mod[0])
        modulation_stage(net, 0, mod[0], w_in0)
        ada_stage(net, 0, 0, TOK)
        project_stage(net, "in0", w_in0, Operand(OR, HR, HT), both, net.PT, None)
        diff_prepare_stage(net)
        diff_attention_stage(net)
        heads = [net.OT[:, h, :] for h in range(4)]
        group_norm_stage(net, "diff_norm", [([o], [o], [net.DER[:, 32:33]], [net.PT[:, h, :]])
                                            for h, o in enumerate(heads)], TOK, 1e-5)
        rwkv_prepare_stage(net)
        for d in range(2):
            rwkv_decay_stage(net, d)
            rwkv_chunks_stage(net, d)
        rwkv_finish_stage(net)
        first_fetch_stage(net, w_out[0])
        mixed_out_stage(net, "out0", w_out[0], Operand(HR, OR, OT), TOK, w_up0[0])
        ada_stage(net, 0, 1, TOK)
        for n, following in enumerate((w_up0[1], mod[1])):
            x = Operand(OR, HR, HT if n == 0 else None)
            relu_squared_stage(net, f"up0_{n}", w_up0[n], x, TOK, halves, w_down0[n])
            deep_stage(net, f"down0_{n}", w_down0[n], halves, TOK, mlp_gated(TOK), following)

        modulation_stage(net, 1, mod[1], w_in1)
        ada_stage(net, 1, 0, TOK)
        project_stage(net, "in1", w_in1, Operand(OR, PR[:, 24:32, :], HT), in1_widths, net.PT, w_out[1], straight=True)
        ssd_steps_stage(net)
        ssd_conv_stage(net)
        ssd_scan_stage(net)
        ssd_gate_stage(net)
        group_norm_stage(net, "ssd_norm", [([net.OT[:, 2 * g + t, 0:LAT] for t in range(2)],) * 2 +
                                           ([net.par("l1_ssm_norm", 2 * g + t) for t in range(2)],
                                            [net.PT[:, 2 * g + t, 0:LAT] for t in range(2)]) for g in range(2)], LAT, EPS)
        gla_gates_stage(net)
        gla_scan_stage(net)
        group_norm_stage(net, "gla_norm", [([net.OT[:, 4 + h, 0:LAT]],) * 2 + ([net.par("l1_gla_norm")],
                                            [net.PT[:, h, 0:LAT]]) for h in range(4)], LAT, EPS)
        times_stage(net, "gla_gate", [(net.OT[:, 4 + h, 0:LAT], net.PT[:, 20 + h, 0:LAT]) for h in range(4)])
        mixed_out_stage(net, "out1", w_out[1], o_lat, LAT, w_up1)
        ada_stage(net, 1, 1, LAT)
        relu_squared_stage(net, "up1", w_up1, h_lat, LAT, hidden, w_down1)
        deep_stage(net, "down1", w_down1, hidden, LAT, mlp_gated(LAT), w_in2[0])
        x = [net.XT[:, t, 0:LAT] for t in range(KT)]
        h = [net.HT[:, t, 0:LAT] for t in range(KT)]
        scratch = [net.PT[:, t, 0:LAT] for t in range(24, 32)]
        gains = lambda name, layer: [net.par(name, KT * layer + t) for t in range(KT)]
        group_norm_stage(net, "final_norm", [(x, x, gains("final_norm", 0), scratch)], LAT, EPS)

        second_load_stage(net)
        mem = SecondMemory(net)
        mem_scratch = [net.PT[:, t, LAT:TOK] for t in range(24, 32)]
        for n in range(2):
            raw, normed = ([v[:, t, :] for t in range(KT)] for v in (mem.memory, mem.memory_normed))
            group_norm_stage(net, f"pre_mix{n}", [(x, h, gains("g_pre_mix_2", n), scratch),
                                                  (raw, normed, gains("g_mem_2", n), mem_scratch)], LAT, EPS)
            project_stage(net, f"second_in{n}", w_in2[n], h_lat, lat, net.PT, w_kv[n])
            project_stage(net, f"memory_in{n}", w_kv[n], Operand(OR[:, :, lats], OR[:, :, LAT:TOK], mem.memory_normed), lat, net.PT, w_out2[n],
                          dst_tile=lambda t: 10 + t)
            second_prepare_stage(net, n)
            fourier_stage(net, n)
            second_attention_stage(net, n)
            o = [net.OT[:, t, 0:LAT] for t in range(KT)]
            gain = gains("g_grp_2", n)
            group_norm_stage(net, f"mix_norm{n}", [(o[a:b], o[a:b], gain[a:b], scratch[a:b])
                                                   for a, b in ((0, 2), (2, 6), (6, 8))], LAT, EPS)
            project_stage(net, f"second_out{n}", w_out2[n], o_lat, lat, net.PT, w_ffn_in[n])
            y = [net.PT[:, t, 0:LAT] for t in range(KT)]
            group_norm_stage(net, f"post_mix{n}", [(y, y, gains("g_post_mix_2", n), scratch)], LAT, EPS, adds=x)
            group_norm_stage(net, f"pre_ffn{n}", [(x, h, gains("g_pre_ffn_2", n), scratch)], LAT, EPS)
            swiglu_stage(net, f"ffn_in{n}", w_ffn_in[n], h_lat, hidden, w_ffn_out[n])
            deep_stage(net, f"ffn_out{n}", w_ffn_out[n], hidden, LAT,
                       lambda tile, bank: nc.vector.tensor_copy(net.OT[:, tile, lats], bank[:, lats]),
                       w_in2[1] if n == 0 else None)
            group_norm_stage(net, f"post_ffn{n}", [(o, o, gains("g_post_ffn_2", n), scratch)], LAT, EPS, adds=x)
        store_stage(net)




def kernel(**inputs):
    import concourse.bacc as bacc
    from concourse.bass_utils import run_bass_kernel_spmd

    nc = bacc.Bacc("TRN2", target_bir_lowering=False, num_devices=1)
    arrays = {name: np.ascontiguousarray(a) for name, a in inputs.items()}
    arrays |= {"const_1": first_constants(), "const_2": second_constants()}
    ins = {name: nc.dram_tensor(f"in_{name}", a.shape, mybir.dt.from_np(a.dtype), kind="ExternalInput").ap()
           for name, a in arrays.items()}
    out = nc.dram_tensor("out", (1, LAT, D), F32, kind="ExternalOutput").ap()
    program(nc, ins, out)
    result = run_bass_kernel_spmd(nc, [{f"in_{name}": a for name, a in arrays.items()}], core_ids=[0])
    return result.results[0]["out"]
```

```python
from contextlib import ExitStack

import numpy as np

import concourse.bass as bass
from concourse import mybir

F32 = mybir.dt.float32
F32R = mybir.dt.float32r
I32 = mybir.dt.int32
ALU = mybir.AluOpType
ACT = mybir.ActivationFunctionType
LOG_EXP = "natural_log_exp_and_others"
AX_X = mybir.AxisListType.X

P = 128
D = 1024
KT = D // P
LAT = 256
TOK = 512
CH = 128
NCH = TOK // CH
HID = 4096
FF = 2816
SLOTS = 4
SW = 256
EPS = 1e-6
LAM_INIT = 0.2
DECAY = float(np.exp(-0.5))
GLA_CLAMP = 43.0


C_IDENT, C_ONES, C_BLK, C_LE, C_GE = (P * n for n in range(5))
C_EPS = 5 * P
EPSILONS = (EPS, 1e-5, 64e-5)
C_OVER = C_EPS + 4
C_MASK4 = C_OVER
C_LEVEL = C_MASK4 + 1024
C_ROTA = C_LEVEL + 2 * 7 * P
C_COSA = C_ROTA + P
C_SINA = C_COSA + LAT
C_FOLD = C_SINA + LAT
N_CONST = C_FOLD + 2
C_DFTC = C_OVER
C_DFTS = C_DFTC + 2 * P
C_WIN = C_DFTS + 4 * LAT
C_ROTB = C_WIN + 2 * LAT
C_INVF = C_ROTB + P
N_CONST2 = C_INVF + 1 - C_OVER


def first_constants():
    j, i = np.arange(P)[:, None], np.arange(P)[None, :]
    out = np.zeros((P, N_CONST), np.float32)
    out[:, C_IDENT:C_IDENT + P] = j == i
    out[:, C_ONES:C_ONES + P] = 1.0
    out[:, C_BLK:C_BLK + P] = j // 64 == i // 64
    out[:, C_LE:C_LE + P] = j <= i
    out[:, C_GE:C_GE + P] = j >= i
    out[:, C_EPS:C_EPS + len(EPSILONS)] = EPSILONS
    for n, (strict, incl) in enumerate(((j < i, j <= i), (j > i, j >= i))):
        out[:, C_MASK4 + 512 * n:C_MASK4 + 512 * (n + 1)] = np.concatenate([strict, incl, strict, incl], 1)
    for lv in range(7):
        b = 1 << lv
        low = (j // (2 * b) == i // (2 * b)) & ((j // b) % 2 == 1) & ((i // b) % 2 == 0)
        out[:, C_LEVEL + P * lv:C_LEVEL + P * (lv + 1)] = low.T
        out[:, C_LEVEL + P * (7 + lv):C_LEVEL + P * (8 + lv)] = low
    rot = np.zeros((P, P), np.float32)
    for r in range(P):
        if r % 32 < 16:
            rot[r, r + 16] = -1.0
        else:
            rot[r, r - 16] = 1.0
    out[:, C_ROTA:C_ROTA + P] = rot.T
    t = np.arange(LAT)
    inv = (np.float32(10000.0) ** (-np.arange(16, dtype=np.float32) / np.float32(16))).astype(np.float32)
    for r in range(P):
        pos = (t // 64 if r % 64 < 32 else t % 64).astype(np.float32)
        ang = pos * inv[r % 16]
        out[r, C_COSA:C_COSA + LAT] = np.cos(ang)
        out[r, C_SINA:C_SINA + LAT] = np.sin(ang)
    for r in range(4):
        out[r, C_FOLD + r % 2] = 1.0
    return out


def second_constants():
    out = np.zeros((P, N_CONST2), np.float32)
    o = -C_OVER
    c = np.arange(64)
    ang = 2 * np.pi * ((c[:, None] * c[None, :]) % 64) / 64
    for n, m in enumerate((np.cos(ang), np.sin(ang))):
        for g in range(2):
            out[64 * g:64 * g + 64, o + C_DFTC + P * n + 64 * g:o + C_DFTC + P * n + 64 * g + 64] = m / 128.0
    s = np.arange(LAT)
    ang = 2 * np.pi * ((s[:, None] * s[None, :]) % LAT) / LAT
    for n, m in enumerate((np.cos(ang), -np.sin(ang))):
        for h in range(2):
            at = o + C_DFTS + (2 * n + h) * LAT
            out[:, at:at + LAT] = m[P * h:P * h + P]
    q, k = np.arange(P)[:, None], np.arange(LAT)[None, :]
    for h in range(2):
        at = o + C_WIN + h * LAT
        out[:, at:at + LAT] = np.where(np.abs(q + P * h - k) <= 128, 0.0, -1e30)
    for r in range(P):
        if r % 64 < 32:
            out[r + 32, o + C_ROTB + r] = -1.0
        else:
            out[r - 32, o + C_ROTB + r] = 1.0
    inv = np.exp(-np.float32(np.log(10000.0)) * np.arange(32, dtype=np.float32) * np.float32(2.0 / 64))
    out[:, o + C_INVF] = inv.astype(np.float32)[np.arange(P) % 32]
    return out


ROWS = [
    [("c", 8), ("c_ctx", 8), ("l0_mod_b", 48), ("l0_norm1", 8), ("l0_norm2", 8), ("l0_mu", 14), ("l0_w0_f", 4),
     ("l0_w0_b", 4), ("l0_a0", 4), ("l0_k_k", 4), ("l0_k_a", 4), ("l0_r_k", 4), ("l0_lnx_w", 4), ("l0_lnx_b", 4),
     ("l0_subln", 1)],
    [("l1_mod_b", 48), ("l1_norm1", 8), ("l1_norm2", 8), ("l1_conv_w", 40), ("l1_conv_b", 8), ("l1_ssm_norm", 4),
     ("l1_gk_b_f", 2), ("l1_gk_b_b", 2), ("l1_gla_norm", 1)],
    [("final_norm", 8), ("g_pre_mix_2", 16), ("g_mem_2", 16), ("g_grp_2", 16), ("g_post_mix_2", 16),
     ("g_pre_ffn_2", 16), ("g_post_ffn_2", 16)],
]
COL = {}
for _n, _tile in enumerate(ROWS):
    _r = 0
    for _name, _count in _tile:
        COL[_name] = P * _n + _r
        _r += _count
    assert _r <= P


class Stage:

    def __init__(self, net, name):
        self.net, self.nc, self.name, self.sems = net, net.nc, name, []

    def sem(self, what):
        s = self.nc.alloc_semaphore(f"{self.name}_{what}")
        self.sems.append(s)
        return s

    def __enter__(self):
        self.block = self.nc.Block(name=self.name, no_gpsimd_drain=True)
        self.block.__enter__()
        self.scalar, self.vector, self.tensor = self.block.scalar, self.block.vector, self.block.tensor
        self.gpsimd, self.sync = self.block.gpsimd, self.block.sync
        return self

    def __exit__(self, *failed):
        self.block.__exit__(*failed)
        if failed[0]:
            return
        for s in self.sems:
            self.nc.gpsimd.sem_clear(s)
        for s in self.net.cleared:
            self.nc.release_semaphore(s)
        self.net.cleared = self.sems


class Chain:

    def __init__(self, engine, sem):
        self.engine, self.sem, self.n = engine, sem, 0

    def __call__(self, step):
        self.n += 1
        step.then_inc(self.sem, 1)
        self.engine.wait_ge(self.sem, self.n)


class Weights:

    def __init__(self, loops, tail, slot, kts=(KT,) * SLOTS, depth=1):
        self.loops, self.tail, self.slot, self.kts, self.depth = loops, tail, slot, kts, depth

    def first(self):
        return SLOTS if self.loops else min(self.tail, SLOTS)

    def last(self):
        return (self.loops, self.tail - 1) if self.tail else (self.loops - 1, SLOTS - 1)


def columns(w, first, count):
    view = w[:, first:first + count].rearrange("(t k) (n m) -> n k t m", k=P, m=SW)
    return Weights(count // SW // SLOTS, count // SW % SLOTS, lambda i, s: view[SLOTS * i + s])


def joined(a, b):
    n, count = SLOTS * a.loops + a.tail, SLOTS * (a.loops + b.loops) + a.tail + b.tail

    def slot(i, s):
        at = SLOTS * i + s
        return a.slot(at // SLOTS, at % SLOTS) if at < n else b.slot((at - n) // SLOTS, (at - n) % SLOTS)

    return Weights(count // SLOTS, count % SLOTS, slot)


def deep(w, parts):
    view = w.rearrange("(t k) (n m) -> n k t m", k=P, m=SW)
    depth = len(parts)
    ends = [0, *(int(n) for n in np.cumsum(parts))]
    across = SLOTS // depth
    return Weights(D // SW // across, 0,
                   lambda i, s: view[across * i + s // depth, :, ends[s % depth]:ends[s % depth + 1], :],
                   tuple(parts) * across, depth)


class Net:

    def __init__(self, nc, ctx, ins, out):
        self.nc, self.ins, self.out, self.cleared = nc, ins, out, []
        self.log_exp_loaded = False

        self.places, self.at = {}, -(-nc.sbuf_base // 32) * 32

        def sb(name, shape):
            self.places[name] = self.at
            tensor = nc.alloc_sbuf_tensor_at(name, shape, F32, offset=self.at)
            self.at += -(-4 * int(np.prod(shape[1:])) // 32) * 32
            return tensor

        self.XT = sb("XT", [P, KT, TOK])
        self.HT = sb("HT", [P, KT, TOK])
        self.PT = sb("PT", [P, 32, TOK])
        self.OT = sb("OT", [P, KT, TOK])
        self.RING = sb("RING", [P, SLOTS, KT * SW])
        self.CONST = sb("CONST", [P, N_CONST])
        self.PAR = sb("PAR", [P, 3 * P])
        self.MOD = sb("MOD", [P, 48, 2])
        self.AFF = sb("AFF", [P, 2, KT, 2])
        self.CACT = sb("CACT", [P, KT, 2])
        self.CSPLIT = nc.alloc_sbuf_tensor_at("CSPLIT", [P, KT, 4], F32R, offset=self.at)
        self.at += 4 * KT * 4
        self.DER = sb("DER", [P, 40])
        self.LORA = sb("LORA", [P, 2, 512])
        self.G2 = sb("G2", [P, 512])
        self.WDG = sb("WDG", [P, KT, 32])
        self.GUP = sb("GUP", [16, 2, 256])
        self.WF = sb("WF", [P, 2, 2, P])
        self.HEADROW = sb("HEADROW", [P, 40])
        self.DSKIP = sb("DSKIP", [P, 4])
        self.SINKROW = sb("SINKROW", [P, 16])
        self.LAMROW = sb("LAMROW", [P, 4, 64])
        self.LAM = sb("LAM", [P, 4])
        self.SC = sb("SC", [P, 7900])
        self.HR, self.OR = (self.rounded(name, [P, KT, TOK]) for name in ("HT", "OT"))
        self.PR = self.rounded("PT", [P, 32, TOK])
        self.RINGR = self.rounded("RING", [P, SLOTS, KT * SW])
        self.SCR = self.rounded("SC", [P, 2 * KT * SW])
        self.ps = [ctx.enter_context(nc.psum_tensor(f"bank{b}", [P, 512], F32)) for b in range(8)]
        self.ring_loaded = [ctx.enter_context(nc.semaphore(f"ring{s}_loaded")) for s in range(SLOTS)]
        self.ring_base = [0] * SLOTS
        self.smalls_in = ctx.enter_context(nc.semaphore("smalls_in"))

    def rounded(self, name, shape):
        return self.nc.alloc_sbuf_tensor_at(name + "_rounded", shape, F32R, offset=self.places[name])

    def const(self, at, width=P):
        return self.CONST[:, at:at + width]

    def eps(self, value):
        at = C_EPS + EPSILONS.index(value)
        return self.CONST[:, at:at + 1]

    def par(self, name, n=0):
        return self.PAR[:, COL[name] + n:COL[name] + n + 1]

    def low(self, s, kt, m):
        return self.RINGR[:, s, kt * SW + m * P:kt * SW + m * P + P]

    def ring_half(self, ring, s, m, kts):
        return ring[:, s, 0:kts * SW].rearrange("p (t m) -> p t m", m=SW)[:, :, m * P:m * P + P]

    def high(self, s, m):
        at = (2 * (s % 2) + m) * KT * P
        return self.SCR[:, at:at + KT * P].rearrange("p (t m) -> p t m", m=P)

    def fetch(self, sync, w, i, s):
        view = self.RING[:, s, 0:w.kts[s] * SW].rearrange("p (t m) -> p t m", m=SW)
        sync.dma_start(view, w.slot(i, s)).then_inc(self.ring_loaded[s], 16)

    def spent(self, w):
        for s in range(SLOTS):
            self.ring_base[s] += 16 * (w.loops + (s < w.tail))


def load_stage(net, first_weights):
    nc, ins = net.nc, net.ins
    rows = net.SC[:, 0:3 * P].rearrange("p (g m) -> p g m", m=P)
    tokens = net.PT[:, 0:2 * NCH, :].rearrange("p t m -> p (t m)").rearrange("p (t d) -> p t d", d=D)
    with Stage(net, "load") as st:
        const_in, rows_in, x_in = st.sem("const_in"), st.sem("rows_in"), st.sem("x_in")
        small_in, zeroed = st.sem("small_in"), st.sem("wf_zeroed")
        turned, copied, cols_ready = st.sem("turned"), st.sem("copied"), st.sem("cols_ready")
        own = st.sem("dve_own")
        lam_exp, lam_sums, act_own = st.sem("lam_exp"), st.sem("lam_sums"), st.sem("act_own")
        smalls_in = net.smalls_in
        n_rows = sum(len(t) for t in ROWS)

        @st.sync
        def _(sp):
            sp.dma_start(net.CONST[:, :], ins["const_1"]).then_inc(const_in, 16)
            for t in range(2):
                sp.dma_start(tokens[:, t, :], ins["x"][0, P * t:P * t + P, :]).then_inc(x_in, 16)
            for t in range(2):
                sp.dma_start(tokens[:, 2 + t, :], ins["ctx"][0, P * t:P * t + P, :]).then_inc(x_in, 16)
            for s in range(first_weights.first()):
                net.fetch(sp, first_weights, 0, s)
            w1 = ins["l1_w_in"]
            for at, col in ((0, 1536), (16, 3088)):
                sp.dma_start(net.WDG[:, :, at:at + 16],
                             w1[:, col:col + 16].rearrange("(t k) m -> k t m", k=P)).then_inc(small_in, 16)
            sp.wait_ge(small_in, 32)

        @st.scalar
        def _(act):
            n = 0
            for g, tile in enumerate(ROWS):
                r = 0
                for name, count in tile:
                    a = ins[name]
                    if len(a.shape) == 2:
                        a = a.rearrange("a b -> (a b)")
                    flat = a.rearrange("(t p) -> t p", p=P)
                    act.dma_start(rows[r:r + count, g, :], flat).then_inc(rows_in, 16)
                    r += count
            link = Chain(act, act_own)
            act.wait_ge(cols_ready, 3)
            for n, name in enumerate(("c", "c_ctx")):
                act.activation(net.CACT[:, :, n], net.PAR[:, COL[name]:COL[name] + 8], ACT.Silu)
            act.wait_ge(lam_sums, 1)
            act.activation(net.LAM[:, 2:4], net.LAM[:, 0:2], ACT.Exp).then_inc(lam_exp, 1)

        @st.gpsimd
        def _(pool):
            pool.memset(net.WF[:, :, :, :], 0.0).then_inc(zeroed, 1)
            small = [(net.LORA[0:64, 0, :], ins["l0_w2_f"]), (net.LORA[0:64, 1, :], ins["l0_w2_b"]),
                     (net.LORA[64:128, 0, :], ins["l0_a2"]), (net.G2[:, :], ins["l0_g2"]),
                     (net.GUP[:, 0, :], ins["l1_gk_up_f"]), (net.GUP[:, 1, :], ins["l1_gk_up_b"])]
            for n, name in enumerate(("l1_dt_bias_f", "l1_dt_bias_b", "l1_a_log_f", "l1_a_log_b",
                                      "l1_d_skip")):
                small.append((net.HEADROW[:, 8 * n:8 * n + 8], ins[name].partition_broadcast(P)))
            small.append((net.SINKROW[:, :], ins["sink_2"].rearrange("a b -> (a b)").partition_broadcast(P)))
            for n, name in enumerate(("l0_lam_q1", "l0_lam_k1", "l0_lam_q2", "l0_lam_k2")):
                small.append((net.LAMROW[:, n, :], ins[name].partition_broadcast(P)))
            for into, of in small:
                pool.dma_start(into, of).then_inc(smalls_in, 16)
            pool.wait_ge(zeroed, 1)
            for layer in range(2):
                for g in range(4):
                    o = 64 * (g % 2)
                    pool.dma_start(net.WF[o:o + 64, layer, g // 2, o:o + 64],
                                   ins["w_fourier_2"][layer, g]).then_inc(smalls_in, 16)
            pool.wait_ge(smalls_in, 16 * (len(small) + 8))

        @st.tensor
        def _(pe):
            ident = net.const(C_IDENT)
            pe.wait_ge(const_in, 16)
            pe.wait_ge(rows_in, 16 * n_rows)
            for g, tile in enumerate(ROWS):
                r = sum(count for _, count in tile)
                nc.tensor.transpose(net.ps[g][:, 0:r], rows[0:r, g, :], ident[0:r, 0:r]).then_inc(turned, 1)
            pe.wait_ge(x_in, 64)
            for f in range(KT):
                bank = (f + 3) % 8
                if f >= 5:
                    pe.wait_ge(cols_ready, f - 4)
                for t in range(4):
                    last = nc.tensor.transpose(net.ps[bank][:, P * t:P * t + P],
                                               tokens[:, t, P * f:P * f + P], ident)
                last.then_inc(turned, 1)

        @st.vector
        def _(dve):
            link = Chain(dve, own)
            for g, tile in enumerate(ROWS):
                r = sum(count for _, count in tile)
                dve.wait_ge(turned, g + 1)
                nc.vector.tensor_copy(net.PAR[:, P * g:P * g + r], net.ps[g][:, 0:r]).then_inc(cols_ready, 1)
            for f in range(KT):
                dve.wait_ge(turned, f + 4)
                nc.vector.tensor_copy(net.XT[:, f, :], net.ps[(f + 3) % 8][:, :])
            dve.wait_ge(cols_ready, 3)
            mu = net.PAR[:, COL["l0_mu"]:COL["l0_mu"] + 14]
            nc.vector.tensor_scalar(net.DER[:, 0:14], mu, 0.5, None, ALU.mult)
            nc.vector.tensor_scalar(net.DER[:, 14:28], mu, -1.0, 1.0, ALU.mult, ALU.add)
            k_a = net.PAR[:, COL["l0_k_a"]:COL["l0_k_a"] + 4]
            nc.vector.tensor_scalar(net.DER[:, 28:32], k_a, -1.0, 1.0, ALU.mult, ALU.add)
            nc.vector.tensor_scalar(net.DER[:, 32:33], net.par("l0_subln"), 1.0 - LAM_INIT, None, ALU.mult)
            dve.wait_ge(smalls_in, 16 * (6 + 5 + 1 + 4 + 8))
            skip = net.HEADROW[:, 32:40].rearrange("p (t h) -> p t h", h=2)
            for h in range(2):
                nc.vector.tensor_copy(net.DSKIP[64 * h:64 * h + 64, :], skip[64 * h:64 * h + 64, :, h])
            lam = net.LAMROW[:, :, :].rearrange("p (a b) d -> p a b d", b=2)
            link(nc.vector.tensor_tensor(lam[:, :, 0, :], lam[:, :, 0, :], lam[:, :, 1, :], ALU.mult))
            nc.vector.tensor_reduce(net.LAM[:, 0:2], lam[:, :, 0, :], AX_X, ALU.add).then_inc(lam_sums, 1)
            dve.wait_ge(lam_exp, 1)
            link(nc.vector.tensor_tensor(net.LAM[:, 0:1], net.LAM[:, 3:4], net.LAM[:, 2:3], ALU.subtract))
            link(nc.vector.tensor_scalar(net.LAM[:, 0:1], net.LAM[:, 0:1], LAM_INIT, None, ALU.subtract))


def feed(net, sp, w, used, following, straight=False):
    if w.loops > 1 and straight:
        for i in range(w.loops - 1):
            for s in range(SLOTS):
                sp.wait_ge(*used(i, s))
                net.fetch(sp, w, i + 1, s)
    elif w.loops > 1:
        with sp.Fori(0, w.loops - 1) as i:
            for s in range(SLOTS):
                sp.wait_ge(*used(i, s))
                net.fetch(sp, w, i + 1, s)
    if w.loops:
        for s in range(w.tail):
            sp.wait_ge(*used(w.loops - 1, s))
            net.fetch(sp, w, w.loops, s)
    if following:
        for s in range(following.first()):
            if w.loops or s < w.tail:
                sp.wait_ge(*used(w.loops - (s >= w.tail), s))
            net.fetch(sp, following, 0, s)


def turns(engine, w, turn, straight=False, peel=False):
    first = w.loops if straight else min(w.loops, 1) if peel else 0
    for i in range(first):
        turn(i, range(SLOTS))
    if w.loops - first == 1:
        turn(first, range(SLOTS))
    elif w.loops > first:
        with engine.Fori(first, w.loops) as i:
            turn(i, range(SLOTS))
    if w.tail:
        turn(w.loops, range(w.tail))


class Operand:

    def __init__(self, high, low, whole=None):
        self.high, self.low, self.whole = high, low, whole

    def tiles(self):
        return self.whole.shape[1]


class Split:

    def __init__(self, st):
        self.high_ready = [st.sem(f"high_ready{m}") for m in range(2)]
        self.split_ready = [st.sem(f"split_ready{m}") for m in range(2)]
        self.used = [st.sem(f"used{m}") for m in range(2)]
        self.operand_high = st.sem("operand_high")
        self.operand_split = st.sem("operand_split")


def is_first(i, s):
    return isinstance(i, int) and i == 0 and s == 0


def high_on_act(net, act, w, sems, x=None, take=None, straight=False, side=None):
    base = list(net.ring_base)

    def turn(i, slots):
        for s in slots:
            for m in range(2):
                if m == 0:
                    act.wait_ge(net.ring_loaded[s], 16 * (i + 1) + base[s])
                if not (isinstance(i, int) and i == 0 and s < 2):
                    act.wait_ge(sems.used[m], SLOTS * i + s - 1)
                act.activation(net.high(s, m)[:, 0:w.kts[s], :], net.ring_half(net.RING, s, m, w.kts[s]),
                               ACT.Copy).then_inc(sems.high_ready[m], 1)
                if is_first(i, s) and m == 0 and x is not None and x.whole is not None:
                    for t in range(x.tiles()):
                        act.activation(x.high[:, t], x.whole[:, t], ACT.Copy).then_inc(sems.operand_high, 1)
                if side and isinstance(i, int) and i == 0 and s == 1 and m == 0:
                    for t in range(side.tiles()):
                        act.activation(side.high[:, t], side.whole[:, t], ACT.Copy).then_inc(sems.operand_high, 1)
                if take and not is_first(i, s):
                    take(*((i, s - 1) if s else (i - 1, SLOTS - 1)), m)

    turns(act, w, turn, straight, peel=True)
    if take:
        for m in range(2):
            take(*w.last(), m)


def low_on_dve(net, dve, w, sems, x=None, take=None, straight=False, side=None):
    def split(operand, before):
        for t in range(operand.tiles()):
            dve.wait_ge(sems.operand_high, before + t + 1)
            net.nc.vector.tensor_tensor(operand.low[:, t], operand.whole[:, t], operand.high[:, t].bitcast(F32),
                                        ALU.subtract).then_inc(sems.operand_split, 1)

    def turn(i, slots):
        for s in slots:
            for m in range(2):
                whole, low = (net.ring_half(ring, s, m, w.kts[s]) for ring in (net.RING, net.RINGR))
                dve.wait_ge(sems.high_ready[m], SLOTS * i + s + 1)
                net.nc.vector.tensor_tensor(low, whole, net.high(s, m)[:, 0:w.kts[s], :].bitcast(F32),
                                            ALU.subtract).then_inc(sems.split_ready[m], 1)
                if is_first(i, s) and m == 0 and x is not None and x.whole is not None:
                    split(x, 0)
                if side and isinstance(i, int) and i == 0 and s == 1 and m == 0:
                    split(side, x.tiles())
                if take and not is_first(i, s):
                    take(*((i, s - 1) if s else (i - 1, SLOTS - 1)), m)

    turns(dve, w, turn, straight, peel=True)
    if take:
        for m in range(2):
            take(*w.last(), m)


def product_on_pe(net, pe, w, sems, x, widths, tile_free, straight=False, side=None, side_from=None):
    def turn(i, slots):
        for s in slots:
            first = is_first(i, s)
            of_side = side is not None and isinstance(i, int) and i == w.loops and s >= side_from
            if of_side and s == side_from:
                pe.wait_ge(sems.operand_split, x.tiles() + side.tiles())
            for m in range(2):
                pe.wait_ge(tile_free[m], SLOTS * i + s + 1)
                pe.wait_ge(sems.split_ready[m], SLOTS * i + s + 1)
                for kt in range(KT):
                    if first and m == 0 and x.whole is not None:
                        pe.wait_ge(sems.operand_split, kt + 1)
                    last = three_passes(net, net.ps[2 * s + m], s, m, kt, side if of_side else x, kt, widths(i, s),
                                        kt == 0, kt == KT - 1)
                last.then_inc(sems.used[m], 1)

    turns(pe, w, turn, straight, peel=True)


def three_passes(net, bank, s, m, kt, x, at, n, start, stop):
    high, low = net.high(s, m)[:, kt, :], net.low(s, kt, m)
    x_high, x_low = x.high[:, at, 0:n], x.low[:, at, 0:n]
    net.nc.tensor.matmul(bank[:, 0:n], high, x_high, start=start, stop=False)
    net.nc.tensor.matmul(bank[:, 0:n], high, x_low, start=False, stop=False)
    return net.nc.tensor.matmul(bank[:, 0:n], low, x_high, start=False, stop=stop)


def deep_on_pe(net, pe, w, sems, x, n, tile_free):
    def turn(i, slots):
        for s in slots:
            part, group, at = s % w.depth, s // w.depth, sum(w.kts[s - s % w.depth:s])
            for m in range(2):
                if part == 0:
                    pe.wait_ge(tile_free[m], SLOTS // w.depth * i + group + 1)
                pe.wait_ge(sems.split_ready[m], SLOTS * i + s + 1)
                for kt in range(w.kts[s]):
                    last = three_passes(net, net.ps[2 * group + m], s, m, kt, x, at + kt, n, part == 0 and kt == 0,
                                        part == w.depth - 1 and kt == w.kts[s] - 1)
                last.then_inc(sems.used[m], 1)

    turns(pe, w, turn)


def modulation_stage(net, layer, w, following):
    nc = net.nc
    high, low = (net.PR[:, t:t + 16, :].rearrange("p t m -> p (t m)").rearrange("p (b m) -> p b m", b=SLOTS)
                 for t in (0, 16))
    rows = net.SC[0:4, 0:SLOTS * SW].rearrange("p (s m) -> p s m", m=SW)
    with Stage(net, f"mod{layer}") as st:
        own, c_split, high_ready, split_ready = (st.sem("dve_own"), st.sem("c_split"), st.sem("high_ready"),
                                                 st.sem("split_ready"))
        used, copied, turned = st.sem("used"), st.sem("copied"), st.sem("turned")
        base = list(net.ring_base)
        columns_at = net.ps[0][:, 0:96].rearrange("p (t n) -> p t n", n=2)

        @st.sync
        def _(sp):
            feed(net, sp, w, lambda i, s: (split_ready, SLOTS * i + s + 1), following)

        @st.scalar
        def _(act):
            def copy_rows(i, s):
                act.wait_ge(used, SLOTS * i + s + 1)
                if not (isinstance(i, int) and i == 0):
                    act.wait_ge(turned, SLOTS * (i - 1) + s + 1)
                act.activation(rows[:, s, :], net.ps[1 + s][0:4, 0:SW], ACT.Copy).then_inc(copied, 1)

            def turn(i, slots):
                for s in slots:
                    first = isinstance(i, int) and i == 0
                    act.wait_ge(net.ring_loaded[s], 16 * (i + 1) + base[s])
                    if not first:
                        act.wait_ge(used, SLOTS * (i - 1) + s + 1)
                    act.activation(high[:, s], net.RING[:, s, :], ACT.Copy).then_inc(high_ready, 1)
                    if s >= 2 or not first:
                        copy_rows(*((i, s - 2) if s >= 2 else (i - 1, s + 2)))

            turn(0, range(SLOTS))
            turn(1, range(SLOTS))
            with act.Fori(2, w.loops) as i:
                turn(i, range(SLOTS))
            for s in (SLOTS - 2, SLOTS - 1):
                copy_rows(w.loops - 1, s)

        @st.tensor
        def _(pe):
            pe.wait_ge(c_split, 1)

            def to_columns(i, s):
                pe.wait_ge(copied, SLOTS * i + s + 1)
                for m in range(2):
                    last = nc.tensor.matmul(columns_at[:, 2 * (SLOTS * i + s) + m, :], rows[:, s, P * m:P * m + P],
                                            net.CONST[0:4, C_FOLD:C_FOLD + 2], start=True, stop=True)
                last.then_inc(turned, 1)

            def turn(i, slots):
                for s in slots:
                    first = isinstance(i, int) and i == 0
                    if not first:
                        pe.wait_ge(copied, SLOTS * (i - 1) + s + 1)
                    pe.wait_ge(split_ready, SLOTS * i + s + 1)
                    for kt in range(KT):
                        c = net.CSPLIT[:, kt, :]
                        at = slice(SW * kt, SW * kt + SW)
                        nc.tensor.matmul(net.ps[1 + s][0:4, 0:SW], c, high[:, s, at], start=(kt == 0), stop=False)
                        last = nc.tensor.matmul(net.ps[1 + s][0:4, 0:SW], c, low[:, s, at], start=False,
                                                stop=(kt == KT - 1))
                    last.then_inc(used, 1)
                    if s >= 2 or not first:
                        to_columns(*((i, s - 2) if s >= 2 else (i - 1, s + 2)))

            turns(pe, w, turn, peel=True)
            for s in (SLOTS - 2, SLOTS - 1):
                to_columns(w.loops - 1, s)

        @st.vector
        def _(dve):
            link = Chain(dve, own)
            c_high, c_low = net.CSPLIT[:, :, 0:2], net.CSPLIT[:, :, 2:4]
            link(nc.vector.tensor_copy(c_high, net.CACT[:, :, :]))
            nc.vector.tensor_tensor(c_low, net.CACT[:, :, :], c_high.bitcast(F32), ALU.subtract).then_inc(c_split, 1)

            def turn(i, slots):
                for s in slots:
                    dve.wait_ge(high_ready, SLOTS * i + s + 1)
                    if not (isinstance(i, int) and i == 0):
                        dve.wait_ge(used, SLOTS * (i - 1) + s + 1)
                    nc.vector.tensor_tensor(low[:, s], net.RING[:, s, :], high[:, s].bitcast(F32),
                                            ALU.subtract).then_inc(split_ready, 1)

            turns(dve, w, turn, peel=True)
            dve.wait_ge(turned, SLOTS * w.loops)
            bias = COL[f"l{layer}_mod_b"]
            link(nc.vector.tensor_tensor(net.MOD[:, :, :], columns_at,
                                         net.PAR[:, bias:bias + 48].unsqueeze(2).to_broadcast([P, 48, 2]), ALU.add))
            for h in range(2):
                gain = COL[f"l{layer}_norm{h + 1}"]
                link(nc.vector.scalar_tensor_tensor(net.AFF[:, h], net.MOD[:, 24 * h + 8:24 * h + 16, :], 1.0,
                                                    net.PAR[:, gain:gain + 8].unsqueeze(2).to_broadcast([P, KT, 2]),
                                                    ALU.add, ALU.mult))
        net.spent(w)


def ada_stage(net, layer, half, n):
    nc, square = net.nc, net.PT
    with Stage(net, f"ada{layer}{half}") as st:
        squared, summed, scaled = st.sem("squared"), st.sem("summed"), st.sem("scaled")
        rstd_ready, act_own = st.sem("rstd_ready"), st.sem("act_own")
        total, rstd = net.ps[0][:, 0:n], net.SC[:, 0:n]
        parts = [(0, 0)] + ([(1, LAT)] if n > LAT else [])

        @st.scalar
        def _(act):
            for t in range(KT):
                act.activation(square[:, t, 0:n], net.XT[:, t, 0:n], ACT.Square).then_inc(squared, 1)
            inverse_roots(net, act, Chain(act, act_own), rstd_ready, [(summed, 1, rstd, total, 1.0 / D, net.eps(EPS))])
            for t in range(KT):
                act.wait_ge(scaled, t + 1)
                for j, at in parts:
                    act.activation(net.HT[:, t, at:at + LAT], net.HT[:, t, at:at + LAT], ACT.Identity,
                                   bias=net.MOD[:, 24 * half + t, j:j + 1])

        @st.tensor
        def _(pe):
            for t in range(KT):
                pe.wait_ge(squared, t + 1)
                last = nc.tensor.matmul(total, net.const(C_ONES), square[:, t, 0:n], start=(t == 0), stop=(t == KT - 1))
            last.then_inc(summed, 1)

        @st.vector
        def _(dve):
            dve.wait_ge(rstd_ready, 1)
            for t in range(KT):
                for j, at in parts:
                    last = nc.vector.scalar_tensor_tensor(net.HT[:, t, at:at + LAT], net.XT[:, t, at:at + LAT],
                                                          net.AFF[:, half, t, j:j + 1], rstd[:, at:at + LAT],
                                                          ALU.mult, ALU.mult)
                last.then_inc(scaled, 1)


def project_stage(net, name, w, x, widths, dst, following, straight=False, side=None, side_from=None):
    with Stage(net, name) as st:
        sems = Split(st)
        tile_free = [st.sem(f"tile_free{m}") for m in range(2)]

        @st.sync
        def _(sp):
            feed(net, sp, w, lambda i, s: (sems.used[1], SLOTS * i + s + 1), following, straight)

        @st.tensor
        def _(pe):
            product_on_pe(net, pe, w, sems, x, widths, tile_free, straight, side, side_from)

        @st.scalar
        def _(act):
            for m in range(2):
                act.sem_inc(tile_free[m], SLOTS)

            def take(i, s, m):
                n = widths(i, s)
                act.wait_ge(sems.used[m], SLOTS * i + s + 1)
                act.activation(dst[:, 2 * (SLOTS * i + s) + m, 0:n], net.ps[2 * s + m][:, 0:n],
                               ACT.Copy).then_inc(tile_free[m], 1)

            high_on_act(net, act, w, sems, x, take, straight, side)

        @st.vector
        def _(dve):
            low_on_dve(net, dve, w, sems, x, straight=straight, side=side)
        net.spent(w)


def relu_squared_stage(net, name, w, x, n, hidden, following):
    nc = net.nc
    with Stage(net, name) as st:
        sems = Split(st)
        raised, squared, high = ([st.sem(f"{what}{m}") for m in range(2)] for what in ("raised", "squared", "hidden_high"))

        @st.sync
        def _(sp):
            feed(net, sp, w, lambda i, s: (sems.used[1], SLOTS * i + s + 1), following)

        @st.tensor
        def _(pe):
            product_on_pe(net, pe, w, sems, x, lambda i, s: n, raised)

        @st.scalar
        def _(act):
            for m in range(2):
                act.sem_inc(raised[m], SLOTS)

            def take(i, s, m):
                act.wait_ge(sems.used[m], SLOTS * i + s + 1)
                act.activation(hidden.whole[:, 2 * (SLOTS * i + s) + m, :], net.ps[2 * s + m][:, 0:n],
                               ACT.Relu).then_inc(raised[m], 1)

            high_on_act(net, act, w, sems, x, take)

        @st.vector
        def _(dve):
            def take(i, s, m):
                low, top, whole = (v[:, 2 * (SLOTS * i + s) + m, :] for v in (hidden.low, hidden.high, hidden.whole))
                done = SLOTS * i + s + 1
                dve.wait_ge(raised[m], SLOTS + done)
                nc.vector.tensor_tensor(whole, whole, whole, ALU.mult).then_inc(squared[m], 1)
                dve.wait_ge(squared[m], done)
                nc.vector.tensor_scalar(top, whole, 1.0, None, ALU.mult).then_inc(high[m], 1)
                dve.wait_ge(high[m], done)
                nc.vector.tensor_tensor(low, whole, top.bitcast(F32), ALU.subtract)

            low_on_dve(net, dve, w, sems, x, take)
        net.spent(w)


def mixed_out_stage(net, name, w, x, n, following):
    with Stage(net, name) as st:
        sems = Split(st)
        tile_free = [st.sem(f"tile_free{m}") for m in range(2)]

        @st.sync
        def _(sp):
            feed(net, sp, w, lambda i, s: (sems.used[1], SLOTS * i + s + 1), following)

        @st.tensor
        def _(pe):
            product_on_pe(net, pe, w, sems, x, lambda i, s: n, tile_free)

        @st.scalar
        def _(act):
            high_on_act(net, act, w, sems, x)

        @st.vector
        def _(dve):
            for m in range(2):
                dve.sem_inc(tile_free[m], SLOTS)

            def take(i, s, m):
                dve.wait_ge(sems.used[m], SLOTS * i + s + 1)
                add_gated(net, 2 * (SLOTS * i + s) + m, net.ps[2 * s + m], 16, n)

            low_on_dve(net, dve, w, sems, x, take)
        net.spent(w)


def add_gated(net, tile, bank, gate, n):
    for j, at in ((0, 0), (1, LAT))[:n // LAT]:
        into = net.XT[:, tile, at:at + LAT]
        step = net.nc.vector.scalar_tensor_tensor(into, bank[:, at:at + LAT], net.MOD[:, gate + tile, j:j + 1], into,
                                                  ALU.mult, ALU.add)
    return step


def deep_stage(net, name, w, x, n, take, following):
    with Stage(net, name) as st:
        sems = Split(st)
        tile_free = [st.sem(f"tile_free{m}") for m in range(2)]
        across = SLOTS // w.depth

        @st.sync
        def _(sp):
            feed(net, sp, w, lambda i, s: (sems.used[1], SLOTS * i + s + 1), following)

        @st.tensor
        def _(pe):
            deep_on_pe(net, pe, w, sems, x, n, tile_free)

        @st.scalar
        def _(act):
            high_on_act(net, act, w, sems)

        @st.vector
        def _(dve):
            for m in range(2):
                dve.sem_inc(tile_free[m], across)

            def take_last(i, s, m):
                if s % w.depth == w.depth - 1:
                    dve.wait_ge(sems.used[m], SLOTS * i + s + 1)
                    group = s // w.depth
                    take(2 * (across * i + group) + m, net.ps[2 * group + m]).then_inc(tile_free[m], 1)

            low_on_dve(net, dve, w, sems, take=take_last)
        net.spent(w)


def first_fetch_stage(net, w):
    with Stage(net, "fetch") as st:
        @st.sync
        def _(sp):
            for s in range(w.first()):
                net.fetch(sp, w, 0, s)


def diff_prepare_stage(net):
    nc = net.nc
    values = net.SC[:, 0:2048].rearrange("p (t m) -> p t m", m=512)
    part = net.SC[:, 2048:2048 + 2 * LAT].rearrange("p (b m) -> p b m", m=LAT)
    with Stage(net, "diff_prepare") as st:
        rotated, added, turned, own = st.sem("rotated"), st.sem("added"), st.sem("turned"), st.sem("dve_own")

        @st.tensor
        def _(pe):
            for t in range(8):
                if t >= 4:
                    pe.wait_ge(added, t - 3)
                nc.tensor.matmul(net.ps[t % 4][:, 0:LAT], net.const(C_ROTA), net.PT[:, t, 0:LAT],
                                 start=True, stop=True).then_inc(rotated, 1)
            for t in range(NCH):
                for h in range(4):
                    last = nc.tensor.transpose(net.ps[4 + t][:, P * h:P * h + P],
                                               net.PT[:, 8 + h, CH * t:CH * t + CH], net.const(C_IDENT))
                last.then_inc(turned, 1)

        @st.scalar
        def _(act):
            for t in range(NCH):
                act.wait_ge(turned, t + 1)
                act.activation(values[:, t, :], net.ps[4 + t][:, :], ACT.Copy)

        @st.vector
        def _(dve):
            link = Chain(dve, own)
            for t in range(8):
                dve.wait_ge(rotated, t + 1)
                x = net.PT[:, t, 0:LAT]
                nc.vector.tensor_tensor(part[:, t % 2], net.ps[t % 4][:, 0:LAT], net.const(C_SINA, LAT),
                                        ALU.mult).then_inc(added, 1)
                link(nc.vector.tensor_tensor(x, x, net.const(C_COSA, LAT), ALU.mult))
                dve.wait_ge(added, t + 1)
                link(nc.vector.tensor_tensor(x, x, part[:, t % 2], ALU.add))


def diff_attention_stage(net):
    nc = net.nc
    near = [net.HT[:, t, :] for t in range(KT)] + [net.PT[:, t, :] for t in range(26, 32)]
    values = net.SC[:, 0:2048].rearrange("p (t m) -> p t m", m=512)
    prob = net.SC[:, 2048:4096].rearrange("p (b m k) -> p b m k", b=2, m=2)
    mixed = net.SC[:, 4096:5120].rearrange("p (b k) -> p b k", b=2)
    mixed_t = net.SC[:, 5120:6144].rearrange("p (b k) -> p b k", b=2)
    stat = net.SC[:, 6144:6144 + 8 * 16].rearrange("p (u n) -> p u n", n=8)
    units = [(h, q) for h in range(4) for q in range(NCH)]
    first_key = lambda q: 0 if q < 2 else 2
    scale = 64 ** -0.5
    with Stage(net, "diff_attention") as st:
        scored, max_ready, exp_ready = st.sem("scored"), st.sem("max_ready"), st.sem("exp_ready")
        mixed_ready, turned, turned_copied = st.sem("mixed_ready"), st.sem("turned"), st.sem("turned_copied")
        out_ready, out_taken, own = st.sem("out_ready"), st.sem("out_taken"), st.sem("dve_own")
        near_ready, damped = st.sem("near_ready"), st.sem("damped")

        @st.gpsimd
        def _(pool):
            by_part = lambda v: v.rearrange("p (s m) -> p s m", m=LAT)
            for t, sums in enumerate(near):
                of, into = by_part(net.PT[:, 12 + t, :]), by_part(sums)
                pool.tensor_tensor(into[:, :, 1:LAT - 1], of[:, :, 0:LAT - 2], of[:, :, 2:LAT],
                                   ALU.add).then_inc(near_ready, 1)
                pool.tensor_copy(into[:, :, 0:1], of[:, :, 1:2]).then_inc(near_ready, 1)
                pool.tensor_copy(into[:, :, LAT - 1:LAT], of[:, :, LAT - 2:LAT - 1]).then_inc(near_ready, 1)

        @st.tensor
        def _(pe):
            def score(u):
                h, q = units[u]
                if u >= 2:
                    pe.wait_ge(exp_ready, 2 * (u - 1))
                k0 = first_key(q) * P
                for m in range(2):
                    rows = slice(64 * m, 64 * m + 64)
                    last = nc.tensor.matmul(net.ps[2 * (u % 2) + m][:, k0:TOK], net.PT[rows, h, P * q:P * q + P],
                                            net.PT[rows, 4 + h, k0:TOK], start=True, stop=True)
                last.then_inc(scored, 1)

            def weigh(u):
                h, q = units[u]
                pe.wait_ge(turned_copied, u + 1)
                if q == 0 and h >= 2:
                    pe.wait_ge(out_taken, h - 1)
                for t in range(first_key(q), NCH):
                    last = nc.tensor.matmul(net.ps[6 + h % 2][:, P * q:P * q + P], values[:, t, P * h:P * h + P],
                                            mixed_t[:, u % 2, P * t:P * t + P],
                                            start=(t == first_key(q)), stop=(t == NCH - 1))
                last.then_inc(out_ready, 1)

            score(0)
            score(1)
            for u, (h, q) in enumerate(units):
                if u + 2 < len(units):
                    score(u + 2)
                pe.wait_ge(mixed_ready, u + 1)
                if u >= 2:
                    pe.wait_ge(turned_copied, u - 1)
                for t in range(first_key(q), NCH):
                    last = nc.tensor.transpose(net.ps[4 + u % 2][:, P * t:P * t + P],
                                               mixed[:, u % 2, P * t:P * t + P], net.const(C_IDENT))
                last.then_inc(turned, 1)
                if u:
                    weigh(u - 1)
            weigh(len(units) - 1)

        @st.scalar
        def _(act):
            def exps(u):
                k0 = first_key(units[u][1]) * P
                act.wait_ge(max_ready, u + 1)
                if u >= 2:
                    act.wait_ge(mixed_ready, u - 1)
                for m in range(2):
                    act.activation(prob[:, u % 2, m, k0:TOK], net.ps[2 * (u % 2) + m][:, k0:TOK], ACT.Exp,
                                   bias=stat[:, u, m:m + 1], scale=scale,
                                   accum_out=stat[:, u, 2 + m:3 + m]).then_inc(exp_ready, 1)

            exps(0)
            exps(1)
            for u, (h, q) in enumerate(units):
                k0 = first_key(q) * P
                act.wait_ge(turned, u + 1)
                if u >= 2:
                    act.wait_ge(out_ready, u - 1)
                act.activation(mixed_t[:, u % 2, k0:TOK], net.ps[4 + u % 2][:, k0:TOK],
                               ACT.Copy).then_inc(turned_copied, 1)
                if u + 2 < len(units):
                    exps(u + 2)
                t = u - 2
                if t >= 0:
                    f = net.PT[:, 12 + t, :]
                    act.wait_ge(near_ready, 3 * (t + 1))
                    act.activation(f, f, ACT.Copy, scale=net.DER[:, 14 + t:15 + t]).then_inc(damped, 1)

        @st.vector
        def _(dve):
            link = Chain(dve, own)

            def maxima(u):
                k0 = first_key(units[u][1]) * P
                dve.wait_ge(scored, u + 1)
                for m in range(2):
                    link(nc.vector.reduce_max(stat[:, u, m:m + 1], net.ps[2 * (u % 2) + m][:, k0:TOK], AX_X))
                nc.vector.tensor_scalar(stat[:, u, 0:2], stat[:, u, 0:2], -scale, None,
                                        ALU.mult).then_inc(max_ready, 1)

            def shift(t):
                f = net.PT[:, 12 + t, :]
                dve.wait_ge(damped, t + 1)
                nc.vector.scalar_tensor_tensor(f, near[t], net.DER[:, t:t + 1], f, ALU.mult, ALU.add)

            maxima(0)
            maxima(1)
            for u, (h, q) in enumerate(units):
                k0 = first_key(q) * P
                dve.wait_ge(exp_ready, 2 * (u + 1))
                link(nc.vector.reciprocal(stat[:, u, 4:6], stat[:, u, 2:4]))
                link(nc.vector.tensor_tensor(stat[:, u, 5:6], stat[:, u, 5:6], net.LAM[:, 0:1], ALU.mult))
                link(nc.vector.tensor_scalar(prob[:, u % 2, 1, k0:TOK], prob[:, u % 2, 1, k0:TOK],
                                             stat[:, u, 5:6], None, ALU.mult))
                if u >= 2:
                    dve.wait_ge(turned, u - 1)
                nc.vector.scalar_tensor_tensor(mixed[:, u % 2, k0:TOK], prob[:, u % 2, 0, k0:TOK], stat[:, u, 4:5],
                                               prob[:, u % 2, 1, k0:TOK], ALU.mult, ALU.add).then_inc(mixed_ready, 1)
                if u + 2 < len(units):
                    maxima(u + 2)
                t = u - 3
                if t >= 0:
                    shift(t)
                if q == 1 and h >= 1:
                    dve.wait_ge(out_ready, 4 * h)
                    nc.vector.tensor_copy(net.OT[:, h - 1, :], net.ps[6 + (h - 1) % 2][:, :]).then_inc(out_taken, 1)
            shift(len(near) - 1)
            dve.wait_ge(out_ready, len(units))
            nc.vector.tensor_copy(net.OT[:, 3, :], net.ps[7][:, :])


def load_log_exp(net, act):
    if not net.log_exp_loaded:
        act.preload_act_table_set(LOG_EXP)
        net.log_exp_loaded = True


def inverse_roots(net, act, own, ready, steps):
    load_log_exp(net, act)
    for n, (sem, value, into, of, scale, eps) in enumerate(steps):
        act.wait_ge(sem, value)
        step = act.activation(into, of, ACT.Ln, scale=scale, bias=eps)
        if n + 1 < len(steps):
            step.then_inc(own.sem, 1)
            own.n += 1
    own(step)
    for _, _, into, _, _, _ in steps:
        act.activation(into, into, ACT.Exp, scale=-0.5).then_inc(ready, 1)


def group_norm_stage(net, name, groups, n, eps, adds=()):
    nc = net.nc
    with Stage(net, name) as st:
        squared, summed, rstd_ready = st.sem("squared"), st.sem("summed"), st.sem("rstd_ready")
        own, act_own = st.sem("dve_own"), st.sem("act_own")
        steps = [t for g in groups for t in zip(g[0], g[3])]

        @st.scalar
        def _(act):
            link = Chain(act, act_own)
            for src, square in steps:
                act.activation(square, src, ACT.Square).then_inc(squared, 1)
            inverse_roots(net, act, link, rstd_ready, [(summed, g + 1, squares[0], net.ps[g % 8][:, 0:n],
                                                   1.0 / (P * len(srcs)), net.eps(eps))
                                                  for g, (srcs, _, _, squares) in enumerate(groups)])

        @st.tensor
        def _(pe):
            at = 0
            for g, (srcs, _, _, squares) in enumerate(groups):
                for k, square in enumerate(squares):
                    at += 1
                    pe.wait_ge(squared, at)
                    last = nc.tensor.matmul(net.ps[g % 8][:, 0:n], net.const(C_ONES), square,
                                            start=(k == 0), stop=(k == len(squares) - 1))
                last.then_inc(summed, 1)

        @st.vector
        def _(dve):
            link = Chain(dve, own)
            for g, (srcs, dsts, gains, squares) in enumerate(groups):
                dve.wait_ge(rstd_ready, g + 1)
                for src, dst, gain in zip(srcs, dsts, gains):
                    last = nc.vector.scalar_tensor_tensor(dst, src, gain, squares[0], ALU.mult, ALU.mult)
                if adds:
                    link(last)
                for dst, x in zip(dsts, adds):
                    nc.vector.tensor_tensor(x, x, dst, ALU.add)


def residual_norm_stage(net, name, y, x, h, squares, side=None):
    nc = net.nc
    (y, y_gains), (h, h_gains) = y, h
    first, second = squares
    sums = [net.ps[n][:, 0:LAT] for n in range(3)]
    with Stage(net, name) as st:
        y_squared, x_squared, side_squared = st.sem("y_squared"), st.sem("x_squared"), st.sem("side_squared")
        summed, rstd_ready, act_own = st.sem("summed"), st.sem("rstd_ready"), st.sem("act_own")
        scaled, added, side_summed, side_ready = (st.sem("scaled"), st.sem("added"), st.sem("side_summed"),
                                                  st.sem("side_ready"))
        root = lambda act, link, sem, value, ready, into, n: inverse_roots(
            net, act, link, ready, [(sem, value, into, sums[n], 1.0 / D, net.eps(EPS))])

        @st.scalar
        def _(act):
            link = Chain(act, act_own)
            for t in range(KT):
                act.activation(first[t], y[t], ACT.Square).then_inc(y_squared, 1)
            root(act, link, summed, 1, rstd_ready, first[0], 0)
            if side:
                for t in range(KT):
                    act.activation(side[3][t], side[0][t], ACT.Square).then_inc(side_squared, 1)
            for t in range(KT):
                act.wait_ge(added, t + 1)
                act.activation(second[t], x[t], ACT.Square).then_inc(x_squared, 1)
            if side:
                root(act, link, side_summed, 1, side_ready, side[3][0], 2)
            root(act, link, summed, 2, rstd_ready, second[0], 1)

        @st.tensor
        def _(pe):
            def add_up(into, squared, tiles, done):
                for t in range(KT):
                    pe.wait_ge(squared, t + 1)
                    last = nc.tensor.matmul(into, net.const(C_ONES), tiles[t], start=(t == 0), stop=(t == KT - 1))
                last.then_inc(done, 1)

            add_up(sums[0], y_squared, first, summed)
            if side:
                add_up(sums[2], side_squared, side[3], side_summed)
            add_up(sums[1], x_squared, second, summed)

        @st.vector
        def _(dve):
            def add(t):
                dve.wait_ge(scaled, t + 1)
                nc.vector.tensor_tensor(x[t], x[t], y[t], ALU.add).then_inc(added, 1)

            dve.wait_ge(rstd_ready, 1)
            for t in range(KT):
                nc.vector.scalar_tensor_tensor(y[t], y[t], y_gains[t], first[0], ALU.mult, ALU.mult).then_inc(scaled, 1)
                if t:
                    add(t - 1)
            add(KT - 1)
            if side:
                dve.wait_ge(side_ready, 1)
                for t in range(KT):
                    nc.vector.scalar_tensor_tensor(side[1][t], side[0][t], side[2][t], side[3][0], ALU.mult, ALU.mult)
            dve.wait_ge(rstd_ready, 2)
            for t in range(KT):
                nc.vector.scalar_tensor_tensor(h[t], x[t], h_gains[t], second[0], ALU.mult, ALU.mult)


def rwkv_prepare_stage(net):
    nc = net.nc
    r0, k0, lora, gate = 12, 16, 24, 25
    kk = net.HT[:, 4:8, :]
    b = net.PT[:, 26:30, :]
    square = net.SC[:, 3584:3584 + 2048].rearrange("p (t m) -> p t m", m=TOK)
    norm = net.SC[:, 5632:5632 + 2048].rearrange("p (t m) -> p t m", m=TOK)
    with Stage(net, "rwkv_prepare") as st:
        own, act_own = st.sem("dve_own"), st.sem("act_own")
        tanh_ready, a_summed, a_ready = st.sem("tanh_ready"), st.sem("a_summed"), st.sem("a_ready")
        squared, normed, floor_ready, root_ready = (st.sem("squared"), st.sem("normed"), st.sem("floor_ready"),
                                                    st.sem("root_ready"))

        @st.vector
        def _(dve):
            link = Chain(dve, own)
            for t in range(4):
                dve.wait_ge(normed, t + 1)
                nc.vector.tensor_scalar(norm[:, t], net.ps[4 + t][:, :], 1e-24, None, ALU.max).then_inc(floor_ready, 1)
            for t in range(4):
                k = net.PT[:, k0 + t, :]
                dve.wait_ge(root_ready, t + 1)
                link(nc.vector.scalar_tensor_tensor(kk[:, t, :], k, net.par("l0_k_k", t), norm[:, t], ALU.mult, ALU.mult))
                dve.wait_ge(a_ready, t + 1)
                link(nc.vector.tensor_scalar(norm[:, t], b[:, t, :], net.par("l0_k_a", t), net.DER[:, 28 + t:29 + t],
                                             ALU.mult, ALU.add))
                link(nc.vector.tensor_tensor(k, k, norm[:, t], ALU.mult))
                link(nc.vector.tensor_tensor(b[:, t, :], b[:, t, :], kk[:, t, :], ALU.mult))

        @st.scalar
        def _(act):
            link = Chain(act, act_own)
            net.log_exp_loaded = False
            for t in range(4):
                act.activation(square[:, t], net.PT[:, k0 + t, :], ACT.Square,
                               scale=net.par("l0_k_k", t)).then_inc(squared, 1)
            act.activation(net.PT[0:64, lora, :], net.PT[0:64, lora, :], ACT.Tanh).then_inc(tanh_ready, 1)
            act.activation(net.PT[:, gate, :], net.PT[:, gate, :], ACT.Sigmoid)
            for t in range(4):
                act.wait_ge(a_summed, t + 1)
                act.activation(b[:, t, :], net.ps[t][:, :], ACT.Sigmoid, bias=net.par("l0_a0", t)).then_inc(a_ready, 1)
            inverse_roots(net, act, link, root_ready, [(floor_ready, t + 1, norm[:, t], norm[:, t], 1.0, 0.0)
                                                  for t in range(4)])

        @st.tensor
        def _(pe):
            for t in range(4):
                nc.tensor.matmul(net.ps[t][:, :], net.LORA[64:128, 0, P * t:P * t + P], net.PT[64:128, lora, :],
                                 start=True, stop=True).then_inc(a_summed, 1)
            for t in range(4):
                pe.wait_ge(squared, t + 1)
                nc.tensor.matmul(net.ps[4 + t][:, :], net.const(C_BLK), square[:, t], start=True,
                                 stop=True).then_inc(normed, 1)


class RwkvMemory:

    def __init__(self, net):
        chunks = lambda v: v.rearrange("p t (c m) -> p t c m", m=CH)
        flat = lambda v, n: v.rearrange("p t m -> p (t m)")[:, 0:n]
        self.r, self.k, self.v = (chunks(net.PT[:, n:n + 4, :]) for n in (12, 16, 20))
        self.kk, self.b = chunks(net.HT[:, 4:8, :]), chunks(net.PT[:, 26:30, :])
        self.kr = flat(net.PT[:, 0:8, :], 4096).rearrange("p (t c n m) -> p t c n m", t=4, c=NCH, n=2)
        self.bd, self.kd = chunks(net.PT[:, 8:12, :]), chunks(net.HT[:, 0:4, :])
        self.sig, self.cum = (net.SC[:, n:n + 2048].rearrange("p (t c m) -> p t c m", t=4, c=NCH) for n in (0, 2048))
        self.vtok = net.SC[:, 4096:6144].rearrange("p (c m) -> p c m", m=512)
        self.state = net.SC[:, 6144:6656].rearrange("p (t m) -> p t m", m=P)
        self.rhs, self.minus_u = net.SC[:, 6656:7168], net.SC[:, 7168:7680]
        small = net.SC[:, 7680:7680 + 64].rearrange("p (n t c) -> p n t c", n=4, t=4)
        self.mid, self.end, self.carry = small[:, 0], small[:, 1], small[:, 2]
        self.btok, self.ktok = net.PT[:, 30, :], net.PT[:, 31, :]
        ring = net.RING[:, :, :].rearrange("p s m -> p (s m)")
        self.grams = [place.rearrange("p (h m) -> p h m", m=512) for place in (ring[:, 0:4096], net.SC[:, 0:4096])]
        four = ring[:, 4096:8192].rearrange("p (q n h m) -> p q n h m", q=2, n=4, h=4)
        self.level, self.inv, self.first_inv_t, self.y = (four[:, :, n] for n in range(4))
        self.out = chunks(net.OT[:, 4:8, :])

    def inv_t(self, order, j, q):
        return (self.bd, self.kd)[q][:, :, order[j - 1], :] if j else self.first_inv_t[:, q]


def rwkv_decay_stage(net, d):
    nc, mem = net.nc, RwkvMemory(net)
    order = [2, 3, 0, 1] if d == 0 else [3, 2, 1, 0]
    mid, end = (63, CH - 1) if d == 0 else (64, 0)
    flat = lambda v: v.rearrange("p t c m -> p (t c) m")
    with Stage(net, f"rwkv_decay{d}") as st:
        summed, gated, cum_ready, exped, own = (st.sem("summed"), st.sem("gated"), st.sem("cum_ready"),
                                                st.sem("exped"), st.sem("dve_own"))
        turned, carry_ready = st.sem("turned"), st.sem("carry_ready")

        @st.tensor
        def _(pe):
            for t in range(4):
                nc.tensor.matmul(net.ps[t][:, :], net.LORA[0:64, d, P * t:P * t + P], net.PT[0:64, 24, :],
                                 start=True, stop=True).then_inc(summed, 1)
            if d == 0:
                for c in range(NCH):
                    for t in range(4):
                        last = nc.tensor.transpose(net.ps[4 + c][:, P * t:P * t + P], mem.v[:, t, c, :],
                                                   net.const(C_IDENT))
                    last.then_inc(turned, 1)

        @st.scalar
        def _(act):
            net.log_exp_loaded = False
            bias = "l0_w0_f" if d == 0 else "l0_w0_b"
            for t in range(4):
                act.wait_ge(summed, t + 1)
                act.activation(mem.sig[:, t].rearrange("p c m -> p (c m)"), net.ps[t][:, :], ACT.Sigmoid,
                               bias=net.par(bias, t)).then_inc(gated, 1)
            if d == 0:
                for c in range(NCH):
                    act.wait_ge(turned, c + 1)
                    act.activation(mem.vtok[:, c, :], net.ps[4 + c][:, :], ACT.Copy)
            kr = mem.kr.rearrange("p t c n m -> p (t c) n m")
            act.wait_ge(cum_ready, 1)
            act.activation(kr[:, :, 1, :], flat(mem.cum), ACT.Exp, scale=-DECAY).then_inc(exped, 1)
            act.activation(flat(mem.bd), flat(mem.cum), ACT.Exp, scale=DECAY).then_inc(exped, 1)
            act.wait_ge(cum_ready, 2)
            act.activation(kr[:, :, 0, :], flat(mem.sig), ACT.Exp, scale=-DECAY).then_inc(exped, 1)
            act.wait_ge(carry_ready, 1)
            act.activation(mem.carry[:, :, 0:3], mem.carry[:, :, 0:3], ACT.Exp, scale=-DECAY)

        @st.vector
        def _(dve):
            link = Chain(dve, own)
            ones = net.const(C_ONES)
            for t in range(4):
                dve.wait_ge(gated, t + 1)
                for c in range(NCH):
                    into, of = mem.cum[:, t, c, :], mem.sig[:, t, c, :]
                    if d:
                        into, of = into[:, ::-1], of[:, ::-1]
                    last = nc.vector.tensor_tensor_scan(into, ones, of, 0.0, ALU.mult, ALU.add)
            link(last)
            link(nc.vector.tensor_copy(mem.mid, mem.cum[:, :, :, mid]))
            link(nc.vector.tensor_copy(mem.end, mem.cum[:, :, :, end]))
            nc.vector.tensor_tensor(flat(mem.cum), flat(mem.cum),
                                    mem.mid.rearrange("p t c -> p (t c)").unsqueeze(2).to_broadcast([P, 16, CH]),
                                    ALU.subtract).then_inc(cum_ready, 1)
            dve.wait_ge(cum_ready, 1)
            nc.vector.tensor_tensor(flat(mem.sig), flat(mem.cum), flat(mem.sig), ALU.subtract).then_inc(cum_ready, 1)
            for j in range(3):
                c, after = order[j], order[j + 1]
                link(nc.vector.tensor_tensor(mem.carry[:, :, j], mem.end[:, :, c], mem.mid[:, :, c], ALU.subtract))
                step = nc.vector.tensor_tensor(mem.carry[:, :, j], mem.carry[:, :, j], mem.mid[:, :, after], ALU.add)
                step.then_inc(carry_ready, 1) if j == 2 else link(step)
            kr = mem.kr.rearrange("p t c n m -> p (t c) n m")
            dve.wait_ge(exped, 2)
            nc.vector.tensor_tensor(kr[:, :, 1, :], kr[:, :, 1, :], flat(mem.r), ALU.mult)
            link(nc.vector.tensor_tensor(flat(mem.kd), flat(mem.bd), flat(mem.k), ALU.mult))
            nc.vector.tensor_tensor(flat(mem.bd), flat(mem.bd), flat(mem.b), ALU.mult)
            dve.wait_ge(exped, 3)
            nc.vector.tensor_tensor(kr[:, :, 0, :], kr[:, :, 0, :], flat(mem.kk), ALU.mult)


def rwkv_chunks_stage(net, d):
    nc, mem = net.nc, RwkvMemory(net)
    order = [2, 3, 0, 1] if d == 0 else [3, 2, 1, 0]
    mask4 = net.const(C_MASK4 + 512 * d, 512)
    level_mask = lambda lv: net.const(C_LEVEL + P * (7 * d + lv)).unsqueeze(1).to_broadcast([P, 4, P])
    ident = net.const(C_IDENT)
    four = lambda bank: bank[:, :].rearrange("p (h m) -> p h m", m=P)
    head = lambda h: (h // 2, slice(64 * (h % 2), 64 * (h % 2) + 64))
    inv_t = lambda j, q: mem.inv_t(order, j, q)
    LV = range(1, 7)
    EVEN_ODD = (0, 2, 4, 6, 1, 3, 5, 7)
    with Stage(net, f"rwkv_chunks{d}") as st:
        gram_ready, gram_masked = st.sem("gram_ready"), st.sem("gram_masked")
        start_ready, start_turned, start_copied = st.sem("start_ready"), st.sem("start_turned"), st.sem("start_copied")
        level_ready, y_ready, y_copied = st.sem("level_ready"), st.sem("y_ready"), st.sem("y_copied")
        dd_ready, inv_doubled, doubled = st.sem("dd_ready"), st.sem("inv_doubled"), st.sem("doubled")
        rhs_ready, rhs_copied, u_ready, u_copied = st.sem("rhs_ready"), st.sem("rhs_copied"), st.sem("u_ready"), st.sem("u_copied")
        tok_turned, tok_copied = st.sem("tok_turned"), st.sem("tok_copied")
        out_ready, out_taken, state_summed, state_ready = (st.sem("out_ready"), st.sem("out_taken"),
                                                           st.sem("state_summed"), st.sem("state_ready"))
        own = st.sem("dve_own")

        @st.tensor
        def _(pe):
            def token_products(j, heads):
                c = order[j]
                for h in heads:
                    t, rows = head(h)
                    bank = net.ps[h % 2]
                    if 8 * j + h >= 2:
                        pe.wait_ge(gram_masked, 8 * j + h - 1)
                    both = mem.kr[rows, t, c].rearrange("p n m -> p (n m)")
                    nc.tensor.matmul(bank[:, 0:256], mem.bd[rows, t, c, :], both, start=True, stop=True)
                    nc.tensor.matmul(bank[:, 256:512], mem.kd[rows, t, c, :], both,
                                     start=True, stop=True).then_inc(gram_ready, 1)

            token_products(0, range(8))
            for j, c in enumerate(order):
                gram = mem.grams[j % 2]
                for q in range(2):
                    pe.wait_ge(start_ready, 2 * j + q + 1)
                    if j:
                        pe.wait_ge(tok_copied, 2 * j)
                    for h in range(4):
                        last = nc.tensor.transpose(net.ps[4 + q][:, P * h:P * h + P], inv_t(j, q)[:, h, :], ident)
                    last.then_inc(start_turned, 1)
                for lv in LV:
                    n = 12 * j + 2 * (lv - 1)
                    for q in range(2):
                        if lv == 1:
                            pe.wait_ge(start_copied, 2 * j + q + 1)
                        else:
                            pe.wait_ge(inv_doubled, 10 * j + 2 * (lv - 2) + q + 1)
                        pe.wait_ge(level_ready, n + q + 1)
                        for h in range(4):
                            last = nc.tensor.matmul(four(net.ps[2 + q])[:, h, :], mem.level[:, q, h, :],
                                                    mem.inv[:, q, h, :], start=True, stop=True)
                        last.then_inc(y_ready, 1)
                    for q in range(2):
                        pe.wait_ge(y_copied, n + q + 1)
                        if lv > 1:
                            pe.wait_ge(doubled, n - 2 + q + 1)
                        if j and lv == 1:
                            pe.wait_ge(out_taken if q else state_ready, j)
                        for h in range(4):
                            if lv < 6:
                                nc.tensor.matmul(four(net.ps[4 + q])[:, h, :], inv_t(j, q)[:, h, :],
                                                 mem.y[:, q, h, :], start=True, stop=True)
                            last = nc.tensor.matmul(four(net.ps[6 + q])[:, h, :], mem.y[:, q, h, :],
                                                    inv_t(j, q)[:, h, :], start=True, stop=True)
                        last.then_inc(dd_ready, 1)
                if j < 3:
                    for bank, part in ((net.ps[4], mem.bd), (net.ps[5], mem.kd)):
                        for t in range(4):
                            last = nc.tensor.transpose(bank[:, P * t:P * t + P], part[:, t, c, :], ident)
                        last.then_inc(tok_turned, 1)
                pe.wait_ge(y_copied, 12 * (j + 1))
                if j:
                    pe.wait_ge(state_ready, j)
                for h in range(8):
                    t, v = h // 2, slice(64 * h, 64 * h + 64)
                    if j and h % 2 == 0:
                        nc.tensor.matmul(net.ps[2][:, P * t:P * t + P], mem.kr[:, t, c, 0, :], mem.state[:, t, :],
                                         start=True, stop=False)
                    last = nc.tensor.matmul(net.ps[2][:, v], gram[:, h, 256:384], mem.vtok[:, c, v],
                                            start=(j == 0), stop=(j == 0 or h % 2 == 1))
                last.then_inc(rhs_ready, 1)
                if j < 3:
                    token_products(j + 1, range(0, 4))
                pe.wait_ge(rhs_copied, j + 1)
                pe.wait_ge(doubled, 12 * (j + 1))
                for h in range(8):
                    last = nc.tensor.matmul(net.ps[3][:, 64 * h:64 * h + 64], inv_t(j, h // 4)[:, h % 4, :],
                                            mem.rhs[:, 64 * h:64 * h + 64], start=True, stop=True)
                last.then_inc(u_ready, 1)
                if j < 3:
                    token_products(j + 1, range(4, 8))
                pe.wait_ge(u_copied, j + 1)
                if j < 3:
                    pe.wait_ge(tok_copied, 2 * (j + 1))
                    for h in EVEN_ODD:
                        t, rows = head(h)
                        into, v = net.ps[6][rows, 64 * t:64 * t + 64], slice(64 * h, 64 * h + 64)
                        nc.tensor.matmul(into, mem.ktok[:, v], mem.vtok[:, c, v], start=True, stop=False)
                        last = nc.tensor.matmul(into, mem.btok[:, v], mem.minus_u[:, v], start=False, stop=True)
                    last.then_inc(state_summed, 1)
                for h in range(8):
                    t, rows = head(h)
                    into, v = net.ps[7][rows, P * t:P * t + P], slice(64 * h, 64 * h + 64)
                    if j and h % 2 == 0:
                        nc.tensor.matmul(net.ps[7][:, P * t:P * t + P], mem.state[:, t, :], mem.kr[:, t, c, 1, :],
                                         start=True, stop=False)
                    nc.tensor.matmul(into, mem.vtok[:, c, v], gram[:, h, 384:512], start=(j == 0), stop=False)
                    last = nc.tensor.matmul(into, mem.minus_u[:, v], gram[:, h, 128:256], start=False, stop=True)
                last.then_inc(out_ready, 1)

        @st.gpsimd
        def _(pool):
            for j in range(NCH):
                for lv in LV:
                    n = 12 * j + 2 * (lv - 1)
                    for q in range(2):
                        if lv == 1:
                            pool.wait_ge(gram_masked, 8 * j + 4 * (q + 1))
                            if j:
                                pool.wait_ge(y_ready, 12 * j)
                        else:
                            pool.wait_ge(y_ready, n - 2 + q + 1)
                        pool.tensor_tensor(mem.level[:, q], mem.grams[j % 2][:, 4 * q:4 * q + 4, 0:P], level_mask(lv),
                                           ALU.mult).then_inc(level_ready, 1)

        @st.scalar
        def _(act):
            for j in range(NCH):
                for q in range(2):
                    act.wait_ge(start_turned, 2 * j + q + 1)
                    act.activation(mem.inv[:, q], four(net.ps[4 + q]), ACT.Copy).then_inc(start_copied, 1)
                for lv in LV:
                    n = 12 * j + 2 * (lv - 1)
                    for q in range(2):
                        act.wait_ge(y_ready, n + q + 1)
                        if n + q >= 2:
                            act.wait_ge(dd_ready, n + q - 1)
                        act.activation(mem.y[:, q], four(net.ps[2 + q]), ACT.Copy).then_inc(y_copied, 1)
                act.wait_ge(rhs_ready, j + 1)
                act.activation(mem.rhs, net.ps[2][:, :], ACT.Copy).then_inc(rhs_copied, 1)
                if j < 3:
                    for n, (bank, part) in enumerate(((net.ps[4], mem.btok), (net.ps[5], mem.ktok))):
                        act.wait_ge(tok_turned, 2 * j + n + 1)
                        if j:
                            act.wait_ge(state_summed, j)
                        act.activation(part, bank[:, :], ACT.Copy).then_inc(tok_copied, 1)

        @st.vector
        def _(dve):
            link = Chain(dve, own)

            def mask_products(j, q):
                gram = mem.grams[j % 2]
                if j >= 2 and q == 0:
                    dve.wait_ge(out_ready, j - 1)
                    dve.wait_ge(level_ready, 12 * (j - 1))
                for h in range(4 * q, 4 * q + 4):
                    dve.wait_ge(gram_ready, 8 * j + h + 1)
                    nc.vector.tensor_tensor(gram[:, h, :], net.ps[h % 2][:, :], mask4, ALU.mult).then_inc(gram_masked, 1)

            def start(j, q):
                dve.wait_ge(gram_masked, 8 * j + 4 * q + 4)
                link(nc.vector.tensor_tensor(inv_t(j, q), mem.grams[j % 2][:, 4 * q:4 * q + 4, 0:P], level_mask(0),
                                             ALU.mult))
                nc.vector.tensor_tensor(inv_t(j, q), ident.unsqueeze(1).to_broadcast([P, 4, P]), inv_t(j, q),
                                        ALU.subtract).then_inc(start_ready, 1)

            for q in range(2):
                mask_products(0, q)
                start(0, q)
            for j, c in enumerate(order):
                for lv in LV:
                    n = 12 * j + 2 * (lv - 1)
                    for q in range(2):
                        dve.wait_ge(dd_ready, n + q + 1)
                        if lv < 6:
                            nc.vector.tensor_tensor(mem.inv[:, q], mem.inv[:, q], four(net.ps[4 + q]),
                                                    ALU.subtract).then_inc(inv_doubled, 1)
                        nc.vector.tensor_tensor(inv_t(j, q), inv_t(j, q), four(net.ps[6 + q]),
                                                ALU.subtract).then_inc(doubled, 1)
                if j < 3:
                    mask_products(j + 1, 0)
                dve.wait_ge(u_ready, j + 1)
                nc.vector.tensor_scalar(mem.minus_u, net.ps[3][:, :], -1.0, None, ALU.mult).then_inc(u_copied, 1)
                if j < 3:
                    start(j + 1, 0)
                    mask_products(j + 1, 1)
                    start(j + 1, 1)
                    sums = net.ps[6][:, 0:256].rearrange("p (t m) -> p t m", m=64)
                    carry = mem.carry[:, :, j].unsqueeze(2).to_broadcast([P, 4, P])
                    dve.wait_ge(state_summed, j + 1)
                    dve.wait_ge(out_ready, j + 1)
                    if j == 0:
                        link(nc.vector.memset(mem.state, 0.0))
                    for o in (0, 64):
                        block = mem.state[o:o + 64, :, o:o + 64]
                        link(nc.vector.tensor_tensor(block, block, sums[o:o + 64], ALU.add))
                    nc.vector.tensor_tensor(mem.state, mem.state, carry, ALU.mult).then_inc(state_ready, 1)
                dve.wait_ge(out_ready, j + 1)
                if d == 0:
                    nc.vector.tensor_copy(mem.out[:, :, c, :], four(net.ps[7])).then_inc(out_taken, 1)
                else:
                    nc.vector.tensor_tensor(mem.out[:, :, c, :], mem.out[:, :, c, :], four(net.ps[7]),
                                            ALU.add).then_inc(out_taken, 1)


def rwkv_finish_stage(net):
    nc, eps = net.nc, 64e-5
    y = net.OT[:, 4:8, :]
    r, k, v = net.PT[:, 12:16, :], net.PT[:, 16:20, :], net.PT[:, 20:24, :]
    rk = net.PT[:, 0:4, :]
    square = net.PT[:, 4:8, :]
    rstd = net.PT[:, 8:12, :]
    with Stage(net, "rwkv_finish") as st:
        rk_ready, bonus_ready, gate_ready = st.sem("rk_ready"), st.sem("bonus_ready"), st.sem("gate_ready")
        mean_ready, centred, squared, var_ready = (st.sem("mean_ready"), st.sem("centred"), st.sem("squared"),
                                                   st.sem("var_ready"))
        root_ready, own, act_own = st.sem("root_ready"), st.sem("dve_own"), st.sem("act_own")
        bonus_used = st.sem("bonus_used")

        @st.gpsimd
        def _(pool):
            pool.tensor_tensor(rk[:, :, :], r, k, ALU.mult).then_inc(rk_ready, 1)

        @st.tensor
        def _(pe):
            for t in range(4):
                nc.tensor.matmul(net.ps[t][:, :], net.const(C_BLK), y[:, t, :], start=True, stop=True).then_inc(mean_ready, 1)
            for t in range(4):
                pe.wait_ge(squared, t + 1)
                nc.tensor.matmul(net.ps[4 + t][:, :], net.const(C_BLK), square[:, t, :], start=True,
                                 stop=True).then_inc(var_ready, 1)
            pe.wait_ge(centred, 4)
            pe.wait_ge(rk_ready, 5)
            for t in range(4):
                nc.tensor.matmul(net.ps[t][:, :], net.const(C_BLK), rk[:, t, :], start=True, stop=True).then_inc(bonus_ready, 1)
            for t in range(4):
                pe.wait_ge(root_ready, t + 1)
                nc.tensor.matmul(net.ps[4 + t][:, :], net.G2[:, P * t:P * t + P], net.PT[:, 25, :], start=True,
                                 stop=True).then_inc(gate_ready, 1)

        @st.scalar
        def _(act):
            link = Chain(act, act_own)
            act.wait_ge(rk_ready, 1)
            for t in range(4):
                act.activation(rk[:, t, :], rk[:, t, :], ACT.Copy, scale=net.par("l0_r_k", t)).then_inc(rk_ready, 1)
            for t in range(4):
                act.wait_ge(centred, t + 1)
                act.activation(square[:, t, :], y[:, t, :], ACT.Square).then_inc(squared, 1)
            inverse_roots(net, act, link, root_ready, [(var_ready, t + 1, rstd[:, t, :], net.ps[4 + t][:, :], 1.0 / 64,
                                                   net.eps(eps)) for t in range(4)])

        @st.vector
        def _(dve):
            link = Chain(dve, own)
            for t in range(4):
                dve.wait_ge(mean_ready, t + 1)
                nc.vector.scalar_tensor_tensor(y[:, t, :], net.ps[t][:, :], -1.0 / 64, y[:, t, :], ALU.mult,
                                               ALU.add).then_inc(centred, 1)
            dve.wait_ge(squared, 4)
            for t in range(4):
                dve.wait_ge(root_ready, t + 1)
                link(nc.vector.tensor_tensor(y[:, t, :], y[:, t, :], rstd[:, t, :], ALU.mult))
                link(nc.vector.tensor_scalar(y[:, t, :], y[:, t, :], net.par("l0_lnx_w", t), net.par("l0_lnx_b", t),
                                             ALU.mult, ALU.add))
                dve.wait_ge(bonus_ready, t + 1)
                link(nc.vector.tensor_tensor(rstd[:, t, :], net.ps[t][:, :], v[:, t, :], ALU.mult))
                link(nc.vector.tensor_tensor(y[:, t, :], y[:, t, :], rstd[:, t, :], ALU.add))
                dve.wait_ge(gate_ready, t + 1)
                link(nc.vector.tensor_tensor(y[:, t, :], y[:, t, :], net.ps[4 + t][:, :], ALU.mult))


def odd_projection(w):
    starts = [0, 256, 512, 768, 1024, 1280, 1552, 1808, 2064, 2320, 2576, 2832]
    views = [w[:, c:c + SW].rearrange("(t k) m -> k t m", k=P) for c in starts]
    latents_only = {0, 1, 5, 6, 10, 11}
    return (Weights(3, 0, lambda i, s: views[SLOTS * i + s]),
            lambda i, s: LAT if SLOTS * i + s in latents_only else TOK)


class SsdMemory:

    def __init__(self, net):
        sc = net.SC
        self.gate_down = sc[0:16, 0:512]
        (self.dt, self.la, self.cum, self.tot, self.to_end, self.e_cum, self.e_tot, self.x, self.e, self.s, self.s2,
         self.poly) = (sc[:, 512 + 64 * n:576 + 64 * n].rearrange("p (c h) -> p c h", h=16) for n in range(12))
        self.e_a = sc[:, 1280:1296]
        self.conv = sc[:, 1600:5696].rearrange("p (t m) -> p t m", m=TOK)
        self.xdt = sc[:, 1600:3648].rearrange("p (c d m) -> p c d m", c=2, d=2)
        self.state = sc[:, 3648:4672].rearrange("p (d m) -> p d m", d=2)
        self.cb = sc[:, 4672:5184].rearrange("p (d g m) -> p d g m", d=2, g=2)
        self.y = sc[:, 5184:6208].rearrange("p (c m) -> p c m", c=2)
        self.part = sc[:, 6208:6720]
        ht = net.HT[:, :, :].rearrange("p t m -> p (t m)")
        self.xtok = ht[:, 0:2048].rearrange("p (c m) -> p c m", c=NCH)
        self.btok = ht[:, 2048:3072].rearrange("p (c m) -> p c m", c=NCH)
        self.xw = net.OT[:, 0:6, :]
        self.att = net.PT[:, 24:32, :].rearrange("p (c t) (h m) -> p c (t h) m", c=2, m=P)


def ssd_inputs_stage(net):
    nc, mem = net.nc, SsdMemory(net)
    by_pool = (6, 7)
    by_dve = (0, 1, 2, 3, 4, 5)
    widths = [TOK if t < 6 else LAT for t in range(8)]

    def convolve(engine, t, link, summed, product=None):
        x = net.PT[:, 4 + t, 0:widths[t]].rearrange("p (s m) -> p s m", m=LAT)
        acc = mem.conv[:, t, 0:widths[t]].rearrange("p (s m) -> p s m", m=LAT)
        tap = lambda k: net.par("l1_conv_w", 8 * k + t)
        link(engine.tensor_scalar(acc, x, tap(2), None, ALU.mult))
        for k in (0, 1, 3, 4):
            o = k - 2
            to, of = slice(max(0, -o), LAT - max(0, o)), slice(max(0, o), LAT - max(0, -o))
            if product is None:
                step = engine.scalar_tensor_tensor(acc[:, :, to], x[:, :, of], tap(k), acc[:, :, to], ALU.mult, ALU.add)
            else:
                part = product[:, 0:widths[t]].rearrange("p (s m) -> p s m", m=LAT)[:, :, to]
                link(engine.tensor_scalar(part, x[:, :, of], tap(k), None, ALU.mult))
                step = engine.tensor_tensor(acc[:, :, to], acc[:, :, to], part, ALU.add)
            step.then_inc(summed, 1) if k == 4 else link(step)

    with Stage(net, "ssd_inputs") as st:
        dt_raw, down_ready, own, pool_own = st.sem("dt_raw"), st.sem("down_ready"), st.sem("dve_own"), st.sem("pool_own")
        abs_ready, e_ready, la_ready, cum_summed = (st.sem("abs_ready"), st.sem("e_ready"), st.sem("la_ready"),
                                                    st.sem("cum_summed"))
        cum_ready, e_a_ready, down_used = st.sem("cum_ready"), st.sem("e_a_ready"), st.sem("down_used")
        dve_summed, pool_summed = st.sem("dve_summed"), st.sem("pool_summed")
        silu_ready, turned = st.sem("silu_ready"), st.sem("turned")
        all_of = lambda v: v.rearrange("p c h -> p (c h)")
        per_head = lambda v: v.unsqueeze(1).to_broadcast([P, NCH, 16])

        @st.tensor
        def _(pe):
            for c in range(NCH):
                for kt in range(KT):
                    last = nc.tensor.matmul(net.ps[0][:, 16 * c:16 * c + 16], net.HT[:, kt, CH * c:CH * c + CH],
                                            net.WDG[:, kt, 0:16], start=(kt == 0), stop=(kt == KT - 1))
            last.then_inc(dt_raw, 1)
            for kt in range(KT):
                last = nc.tensor.matmul(net.ps[1][0:16, :], net.WDG[:, kt, 16:32], net.HT[:, kt, :],
                                        start=(kt == 0), stop=(kt == KT - 1))
            last.then_inc(down_ready, 1)
            pe.wait_ge(la_ready, 1)
            for c in range(NCH):
                for d, tri in enumerate((C_LE, C_GE)):
                    nc.tensor.matmul(net.ps[2][:, 16 * c + 8 * d:16 * c + 8 * d + 8], net.const(tri),
                                     mem.la[:, c, 8 * d:8 * d + 8], start=True, stop=True)
            nc.tensor.matmul(net.ps[3][:, 0:64], net.const(C_ONES), all_of(mem.la), start=True,
                             stop=True).then_inc(cum_summed, 1)
            pe.wait_ge(silu_ready, 8)
            for at, c in enumerate((2, 3, 0, 1)):
                if at == 2:
                    pe.wait_ge(down_used, 1)
                    pe.wait_ge(cum_ready, 1)
                for n, (first, count) in enumerate(((4, 4), (8, 2))):
                    for t in range(count):
                        last = nc.tensor.transpose(net.ps[2 * c + n][:, P * t:P * t + P],
                                                   net.PT[:, first + t, CH * c:CH * c + CH], net.const(C_IDENT))
                    last.then_inc(turned, 1)

        @st.scalar
        def _(act):
            net.log_exp_loaded = False
            act.activation(mem.e_a, net.HEADROW[:, 16:32], ACT.Exp).then_inc(e_a_ready, 1)
            act.wait_ge(abs_ready, 1)
            act.activation(mem.e, mem.e, ACT.Exp, scale=-1.0).then_inc(e_ready, 1)
            act.wait_ge(down_ready, 1)
            act.activation(mem.gate_down, net.ps[1][0:16, :], ACT.Copy).then_inc(down_used, 1)
            act.wait_ge(cum_ready, 1)
            for into, of in ((mem.e_cum, mem.cum), (mem.e_tot, mem.tot), (mem.to_end, mem.to_end)):
                act.activation(into, of, ACT.Exp)
            for t in (0, 1, 2, 3, 4, 6, 7, 5):
                if t in by_dve:
                    act.wait_ge(dve_summed, by_dve.index(t) + 1)
                else:
                    act.wait_ge(pool_summed, by_pool.index(t) + 1)
                act.activation(net.PT[:, 4 + t, 0:widths[t]], mem.conv[:, t, 0:widths[t]], ACT.Silu,
                               bias=net.par("l1_conv_b", t)).then_inc(silu_ready, 1)
            for gate in (net.PT[:, 0:4, 0:LAT], net.PT[:, 20:24, 0:LAT]):
                act.activation(gate, gate, ACT.Silu)
            for at, c in enumerate((2, 3, 0, 1)):
                act.wait_ge(turned, 2 * at + 2)
                act.activation(mem.btok[:, c, :], net.ps[2 * c + 1][:, 0:256], ACT.Copy)

        @st.gpsimd
        def _(pool):
            link = Chain(pool, pool_own)
            for n, t in enumerate(by_pool):
                convolve(nc.gpsimd, t, link, pool_summed, mem.part)
                pool.wait_ge(pool_summed, n + 1)

        @st.vector
        def _(dve):
            link = Chain(dve, own)
            raw = net.ps[0][:, 0:64].rearrange("p (c h) -> p c h", h=16)
            for t in by_dve[:3]:
                convolve(nc.vector, t, link, dve_summed)
            dve.wait_ge(dt_raw, 1)
            link(nc.vector.tensor_tensor(mem.x, raw, per_head(net.HEADROW[:, 0:16]), ALU.add))
            link(nc.vector.tensor_scalar(mem.s, mem.x, -1.0, None, ALU.mult))
            nc.vector.tensor_tensor(mem.e, mem.x, mem.s, ALU.max).then_inc(abs_ready, 1)
            convolve(nc.vector, by_dve[3], link, dve_summed)
            dve.wait_ge(e_ready, 1)
            link(nc.vector.tensor_scalar(mem.s, mem.e, 2.0, None, ALU.add))
            link(nc.vector.reciprocal(mem.s, mem.s))
            link(nc.vector.tensor_tensor(mem.s, mem.s, mem.e, ALU.mult))
            link(nc.vector.tensor_tensor(mem.s2, mem.s, mem.s, ALU.mult))
            link(nc.vector.tensor_scalar(mem.poly, mem.s2, 1.0 / 15, None, ALU.mult))
            for odd in (13, 11, 9, 7, 5, 3):
                link(nc.vector.scalar_tensor_tensor(mem.poly, mem.poly, 1.0 / odd, mem.s2, ALU.add, ALU.mult))
            link(nc.vector.scalar_tensor_tensor(mem.poly, mem.poly, 1.0, mem.s, ALU.add, ALU.mult))
            link(nc.vector.tensor_scalar(mem.x, mem.x, 0.0, None, ALU.max))
            link(nc.vector.scalar_tensor_tensor(mem.dt, mem.poly, 2.0, mem.x, ALU.mult, ALU.add))
            dve.wait_ge(e_a_ready, 1)
            nc.vector.scalar_tensor_tensor(mem.la, mem.dt, -1.0, per_head(mem.e_a), ALU.mult, ALU.mult).then_inc(la_ready, 1)
            convolve(nc.vector, by_dve[4], link, dve_summed)
            dve.wait_ge(cum_summed, 1)
            link(nc.vector.tensor_copy(all_of(mem.cum), net.ps[2][:, 0:64]))
            link(nc.vector.tensor_copy(all_of(mem.tot), net.ps[3][:, 0:64]))
            nc.vector.tensor_tensor(mem.to_end, mem.tot, mem.cum, ALU.subtract).then_inc(cum_ready, 1)
            convolve(nc.vector, by_dve[5], link, dve_summed)
            dve.wait_ge(down_ready, 1)
            for at, c in enumerate((2, 3, 0, 1)):
                dve.wait_ge(turned, 2 * at + 1)
                nc.vector.tensor_copy(mem.xtok[:, c, :], net.ps[2 * c][:, :])


def ssd_scan_stage(net):
    nc, mem = net.nc, SsdMemory(net)
    heads = lambda v: v.rearrange("p (h m) -> p h m", m=64)
    wide = lambda v: v.unsqueeze(2).to_broadcast([P, 8, 64])
    updates = [(0, 2), (1, 3), (0, 3), (1, 2), (0, 0), (1, 1)]
    serves = {2: 0, 3: 1, 4: 1, 5: 0}
    served_bank = {2: 0, 3: 1, 4: 2, 5: 3}
    with Stage(net, "ssd_scan") as st:
        row_ready, row_used, exp_ready, att_ready = (st.sem("row_ready"), st.sem("row_used"), st.sem("exp_ready"),
                                                     st.sem("att_ready"))
        cb_ready, cb_masked, xdt_ready = st.sem("cb_ready"), st.sem("cb_masked"), st.sem("xdt_ready")
        y_ready, xw_ready, state_summed, state_ready = (st.sem("y_ready"), st.sem("xw_ready"), st.sem("state_summed"),
                                                        st.sem("state_ready"))
        served, own, weights_ready = st.sem("served"), st.sem("dve_own"), st.sem("weights_ready")

        @st.tensor
        def _(pe):
            def sum_state(n):
                d, c = updates[n]
                pe.wait_ge(xw_ready, n + 1)
                if n >= 2:
                    pe.wait_ge(state_ready, n - 1)
                for g in range(2):
                    last = nc.tensor.matmul(net.ps[6 + d][:, 256 * g:256 * g + 256], mem.btok[:, c, P * g:P * g + P],
                                            mem.xw[:, n, 256 * g:256 * g + 256], start=True, stop=True)
                last.then_inc(state_summed, 1)

            def serve(n):
                d, to = updates[n][0], serves[n]
                pe.wait_ge(state_ready, n + 1)
                for g in range(2):
                    last = nc.tensor.matmul(net.ps[served_bank[n]][:, 256 * g:256 * g + 256],
                                            net.PT[:, 10 + g, CH * to:CH * to + CH],
                                            mem.state[:, d, 256 * g:256 * g + 256], start=True, stop=True)
                last.then_inc(served, 1)

            def inside(c, some):
                for h in some:
                    v = slice(64 * h, 64 * h + 64)
                    for d in range(2):
                        last = nc.tensor.matmul(net.ps[4 + c][:, v], mem.att[:, c, 8 * d + h, :], mem.xdt[:, c, d, v],
                                                start=(d == 0), stop=(d == 1))
                return last

            for c in range(2):
                for n in range(4):
                    at = 4 * c + n
                    if at >= 2:
                        pe.wait_ge(row_used, at - 1)
                    for h in range(4 * n, 4 * n + 4):
                        last = nc.tensor.matmul(net.ps[at % 2][:, P * (h % 4):P * (h % 4) + P],
                                                mem.la[:, c, h:h + 1].to_broadcast([P, P]),
                                                net.const(C_LE if h < 8 else C_GE), start=True, stop=True)
                    last.then_inc(row_ready, 1)
                for g in range(2):
                    last = nc.tensor.matmul(net.ps[2 + c][:, P * g:P * g + P], net.PT[:, 8 + g, CH * c:CH * c + CH],
                                            net.PT[:, 10 + g, CH * c:CH * c + CH], start=True, stop=True)
                last.then_inc(cb_ready, 1)
            for n in range(4):
                sum_state(n)
            pe.wait_ge(xdt_ready, 4)
            pe.wait_ge(att_ready, 4)
            inside(0, range(8)).then_inc(y_ready, 1)
            pe.wait_ge(row_used, 8)
            serve(2)
            serve(3)
            sum_state(4)
            sum_state(5)
            pe.wait_ge(att_ready, 8)
            inside(1, range(4))
            pe.wait_ge(cb_masked, 2)
            serve(4)
            serve(5)
            inside(1, range(4, 8)).then_inc(y_ready, 1)

        @st.gpsimd
        def _(pool):
            pool.wait_ge(weights_ready, 1)
            for n, (d, c) in enumerate(updates):
                pool.tensor_tensor(heads(mem.xw[:, n, :]), heads(mem.xtok[:, c, :]),
                                   wide(mem.to_end[:, c, 8 * d:8 * d + 8]), ALU.mult).then_inc(xw_ready, 1)
            for c in range(2):
                for d in range(2):
                    pool.tensor_tensor(heads(mem.xdt[:, c, d, :]), heads(mem.xtok[:, c, :]),
                                       wide(mem.dt[:, c, 8 * d:8 * d + 8]), ALU.mult).then_inc(xdt_ready, 1)
            pool.wait_ge(xdt_ready, 4)

        @st.scalar
        def _(act):
            load_log_exp(net, act)
            for c in range(2):
                act.wait_ge(row_used, 4 * (c + 1))
                act.activation(mem.att[:, c], mem.att[:, c], ACT.Exp).then_inc(exp_ready, 1)

        @st.vector
        def _(dve):
            link = Chain(dve, own)

            def weigh(c):
                dve.wait_ge(cb_ready, c + 1)
                if c:
                    dve.wait_ge(att_ready, 4)
                for d, tri in enumerate((C_LE, C_GE)):
                    for g in range(2):
                        step = nc.vector.tensor_tensor(mem.cb[:, d, g, :], net.ps[2 + c][:, P * g:P * g + P],
                                                       net.const(tri), ALU.mult)
                step.then_inc(cb_masked, 1)
                dve.wait_ge(exp_ready, c + 1)
                dve.wait_ge(cb_masked, c + 1)
                for d in range(2):
                    for g in range(2):
                        four = mem.att[:, c, 8 * d + 4 * g:8 * d + 4 * g + 4, :]
                        nc.vector.tensor_tensor(four, four, mem.cb[:, d, g, :].unsqueeze(1).to_broadcast([P, 4, P]),
                                                ALU.mult).then_inc(att_ready, 1)

            def update(pair):
                for n in pair:
                    d, c = updates[n]
                    if n >= 4:
                        dve.wait_ge(served, n - 3)
                    dve.wait_ge(state_ready, n - 1)
                    step = nc.vector.tensor_tensor(heads(mem.state[:, d, :]), heads(mem.state[:, d, :]),
                                                   wide(mem.e_tot[:, c, 8 * d:8 * d + 8]), ALU.mult)
                link(step)
                for n in pair:
                    d = updates[n][0]
                    dve.wait_ge(state_summed, n + 1)
                    nc.vector.tensor_tensor(mem.state[:, d, :], mem.state[:, d, :], net.ps[6 + d][:, :],
                                            ALU.add).then_inc(state_ready, 1)

            def add_served(n, into):
                dve.wait_ge(served, n - 1)
                d, to = updates[n][0], serves[n]
                link(nc.vector.tensor_tensor(heads(into), heads(net.ps[served_bank[n]][:, :]),
                                             wide(mem.e_cum[:, to, 8 * d:8 * d + 8]), ALU.mult))
                if n >= 4:
                    link(nc.vector.tensor_tensor(mem.y[:, to, :], mem.y[:, to, :], into, ALU.add))

            nc.vector.tensor_tensor(mem.to_end, mem.to_end, mem.dt, ALU.mult).then_inc(weights_ready, 1)
            for c in range(2):
                for n in range(4):
                    dve.wait_ge(row_ready, 4 * c + n + 1)
                    for h in range(4 * n, 4 * n + 4):
                        last = nc.vector.tensor_scalar(mem.att[:, c, h, :],
                                                       net.ps[(4 * c + n) % 2][:, P * (h % 4):P * (h % 4) + P],
                                                       mem.cum[:, c, h:h + 1], 0.0, ALU.subtract, ALU.min)
                    last.then_inc(row_used, 1)
            weigh(0)
            for n in range(2):
                dve.wait_ge(state_summed, n + 1)
                nc.vector.tensor_copy(mem.state[:, updates[n][0], :], net.ps[6 + updates[n][0]][:, :]).then_inc(state_ready, 1)
            weigh(1)
            update((2, 3))
            for n in (2, 3):
                add_served(n, mem.y[:, serves[n], :])
            update((4, 5))
            dve.wait_ge(y_ready, 1)
            link(nc.vector.tensor_tensor(mem.y[:, 0, :], mem.y[:, 0, :], net.ps[4][:, :], ALU.add))
            for n in (4, 5):
                add_served(n, mem.part)
            dve.wait_ge(y_ready, 2)
            nc.vector.tensor_tensor(mem.y[:, 1, :], mem.y[:, 1, :], net.ps[5][:, :], ALU.add)


def ssd_gate_stage(net):
    nc, mem = net.nc, SsdMemory(net)
    with Stage(net, "ssd_gate") as st:
        turned, own = st.sem("turned"), st.sem("dve_own")

        @st.tensor
        def _(pe):
            for t in range(4):
                for c in range(2):
                    last = nc.tensor.transpose(net.ps[t][:, P * c:P * c + P], mem.y[:, c, P * t:P * t + P],
                                               net.const(C_IDENT))
                last.then_inc(turned, 1)

        @st.vector
        def _(dve):
            link = Chain(dve, own)
            for t in range(4):
                dve.wait_ge(turned, t + 1)
                link(nc.vector.scalar_tensor_tensor(net.OT[:, t, 0:LAT], net.PT[:, 4 + t, 0:LAT], net.DSKIP[:, t:t + 1],
                                                    net.ps[t][:, 0:LAT], ALU.mult, ALU.add))
                link(nc.vector.tensor_tensor(net.OT[:, t, 0:LAT], net.OT[:, t, 0:LAT], net.PT[:, t, 0:LAT], ALU.mult))


class GlaMemory:

    def __init__(self, net):
        sc = net.SC
        self.gate_down = sc[0:16, 0:512]
        self.cum = sc[:, 512:2560].rearrange("p (d t c m) -> p d t c m", d=2, t=2, c=NCH)
        lat = lambda at: sc[:, at:at + 1024].rearrange("p (d t c m) -> p d t c m", d=2, t=2, c=2)
        self.q_in, self.k_in, self.q_state = lat(2560), lat(3584), lat(4608)
        half = lambda at: sc[:, at:at + 512].rearrange("p (d t c m) -> p d t c m", d=2, t=2, c=2)
        self.q_cross, self.k_cross = half(5632), half(6144)
        self.e_end = sc[:, 6656:6672].rearrange("p (d t c) -> p d t c", d=2, t=2)
        ht = net.HT[:, :, :].rearrange("p t m -> p (t m)")
        self.k_end = ht[:, 0:2048].rearrange("p (d t c m) -> p d t c m", d=2, t=2, c=NCH)
        self.vtok = ht[:, 2048:4096].rearrange("p (c m) -> p c m", c=NCH)
        pt = net.PT[:, 0:12, :].rearrange("p t m -> p (t m)")
        self.gate = pt[:, 0:2048].rearrange("p (d t m) -> p d t m", d=2, t=2)
        self.low = pt[:, 2048:4096].rearrange("p (d t m) -> p d t m", d=2, t=2)
        self.shift = pt[:, 4096:6144].rearrange("p (d t c m) -> p d t c m", d=2, t=2, c=NCH)
        pt = net.PT[:, 24:32, :].rearrange("p t m -> p (t m)")
        self.att = pt[:, 0:2048].rearrange("p (d c h m) -> p d c h m", d=2, c=2, h=4)
        self.state = pt[:, 2048:3072].rearrange("p (d c t m) -> p d c t m", d=2, c=2, t=2)
        self.ktok = pt[:, 3072:4096].rearrange("p (b m) -> p b m", b=4)


def gla_gates_stage(net):
    nc, mem = net.nc, GlaMemory(net)
    q, k = (net.PT[:, n:n + 2, :].rearrange("p t (c m) -> p t c m", m=CH) for n in (12, 14))
    tau = 1.0 / 16.0
    raw_of = lambda d, t: net.ps[2 * d + t][:, :]
    bias = lambda d, t: net.par("l1_gk_b_f" if d == 0 else "l1_gk_b_b", t)
    cross = (((64, 0), (31, 95), 63, CH - 1), ((0, 64), (32, 96), 64, 0))
    with Stage(net, "gla_gates") as st:
        gate_raw, low_ready, log_ready, turned = (st.sem("gate_raw"), st.sem("low_ready"), st.sem("log_ready"),
                                                  st.sem("turned"))
        own, act_own, shifted, exped = st.sem("dve_own"), st.sem("act_own"), st.sem("shifted"), st.sem("exped")
        abs_ready, k_scaled, zeroed = st.sem("abs_ready"), st.sem("k_scaled"), st.sem("zeroed")

        @st.tensor
        def _(pe):
            for d in range(2):
                for t in range(2):
                    nc.tensor.matmul(raw_of(d, t), net.GUP[:, d, P * t:P * t + P], mem.gate_down,
                                     start=True, stop=True).then_inc(gate_raw, 1)
            for c in range(NCH):
                for t in range(4):
                    last = nc.tensor.transpose(net.ps[4 + c][:, P * t:P * t + P], net.PT[:, 16 + t, CH * c:CH * c + CH],
                                               net.const(C_IDENT))
                last.then_inc(turned, 1)

        @st.scalar
        def _(act):
            load_log_exp(net, act)
            link = Chain(act, act_own)
            for d in range(2):
                for t in range(2):
                    act.wait_ge(gate_raw, 2 * d + t + 1)
                    act.activation(mem.gate[:, d, t, :], raw_of(d, t), ACT.Abs, bias=bias(d, t)).then_inc(abs_ready, 1)
                act.wait_ge(abs_ready, 2 * d + 2)
                link(act.activation(mem.gate[:, d], mem.gate[:, d], ACT.Exp, scale=-1.0))
                act.activation(mem.gate[:, d], mem.gate[:, d], ACT.Ln, bias=1.0).then_inc(log_ready, 1)
            for c in range(NCH):
                act.wait_ge(turned, c + 1)
                act.activation(mem.vtok[:, c, :], net.ps[4 + c][:, :], ACT.Copy)
            for d in range(2):
                lat = mem.shift[:, d, :, 0:2, :]
                act.wait_ge(shifted, d + 1)
                act.activation(mem.k_in[:, d], lat, ACT.Exp, scale=-tau).then_inc(exped, 1)
                act.activation(mem.q_in[:, d], lat, ACT.Exp, scale=tau).then_inc(exped, 1)
            for d in range(2):
                (qh, kh), lat = cross[d][0], mem.shift[:, d, :, 0:2, :]
                act.wait_ge(shifted, d + 3)
                for t in range(2):
                    act.activation(mem.k_cross[:, d, t], lat[:, t, :, kh:kh + 64], ACT.Exp, scale=-tau)
                    last = act.activation(mem.q_cross[:, d, t], lat[:, t, :, qh:qh + 64], ACT.Exp, scale=tau)
                last.then_inc(exped, 1)
            for d in range(2):
                act.wait_ge(shifted, d + 5)
                act.activation(mem.k_end[:, d], mem.shift[:, d], ACT.Exp, scale=-tau).then_inc(exped, 1)
                for t in range(2):
                    last = act.activation(mem.q_state[:, d, t], mem.cum[:, d, t, 0:2], ACT.Exp, scale=tau)
                last.then_inc(exped, 1)
                act.activation(mem.e_end[:, d], mem.e_end[:, d], ACT.Exp, scale=tau)

        @st.gpsimd
        def _(pool):
            pool.memset(mem.att, 0.0).then_inc(zeroed, 1)
            for d in range(2):
                pool.wait_ge(exped, 2 * d + 1)
                for t in range(2):
                    pool.tensor_tensor(mem.k_in[:, d, t], mem.k_in[:, d, t], k[:, t, 0:2], ALU.mult).then_inc(k_scaled, 1)
            for d in range(2):
                kh = cross[d][0][1]
                pool.wait_ge(exped, d + 5)
                for t in range(2):
                    pool.tensor_tensor(mem.k_cross[:, d, t], mem.k_cross[:, d, t], k[:, t, 0:2, kh:kh + 64],
                                       ALU.mult).then_inc(k_scaled, 1)
            for d in range(2):
                pool.wait_ge(exped, 2 * d + 7)
                pool.tensor_tensor(mem.k_end[:, d, 0], mem.k_end[:, d, 0], k[:, 0], ALU.mult).then_inc(k_scaled, 1)
            pool.wait_ge(zeroed, 1)
            pool.wait_ge(k_scaled, 10)

        @st.vector
        def _(dve):
            link = Chain(dve, own)
            ones = net.const(C_ONES)
            clamp = GLA_CLAMP / tau
            for d in range(2):
                for t in range(2):
                    dve.wait_ge(abs_ready, 2 * d + t + 1)
                    last = nc.vector.tensor_scalar(mem.low[:, d, t, :], raw_of(d, t), bias(d, t), 0.0, ALU.add, ALU.min)
                link(last)
                dve.wait_ge(log_ready, d + 1)
                link(nc.vector.tensor_tensor(mem.low[:, d], mem.low[:, d], mem.gate[:, d], ALU.subtract))
                for t in range(2):
                    for c in range(NCH):
                        into, of = mem.cum[:, d, t, c, :], mem.low[:, d, t, CH * c:CH * c + CH]
                        if d:
                            into, of = into[:, ::-1], of[:, ::-1]
                        last = nc.vector.tensor_tensor_scan(into, ones, of, 0.0, ALU.mult, ALU.add)
                link(last)
                cum, shift, mids = mem.cum[:, d], mem.shift[:, d], cross[d][1]
                for t in range(2):
                    for h in range(2):
                        part = slice(64 * h, 64 * h + 64)
                        last = nc.vector.tensor_tensor(shift[:, t, 0:2, part], cum[:, t, 0:2, part],
                                                       cum[:, t, 0:2, mids[h]:mids[h] + 1].to_broadcast([P, 2, 64]),
                                                       ALU.subtract)
                link(last)
                nc.vector.tensor_scalar(shift[:, :, 0:2, :], shift[:, :, 0:2, :], clamp, -clamp, ALU.min,
                                        ALU.max).then_inc(shifted, 1)
            for d in range(2):
                cum, shift, edge = mem.cum[:, d], mem.shift[:, d], cross[d][2]
                dve.wait_ge(exped, 2 * d + 2)
                for t in range(2):
                    last = nc.vector.tensor_tensor(shift[:, t, 0:2, :], cum[:, t, 0:2, :],
                                                   cum[:, t, 0:2, edge:edge + 1].to_broadcast([P, 2, CH]), ALU.subtract)
                last.then_inc(shifted, 1)
                for t in range(2):
                    nc.vector.scalar_tensor_tensor(mem.q_in[:, d, t], mem.q_in[:, d, t], 0.125, q[:, t, 0:2],
                                                   ALU.mult, ALU.mult)
            for d in range(2):
                qh, cum, shift, end = cross[d][0][0], mem.cum[:, d], mem.shift[:, d], cross[d][3]
                dve.wait_ge(exped, d + 5)
                nc.vector.tensor_copy(mem.e_end[:, d], cum[:, :, :, end])
                for t in range(2):
                    last = nc.vector.tensor_tensor(shift[:, t], cum[:, t],
                                                   cum[:, t, :, end:end + 1].to_broadcast([P, NCH, CH]), ALU.subtract)
                last.then_inc(shifted, 1)
                for t in range(2):
                    nc.vector.scalar_tensor_tensor(mem.q_cross[:, d, t], mem.q_cross[:, d, t], 0.125,
                                                   q[:, t, 0:2, qh:qh + 64], ALU.mult, ALU.mult)
            for d in range(2):
                dve.wait_ge(exped, 2 * d + 8)
                nc.vector.tensor_tensor(mem.k_end[:, d, 1], mem.k_end[:, d, 1], k[:, 1], ALU.mult)
                for t in range(2):
                    nc.vector.scalar_tensor_tensor(mem.q_state[:, d, t], mem.q_state[:, d, t], 0.125, q[:, t, 0:2],
                                                   ALU.mult, ALU.mult)


def gla_scan_stage(net):
    nc, mem = net.nc, GlaMemory(net)
    head = lambda h: (h // 2, slice(64 * (h % 2), 64 * (h % 2) + 64))
    ident = net.const(C_IDENT)
    updates = [(0, 2, None), (1, 3, None), (0, 3, 0), (1, 2, 1), (0, 0, 1), (1, 1, 0)]
    units = [(d, c) for d in range(2) for c in range(2)]
    unit_banks = lambda n: (0, 1) if n % 2 == 0 else (4, 5)
    update_bank = lambda n: net.ps[(2, 3, 6, 7)[n % 4]]
    with Stage(net, "gla_scan") as st:
        att_raw, att_ready = st.sem("att_raw"), st.sem("att_ready")
        turned, ktok_ready, state_summed, state_ready = (st.sem("turned"), st.sem("ktok_ready"), st.sem("state_summed"),
                                                         st.sem("state_ready"))
        y_ready, own = st.sem("y_ready"), st.sem("dve_own")

        @st.tensor
        def _(pe):
            def attend(n):
                d, c = units[n]
                if n >= 2:
                    pe.wait_ge(att_ready, 4 * (n - 1))
                for h in range(4):
                    t, rows = head(h)
                    bank, at = net.ps[unit_banks(n)[h % 2]], P * (h // 2)
                    for half in range(2):
                        part = slice(64 * half, 64 * half + 64)
                        nc.tensor.matmul(bank[part, at + 64 * half:at + 64 * half + 64], mem.k_in[rows, d, t, c, part],
                                         mem.q_in[rows, d, t, c, part], start=True, stop=True)
                    jh, ih = ((0, 1), (1, 0))[d]
                    last = nc.tensor.matmul(bank[64 * jh:64 * jh + 64, at + 64 * ih:at + 64 * ih + 64],
                                            mem.k_cross[rows, d, t, c], mem.q_cross[rows, d, t, c], start=True, stop=True)
                    if h >= 2:
                        last.then_inc(att_raw, 1)

            def update(pair):
                for n in pair:
                    d, c, _ = updates[n]
                    if n >= 4:
                        pe.wait_ge(state_ready, n - 3)
                    for t in range(2):
                        last = nc.tensor.transpose(update_bank(n)[:, P * t:P * t + P], mem.k_end[:, d, t, c, :], ident)
                    last.then_inc(turned, 1)
                for n in pair:
                    c = updates[n][1]
                    pe.wait_ge(ktok_ready, n + 1)
                    for h in range(4):
                        t, rows = head(h)
                        last = nc.tensor.matmul(update_bank(n)[rows, 256 + P * t:384 + P * t],
                                                mem.ktok[:, n % 4, 64 * h:64 * h + 64], mem.vtok[:, c, P * h:P * h + P],
                                                start=True, stop=True)
                    last.then_inc(state_summed, 1)

            attend(0)
            attend(1)
            update((0, 1))
            attend(2)
            update((2, 3))
            attend(3)
            update((4, 5))
            pe.wait_ge(state_ready, len(updates))
            pe.wait_ge(att_ready, 16)
            for h in range(4):
                t, rows = head(h)
                for c in range(2):
                    into = net.ps[4 + h][:, P * c:P * c + P]
                    for d in range(2):
                        nc.tensor.matmul(into, mem.vtok[:, c, P * h:P * h + P], mem.att[:, d, c, h, :],
                                         start=(d == 0), stop=False)
                    for d in range(2):
                        last = nc.tensor.matmul(into, mem.state[rows, d, c, t, :], mem.q_state[rows, d, t, c, :],
                                                start=False, stop=(d == 1))
                last.then_inc(y_ready, 1)

        @st.scalar
        def _(act):
            for n in range(len(updates)):
                act.wait_ge(turned, n + 1)
                if n >= 4:
                    act.wait_ge(state_summed, n - 3)
                act.activation(mem.ktok[:, n % 4, :], update_bank(n)[:, 0:256], ACT.Copy).then_inc(ktok_ready, 1)

        @st.vector
        def _(dve):
            link = Chain(dve, own)

            def mask(n):
                d, c = units[n]
                tri = net.const((C_LE, C_GE)[d]).unsqueeze(1).to_broadcast([P, 2, P])
                whole, rest = ((slice(0, 64), slice(64, 128)), (slice(64, 128), slice(0, 64)))[d]
                dve.wait_ge(att_raw, 2 * n + 2)
                for odd in range(2):
                    raw = net.ps[unit_banks(n)[odd]][:, 0:256].rearrange("p (h m) -> p h m", m=P)
                    into = mem.att[:, d, c, odd::2, :]
                    nc.vector.tensor_tensor(into[whole], raw[whole], tri[whole], ALU.mult).then_inc(att_ready, 1)
                    nc.vector.tensor_tensor(into[rest, :, rest], raw[rest, :, rest], tri[rest, :, rest],
                                            ALU.mult).then_inc(att_ready, 1)

            held = {}

            def update(n):
                d, c, to = updates[n]
                sums = update_bank(n)[:, 256:512].rearrange("p (t m) -> p t m", m=P)
                if n < 2:
                    into = mem.state[:, d, 1 - d]
                    dve.wait_ge(state_summed, n + 1)
                    last = nc.vector.tensor_copy(into, sums)
                else:
                    into = mem.state[:, d, to]
                    dve.wait_ge(state_ready, n - 1)
                    decay = mem.e_end[:, d, :, c:c + 1].to_broadcast([P, 2, P])
                    link(nc.vector.tensor_tensor(into, held[d], decay, ALU.mult))
                    dve.wait_ge(state_summed, n + 1)
                    last = nc.vector.tensor_tensor(into, into, sums, ALU.add)
                last.then_inc(state_ready, 1)
                held[d] = into

            mask(0)
            mask(1)
            update(0)
            update(1)
            mask(2)
            update(2)
            update(3)
            mask(3)
            update(4)
            update(5)
            for h in range(4):
                dve.wait_ge(y_ready, h + 1)
                nc.vector.tensor_copy(net.OT[:, 4 + h, 0:LAT], net.ps[4 + h][:, 0:LAT])


def times_stage(net, name, pairs):
    with Stage(net, name) as st:
        @st.vector
        def _(dve):
            for a, b in pairs:
                net.nc.vector.tensor_tensor(a, a, b, ALU.mult)


class SecondMemory:

    def __init__(self, net):
        sc = net.SC
        self.spectrum_in = sc[:, 0:1024].rearrange("p (a t n m) -> p a t n m", a=2, t=2, n=2)
        self.spectrum = sc[:, 1024:1536].rearrange("p (t m) -> p t m", m=LAT)
        self.vtok = sc[:, 1536:1792].rearrange("p (a m) -> p a m", a=2)
        self.mem_vtok = sc[:, 1792:2304].rearrange("p (a m) -> p a m", a=2)
        self.prob = sc[:, 2304:3328].rearrange("p (b q k) -> p b q k", b=2, q=2)
        self.prob_t = sc[:, 3328:4352].rearrange("p (b m) -> p b m", b=2)
        self.stat = sc[:, 4352:4352 + 12 * 8].rearrange("p (h n) -> p h n", n=8)
        self.part = sc[:, 4500:5012].rearrange("p (b m) -> p b m", m=LAT)
        self.angle, self.turn = sc[:, 5100:5356], sc[:, 5356:5612]
        self.sin, self.cos = sc[:, 6300:6556], sc[:, 6556:6812]
        self.memory, self.memory_normed = net.HT[:, :, LAT:TOK], net.OT[:, :, LAT:TOK]
        self.k_swapped = net.PT[:, 14, 0:LAT]


def second_load_stage(net):
    nc, mem = net.nc, SecondMemory(net)
    rows = net.PT[:, 24:28, :].rearrange("p t m -> p (t m)").rearrange("p (a d) -> p a d", a=2)
    where = mem.turn.bitcast(I32)
    with Stage(net, "second_load") as st:
        const_in, memory_in, where_in, turned = (st.sem("const_in"), st.sem("memory_in"), st.sem("where_in"),
                                                 st.sem("turned"))
        own, reduced, sin_ready = st.sem("dve_own"), st.sem("reduced"), st.sem("sin_ready")

        @st.sync
        def _(sp):
            sp.dma_start(where, net.ins["positions_2"][0].partition_broadcast(P)).then_inc(where_in, 16)
            sp.dma_start(net.CONST[:, C_OVER:C_OVER + N_CONST2], net.ins["const_2"]).then_inc(const_in, 16)
            sp.dma_start(rows, net.ins["mem_2"][0].rearrange("(a p) d -> p a d", p=P)).then_inc(memory_in, 16)

        @st.tensor
        def _(pe):
            pe.wait_ge(memory_in, 16)
            for f in range(KT):
                for a in range(2):
                    last = nc.tensor.transpose(net.ps[f][:, P * a:P * a + P], rows[:, a, P * f:P * f + P],
                                               net.const(C_IDENT))
                last.then_inc(turned, 1)

        @st.scalar
        def _(act):
            net.log_exp_loaded = False
            for f in range(KT):
                act.wait_ge(turned, f + 1)
                act.activation(mem.memory[:, f, :], net.ps[f][:, 0:LAT], ACT.Copy)
            act.wait_ge(reduced, 2)
            act.activation(mem.sin, mem.angle, ACT.Sin)
            act.activation(mem.cos, mem.angle, ACT.Sin, scale=0.5).then_inc(sin_ready, 1)

        @st.vector
        def _(dve):
            link = Chain(dve, own)
            two_pi = 2.0 * np.pi
            high = float(np.float32(6.28125))
            middle = float(np.float32(np.float64(two_pi - high)))
            low = float(np.float32(two_pi - high - middle))
            rounder = 1.5 * 2.0 ** 23
            dve.wait_ge(where_in, 16)
            dve.wait_ge(const_in, 16)
            link(nc.vector.tensor_copy(mem.angle, where))
            link(nc.vector.tensor_scalar(mem.angle, mem.angle, net.CONST[:, C_INVF:C_INVF + 1], None, ALU.mult))
            link(nc.vector.tensor_scalar(mem.turn, mem.angle, 1.0 / two_pi, rounder, ALU.mult, ALU.add))
            link(nc.vector.tensor_scalar(mem.turn, mem.turn, -rounder, None, ALU.add))
            for part in (high, middle, low):
                link(nc.vector.scalar_tensor_tensor(mem.angle, mem.turn, -part, mem.angle, ALU.mult, ALU.add))
            nc.vector.tensor_scalar(mem.angle, mem.angle, 3.1415925, -3.1415925, ALU.min, ALU.max).then_inc(reduced, 2)
            dve.wait_ge(sin_ready, 1)
            link(nc.vector.tensor_tensor(mem.cos, mem.cos, mem.cos, ALU.mult))
            nc.vector.tensor_scalar(mem.cos, mem.cos, -2.0, 1.0, ALU.mult, ALU.add)


def second_prepare_stage(net, layer):
    nc, mem = net.nc, SecondMemory(net)
    with Stage(net, f"second_prepare{layer}") as st:
        rotated, added, turned, own = st.sem("rotated"), st.sem("added"), st.sem("turned"), st.sem("dve_own")

        @st.tensor
        def _(pe):
            for n in range(5):
                if n == 4:
                    pe.wait_ge(added, 1)
                nc.tensor.matmul(net.ps[n % 4][:, 0:LAT], net.const(C_ROTB), net.PT[:, 2 + n, 0:LAT],
                                 start=True, stop=True).then_inc(rotated, 1)
            for a in range(2):
                for n, t in enumerate((7, 12, 13)):
                    last = nc.tensor.transpose(net.ps[4 + a][:, P * n:P * n + P], net.PT[:, t, P * a:P * a + P],
                                               net.const(C_IDENT))
                last.then_inc(turned, 1)

        @st.scalar
        def _(act):
            for a in range(2):
                act.wait_ge(turned, a + 1)
                act.activation(mem.vtok[:, a, :], net.ps[4 + a][:, 0:P], ACT.Copy)
                act.activation(mem.mem_vtok[:, a, :], net.ps[4 + a][:, P:3 * P], ACT.Copy)

        @st.vector
        def _(dve):
            link = Chain(dve, own)
            for n in range(5):
                x = net.PT[:, 2 + n, 0:LAT]
                dve.wait_ge(rotated, n + 1)
                nc.vector.tensor_tensor(mem.part[:, n % 2], net.ps[n % 4][:, 0:LAT], mem.sin, ALU.mult).then_inc(added, 1)
                link(nc.vector.tensor_tensor(x, x, mem.cos, ALU.mult))
                dve.wait_ge(added, n + 1)
                link(nc.vector.tensor_tensor(x, x, mem.part[:, n % 2], ALU.add))
            keys = net.PT[:, 6, 0:LAT]
            nc.vector.tensor_copy(mem.k_swapped[64:128], keys[0:64])
            nc.vector.tensor_copy(mem.k_swapped[0:64], keys[64:128])


def fourier_stage(net, layer):
    nc, mem = net.nc, SecondMemory(net)
    with Stage(net, f"fourier{layer}") as st:
        by_channel, by_channel_copied, by_token, by_token_copied, mixed = (
            st.sem("by_channel"), st.sem("by_channel_copied"), st.sem("by_token"), st.sem("by_token_copied"), st.sem("mixed"))

        @st.tensor
        def _(pe):
            for a in range(2):
                for t in range(2):
                    last = nc.tensor.matmul(net.ps[a][:, 256 * t:256 * t + 256], net.PT[:, t, P * a:P * a + P],
                                            net.const(C_DFTC, 256), start=True, stop=True)
                last.then_inc(by_channel, 1)
            pe.wait_ge(by_channel_copied, 2)
            for t in range(2):
                for n in range(2):
                    for a in range(2):
                        last = nc.tensor.matmul(net.ps[2 + t][:, 0:LAT], mem.spectrum_in[:, a, t, n, :],
                                                net.const(C_DFTS + (2 * n + a) * LAT, LAT),
                                                start=(n == 0 and a == 0), stop=(n == 1 and a == 1))
                last.then_inc(by_token, 1)
            for t in range(2):
                pe.wait_ge(by_token_copied, t + 1)
                nc.tensor.matmul(net.ps[4 + t][:, 0:LAT], net.WF[:, layer, t, :], mem.spectrum[:, t, :], start=True,
                                 stop=True).then_inc(mixed, 1)

        @st.scalar
        def _(act):
            for a in range(2):
                act.wait_ge(by_channel, a + 1)
                act.activation(mem.spectrum_in[:, a].rearrange("p t n m -> p (t n m)"), net.ps[a][:, :],
                               ACT.Copy).then_inc(by_channel_copied, 1)
            for t in range(2):
                act.wait_ge(by_token, t + 1)
                act.activation(mem.spectrum[:, t, :], net.ps[2 + t][:, 0:LAT], ACT.Copy).then_inc(by_token_copied, 1)
            for t in range(2):
                act.wait_ge(mixed, t + 1)
                act.activation(net.OT[:, t, 0:LAT], net.ps[4 + t][:, 0:LAT], ACT.Copy)


def second_attention_stage(net, layer):
    nc, mem = net.nc, SecondMemory(net)
    scale = 64 ** -0.5
    window = net.const(C_WIN, 2 * LAT)
    heads = []
    for h in range(8):
        rows, kv = slice(64 * (h % 2), 64 * (h % 2) + 64), h // 4
        keys = net.PT[rows, 6, 0:LAT] if kv == h % 2 else mem.k_swapped[rows]
        heads.append((net.PT[rows, 2 + h // 2, 0:LAT], keys, mem.vtok[:, :, 64 * kv:64 * kv + 64],
                      net.SINKROW[:, 8 * layer + h:8 * layer + h + 1]))
    for h in range(4):
        rows = slice(64 * (h % 2), 64 * (h % 2) + 64)
        heads.append((net.PT[rows, 8 + h // 2, 0:LAT], net.PT[rows, 10 + h // 2, 0:LAT],
                      mem.mem_vtok[:, :, 64 * h:64 * h + 64], None))
    N = len(heads)
    with Stage(net, f"attention{layer}") as st:
        scored, score_used, max_ready, exp_ready = (st.sem("scored"), st.sem("score_used"), st.sem("max_ready"),
                                                    st.sem("exp_ready"))
        prob_ready, turned, turned_copied, out_ready = (st.sem("prob_ready"), st.sem("turned"), st.sem("turned_copied"),
                                                        st.sem("out_ready"))
        out_taken, own = st.sem("out_taken"), st.sem("dve_own")

        @st.tensor
        def _(pe):
            def score(u):
                q, k, _, _ = heads[u]
                if u >= 2:
                    pe.wait_ge(score_used, u - 1)
                for t in range(2):
                    last = nc.tensor.matmul(net.ps[u % 2][:, LAT * t:LAT * t + LAT], q[:, P * t:P * t + P], k,
                                            start=True, stop=True)
                last.then_inc(scored, 1)

            def weigh(u):
                v = heads[u][2]
                pe.wait_ge(turned_copied, u + 1)
                if u % 2 == 0 and u >= 4:
                    pe.wait_ge(out_taken, u // 2 - 1)
                rows = slice(64 * (u % 2), 64 * (u % 2) + 64)
                for kt in range(2):
                    last = nc.tensor.matmul(net.ps[4 + (u // 2) % 2][rows, 0:LAT], v[:, kt, :],
                                            mem.prob_t[:, u % 2, LAT * kt:LAT * kt + LAT], start=(kt == 0), stop=(kt == 1))
                last.then_inc(out_ready, 1)

            score(0)
            score(1)
            for u in range(N):
                if u + 2 < N:
                    score(u + 2)
                pe.wait_ge(prob_ready, u + 1)
                if u >= 2:
                    pe.wait_ge(turned_copied, u - 1)
                for kt in range(2):
                    for t in range(2):
                        last = nc.tensor.transpose(net.ps[2 + u % 2][:, LAT * kt + P * t:LAT * kt + P * t + P],
                                                   mem.prob[:, u % 2, t, P * kt:P * kt + P], net.const(C_IDENT))
                last.then_inc(turned, 1)
                if u:
                    weigh(u - 1)
            weigh(N - 1)

        @st.scalar
        def _(act):
            def exps(u):
                act.wait_ge(max_ready, u + 1)
                for t in range(2):
                    act.activation(mem.prob[:, u % 2, t, :], mem.prob[:, u % 2, t, :], ACT.Exp,
                                   bias=mem.stat[:, u, t:t + 1], accum_out=mem.stat[:, u, 2 + t:3 + t]).then_inc(exp_ready, 1)
                sink = heads[u][3]
                if sink is not None:
                    act.activation(mem.stat[:, u, 4:6], mem.stat[:, u, 0:2], ACT.Exp, bias=sink).then_inc(exp_ready, 1)

            exps(0)
            for u in range(N):
                if u + 1 < N:
                    exps(u + 1)
                act.wait_ge(turned, u + 1)
                if u >= 2:
                    act.wait_ge(out_ready, u - 1)
                act.activation(mem.prob_t[:, u % 2, :], net.ps[2 + u % 2][:, :], ACT.Copy).then_inc(turned_copied, 1)

        @st.vector
        def _(dve):
            link = Chain(dve, own)
            exps_before = [sum(3 if x[3] is not None else 2 for x in heads[:u]) for u in range(N + 1)]

            def maxima(u):
                sink, most = heads[u][3], mem.stat[:, u, 0:2]
                dve.wait_ge(scored, u + 1)
                if u >= 2:
                    dve.wait_ge(turned, u - 1)
                both = mem.prob[:, u % 2].rearrange("p q k -> p (q k)")
                if sink is not None:
                    step = nc.vector.scalar_tensor_tensor(both, net.ps[u % 2][:, :], scale, window, ALU.mult, ALU.add)
                else:
                    step = nc.vector.tensor_scalar(both, net.ps[u % 2][:, :], scale, None, ALU.mult)
                step.then_inc(score_used, 1)
                dve.wait_ge(score_used, u + 1)
                link(nc.vector.reduce_max(most, mem.prob[:, u % 2], AX_X))
                if sink is not None:
                    nc.vector.tensor_scalar(most, most, sink, -1.0, ALU.max, ALU.mult).then_inc(max_ready, 1)
                else:
                    nc.vector.tensor_scalar(most, most, -1.0, None, ALU.mult).then_inc(max_ready, 1)

            maxima(0)
            for u in range(N):
                if u + 1 < N:
                    maxima(u + 1)
                dve.wait_ge(exp_ready, exps_before[u + 1])
                total = mem.stat[:, u, 2:4]
                if heads[u][3] is not None:
                    link(nc.vector.tensor_tensor(total, total, mem.stat[:, u, 4:6], ALU.add))
                link(nc.vector.reciprocal(total, total))
                for t in range(2):
                    last = nc.vector.tensor_scalar(mem.prob[:, u % 2, t, :], mem.prob[:, u % 2, t, :],
                                                   mem.stat[:, u, 2 + t:3 + t], None, ALU.mult)
                last.then_inc(prob_ready, 1)
                if u % 2 == 0 and u >= 2:
                    dve.wait_ge(out_ready, u)
                    pair = u // 2 - 1
                    nc.vector.tensor_copy(net.OT[:, 2 + pair, 0:LAT], net.ps[4 + pair % 2][:, 0:LAT]).then_inc(out_taken, 1)
            dve.wait_ge(out_ready, N)
            nc.vector.tensor_copy(net.OT[:, 7, 0:LAT], net.ps[5][:, 0:LAT])


def swiglu_weights(w):
    gate, up = (w[:, o:o + FF].rearrange("(t k) (n m) -> n k t m", k=P, m=SW) for o in (0, FF))
    pairs = FF // SW
    return Weights(pairs // 2, 2 * (pairs % 2), lambda i, s: (up if s % 2 else gate)[2 * i + s // 2])


def swiglu_stage(net, name, w, x, hidden, following):
    nc = net.nc
    with Stage(net, name) as st:
        sems = Split(st)
        gate_free, up_free, high = ([st.sem(f"{what}{m}") for m in range(2)]
                                           for what in ("gate_free", "up_free", "hidden_high"))

        @st.sync
        def _(sp):
            feed(net, sp, w, lambda i, s: (sems.used[1], SLOTS * i + s + 1), following)

        @st.tensor
        def _(pe):
            def turn(i, slots):
                for s in slots:
                    first = is_first(i, s)
                    for m in range(2):
                        pe.wait_ge((up_free if s % 2 else gate_free)[m], 2 * i + s // 2 + 1)
                        pe.wait_ge(sems.split_ready[m], SLOTS * i + s + 1)
                        for kt in range(KT):
                            if first and m == 0:
                                pe.wait_ge(sems.operand_split, kt + 1)
                            last = three_passes(net, net.ps[2 * s + m], s, m, kt, x, kt, LAT, kt == 0, kt == KT - 1)
                        last.then_inc(sems.used[m], 1)

            turns(pe, w, turn, peel=True)

        @st.scalar
        def _(act):
            net.log_exp_loaded = False
            for m in range(2):
                act.sem_inc(gate_free[m], 2)

            def take(i, s, m):
                if s % 2 == 0:
                    act.wait_ge(sems.used[m], SLOTS * i + s + 1)
                    act.activation(hidden.whole[:, 4 * i + s + m, :], net.ps[2 * s + m][:, 0:LAT],
                                   ACT.Silu).then_inc(gate_free[m], 1)

            high_on_act(net, act, w, sems, x, take)

        @st.vector
        def _(dve):
            for m in range(2):
                dve.sem_inc(up_free[m], 2)

            def take(i, s, m):
                if s % 2 == 0:
                    return
                low, top, whole = (v[:, 4 * i + s - 1 + m, :] for v in (hidden.low, hidden.high, hidden.whole))
                done = 2 * i + s // 2 + 1
                dve.wait_ge(gate_free[m], 2 + done)
                dve.wait_ge(sems.used[m], SLOTS * i + s + 1)
                nc.vector.tensor_tensor(whole, whole, net.ps[2 * s + m][:, 0:LAT], ALU.mult).then_inc(up_free[m], 1)
                dve.wait_ge(up_free[m], 2 + done)
                nc.vector.tensor_scalar(top, whole, 1.0, None, ALU.mult).then_inc(high[m], 1)
                dve.wait_ge(high[m], done)
                nc.vector.tensor_tensor(low, whole, top.bitcast(F32), ALU.subtract)

            low_on_dve(net, dve, w, sems, x, take)
        net.spent(w)


def store_stage(net):
    nc = net.nc
    rows = net.PT[:, 0:4, :].rearrange("p t m -> p (t m)").rearrange("p (a d) -> p a d", a=2)
    with Stage(net, "store") as st:
        turned, copied, stored = st.sem("turned"), st.sem("copied"), st.sem("stored")

        @st.tensor
        def _(pe):
            for a in range(2):
                for f in range(KT):
                    last = nc.tensor.transpose(net.ps[2 * a + f // 4][:, P * (f % 4):P * (f % 4) + P],
                                               net.XT[:, f, P * a:P * a + P], net.const(C_IDENT))
                    if f % 4 == 3:
                        last.then_inc(turned, 1)

        @st.vector
        def _(dve):
            for n in range(4):
                dve.wait_ge(turned, n + 1)
                nc.vector.tensor_copy(rows[:, n // 2, 512 * (n % 2):512 * (n % 2) + 512], net.ps[n][:, :]).then_inc(copied, 1)

        @st.sync
        def _(sp):
            for a in range(2):
                sp.wait_ge(copied, 2 * (a + 1))
                sp.dma_start(net.out[0, P * a:P * a + P, :], rows[:, a, :]).then_inc(stored, 16)
            sp.wait_ge(stored, 32)


def program(nc, ins, out):
    with ExitStack() as ctx:
        net = Net(nc, ctx, ins, out)
        both, lat = (lambda i, s: TOK), (lambda i, s: LAT)
        mod = [columns(ins[f"l{n}_mod_w"], 0, 6 * D) for n in range(2)]
        w_in0 = columns(ins["l0_w_in"], 0, 3328)
        w_in1, in1_widths = odd_projection(ins["l1_w_in"])
        w_out = [columns(ins[f"l{n}_w_out"], 0, D) for n in range(2)]
        half = HID // 2
        w_up0 = [columns(ins["l0_mlp_w1"], half * n, half) for n in range(2)]
        w_down0 = [deep(ins["l0_mlp_w2"][half * n:half * n + half, :], (8, 8)) for n in range(2)]
        w_up1, w_down1 = columns(ins["l1_mlp_w1"], 0, HID), deep(ins["l1_mlp_w2"], (8, 8, 8, 8))

        w_in2 = [joined(columns(ins["w_in_2"][n], 0, 1280), columns(ins["w_mem_kv_2"][n], 0, 512)) for n in range(2)]
        w_out2 = [columns(ins["w_out_2"][n], 0, D) for n in range(2)]
        w_ffn_in = [swiglu_weights(ins["w_ffn_in_2"][n]) for n in range(2)]
        w_ffn_out = [deep(ins["w_ffn_out_2"][n], (6, 6, 5, 5)) for n in range(2)]

        HT, PT, OT = net.HT[:, :, :], net.PT[:, :, :], net.OT[:, :, :]
        lats = slice(0, LAT)
        HR, PR, OR = net.HR[:, :, :], net.PR[:, :, :], net.OR[:, :, :]
        halves = Operand(PR[:, 0:16, :], PR[:, 16:32, :], PT[:, 16:32, :])
        hidden = Operand(PR[:, :, lats], PR[:, :, LAT:TOK], PT[:, :, LAT:TOK])
        h_lat = Operand(OR[:, :, lats], HR[:, :, lats], HT[:, :, lats])
        o_lat = Operand(HR[:, :, lats], OR[:, :, lats], OT[:, :, lats])
        of_memory = Operand(PR[:, 16:24, lats], OR[:, :, LAT:TOK], OT[:, :, LAT:TOK])
        mlp_gated = lambda n: lambda tile, bank: add_gated(net, tile, bank, 40, n)

        load_stage(net, mod[0])
        modulation_stage(net, 0, mod[0], w_in0)
        ada_stage(net, 0, 0, TOK)
        project_stage(net, "in0", w_in0, Operand(OR, HR, HT), both, net.PT, None)
        diff_prepare_stage(net)
        diff_attention_stage(net)
        heads = [net.OT[:, h, :] for h in range(4)]
        group_norm_stage(net, "diff_norm", [([o], [o], [net.DER[:, 32:33]], [net.PT[:, h, :]])
                                            for h, o in enumerate(heads)], TOK, 1e-5)
        rwkv_prepare_stage(net)
        for d in range(2):
            rwkv_decay_stage(net, d)
            rwkv_chunks_stage(net, d)
        rwkv_finish_stage(net)
        first_fetch_stage(net, w_out[0])
        mixed_out_stage(net, "out0", w_out[0], Operand(HR, OR, OT), TOK, w_up0[0])
        ada_stage(net, 0, 1, TOK)
        for n, following in enumerate((w_up0[1], mod[1])):
            x = Operand(OR, HR, HT if n == 0 else None)
            relu_squared_stage(net, f"up0_{n}", w_up0[n], x, TOK, halves, w_down0[n])
            deep_stage(net, f"down0_{n}", w_down0[n], halves, TOK, mlp_gated(TOK), following)

        modulation_stage(net, 1, mod[1], w_in1)
        ada_stage(net, 1, 0, TOK)
        project_stage(net, "in1", w_in1, Operand(OR, PR[:, 24:32, :], HT), in1_widths, net.PT, w_out[1], straight=True)
        ssd_inputs_stage(net)
        ssd_scan_stage(net)
        ssd_gate_stage(net)
        group_norm_stage(net, "ssd_norm", [([net.OT[:, 2 * g + t, 0:LAT] for t in range(2)],) * 2 +
                                           ([net.par("l1_ssm_norm", 2 * g + t) for t in range(2)],
                                            [net.PT[:, 2 * g + t, 0:LAT] for t in range(2)]) for g in range(2)], LAT, EPS)
        gla_gates_stage(net)
        gla_scan_stage(net)
        group_norm_stage(net, "gla_norm", [([net.OT[:, 4 + h, 0:LAT]],) * 2 + ([net.par("l1_gla_norm")],
                                            [net.PT[:, h, 0:LAT]]) for h in range(4)], LAT, EPS)
        times_stage(net, "gla_gate", [(net.OT[:, 4 + h, 0:LAT], net.PT[:, 20 + h, 0:LAT]) for h in range(4)])
        mixed_out_stage(net, "out1", w_out[1], o_lat, LAT, w_up1)
        ada_stage(net, 1, 1, LAT)
        relu_squared_stage(net, "up1", w_up1, h_lat, LAT, hidden, w_down1)
        deep_stage(net, "down1", w_down1, hidden, LAT, mlp_gated(LAT), w_in2[0])
        x = [net.XT[:, t, 0:LAT] for t in range(KT)]
        h = [net.HT[:, t, 0:LAT] for t in range(KT)]
        scratch = [net.PT[:, t, 0:LAT] for t in range(24, 32)]
        gains = lambda name, layer: [net.par(name, KT * layer + t) for t in range(KT)]
        group_norm_stage(net, "final_norm", [(x, x, gains("final_norm", 0), scratch)], LAT, EPS)

        second_load_stage(net)
        mem = SecondMemory(net)
        scratch_2 = [net.PT[:, t, LAT:TOK] for t in range(24, 32)]
        raw, normed = ([v[:, t, :] for t in range(KT)] for v in (mem.memory, mem.memory_normed))
        memory = lambda n: (raw, normed, gains("g_mem_2", n), [net.PT[:, t, 0:LAT] for t in range(16, 24)])
        group_norm_stage(net, "pre_mix0", [(x, h, gains("g_pre_mix_2", 0), scratch), memory(0)], LAT, EPS)
        for n in range(2):
            project_stage(net, f"second_in{n}", w_in2[n], h_lat, lat, PT, w_out2[n], side=of_memory, side_from=1)
            second_prepare_stage(net, n)
            fourier_stage(net, n)
            second_attention_stage(net, n)
            o = [net.OT[:, t, 0:LAT] for t in range(KT)]
            gain = gains("g_grp_2", n)
            group_norm_stage(net, f"mix_norm{n}", [(o[a:b], o[a:b], gain[a:b], scratch[a:b])
                                                   for a, b in ((0, 2), (2, 6), (6, 8))], LAT, EPS)
            project_stage(net, f"second_out{n}", w_out2[n], o_lat, lat, net.PT, w_ffn_in[n])
            y = [net.PT[:, t, 0:LAT] for t in range(KT)]
            residual_norm_stage(net, f"post_mix{n}", (y, gains("g_post_mix_2", n)), x, (h, gains("g_pre_ffn_2", n)),
                                (scratch, scratch_2))
            swiglu_stage(net, f"ffn_in{n}", w_ffn_in[n], h_lat, hidden, w_ffn_out[n])
            deep_stage(net, f"ffn_out{n}", w_ffn_out[n], hidden, LAT,
                       lambda tile, bank: nc.vector.tensor_copy(net.OT[:, tile, lats], bank[:, lats]),
                       w_in2[1] if n == 0 else None)
            if n == 0:
                residual_norm_stage(net, "post_ffn0", (o, gains("g_post_ffn_2", 0)), x, (h, gains("g_pre_mix_2", 1)),
                                    (scratch, scratch_2), memory(1))
            else:
                group_norm_stage(net, "post_ffn1", [(o, o, gains("g_post_ffn_2", 1), scratch)], LAT, EPS, adds=x)
        store_stage(net)




def kernel(**inputs):
    import concourse.bacc as bacc
    from concourse.bass_utils import run_bass_kernel_spmd

    nc = bacc.Bacc("TRN2", target_bir_lowering=False, num_devices=1)
    arrays = {name: np.ascontiguousarray(a) for name, a in inputs.items()}
    arrays |= {"const_1": first_constants(), "const_2": second_constants()}
    ins = {name: nc.dram_tensor(f"in_{name}", a.shape, mybir.dt.from_np(a.dtype), kind="ExternalInput").ap()
           for name, a in arrays.items()}
    out = nc.dram_tensor("out", (1, LAT, D), F32, kind="ExternalOutput").ap()
    program(nc, ins, out)
    result = run_bass_kernel_spmd(nc, [{f"in_{name}": a for name, a in arrays.items()}], core_ids=[0])
    return result.results[0]["out"]
```
